# Optimizing a Trainium2 kernel written in Bass

```python
import jax, jax.numpy as jnp
from jax import lax
import numpy as np

D_MODEL = 1024
BATCH = 1
SEQ = 512
DEPTH = 2

D_MIX = D_MODEL
CONV_W = D_MIX // 4
CONV_K = 31
POOL_W = D_MIX // 4
POOL_WINDOWS = (2, 4, 8, 16)
POOL_G = 4
POOL_GW = POOL_W // POOL_G
HEAD_DIM = 64
ATTN_W = D_MIX // 2
N_HEADS = ATTN_W // HEAD_DIM
IDX_HEADS = 4
IDX_DIM = 64
TOPK_MAX = 256
Q_BLOCK = 128
ROPE_THETA = 10000.0
PLE_DIM = 256
EPS = 1e-6
SPLITS = (CONV_W, CONV_W, CONV_W,
          POOL_W, POOL_W,
          ATTN_W, ATTN_W, ATTN_W, ATTN_W,
          IDX_HEADS * IDX_DIM, IDX_DIM, IDX_HEADS)
D_IN = 3 * CONV_W + 2 * POOL_W + 4 * ATTN_W + IDX_HEADS * IDX_DIM + IDX_DIM + IDX_HEADS


def rmsnorm(x, g):
    xf = x.astype(jnp.float32)
    y = xf * lax.rsqrt(jnp.mean(xf * xf, axis=-1, keepdims=True) + EPS)
    return (y * g.astype(jnp.float32)).astype(x.dtype)

def layernorm(x, g, b):
    xf = x.astype(jnp.float32)
    mu = jnp.mean(xf, axis=-1, keepdims=True)
    xc = xf - mu
    y = xc * lax.rsqrt(jnp.mean(xc * xc, axis=-1, keepdims=True) + EPS)
    return (y * g.astype(jnp.float32) + b.astype(jnp.float32)).astype(x.dtype)

def rope(x, pos):
    half = x.shape[-1] // 2
    inv = ROPE_THETA ** (-jnp.arange(half, dtype=jnp.float32) / half)
    ang = pos.astype(jnp.float32)[:, None] * inv[None, :]
    cos = jnp.cos(ang)[None, :, None, :]
    sin = jnp.sin(ang)[None, :, None, :]
    xf = x.astype(jnp.float32)
    x1, x2 = xf[..., :half], xf[..., half:]
    return jnp.concatenate([x1 * cos - x2 * sin, x2 * cos + x1 * sin], axis=-1).astype(x.dtype)

def conv_module(val, glu, dw_w, dw_b, ln_g, ln_b, pw_w, pw_b):
    u = val * jax.nn.sigmoid(glu)
    u = lax.conv_general_dilated(u, dw_w[:, None, :], window_strides=(1,),
                                 padding=[(CONV_K - 1, 0)],
                                 dimension_numbers=('NWC', 'WIO', 'NWC'),
                                 feature_group_count=CONV_W) + dw_b
    u = jax.nn.silu(layernorm(u, ln_g, ln_b))
    return u @ pw_w + pw_b

def pool_mixer(u, w, b, scale):
    B, S, _ = u.shape
    ug = u.reshape(B, S, POOL_G, POOL_GW)
    t = jnp.arange(S)
    outs = []
    for g, win in enumerate(POOL_WINDOWS):
        xg = ug[:, :, g].astype(jnp.float32)
        cs = jnp.cumsum(xg, axis=1)
        lag = jnp.pad(cs, ((0, 0), (win, 0), (0, 0)))[:, :S]
        cnt = jnp.minimum(t + 1, win).astype(jnp.float32)[None, :, None]
        outs.append((cs - lag) / cnt - xg)
    d = jnp.stack(outs, axis=2).astype(u.dtype)
    y = jnp.einsum('bsgc,gcd->bsgd', d, w).reshape(B, S, POOL_W) + b
    return y * scale

def sparse_attention(q, k, v, qi, ki, wi):
    B, S, H, Dh = q.shape
    L = k.shape[1]
    topk = min(TOPK_MAX, L // 4)
    nb = S // Q_BLOCK
    key_pos = jnp.arange(L)
    kf = ki.astype(jnp.float32)

    def to_blocks(a):
        return a.reshape((B, nb, Q_BLOCK) + a.shape[2:]).swapaxes(0, 1)

    def gather(a, i):
        return a[i]

    def block(args):
        qb, qib, wib, start = args
        qpos = start + jnp.arange(Q_BLOCK)
        causal = key_pos[None, :] <= qpos[:, None]
        s = jnp.einsum('bqhd,bsd->bqhs', qib.astype(jnp.float32), kf) * (IDX_DIM ** -0.5)
        score = jnp.einsum('bqh,bqhs->bqs', wib.astype(jnp.float32), jax.nn.relu(s))
        score = jnp.where(causal[None], score, -jnp.inf)
        _, idx = lax.top_k(score, topk)
        kg = jax.vmap(gather)(k, idx)
        vg = jax.vmap(gather)(v, idx)
        logits = jnp.einsum('bqhd,bqkhd->bhqk', qb.astype(jnp.float32),
                            kg.astype(jnp.float32)) * (HEAD_DIM ** -0.5)
        valid = idx <= qpos[None, :, None]
        logits = jnp.where(valid[:, None], logits, -jnp.inf)
        pr = jax.nn.softmax(logits, axis=-1)
        o = jnp.einsum('bhqk,bqkhd->bqhd', pr, vg.astype(jnp.float32))
        return o.astype(q.dtype)

    starts = jnp.arange(nb) * Q_BLOCK
    o = lax.map(block, (to_blocks(q), to_blocks(qi), to_blocks(wi), starts))
    return o.swapaxes(0, 1).reshape(B, S, H * Dh)

def first_inputs(seed: int = 0) -> dict:
    key = jax.random.key(seed)
    ks = jax.random.split(key, 20)
    f32 = jnp.float32

    def nrm(k, shape, scale):
        return jax.random.normal(k, shape, f32) * scale

    return {
        'x': nrm(ks[0], (BATCH, SEQ, D_MODEL), 1.0),
        'p': nrm(ks[1], (DEPTH, BATCH, SEQ, PLE_DIM), 1.0),
        'norm_g': 1.0 + nrm(ks[2], (DEPTH, D_MODEL), 0.1),
        'w_in': nrm(ks[3], (DEPTH, D_MODEL, D_IN), D_MODEL ** -0.5),
        'b_in': nrm(ks[4], (DEPTH, D_IN), 0.02),
        'conv_dw_w': nrm(ks[5], (DEPTH, CONV_K, CONV_W), CONV_K ** -0.5),
        'conv_dw_b': nrm(ks[6], (DEPTH, CONV_W), 0.02),
        'conv_ln_g': 1.0 + nrm(ks[7], (DEPTH, CONV_W), 0.1),
        'conv_ln_b': nrm(ks[8], (DEPTH, CONV_W), 0.02),
        'conv_pw_w': nrm(ks[9], (DEPTH, CONV_W, CONV_W), CONV_W ** -0.5),
        'conv_pw_b': nrm(ks[10], (DEPTH, CONV_W), 0.02),
        'pool_w': nrm(ks[11], (DEPTH, POOL_G, POOL_GW, POOL_GW), POOL_GW ** -0.5),
        'pool_b': nrm(ks[12], (DEPTH, POOL_W), 0.02),
        'pool_scale': 1.0 + nrm(ks[13], (DEPTH, POOL_W), 0.1),
        'w_out': nrm(ks[14], (DEPTH, D_MIX, D_MODEL), D_MIX ** -0.5),
        'ple_w': nrm(ks[15], (DEPTH, PLE_DIM, D_MODEL), PLE_DIM ** -0.5),
        'ple_gate_w': nrm(ks[16], (DEPTH, D_MODEL, D_MODEL), D_MODEL ** -0.5),
        'final_norm_g': 1.0 + nrm(ks[17], (D_MODEL,), 0.1),
    }

def first_block(x, p, norm_g, w_in, b_in, conv_dw_w, conv_dw_b, conv_ln_g, conv_ln_b,
              conv_pw_w, conv_pw_b, pool_w, pool_b, pool_scale, w_out, ple_w,
              ple_gate_w, final_norm_g):
    B, S, _ = x.shape
    pos = jnp.arange(S)
    cut = [int(c) for c in np.cumsum(SPLITS)[:-1]]
    h = x
    for i in range(DEPTH):
        n = rmsnorm(h, norm_g[i])
        z = n @ w_in[i] + b_in[i]
        (c_val, c_glu, c_gate, p_in, p_gate, q, k, v, a_gate,
         qi, ki, wi) = jnp.split(z, cut, axis=-1)
        ya = conv_module(c_val, c_glu, conv_dw_w[i], conv_dw_b[i], conv_ln_g[i],
                         conv_ln_b[i], conv_pw_w[i], conv_pw_b[i]) * jax.nn.silu(c_gate)
        yb = pool_mixer(p_in, pool_w[i], pool_b[i], pool_scale[i]) * jax.nn.silu(p_gate)
        q = rope(q.reshape(B, S, N_HEADS, HEAD_DIM), pos)
        k = rope(k.reshape(B, S, N_HEADS, HEAD_DIM), pos)
        v = v.reshape(B, S, N_HEADS, HEAD_DIM)
        qi = rope(qi.reshape(B, S, IDX_HEADS, IDX_DIM), pos)
        ki = rope(ki[:, :, None, :], pos)[:, :, 0, :]
        yc = sparse_attention(q, k, v, qi, ki, wi) * jax.nn.silu(a_gate)
        h = h + jnp.concatenate([ya, yb, yc], axis=-1) @ w_out[i]
        h = h + (p[i] @ ple_w[i]) * jax.nn.sigmoid(h @ ple_gate_w[i])
    return rmsnorm(h, final_norm_g)


N_META = 16
H_A = 4
QK_NOPE = 128
QK_ROPE = 64
V_DIM = 128
Q_LORA = 256
KV_LORA = 128
H_B = 8
N_B = 64
RW = H_B * N_B
DECAY_LORA = 64
AAA_LORA = 64
GATE_LORA = 128
VRES_LORA = 32
RWKV_GN_EPS = 64e-5
MIX = H_A * V_DIM + RW
MLA_COLS = Q_LORA + KV_LORA + QK_ROPE
RWKV_COLS = 3 * RW + 2 * DECAY_LORA + 2 * AAA_LORA + GATE_LORA
IN_COLS = MLA_COLS + RWKV_COLS
N_GROUPS = 4
EXPERTS_PER_GROUP = 8
N_EXPERTS = N_GROUPS * EXPERTS_PER_GROUP
TOP_K = 2
E_HID = 256
MOE_BLOCK = 128
DN_ALPHA = (2 * DEPTH) ** 0.25
DN_BETA = (8 * DEPTH) ** -0.25
LN_EPS = 1e-5
RMS_EPS = 1e-6


def _split(t, sizes):
    return jnp.split(t, np.cumsum(sizes)[:-1].tolist(), axis=-1)

def _layer_norm(x, g, b):
    xf = x.astype(jnp.float32)
    mu = jnp.mean(xf, -1, keepdims=True)
    var = jnp.mean(jnp.square(xf - mu), -1, keepdims=True)
    return ((xf - mu) * lax.rsqrt(var + LN_EPS) * g + b).astype(x.dtype)

def _rms_norm(x, g):
    xf = x.astype(jnp.float32)
    return (xf * lax.rsqrt(jnp.mean(xf * xf, -1, keepdims=True) + RMS_EPS) * g).astype(x.dtype)

def _rope(t, cos, sin):
    half = t.shape[-1] // 2
    t1, t2 = t[..., :half], t[..., half:]
    return jnp.concatenate([t1 * cos - t2 * sin, t2 * cos + t1 * sin], -1).astype(t.dtype)

def _centred_shift(p, mu_prev, mu_next):
    prev = jnp.pad(p[:, :-1], ((0, 0), (1, 0), (0, 0)))
    nxt = jnp.pad(p[:, 1:], ((0, 0), (0, 1), (0, 0)))
    return p + mu_prev * (prev - p) + mu_next * (nxt - p)

def _mla(c_q, c_kv, k_pe, cos, sin, q_norm, kv_norm, w_uq, w_ukv, out_norm):
    B, L, _ = c_q.shape
    q = (_rms_norm(c_q, q_norm) @ w_uq).reshape(B, L, H_A, QK_NOPE + QK_ROPE)
    q_nope = q[..., :QK_NOPE]
    q_pe = _rope(q[..., QK_NOPE:], cos[:, :, None, :], sin[:, :, None, :])
    kv = (_rms_norm(c_kv, kv_norm) @ w_ukv).reshape(B, L, H_A, QK_NOPE + V_DIM)
    k_nope, v = kv[..., :QK_NOPE], kv[..., QK_NOPE:]
    k_pe = _rope(k_pe, cos, sin)
    scale = (QK_NOPE + QK_ROPE) ** -0.5

    def attend(blk):
        qn, qp = blk
        s = jnp.einsum('bqhd,bkhd->bhqk', qn, k_nope) + jnp.einsum('bqhd,bkd->bhqk', qp, k_pe)
        p = jax.nn.softmax(s.astype(jnp.float32) * scale, axis=-1).astype(v.dtype)
        return jnp.einsum('bhqk,bkhd->bqhd', p, v)

    out_meta = attend((q_nope[:, :N_META], q_pe[:, :N_META]))
    n_blk = (L - N_META) // Q_BLOCK

    def to_blocks(t):
        return jnp.moveaxis(t[:, N_META:].reshape(B, n_blk, Q_BLOCK, H_A, t.shape[-1]), 1, 0)

    out_real = lax.map(attend, (to_blocks(q_nope), to_blocks(q_pe)))
    out_real = jnp.moveaxis(out_real, 0, 1).reshape(B, L - N_META, H_A, V_DIM)
    out = jnp.concatenate([out_meta, out_real], axis=1)
    out = _rms_norm(out, out_norm.reshape(H_A, V_DIM))
    return out.reshape(B, L, H_A * V_DIM)

def _wkv_scan(r, decay, k, v, kk, a, reverse):
    B = r.shape[0]

    def step(S, inp):
        r_t, w_t, k_t, v_t, kk_t, b_t = inp
        sa = jnp.einsum('bhvk,bhk->bhv', S, kk_t)
        S = S * w_t[:, :, None, :] - sa[..., None] * b_t[:, :, None, :] + v_t[..., None] * k_t[:, :, None, :]
        return S, jnp.einsum('bhvk,bhk->bhv', S, r_t)

    xs = tuple(jnp.moveaxis(t, 1, 0) for t in (r, decay, k, v, kk, kk * a))
    S0 = jnp.zeros((B, H_B, N_B, N_B), jnp.float32)
    _, ys = lax.scan(step, S0, xs, reverse=reverse)
    return jnp.moveaxis(ys, 0, 1)

def _rwkv_bidir(u, v_first, vres, w0, w2, a0, a2, g2, k_k, k_a, r_k, gn_g, gn_b):
    dt = u.dtype
    u = u.astype(jnp.float32)
    B, L, _ = u.shape
    r, k, v, wd_f, wd_b, ad_f, ad_b, gd = _split(
        u, [RW, RW, RW, DECAY_LORA, DECAY_LORA, AAA_LORA, AAA_LORA, GATE_LORA])
    if vres is None:
        v_first = v
    else:
        v0, v1, v2 = vres
        v = v + (v_first - v) * jax.nn.sigmoid(v0 + (v @ v1) @ v2)
    g = jax.nn.sigmoid(gd) @ g2

    def heads(t):
        return t.reshape(B, L, H_B, N_B)

    kk = heads(k * k_k)
    kk = kk * lax.rsqrt(jnp.sum(kk * kk, -1, keepdims=True) + 1e-12)
    rh, vh = heads(r), heads(v)

    def direction(d, wd, ad, reverse):
        wl = w0[d] + jnp.tanh(wd) @ w2[d]
        decay = jnp.exp(-jnp.exp(-jax.nn.softplus(-wl) - 0.5))
        a = jax.nn.sigmoid(a0[d] + ad @ a2[d])
        kd = heads(k * (1.0 + (a - 1.0) * k_a))
        y = _wkv_scan(rh, heads(decay), kd, vh, kk, heads(a), reverse)
        bonus = jnp.sum(rh * kd * r_k, -1, keepdims=True) * vh
        return y, bonus

    y_f, bonus_f = direction(0, wd_f, ad_f, False)
    y_b, bonus_b = direction(1, wd_b, ad_b, True)
    y = y_f + y_b
    mu = jnp.mean(y, -1, keepdims=True)
    var = jnp.mean(jnp.square(y - mu), -1, keepdims=True)
    yn = ((y - mu) * lax.rsqrt(var + RWKV_GN_EPS)).reshape(B, L, RW) * gn_g + gn_b
    out = (yn + (bonus_f + bonus_b).reshape(B, L, RW)) * g
    return out.astype(dt), v_first

def _hier_moe(h, w_group, b_group, w_expert, b_expert, w1, w3, w2):
    T, D = h.shape
    g_prob = jax.nn.softmax((h @ w_group).astype(jnp.float32) + b_group, axis=-1)
    g_top_p, g_top = lax.top_k(g_prob, 1)
    e_logits = ((h @ w_expert).astype(jnp.float32) + b_expert).reshape(T, N_GROUPS, EXPERTS_PER_GROUP)
    e_logits = jnp.take_along_axis(e_logits, g_top[:, :, None], axis=1)[:, 0]
    e_top_p, e_top = lax.top_k(jax.nn.softmax(e_logits, axis=-1), TOP_K)
    gate = (g_top_p * e_top_p).reshape(-1)
    flat_e = (g_top * EXPERTS_PER_GROUP + e_top).reshape(-1)
    flat_tok = jnp.repeat(jnp.arange(T, dtype=jnp.int32), TOP_K)
    order = jnp.argsort(flat_e)
    se = flat_e[order]
    counts = jnp.bincount(flat_e, length=N_EXPERTS)
    starts = jnp.cumsum(counts) - counts
    padded = (counts + MOE_BLOCK - 1) // MOE_BLOCK * MOE_BLOCK
    pends = jnp.cumsum(padded)
    dest = (pends - padded)[se] + jnp.arange(T * TOP_K) - starts[se]
    n_rows = (T * TOP_K + N_EXPERTS * (MOE_BLOCK - 1) + MOE_BLOCK - 1) // MOE_BLOCK * MOE_BLOCK
    n_blocks = n_rows // MOE_BLOCK
    row_tok = jnp.zeros((n_rows,), jnp.int32).at[dest].set(flat_tok[order])
    row_gate = jnp.zeros((n_rows,), jnp.float32).at[dest].set(gate[order])
    block_e = jnp.clip(jnp.searchsorted(pends, jnp.arange(n_blocks) * MOE_BLOCK, side='right'),
                       0, N_EXPERTS - 1)
    xb = h[row_tok].reshape(n_blocks, MOE_BLOCK, D)

    def expert_block(args):
        xe, e = args
        return (jax.nn.silu(xe @ w1[e]) * (xe @ w3[e])) @ w2[e]

    yb = lax.map(expert_block, (xb, block_e)).reshape(n_rows, D)
    y = jnp.zeros((T, D), jnp.float32).at[row_tok].add(yb.astype(jnp.float32) * row_gate[:, None])
    return y.astype(h.dtype)

def second_inputs(seed: int = 0) -> dict:
    key = jax.random.key(seed)
    ks = iter(jax.random.split(key, 48))

    def nrm(shape, s):
        return jax.random.normal(next(ks), shape, jnp.float32) * s

    def uni(shape, lo, hi):
        return jax.random.uniform(next(ks), shape, jnp.float32, lo, hi)

    D = D_MODEL
    return {
        'x': nrm((BATCH, SEQ, D), 1.0),
        'positions': jnp.tile(jnp.arange(SEQ, dtype=jnp.int32)[None], (BATCH, 1)),
        'meta_tokens': nrm((N_META, D), 1.0),
        'emb_ln_g': 1.0 + nrm((D,), 0.02),
        'emb_ln_b': nrm((D,), 0.02),
        'w_in': nrm((DEPTH, D, IN_COLS), D ** -0.5),
        'mla_q_norm': 1.0 + nrm((DEPTH, Q_LORA), 0.02),
        'mla_kv_norm': 1.0 + nrm((DEPTH, KV_LORA), 0.02),
        'mla_w_uq': nrm((DEPTH, Q_LORA, H_A * (QK_NOPE + QK_ROPE)), Q_LORA ** -0.5),
        'mla_w_ukv': nrm((DEPTH, KV_LORA, H_A * (QK_NOPE + V_DIM)), KV_LORA ** -0.5),
        'mla_out_norm': 1.0 + nrm((DEPTH, H_A * V_DIM), 0.02),
        'rwkv_mu_prev': uni((DEPTH, RWKV_COLS), 0.0, 0.5),
        'rwkv_mu_next': uni((DEPTH, RWKV_COLS), 0.0, 0.5),
        'rwkv_w0': uni((DEPTH, 2, RW), -4.0, 0.0),
        'rwkv_w2': nrm((DEPTH, 2, DECAY_LORA, RW), 0.1),
        'rwkv_a0': nrm((DEPTH, 2, RW), 0.3),
        'rwkv_a2': nrm((DEPTH, 2, AAA_LORA, RW), 0.1),
        'rwkv_g2': nrm((DEPTH, GATE_LORA, RW), GATE_LORA ** -0.5),
        'rwkv_k_k': 0.85 + nrm((DEPTH, RW), 0.05),
        'rwkv_k_a': 1.0 + nrm((DEPTH, RW), 0.05),
        'rwkv_r_k': nrm((DEPTH, H_B, N_B), 0.1),
        'rwkv_gn_g': 1.0 + nrm((DEPTH, RW), 0.02),
        'rwkv_gn_b': nrm((DEPTH, RW), 0.02),
        'rwkv_v0': nrm((DEPTH - 1, RW), 0.3),
        'rwkv_v1': nrm((DEPTH - 1, RW, VRES_LORA), RW ** -0.5),
        'rwkv_v2': nrm((DEPTH - 1, VRES_LORA, RW), 0.5 * VRES_LORA ** -0.5),
        'w_out': nrm((DEPTH, MIX, D), DN_BETA * MIX ** -0.5),
        'ln1_g': 1.0 + nrm((DEPTH, D), 0.02),
        'ln1_b': nrm((DEPTH, D), 0.02),
        'moe_w_group': nrm((DEPTH, D, N_GROUPS), D ** -0.5),
        'moe_b_group': nrm((DEPTH, N_GROUPS), 0.01),
        'moe_w_expert': nrm((DEPTH, D, N_EXPERTS), D ** -0.5),
        'moe_b_expert': nrm((DEPTH, N_EXPERTS), 0.01),
        'moe_w1': nrm((DEPTH, N_EXPERTS, D, E_HID), D ** -0.5),
        'moe_w3': nrm((DEPTH, N_EXPERTS, D, E_HID), D ** -0.5),
        'moe_w2': nrm((DEPTH, N_EXPERTS, E_HID, D), DN_BETA * E_HID ** -0.5),
        'ln2_g': 1.0 + nrm((DEPTH, D), 0.02),
        'ln2_b': nrm((DEPTH, D), 0.02),
    }

def second_block(x, positions, meta_tokens, emb_ln_g, emb_ln_b, w_in, mla_q_norm, mla_kv_norm,
              mla_w_uq, mla_w_ukv, mla_out_norm, rwkv_mu_prev, rwkv_mu_next, rwkv_w0, rwkv_w2,
              rwkv_a0, rwkv_a2, rwkv_g2, rwkv_k_k, rwkv_k_a, rwkv_r_k, rwkv_gn_g, rwkv_gn_b,
              rwkv_v0, rwkv_v1, rwkv_v2, w_out, ln1_g, ln1_b, moe_w_group, moe_b_group,
              moe_w_expert, moe_b_expert, moe_w1, moe_w3, moe_w2, ln2_g, ln2_b):
    B = x.shape[0]
    meta = jnp.broadcast_to(meta_tokens.astype(x.dtype)[None], (B, N_META, D_MODEL))
    h = _layer_norm(jnp.concatenate([meta, x], axis=1), emb_ln_g, emb_ln_b)
    L = h.shape[1]
    pos = jnp.concatenate([jnp.broadcast_to(jnp.arange(N_META, dtype=jnp.int32), (B, N_META)),
                           positions + N_META], axis=1)
    inv_freq = ROPE_THETA ** (-jnp.arange(0, QK_ROPE, 2, dtype=jnp.float32) / QK_ROPE)
    ang = pos.astype(jnp.float32)[..., None] * inv_freq
    cos, sin = jnp.cos(ang), jnp.sin(ang)
    v_first = None
    for li in range(DEPTH):
        proj = h @ w_in[li]
        c_q, c_kv, k_pe, rw = _split(proj, [Q_LORA, KV_LORA, QK_ROPE, RWKV_COLS])
        y_att = _mla(c_q, c_kv, k_pe, cos, sin, mla_q_norm[li], mla_kv_norm[li],
                     mla_w_uq[li], mla_w_ukv[li], mla_out_norm[li])
        u = _centred_shift(rw, rwkv_mu_prev[li], rwkv_mu_next[li])
        vres = None if li == 0 else (rwkv_v0[li - 1], rwkv_v1[li - 1], rwkv_v2[li - 1])
        y_rwkv, v_first = _rwkv_bidir(u, v_first, vres, rwkv_w0[li], rwkv_w2[li], rwkv_a0[li],
                                      rwkv_a2[li], rwkv_g2[li], rwkv_k_k[li], rwkv_k_a[li],
                                      rwkv_r_k[li], rwkv_gn_g[li], rwkv_gn_b[li])
        mixed = jnp.concatenate([y_att, y_rwkv], axis=-1) @ w_out[li]
        h = _layer_norm(DN_ALPHA * h + mixed, ln1_g[li], ln1_b[li])
        ff = _hier_moe(h.reshape(B * L, D_MODEL), moe_w_group[li], moe_b_group[li],
                       moe_w_expert[li], moe_b_expert[li], moe_w1[li], moe_w3[li],
                       moe_w2[li]).reshape(B, L, D_MODEL)
        h = _layer_norm(DN_ALPHA * h + ff, ln2_g[li], ln2_b[li])
    return h[:, N_META:]


def setup_inputs(seed=0):
    out = dict(first_inputs(seed))
    for name, value in second_inputs(seed + 1).items():
        if name != "x":
            out[name + "_2"] = value
    return out


def reference(
    x, p, norm_g, w_in, b_in, conv_dw_w, conv_dw_b, conv_ln_g, conv_ln_b, conv_pw_w, conv_pw_b,
    pool_w, pool_b, pool_scale, w_out, ple_w, ple_gate_w, final_norm_g, positions_2,
    meta_tokens_2, emb_ln_g_2, emb_ln_b_2, w_in_2, mla_q_norm_2, mla_kv_norm_2, mla_w_uq_2,
    mla_w_ukv_2, mla_out_norm_2, rwkv_mu_prev_2, rwkv_mu_next_2, rwkv_w0_2, rwkv_w2_2,
    rwkv_a0_2, rwkv_a2_2, rwkv_g2_2, rwkv_k_k_2, rwkv_k_a_2, rwkv_r_k_2, rwkv_gn_g_2,
    rwkv_gn_b_2, rwkv_v0_2, rwkv_v1_2, rwkv_v2_2, w_out_2, ln1_g_2, ln1_b_2, moe_w_group_2,
    moe_b_group_2, moe_w_expert_2, moe_b_expert_2, moe_w1_2, moe_w3_2, moe_w2_2, ln2_g_2,
    ln2_b_2,
):
    x = first_block(
        x, p, norm_g, w_in, b_in, conv_dw_w, conv_dw_b, conv_ln_g, conv_ln_b, conv_pw_w,
        conv_pw_b, pool_w, pool_b, pool_scale, w_out, ple_w, ple_gate_w, final_norm_g,
    )
    return second_block(
        x, positions_2, meta_tokens_2, emb_ln_g_2, emb_ln_b_2, w_in_2, mla_q_norm_2,
        mla_kv_norm_2, mla_w_uq_2, mla_w_ukv_2, mla_out_norm_2, rwkv_mu_prev_2, rwkv_mu_next_2,
        rwkv_w0_2, rwkv_w2_2, rwkv_a0_2, rwkv_a2_2, rwkv_g2_2, rwkv_k_k_2, rwkv_k_a_2,
        rwkv_r_k_2, rwkv_gn_g_2, rwkv_gn_b_2, rwkv_v0_2, rwkv_v1_2, rwkv_v2_2, w_out_2, ln1_g_2,
        ln1_b_2, moe_w_group_2, moe_b_group_2, moe_w_expert_2, moe_b_expert_2, moe_w1_2,
        moe_w3_2, moe_w2_2, ln2_g_2, ln2_b_2,
    )


_drawn_inputs = setup_inputs


def setup_inputs(seed=0):
    import zlib

    import numpy as np

    out = dict(_drawn_inputs(seed))
    spreads = {}
    factors = {'conv_dw_b': 4.052,
     'conv_ln_b': 8.0,
     'conv_pw_b': 4.11,
     'pool_b': 4.48,
     'mla_q_norm_2': 8.0,
     'mla_kv_norm_2': 4.697,
     'mla_out_norm_2': 6.317,
     'rwkv_w2_2': 4.129,
     'rwkv_k_k_2': 8.0,
     'rwkv_k_a_2': 4.715,
     'rwkv_gn_g_2': 8.0,
     'rwkv_gn_b_2': 8.0,
     'rwkv_v0_2': 3.174,
     'rwkv_v1_2': 2.749,
     'rwkv_v2_2': 2.78,
     'moe_b_group_2': 8.0,
     'moe_b_expert_2': 8.0}
    for name, (base, spread) in spreads.items():
        noise = np.random.default_rng([zlib.crc32(name.encode()), seed]).standard_normal(out[name].shape)
        drawn = base * np.exp(spread * noise) if base else spread * noise
        out[name] = __import__('jax').numpy.asarray(drawn.astype(out[name].dtype))
    for name, factor in factors.items():
        out[name] = (out[name] * factor).astype(out[name].dtype)
    return out
```

```python
from contextlib import ExitStack

import numpy as np

import concourse.bass as bass
from concourse import mybir

F32 = mybir.dt.float32
I32 = mybir.dt.int32
ALU = mybir.AluOpType
ACT = mybir.ActivationFunctionType
AX = mybir.AxisListType.X

P = 128
D = 1024
KT = D // P
SEQ = 512
DEPTH = 2
BIG = 1e30

CONV_K = 31
TOPK = 128
IDX_HEADS = 4
Z_TILES = 30
Z_VAL, Z_GLU, Z_CGATE, Z_PIN, Z_PGATE, Z_Q, Z_K, Z_V, Z_AGATE, Z_QI, Z_KI, Z_WI = (
    0, 2, 4, 6, 8, 10, 14, 18, 22, 26, 28, 29)
PAIRS1 = 14

N_META = 16
L = SEQ + N_META
HALF = L // 2
H_A = 4
MLA_SCALE = 192 ** -0.5
RW_TILES = 4
CH = 64
N_CH = -(-L // CH)
LP = N_CH * CH
WIDE = 2 * RW_TILES * LP
LEVELS = 6
N_EXP = 32
E_HID = 256
ALPHA = (2 * DEPTH) ** 0.25
EXP_HALF = float(np.exp(-0.5))
T_CQ, T_CKV, T_KPE, T_R, T_K, T_V, T_WD, T_AD, T_GD = 0, 2, 3, 4, 8, 12, 16, 17, 18
TOK = [(t * P, min(P, L - t * P)) for t in range(-(-L // P))]


class Sems:

    def __init__(self, nc):
        self.nc = nc
        self.old = []
        self.new = []
        self.stack = ExitStack()
        self.last = ExitStack()
        self.stage = 0

    def open(self):
        self.last.close()
        self.stage += 1
        self.old, self.new = self.new, []
        self.last, self.stack = self.stack, ExitStack()

    def take(self, name):
        s = self.stack.enter_context(self.nc.semaphore(f"{name}_{self.stage}"))
        self.new.append(s)
        return s

    def clear_old(self, pool):
        for s in self.old:
            pool.sem_clear(s)


class Chain:

    def __init__(self, eng, sem):
        self.eng, self.sem, self.n = eng, sem, 0

    def add(self, ins):
        ins.then_inc(self.sem, 1)
        self.n += 1
        return self.n

    def wait(self, n=None):
        self.eng.wait_ge(self.sem, self.n if n is None else n)

    def link(self, ins):
        self.add(ins)
        self.wait()


def in_pairs(eng, n, body):
    if n >= 2:
        with eng.Fori(0, n // 2) as i:
            body(i * 2, 0, i)
            body(i * 2 + 1, 1, i)
    if n % 2:
        body(n - 1, 0, n // 2)


def halves(ap, nh):
    return ap.rearrange("p (a n) -> p a n", a=nh)


class Env:
    pass


def sweep(nc, S):
    S.open()
    with nc.Block() as block:
        @block.gpsimd
        def _(pool):
            S.clear_old(pool)
    S.open()


def load_constants(nc, S, pairs):
    S.open()
    loaded = S.take("constants_loaded")
    with nc.Block() as block:
        @block.gpsimd
        def _(pool):
            S.clear_old(pool)

        @block.sync
        def _(sp):
            for dst, src in pairs:
                sp.dma_start(dst, src).then_inc(loaded, 16)
            sp.wait_ge(loaded, 16 * len(pairs))


def transpose_rows(nc, S, E, dst, ntiles, parts):
    S.open()
    turned = S.take("turned")
    copied = S.take("copied")
    with nc.Block() as block:
        @block.gpsimd
        def _(pool):
            S.clear_old(pool)

        @block.tensor
        def _(pe):
            for k in range(ntiles):
                if k >= 8:
                    pe.wait_ge(copied, k - 7)
                for n, (tile_ap, c0, rows_n) in enumerate(parts):
                    last = pe.transpose(E.PS[:, k % 8, c0:c0 + rows_n], tile_ap[:, k * P:(k + 1) * P],
                                        E.ident[0:rows_n, 0:rows_n])
                last.then_inc(turned, 1)

        @block.scalar
        def _(act):
            w = parts[-1][1] + parts[-1][2]
            for k in range(ntiles):
                act.wait_ge(turned, k + 1)
                act.copy(dst(k), E.PS[:, k % 8, 0:w]).then_inc(copied, 1)


def load_params(nc, S, E, rows):
    S.open()
    blank = S.take("blank")
    loaded = S.take("rows_loaded")
    turned = S.take("turned")
    with nc.Block() as block:
        @block.gpsimd
        def _(pool):
            S.clear_old(pool)

        @block.vector
        def _(dve):
            dve.memset(E.praw[:, :], 0.0).then_inc(blank, 1)

        @block.sync
        def _(sp):
            sp.wait_ge(blank, 1)
            for r, n, src, c0, w in rows:
                sp.dma_start(E.praw[r:r + n, c0:c0 + w], src).then_inc(loaded, 16)

        @block.tensor
        def _(pe):
            pe.wait_ge(loaded, 16 * len(rows))
            pe.transpose(E.PS[:, 0, 0:P], E.praw[:, :], E.ident[:, :]).then_inc(turned, 1)

        @block.scalar
        def _(act):
            act.wait_ge(turned, 1)
            act.copy(E.par[:, :], E.PS[:, 0, 0:P])


def norm(nc, S, E, src, dst, nk, nh, nw, g, eps, b=None, func=None):
    S.open()
    centred = b is not None
    sum_ready = S.take("sum_ready")
    xc_ready = S.take("xc_ready")
    sq_ready = S.take("sq_ready")
    ssq_ready = S.take("ssq_ready")
    var_ready = S.take("var_ready")
    std_ready = S.take("std_ready")
    scaled = S.take("scaled")
    own = S.take("dve_steps")
    width = nk * P
    bank_sum = E.PS[:, 0:nh, 0:nw]
    bank_sq = E.PS[:, 2:2 + nh, 0:nw]
    sq = E.normbuf
    stat = halves(E.stat[:, 0:nh * nw], nh)

    with nc.Block() as block:
        @block.gpsimd
        def _(pool):
            S.clear_old(pool)

        @block.tensor
        def _(pe):
            if centred:
                for k in range(nk):
                    for a in range(nh):
                        last = pe.matmul(E.PS[:, a, 0:nw], E.ones[:, :], halves(src(k), nh)[:, a, :],
                                         start=(k == 0), stop=(k == nk - 1))
                last.then_inc(sum_ready, 1)
            for k in range(nk):
                pe.wait_ge(sq_ready, k + 1)
                for a in range(nh):
                    last = pe.matmul(E.PS[:, 2 + a, 0:nw], E.ones[:, :],
                                     halves(sq[:, k, 0:nh * nw], nh)[:, a, :],
                                     start=(k == 0), stop=(k == nk - 1))
            last.then_inc(ssq_ready, 1)

        @block.scalar
        def _(act):
            for k in range(nk):
                if centred:
                    act.wait_ge(xc_ready, k + 1)
                act.activation(sq[:, k, 0:nh * nw], dst(k) if centred else src(k),
                               ACT.Square).then_inc(sq_ready, 1)
            act.wait_ge(var_ready, 1)
            act.activation(stat, stat, ACT.Sqrt).then_inc(std_ready, 1)
            if centred:
                for k in range(nk):
                    act.wait_ge(scaled, k + 1)
                    act.activation(dst(k), dst(k), func or ACT.Identity, bias=b(k))

        @block.vector
        def _(dve):
            c = Chain(dve, own)
            if centred:
                dve.wait_ge(sum_ready, 1)
                c.link(dve.tensor_scalar(stat, bank_sum, 1.0 / width, None, ALU.mult))
                for k in range(nk):
                    dve.tensor_tensor(dst(k), src(k), E.stat[:, 0:nh * nw], ALU.subtract).then_inc(xc_ready, 1)
                dve.wait_ge(xc_ready, nk)
            dve.wait_ge(ssq_ready, 1)
            dve.tensor_scalar(stat, bank_sq, 1.0 / width, eps, ALU.mult, ALU.add).then_inc(var_ready, 1)
            dve.wait_ge(std_ready, 1)
            c.link(dve.reciprocal(E.stat[:, 0:nh * nw], E.stat[:, 0:nh * nw]))
            for k in range(nk):
                dve.scalar_tensor_tensor(dst(k), dst(k) if centred else src(k), g(k), E.stat[:, 0:nh * nw],
                                         ALU.mult, ALU.mult).then_inc(scaled, 1)


def project(nc, S, E, w_of, rhs, nk, npairs, nh, nw, evac, on="scalar"):
    S.open()
    loaded = [S.take("w_loaded_0"), S.take("w_loaded_1")]
    done = S.take("tile_done")
    freed = S.take("tile_out")
    with nc.Block() as block:
        @block.gpsimd
        def _(pool):
            S.clear_old(pool)

        @block.sync
        def _(sp):
            def load(j, slot, turn):
                sp.wait_ge(done, j * 2 + 1)
                sp.dma_start(E.wring[:, slot, 0:nk, :], w_of(j)).then_inc(loaded[slot], 16)
            in_pairs(sp, npairs, load)

        @block.tensor
        def _(pe):
            pe.sem_inc(done, 3)

            def multiply(j, slot, turn):
                pe.wait_ge(loaded[slot], turn * 16 + 16)
                for t in range(2):
                    pe.wait_ge(freed, j * 2 + (t + 1))
                    for k in range(nk):
                        for a in range(nh):
                            last = pe.matmul(E.PS[:, 4 * slot + 2 * t + a, 0:nw],
                                             E.wring[:, slot, k, t * P:(t + 1) * P],
                                             halves(rhs(k), nh)[:, a, :], start=(k == 0), stop=(k == nk - 1))
                    last.then_inc(done, 1)
            in_pairs(pe, npairs, multiply)

        def take_out(eng):
            eng.sem_inc(freed, 4)

            def body(j, slot, turn):
                for t in range(2):
                    eng.wait_ge(done, j * 2 + (t + 4))
                    b = 4 * slot + 2 * t
                    evac(eng, j, t, E.PS[:, b:b + nh, 0:nw]).then_inc(freed, 1)
            in_pairs(eng, npairs, body)

        if on == "scalar":
            @block.scalar
            def _(act):
                take_out(act)
        else:
            @block.vector
            def _(dve):
                take_out(dve)


def conv_taps(nc, S, E):
    S.open()
    sig_ready = S.take("sig_ready")
    padded = S.take("padded")
    gated = S.take("gated")
    own = S.take("tap_steps")
    pad = CONV_K - 1
    with nc.Block() as block:
        @block.gpsimd
        def _(pool):
            S.clear_old(pool)

        @block.scalar
        def _(act):
            act.activation(E.z[:, Z_GLU:Z_GLU + 2, :], E.z[:, Z_GLU:Z_GLU + 2, :],
                           ACT.Sigmoid).then_inc(sig_ready, 1)

        @block.vector
        def _(dve):
            dve.memset(E.upad[:, :, 0:pad], 0.0).then_inc(padded, 1)
            dve.wait_ge(sig_ready, 1)
            dve.tensor_tensor(E.upad[:, :, pad:pad + SEQ], E.z[:, Z_VAL:Z_VAL + 2, :],
                              E.z[:, Z_GLU:Z_GLU + 2, :], ALU.mult).then_inc(gated, 1)
            dve.wait_ge(padded, 1)
            dve.wait_ge(gated, 1)
            c = Chain(dve, own)
            for tap in range(CONV_K):
                for t in range(2):
                    acc, u = E.conv[:, t, :], E.upad[:, t, tap:tap + SEQ]
                    w = E.par[:, R_DW + 2 * tap + t:R_DW + 2 * tap + t + 1]
                    if tap == 0:
                        c.add(dve.tensor_scalar(acc, u, w, E.par[:, R_DWB + t:R_DWB + t + 1],
                                                ALU.mult, ALU.add))
                    else:
                        c.wait(2 * tap - 1 + t)
                        c.add(dve.scalar_tensor_tensor(acc, u, w, acc, ALU.mult, ALU.add))


def conv_point(nc, S, E):
    S.open()
    loaded = S.take("pw_loaded")
    silu_ready = S.take("silu_ready")
    done = S.take("point_done")
    with nc.Block() as block:
        @block.gpsimd
        def _(pool):
            S.clear_old(pool)

        @block.sync
        def _(sp):
            sp.dma_start(E.wring[:, 0, 0:2, :],
                         E.A["conv_pw_w"][E.li].rearrange("(k p) m -> p k m", p=P)).then_inc(loaded, 16)
            sp.wait_ge(loaded, 16)

        @block.scalar
        def _(act):
            act.activation(E.z[:, Z_CGATE:Z_CGATE + 2, :], E.z[:, Z_CGATE:Z_CGATE + 2, :],
                           ACT.Silu).then_inc(silu_ready, 1)

        @block.tensor
        def _(pe):
            pe.wait_ge(loaded, 16)
            for m in range(2):
                for k in range(2):
                    last = pe.matmul(E.PS[:, m, :], E.wring[:, 0, k, m * P:(m + 1) * P], E.conv[:, k, :],
                                     start=(k == 0), stop=(k == 1))
                last.then_inc(done, 1)

        @block.vector
        def _(dve):
            dve.wait_ge(silu_ready, 1)
            for m in range(2):
                dve.wait_ge(done, m + 1)
                dve.scalar_tensor_tensor(E.y[:, m, 0:SEQ], E.PS[:, m, :], E.par[:, R_PWB + m:R_PWB + m + 1],
                                         E.z[:, Z_CGATE + m, :], ALU.add, ALU.mult)


def pool_mix(nc, S, E):
    S.open()
    loaded = S.take("pool_w_loaded")
    own = S.take("window_steps")
    d_ready = S.take("d_ready")
    silu_ready = S.take("silu_ready")
    done = S.take("pool_done")
    G = 64
    with nc.Block() as block:
        @block.gpsimd
        def _(pool):
            S.clear_old(pool)

        @block.sync
        def _(sp):
            for g in range(4):
                r = (g % 2) * G
                sp.dma_start(E.wring[r:r + G, 0, 0, (g // 2) * G:(g // 2) * G + G],
                             E.A["pool_w"][E.li, g]).then_inc(loaded, 16)
            sp.wait_ge(loaded, 64)

        @block.scalar
        def _(act):
            act.activation(E.z[:, Z_PGATE:Z_PGATE + 2, :], E.z[:, Z_PGATE:Z_PGATE + 2, :],
                           ACT.Silu).then_inc(silu_ready, 1)

        @block.vector
        def _(dve):
            c = Chain(dve, own)
            x = E.z[:, Z_PIN:Z_PIN + 2, :]
            a, b = E.win[:, 0, :, :], E.win[:, 1, :, :]
            c.add(dve.memset(E.win[:, :, :, 0:16], 0.0))
            c.link(dve.tensor_copy(a[:, :, 16:16 + SEQ], x))

            def double(dst, src, by):
                c.link(dve.tensor_tensor(dst[:, :, 16:16 + SEQ], src[:, :, 16:16 + SEQ],
                                         src[:, :, 16 - by:16 - by + SEQ], ALU.add))

            def use(src, g):
                r, t = (g % 2) * G, g // 2
                c.add(dve.tensor_copy(E.avg[r:r + G, t, :], src[r:r + G, t, 16:16 + SEQ]))
            double(b, a, 1)
            use(b, 0)
            double(a, b, 2)
            use(a, 1)
            double(b, a, 4)
            use(b, 2)
            double(a, b, 8)
            use(a, 3)
            c.wait()
            c.link(dve.tensor_tensor(E.avg[:, :, :], E.avg[:, :, :], E.invcnt[:, :, :], ALU.mult))
            dve.tensor_tensor(E.avg[:, :, :], E.avg[:, :, :], x, ALU.subtract).then_inc(d_ready, 1)
            dve.wait_ge(silu_ready, 1)
            dve.wait_ge(done, 1)
            for t in range(2):
                c.add(dve.tensor_scalar(E.avg[:, t, :], E.PS[:, t, :], E.par[:, R_PB + t:R_PB + t + 1],
                                        E.par[:, R_PS + t:R_PS + t + 1], ALU.add, ALU.mult))
            c.wait()
            dve.tensor_tensor(E.y[:, 2:4, 0:SEQ], E.avg[:, :, :], E.z[:, Z_PGATE:Z_PGATE + 2, :], ALU.mult)

        @block.tensor
        def _(pe):
            pe.wait_ge(loaded, 64)
            pe.wait_ge(d_ready, 1)
            for g in range(4):
                r, t = (g % 2) * G, g // 2
                last = pe.matmul(E.PS[r:r + G, t, :], E.wring[r:r + G, 0, 0, t * G:t * G + G],
                                 E.avg[r:r + G, t, :], start=True, stop=True)
            last.then_inc(done, 1)


def rotate(nc, S, E, tiles, n_tokens, nh):
    S.open()
    turned = S.take("turned")
    cos_done = S.take("cos_done")
    sin_done = S.take("sin_done")
    added = S.take("added")
    nw = n_tokens // nh
    with nc.Block() as block:
        @block.gpsimd
        def _(pool):
            S.clear_old(pool)
            for i, x in enumerate(tiles):
                pool.wait_ge(cos_done, i + 1)
                pool.wait_ge(sin_done, i + 1)
                pool.tensor_tensor(x, E.rotbuf[:, 0, i % 2, 0:n_tokens], E.rotbuf[:, 1, i % 2, 0:n_tokens],
                                   ALU.add).then_inc(added, 1)

        @block.tensor
        def _(pe):
            for i, x in enumerate(tiles):
                if i >= 4:
                    pe.wait_ge(sin_done, i - 3)
                for a in range(nh):
                    last = pe.matmul(E.PS[:, 2 * (i % 4) + a, 0:nw], E.rot[:, :], halves(x, nh)[:, a, :],
                                     start=True, stop=True)
                last.then_inc(turned, 1)

        @block.vector
        def _(dve):
            for i, x in enumerate(tiles):
                if i >= 2:
                    dve.wait_ge(added, i - 1)
                dve.tensor_tensor(E.rotbuf[:, 0, i % 2, 0:n_tokens], x, E.cos[:, 0:n_tokens],
                                  ALU.mult).then_inc(cos_done, 1)
                dve.wait_ge(turned, i + 1)
                b = 2 * (i % 4)
                dve.tensor_tensor(halves(E.rotbuf[:, 1, i % 2, 0:n_tokens], nh), E.PS[:, b:b + nh, 0:nw],
                                  halves(E.sin[:, 0:n_tokens], nh), ALU.mult).then_inc(sin_done, 1)


def turn_values(nc, S, E):
    S.open()
    turned = S.take("turned")
    with nc.Block() as block:
        @block.gpsimd
        def _(pool):
            S.clear_old(pool)

        @block.tensor
        def _(pe):
            for t in range(4):
                for m in range(4):
                    last = pe.transpose(E.PS[:, t, m * P:(m + 1) * P], E.z[:, Z_V + m, t * P:(t + 1) * P],
                                        E.ident[:, :])
                last.then_inc(turned, 1)
            for t in range(4):
                last = pe.transpose(E.PS[:, 4, 4 * t:4 * t + 4], E.z[0:4, Z_WI, t * P:(t + 1) * P],
                                    E.ident[0:4, 0:4])
            last.then_inc(turned, 1)

        @block.scalar
        def _(act):
            for t in range(4):
                act.wait_ge(turned, t + 1)
                act.copy(E.vn[:, t, :], E.PS[:, t, :])
            act.wait_ge(turned, 5)
            act.copy(E.wi[:, :], E.PS[:, 4, 0:16])


def select_keys(nc, S, E):
    S.open()
    s_done = S.take("s_done")
    relu_done = S.take("relu_done")
    score_done = S.take("score_done")
    causal = S.take("causal")
    own = S.take("select_steps")
    blank = S.take("blank")
    units = [(qb, h) for qb in (1, 2, 3) for h in range(IDX_HEADS)]
    with nc.Block() as block:
        @block.tensor
        def _(pe):
            for i, (qb, h) in enumerate(units):
                if i >= 8:
                    pe.wait_ge(relu_done, i - 7)
                r, nk = (h % 2) * 64, (qb + 1) * P
                pe.matmul(E.PS[:, i % 8, 0:nk], E.z[r:r + 64, Z_QI + h // 2, qb * P:(qb + 1) * P],
                          E.z[r:r + 64, Z_KI, 0:nk], start=True, stop=True).then_inc(s_done, 1)

        @block.scalar
        def _(act):
            for i, (qb, h) in enumerate(units):
                act.wait_ge(s_done, i + 1)
                if i >= 4:
                    act.wait_ge(own, i - 3)
                nk = (qb + 1) * P
                act.activation(E.relu[:, i % 4, 0:nk], E.PS[:, i % 8, 0:nk], ACT.Relu,
                               scale=0.125).then_inc(relu_done, 1)

        @block.gpsimd
        def _(pool):
            S.clear_old(pool)
            pool.memset(E.mask[:, 0, 0:P], 0.0).then_inc(blank, 1)
            pool.wait_ge(blank, 1)
            pool.affine_select(out=E.mask[:, 0, 0:P], in_=E.mask[:, 0, 0:P], compare_op=ALU.is_ge, fill=-BIG,
                               base=0, pattern=[[-1, P]], channel_multiplier=1)
            for n, qb in enumerate((1, 2, 3)):
                pool.wait_ge(score_done, n + 1)
                x = E.score[:, qb, qb * P:(qb + 1) * P]
                pool.affine_select(out=x, in_=x, compare_op=ALU.is_ge, fill=-3e38, base=0,
                                   pattern=[[-1, P]], channel_multiplier=1).then_inc(causal, 1)

        @block.vector
        def _(dve):
            c = Chain(dve, own)
            for i, (qb, h) in enumerate(units):
                dve.wait_ge(relu_done, i + 1)
                nk = (qb + 1) * P
                acc, w = E.score[:, qb, 0:nk], E.wi[:, 4 * qb + h:4 * qb + h + 1]
                if h == 0:
                    c.link(dve.tensor_scalar(acc, E.relu[:, i % 4, 0:nk], w, None, ALU.mult))
                else:
                    c.link(dve.scalar_tensor_tensor(acc, E.relu[:, i % 4, 0:nk], w, acc, ALU.mult, ALU.add))
                if h == IDX_HEADS - 1:
                    dve.sem_inc(score_done, 1)
            dve.wait_ge(causal, 3)
            ROUNDS = TOPK // 8
            for r in range(ROUNDS):
                for qb in (1, 2, 3):
                    nk = (qb + 1) * P
                    if r:
                        c.wait(last_rep[qb])
                    src = E.work[:, qb, 0:nk] if r else E.score[:, qb, 0:nk]
                    c.add(dve.max(out=E.best[:, qb, :], in_=src))
                top = c.n
                last_rep = {}
                for qb in (1, 2, 3):
                    nk = (qb + 1) * P
                    c.wait(top)
                    src = E.work[:, qb, 0:nk] if r else E.score[:, qb, 0:nk]
                    if r < ROUNDS - 1:
                        last_rep[qb] = c.add(dve.match_replace(out=E.work[:, qb, 0:nk], in_to_replace=E.best[:, qb, :],
                                                               in_values=src, imm_value=-3e38))
            for qb in (1, 2, 3):
                nk = (qb + 1) * P
                s, m = E.score[:, qb, 0:nk], E.mask[:, qb, 0:nk]
                eq, cum = E.work[:, qb, 0:nk], E.relu[:, qb, 0:nk]
                thr, need = E.best[:, qb, 7:8], E.count[:, qb:qb + 1]
                c.add(dve.tensor_scalar(eq, s, thr, None, ALU.is_equal))
                c.link(dve.tensor_scalar(m, s, thr, 0.0, ALU.is_gt, ALU.add, accum_out=need))
                c.add(dve.tensor_scalar(need, need, -1.0, float(TOPK), ALU.mult, ALU.add))
                c.link(dve.tensor_tensor_scan(cum, E.onesrow[:, 0:nk], eq, 0.0, ALU.mult, ALU.add))
                c.link(dve.scalar_tensor_tensor(eq, cum, need, eq, ALU.is_le, ALU.mult))
                c.link(dve.tensor_tensor(m, m, eq, ALU.add))
                c.add(dve.tensor_scalar(m, m, BIG, -BIG, ALU.mult, ALU.add))
            c.wait()


def attend(nc, S, E):
    S.open()
    logit_done = S.take("logit_done")
    masked = S.take("masked")
    neg_max = S.take("neg_max")
    exp_done = S.take("exp_done")
    turned = S.take("probs_turned")
    copied = S.take("probs_copied")
    pv_done = S.take("pv_done")
    rsum = S.take("sum_inverse")
    o_ready = S.take("o_ready")
    o_turned = S.take("o_turned")
    gate = S.take("gate_ready")
    used = S.take("o_used")
    units = [(qb, h) for qb in range(4) for h in range(8)]
    SCALE = 0.125
    with nc.Block() as block:
        @block.gpsimd
        def _(pool):
            S.clear_old(pool)

        @block.tensor
        def _(pe):
            def logits(i):
                qb, h = units[i]
                r, nk = (h % 2) * 64, (qb + 1) * P
                if i >= 2:
                    pe.wait_ge(masked, i - 1)
                pe.matmul(E.PS[:, i % 2, 0:nk], E.z[r:r + 64, Z_Q + h // 2, qb * P:(qb + 1) * P],
                          E.z[r:r + 64, Z_K + h // 2, 0:nk], start=True, stop=True).then_inc(logit_done, 1)

            def turn(i):
                qb, h = units[i]
                pe.wait_ge(exp_done, i + 1)
                if i >= 2:
                    pe.wait_ge(copied, i - 1)
                for kb in range(qb + 1):
                    last = pe.transpose(E.PS[:, 2 + i % 2, kb * P:(kb + 1) * P],
                                        E.prob[:, i % 2, kb * P:(kb + 1) * P], E.ident[:, :])
                last.then_inc(turned, 1)

            def values(i):
                qb, h = units[i]
                pe.wait_ge(copied, i + 1)
                if h == 0 and qb >= 2:
                    pe.wait_ge(o_ready, qb - 1)
                for kb in range(qb + 1):
                    last = pe.matmul(E.PS[:, 4 + qb % 2, h * 64:h * 64 + 64],
                                     E.probT[:, i % 2, kb * P:(kb + 1) * P],
                                     E.vn[:, kb, h * 64:h * 64 + 64], start=(kb == 0), stop=(kb == qb))
                last.then_inc(pv_done, 1)

            def turn_out(qb):
                pe.wait_ge(o_ready, qb + 1)
                if qb >= 2:
                    pe.wait_ge(used, qb - 1)
                for m in range(4):
                    last = pe.transpose(E.PS[:, 6 + qb % 2, m * P:(m + 1) * P], E.o[:, qb % 2, m * P:(m + 1) * P],
                                        E.ident[:, :])
                last.then_inc(o_turned, 1)

            n = len(units)
            logits(0)
            for i in range(n + 2):
                if i + 1 < n:
                    logits(i + 1)
                if i < n:
                    turn(i)
                if 1 <= i <= n:
                    values(i - 1)
                if i >= 9 and (i - 9) % 8 == 0:
                    turn_out((i - 9) // 8)

        @block.vector
        def _(dve):
            def mask(i):
                qb, h = units[i]
                nk = (qb + 1) * P
                dve.wait_ge(logit_done, i + 1)
                if i >= 2:
                    dve.wait_ge(exp_done, i - 1)
                dve.tensor_tensor_reduce(E.logit[:, i % 2, 0:nk], E.PS[:, i % 2, 0:nk], E.mask[:, qb, 0:nk],
                                         1.0, -3e38, ALU.add, ALU.max, E.mx[:, i:i + 1]).then_inc(masked, 1)
                dve.wait_ge(masked, i + 1)
                dve.tensor_scalar(E.mx[:, i:i + 1], E.mx[:, i:i + 1], -SCALE, None, ALU.mult).then_inc(neg_max, 1)

            def copy(i):
                qb, h = units[i]
                nk = (qb + 1) * P
                dve.wait_ge(turned, i + 1)
                if i >= 2:
                    dve.wait_ge(pv_done, i - 1)
                dve.tensor_copy(E.probT[:, i % 2, 0:nk], E.PS[:, 2 + i % 2, 0:nk]).then_inc(copied, 1)

            def out(qb):
                dve.wait_ge(exp_done, 8 * qb + 8)
                dve.reciprocal(E.sums[:, 8 * qb:8 * qb + 8], E.sums[:, 8 * qb:8 * qb + 8]).then_inc(rsum, 1)
                dve.wait_ge(pv_done, 8 * qb + 8)
                dve.wait_ge(rsum, qb + 1)
                if qb >= 2:
                    dve.wait_ge(o_turned, qb - 1)
                dve.tensor_tensor(E.o[:, qb % 2, :].rearrange("p (h n) -> p h n", h=8),
                                  E.PS[:, 4 + qb % 2, :].rearrange("p (h n) -> p h n", h=8),
                                  E.sums[:, 8 * qb:8 * qb + 8].unsqueeze(2).broadcast_to([P, 8, 64]),
                                  ALU.mult).then_inc(o_ready, 1)

            def store(qb):
                dve.wait_ge(o_turned, qb + 1)
                dve.wait_ge(gate, 1)
                dve.tensor_tensor(E.y[:, 4:8, qb * P:(qb + 1) * P],
                                  E.PS[:, 6 + qb % 2, :].rearrange("p (m n) -> p m n", m=4),
                                  E.z[:, Z_AGATE:Z_AGATE + 4, qb * P:(qb + 1) * P], ALU.mult).then_inc(used, 1)

            n = len(units)
            mask(0)
            for i in range(n + 3):
                if i + 1 < n:
                    mask(i + 1)
                if i < n:
                    copy(i)
                if i >= 8 and (i - 8) % 8 == 0 and i <= n:
                    out(i // 8 - 1)
                if i >= 10 and (i - 10) % 8 == 0:
                    store((i - 10) // 8)

        @block.scalar
        def _(act):
            act.activation(E.z[:, Z_AGATE:Z_AGATE + 4, :], E.z[:, Z_AGATE:Z_AGATE + 4, :],
                           ACT.Silu).then_inc(gate, 1)
            for i, (qb, h) in enumerate(units):
                nk = (qb + 1) * P
                act.wait_ge(neg_max, i + 1)
                if i >= 2:
                    act.wait_ge(turned, i - 1)
                act.activation(E.prob[:, i % 2, 0:nk], E.logit[:, i % 2, 0:nk], ACT.Exp, bias=E.mx[:, i:i + 1],
                               scale=SCALE, accum_out=E.sums[:, i:i + 1]).then_inc(exp_done, 1)


def index_weights(nc, S, E):
    S.open()
    loaded = S.take("w_loaded")
    done = S.take("tile_done")
    ki0 = Z_KI * P
    w = E.A["w_in"][E.li].rearrange("(k p) m -> p k m", p=P)
    with nc.Block() as block:
        @block.gpsimd
        def _(pool):
            S.clear_old(pool)

        @block.sync
        def _(sp):
            sp.dma_start(E.wring[:, 0, :, 0:64], w[:, :, ki0:ki0 + 64]).then_inc(loaded, 16)
            sp.dma_start(E.wring[:, 0, :, 64:128], w[:, :, ki0:ki0 + 64]).then_inc(loaded, 16)
            sp.dma_start(E.wring[:, 0, :, 128:132], w[:, :, ki0 + 64:ki0 + 68]).then_inc(loaded, 16)
            sp.wait_ge(loaded, 48)

        @block.tensor
        def _(pe):
            pe.wait_ge(loaded, 48)
            for n, (c0, m) in enumerate(((0, P), (P, 4))):
                for k in range(KT):
                    last = pe.matmul(E.PS[0:m, n, :], E.wring[:, 0, k, c0:c0 + m], E.n[:, k, 0:SEQ],
                                     start=(k == 0), stop=(k == KT - 1))
                last.then_inc(done, 1)

        @block.scalar
        def _(act):
            for n, m in enumerate((P, 4)):
                act.wait_ge(done, n + 1)
                act.activation(E.z[0:m, Z_KI + n, :], E.PS[0:m, n, :], ACT.Identity,
                               bias=E.par[0:m, R_B + Z_KI + n:R_B + Z_KI + n + 1])


def gated_skip(nc, S, E):
    S.open()
    loaded = S.take("ple_loaded")
    done = S.take("tile_done")
    times = S.take("times_gate")
    freed = S.take("bank_out")
    with nc.Block() as block:
        @block.gpsimd
        def _(pool):
            S.clear_old(pool)
            for m in range(KT):
                pool.wait_ge(times, m + 1)
                pool.tensor_tensor(E.h[:, m, 0:SEQ], E.h1[:, m, 0:SEQ], E.n[:, m, 0:SEQ], ALU.add)

        @block.sync
        def _(sp):
            sp.dma_start(E.plew[:, :, :], E.A["ple_w"][E.li].rearrange("(k p) m -> p k m", p=P)).then_inc(loaded, 16)
            sp.wait_ge(loaded, 16)

        @block.tensor
        def _(pe):
            pe.wait_ge(loaded, 16)
            for m in range(KT):
                for k in range(2):
                    last = pe.matmul(E.PS[:, m, :], E.plew[:, k, m * P:(m + 1) * P], E.pT[:, k, :],
                                     start=(k == 0), stop=(k == 1))
                last.then_inc(done, 1)

        @block.vector
        def _(dve):
            for m in range(KT):
                dve.wait_ge(done, m + 1)
                dve.tensor_tensor(E.n[:, m, 0:SEQ], E.PS[:, m, :], E.n[:, m, 0:SEQ], ALU.mult).then_inc(times, 1)


R_NG, R_B, R_DW, R_DWB, R_LG, R_LB, R_PWB, R_PB, R_PS = 0, 8, 38, 100, 102, 104, 106, 108, 110


def first_block(nc, S, E, scope):
    A = E.A

    def sb(name, shape):
        return scope.enter_context(nc.sbuf_tensor(name, shape, F32))
    E.z = sb("z", [P, Z_TILES, SEQ])
    h1 = E.h1_flat
    padded = SEQ + CONV_K - 1
    E.upad = h1[:, 0:2 * padded].rearrange("p (a n) -> p a n", a=2)
    at = 2 * padded
    E.conv = h1[:, at:at + 2 * SEQ].rearrange("p (a n) -> p a n", a=2)
    at += 2 * SEQ
    E.win = h1[:, at:at + 4 * (SEQ + 16)].rearrange("p (b a n) -> p b a n", b=2, a=2)
    E.avg = E.conv
    n = E.n_flat
    E.vn = n[:, 0:4 * SEQ].rearrange("p (a n) -> p a n", a=4)
    E.relu = n[:, 4 * SEQ:8 * SEQ].rearrange("p (a n) -> p a n", a=4)
    E.invcnt = sb("invcnt", [P, 2, SEQ])
    E.wi = sb("wi", [P, 16])
    E.score = sb("score", [P, 4, SEQ])
    E.work = E.normbuf[:, 0:4, 0:SEQ]
    E.mask = E.normbuf[:, 4:8, 0:SEQ]
    E.best = sb("best", [P, 4, 8])
    E.count = sb("count", [P, 4])
    E.onesrow = sb("onesrow", [P, SEQ])
    E.logit = E.relu[:, 0:2, :]
    E.prob = E.relu[:, 2:4, :]
    E.probT = E.score[:, 0:2, :]
    E.o = E.score[:, 2:4, :]
    E.mx = sb("mx", [P, 32])
    E.sums = sb("sums", [P, 32])
    E.plew = E.z[:, 0:4, :].rearrange("p a n -> p (a n)").rearrange("p (k m) -> p k m", k=2)
    E.pT = E.z[:, 4:6, :]
    xn = E.z[:, 0:8, :].rearrange("p a n -> p (a n)").rearrange("p (t d) -> p t d", t=4)
    pn = E.z[:, 8:10, :].rearrange("p a n -> p (a n)").rearrange("p (t d) -> p t d", t=4)

    load_constants(nc, S, [(E.invcnt[:, :, :], A["invcnt"]), (E.cos[:, 0:SEQ], A["cos1"]), (E.sin[:, 0:SEQ], A["sin1"]),
                           (E.onesrow[:, :], A["onesrow"]),
                           (xn, A["x"][0].rearrange("(t p) d -> p t d", p=P))])
    transpose_rows(nc, S, E, lambda k: E.h[:, k, 0:SEQ], KT,
                   parts=[(xn[:, t, :], t * P, P) for t in range(4)])
    sweep(nc, S)
    with nc.Fori(0, E.depth) as li:
        E.li = li

        def rows(name, n):
            return A[name][li].rearrange("(t p) -> t p", p=P)[0:n]
        b = A["b_in"][li]
        ki0 = Z_KI * P
        load_params(nc, S, E, [
            (R_NG, 8, rows("norm_g", 8), 0, P),
            (R_B, 28, b[0:28 * P].rearrange("(t p) -> t p", p=P), 0, P),
            (R_B + 28, 1, b[ki0:ki0 + 64].unsqueeze(0), 0, 64),
            (R_B + 28, 1, b[ki0:ki0 + 64].unsqueeze(0), 64, 64),
            (R_B + 29, 1, b[ki0 + 64:ki0 + 68].unsqueeze(0), 0, 4),
            (R_DW, 62, A["conv_dw_w"][li].rearrange("k (t p) -> (k t) p", p=P), 0, P),
            (R_DWB, 2, rows("conv_dw_b", 2), 0, P), (R_LG, 2, rows("conv_ln_g", 2), 0, P),
            (R_LB, 2, rows("conv_ln_b", 2), 0, P), (R_PWB, 2, rows("conv_pw_b", 2), 0, P),
            (R_PB, 2, rows("pool_b", 2), 0, P), (R_PS, 2, rows("pool_scale", 2), 0, P)])

        def par(r):
            return lambda k: E.par[:, r + k:r + k + 1]
        norm(nc, S, E, lambda k: E.h[:, k, 0:SEQ], lambda k: E.n[:, k, 0:SEQ], KT, 1, SEQ, par(R_NG), 1e-6)
        w_in = A["w_in"][li].rearrange("(k p) m -> p k m", p=P)
        par_b = E.par[:, R_B:R_B + 30]

        def to_z(eng, j, t, psum):
            q = j * 2 + t
            return eng.activation(E.z[:, bass.ds(q, 1), :], psum, ACT.Identity, bias=par_b[:, bass.ds(q, 1)])
        project(nc, S, E, lambda j: w_in[:, :, bass.ds(j * 256, 256)], lambda k: E.n[:, k, 0:SEQ], KT, PAIRS1,
                1, SEQ, to_z)
        index_weights(nc, S, E)
        conv_taps(nc, S, E)
        norm(nc, S, E, lambda k: E.conv[:, k, :], lambda k: E.conv[:, k, :], 2, 1, SEQ, par(R_LG), 1e-6,
             b=par(R_LB), func=ACT.Silu)
        conv_point(nc, S, E)
        pool_mix(nc, S, E)
        rotate(nc, S, E, [E.z[:, m, :] for m in [*range(Z_Q, Z_V), Z_QI, Z_QI + 1, Z_KI]], SEQ, 1)
        turn_values(nc, S, E)
        select_keys(nc, S, E)
        attend(nc, S, E)
        w_out = A["w_out"][li].rearrange("(k p) m -> p k m", p=P)

        def add_h(eng, j, t, psum):
            q = j * 2 + t
            return eng.tensor_tensor(E.h1[:, bass.ds(q, 1), 0:SEQ], psum, E.h[:, bass.ds(q, 1), 0:SEQ], ALU.add)
        project(nc, S, E, lambda j: w_out[:, :, bass.ds(j * 256, 256)], lambda k: E.y[:, k, 0:SEQ], KT, KT // 2,
                1, SEQ, add_h, on="vector")
        ple_gate = A["ple_gate_w"][li].rearrange("(k p) m -> p k m", p=P)

        def sigmoids(eng, j, t, psum):
            return eng.activation(E.n[:, bass.ds(j * 2 + t, 1), 0:SEQ], psum, ACT.Sigmoid)
        project(nc, S, E, lambda j: ple_gate[:, :, bass.ds(j * 256, 256)], lambda k: E.h1[:, k, 0:SEQ], KT, KT // 2,
                1, SEQ, sigmoids)
        load_constants(nc, S, [(pn, A["p"][li, 0].rearrange("(t p) d -> p t d", p=P))])
        transpose_rows(nc, S, E, lambda k: E.pT[:, k, :], 2, parts=[(pn[:, t, :], t * P, P) for t in range(4)])
        gated_skip(nc, S, E)
        sweep(nc, S)
    load_params(nc, S, E, [(0, 8, A["final_norm_g"].rearrange("(t p) -> t p", p=P), 0, P),
                           (8, 8, A["emb_ln_g_2"].rearrange("(t p) -> t p", p=P), 0, P),
                           (16, 8, A["emb_ln_b_2"].rearrange("(t p) -> t p", p=P), 0, P)])
    norm(nc, S, E, lambda k: E.h[:, k, 0:SEQ], lambda k: E.h1[:, k, N_META:L], KT, 1, SEQ,
         lambda k: E.par[:, k:k + 1], 1e-6)


(Q_QN, Q_KVN, Q_MP, Q_MN, Q_W0, Q_A0, Q_KK, Q_KA, Q_RK, Q_GG, Q_GB, Q_V0, Q_L1G, Q_L1B, Q_L2G, Q_L2B, Q_FIRST,
 Q_C0) = (0, 2, 3, 18, 33, 41, 49, 53, 57, 61, 65, 69, 73, 81, 89, 97, 105, 106)


def angles(nc, S, E):
    S.open()
    loaded = S.take("positions_loaded")
    own = S.take("angle_steps")
    r_ready = S.take("r_ready")
    TURN = 2 * np.pi
    C1 = 6.28125
    C2 = float(np.float32(np.round((TURN - C1) * 2 ** 21) / 2 ** 21))
    C3 = TURN - C1 - C2
    MAGIC = 1.5 * 2 ** 23
    with nc.Block() as block:
        @block.gpsimd
        def _(pool):
            S.clear_old(pool)

        @block.sync
        def _(sp):
            sp.dma_start(E.pos_int[:, :], E.A["positions_2"][0].partition_broadcast(P)).then_inc(loaded, 16)
            sp.dma_start(E.cos[:, 0:N_META], E.A["meta_pos"]).then_inc(loaded, 16)
            sp.dma_start(E.invf[:, :], E.A["inv_freq"]).then_inc(loaded, 16)
            sp.wait_ge(loaded, 48)

        @block.vector
        def _(dve):
            c = Chain(dve, own)
            dve.wait_ge(loaded, 48)
            c.link(dve.tensor_copy(E.cos[:, N_META:L], E.pos_int[:, :]))
            c.link(dve.tensor_scalar(E.cos[:, N_META:L], E.cos[:, N_META:L], float(N_META), None, ALU.add))
            c.link(dve.tensor_scalar(E.cos[:, :], E.cos[:, :], E.invf[:, 0:1], None, ALU.mult))
            turns = E.stat[:, 0:L]
            c.link(dve.tensor_scalar(turns, E.cos[:, :], 1.0 / TURN, MAGIC, ALU.mult, ALU.add))
            c.link(dve.tensor_scalar(turns, turns, -MAGIC, None, ALU.add))
            for part in (C1, C2, C3):
                c.link(dve.scalar_tensor_tensor(E.cos[:, :], turns, -part, E.cos[:, :], ALU.mult, ALU.add))
            PI = 3.1415925
            c.link(dve.tensor_scalar(E.cos[:, :], E.cos[:, :], PI, -PI, ALU.min, ALU.max))
            c.link(dve.tensor_scalar(E.stat[:, 0:L], E.cos[:, :], -1.0, None, ALU.mult))
            c.link(dve.tensor_tensor(E.stat[:, 0:L], E.stat[:, 0:L], E.cos[:, :], ALU.max))
            dve.tensor_scalar(E.stat[:, 0:L], E.stat[:, 0:L], -1.0, float(np.pi / 2), ALU.mult,
                              ALU.add).then_inc(r_ready, 1)

        @block.scalar
        def _(act):
            act.wait_ge(r_ready, 1)
            act.activation(E.sin[:, :], E.cos[:, :], ACT.Sin).then_inc(r_ready, 1)
            act.wait_ge(r_ready, 2)
            act.activation(E.cos[:, :], E.stat[:, 0:L], ACT.Sin)


def project_tail(nc, S, E):
    S.open()
    loaded = S.take("w_loaded")
    done = S.take("tile_done")
    w = E.A["w_in_2"][E.li].rearrange("(k p) m -> p k m", p=P)
    first_rw = 3 * P + 64
    out = S.take("tile_out")
    tiles = (0, 1, 2, 3, T_GD)
    wt = E.norm_flat[:, 0:KT * 512].rearrange("p (k m) -> p k m", k=KT)
    w_gd = E.wring[:, 0, :, 0:P]
    with nc.Block() as block:
        @block.gpsimd
        def _(pool):
            S.clear_old(pool)

        @block.sync
        def _(sp):
            sp.dma_start(wt[:, :, 0:448], w[:, :, 0:448]).then_inc(loaded, 16)
            sp.dma_start(wt[:, :, 448:512], w[:, :, 384:448]).then_inc(loaded, 16)
            c0 = first_rw + 14 * P
            sp.dma_start(w_gd, w[:, :, c0:c0 + P]).then_inc(loaded, 16)
            sp.wait_ge(loaded, 48)

        @block.tensor
        def _(pe):
            pe.wait_ge(loaded, 48)
            for i, m in enumerate(tiles):
                if i == 4:
                    pe.wait_ge(out, 1)
                for k in range(KT):
                    wk = wt[:, k, i * P:(i + 1) * P] if i < 4 else w_gd[:, k, :]
                    for a in range(2):
                        last = pe.matmul(E.PS[:, 2 * (i % 4) + a, 0:HALF], wk,
                                         halves(E.h[:, k, :], 2)[:, a, :], start=(k == 0), stop=(k == KT - 1))
                last.then_inc(done, 1)

        @block.scalar
        def _(act):
            for i, m in enumerate(tiles):
                act.wait_ge(done, i + 1)
                act.activation(halves(E.zs[m], 2), E.PS[:, 2 * (i % 4):2 * (i % 4) + 2, 0:HALF],
                               ACT.Identity).then_inc(out, 1)


def shift(nc, S, E):
    S.open()
    c0_ready = S.take("c0_ready")
    own = S.take("shift_steps")
    centre = S.take("centre_ready")
    both = S.take("neighbours_added")
    back = S.take("copied_back")
    n_t = 15
    with nc.Block() as block:
        @block.gpsimd
        def _(pool):
            S.clear_old(pool)

        @block.scalar
        def _(act):
            act.wait_ge(c0_ready, 1)

            def return_tile(i):
                act.wait_ge(both, i + 1)
                act.copy(E.zs[T_R + i], E.shifted[:, i % 4, :]).then_inc(back, 1)
            for i in range(n_t):
                if i >= 4:
                    act.wait_ge(back, i - 3)
                act.mul(E.shifted[:, i % 4, :], E.zs[T_R + i], E.par[:, Q_C0 + i:Q_C0 + i + 1]).then_inc(centre, 1)
                if i >= 2:
                    return_tile(i - 2)
            for i in (n_t - 2, n_t - 1):
                return_tile(i)

        @block.vector
        def _(dve):
            c = Chain(dve, own)
            c0 = E.par[:, Q_C0:Q_C0 + n_t]
            c.link(dve.tensor_tensor(c0, E.par[:, Q_MP:Q_MP + n_t], E.par[:, Q_MN:Q_MN + n_t], ALU.add))
            dve.tensor_scalar(c0, c0, -1.0, 1.0, ALU.mult, ALU.add).then_inc(c0_ready, 1)
            for i in range(n_t):
                x, u = E.zs[T_R + i], E.shifted[:, i % 4, :]
                dve.wait_ge(centre, i + 1)
                c.link(dve.scalar_tensor_tensor(u[:, 1:L], x[:, 0:L - 1], E.par[:, Q_MP + i:Q_MP + i + 1],
                                                u[:, 1:L], ALU.mult, ALU.add))
                dve.scalar_tensor_tensor(u[:, 0:L - 1], x[:, 1:L], E.par[:, Q_MN + i:Q_MN + i + 1],
                                         u[:, 0:L - 1], ALU.mult, ALU.add).then_inc(both, 1)


def mla_project(nc, S, E):
    S.open()
    loaded = S.take("w_loaded")
    done = S.take("tile_done")
    out = S.take("tile_out")
    flat = E.wring[:, :, :, :].rearrange("p s k m -> p (s k m)")
    uq = flat[:, 0:1536].rearrange("p (k h c) -> p k h c", k=2, h=H_A)
    ukv = flat[:, 1536:2560].rearrange("p (h c) -> p h c", h=H_A)
    pe_w = flat[:, 2560:3072].rearrange("p (k h c) -> p k h c", k=2, h=H_A)
    tiles = [([uq[:, k, h, 0:P] for k in range(2)], 0, E.qn[:, h, :]) for h in range(H_A)]
    tiles += [([pe_w[:, k, 2 * j:2 * j + 2, :].rearrange("p h c -> p (h c)") for k in range(2)], 0, E.qp[:, j, :])
              for j in range(2)]
    tiles += [([ukv[:, h, 0:P]], 2, E.kn[:, h, :]) for h in range(H_A)]
    with nc.Block() as block:
        @block.gpsimd
        def _(pool):
            S.clear_old(pool)

        @block.sync
        def _(sp):
            w = E.A["mla_w_uq_2"][E.li].rearrange("(k p) (h c) -> p k h c", p=P, h=H_A)
            for k in range(2):
                sp.dma_start(uq[:, k], w[:, k]).then_inc(loaded, 16)
                sp.dma_start(pe_w[:, k], w[:, k, :, P:192]).then_inc(loaded, 16)
            sp.dma_start(ukv, E.A["mla_w_ukv_2"][E.li].rearrange("p (h c) -> p h c", h=H_A)).then_inc(loaded, 16)
            sp.wait_ge(loaded, 80)

        @block.tensor
        def _(pe):
            pe.wait_ge(loaded, 80)
            for i, (w, k0, _) in enumerate(tiles):
                if i >= 4:
                    pe.wait_ge(out, i - 3)
                for k in range(len(w)):
                    for a in range(2):
                        last = pe.matmul(E.PS[:, 2 * (i % 4) + a, 0:HALF], w[k],
                                         halves(E.n[:, k0 + k, :], 2)[:, a, :], start=(k == 0), stop=(k == len(w) - 1))
                last.then_inc(done, 1)
            pe.wait_ge(out, 10)
            for t, (t0, rows) in enumerate(TOK):
                last = pe.matmul(E.PS[0:rows, t, :], E.n[:, 2, t0:t0 + rows], ukv[:, :, P:2 * P], start=True, stop=True)
                last.then_inc(done, 1)

        @block.scalar
        def _(act):
            for i, (_, _, dst) in enumerate(tiles):
                act.wait_ge(done, i + 1)
                act.activation(halves(dst, 2), E.PS[:, 2 * (i % 4):2 * (i % 4) + 2, 0:HALF],
                               ACT.Identity).then_inc(out, 1)
            for t, (t0, rows) in enumerate(TOK):
                act.wait_ge(done, 11 + t)
                act.copy(E.vn2[0:rows, t, :], E.PS[0:rows, t, :])


def mla_attend(nc, S, E):
    S.open()
    logit_done = S.take("logit_done")
    neg_max = S.take("neg_max")
    max_steps = S.take("max_steps")
    exp_done = S.take("exp_done")
    turned = S.take("probs_turned")
    copied = S.take("probs_copied")
    copied_end = S.take("probs_end_copied")
    pv_done = S.take("pv_done")
    inv_ready = S.take("sum_inverse")
    o_ready = S.take("o_ready")
    blank = S.take("blank")
    units = [(t, h) for t in range(len(TOK)) for h in range(H_A)]
    n = len(units)
    nt = len(TOK)
    with nc.Block() as block:
        @block.gpsimd
        def _(pool):
            S.clear_old(pool)
            pool.memset(E.on[:, nt - 1, :], 1.0).then_inc(blank, 1)

        @block.tensor
        def _(pe):
            def logits(i):
                t, h = units[i]
                t0, rows = TOK[t]
                r = (h % 2) * 64
                if i >= 2:
                    pe.wait_ge(exp_done, i - 1)
                for a in range(2):
                    dst = E.PS[0:rows, 2 * (i % 2) + a, 0:HALF]
                    pe.matmul(dst, E.qn[:, h, t0:t0 + rows], halves(E.kn[:, h, :], 2)[:, a, :], start=True, stop=False)
                    last = pe.matmul(dst, E.qp[r:r + 64, h // 2, t0:t0 + rows],
                                     halves(E.zs[T_KPE], 2)[r:r + 64, a, :], start=False, stop=True)
                last.then_inc(logit_done, 1)

            def turn(i):
                t, h = units[i]
                rows = TOK[t][1]
                pe.wait_ge(exp_done, i + 1)
                if i >= 2:
                    pe.wait_ge(copied, i - 1)
                    pe.wait_ge(copied_end, i - 1)
                for b, (b0, br) in enumerate(TOK):
                    dst = (E.PS[0:br, 4 + i % 2, b * P:b * P + rows] if b < 4 else
                           E.PS[0:br, 6, (i % 2) * P:(i % 2) * P + rows])
                    last = pe.transpose(dst, E.prob2[0:rows, i % 2, b0:b0 + br], E.ident[0:rows, 0:rows])
                last.then_inc(turned, 1)

            def values(i):
                t, h = units[i]
                rows = TOK[t][1]
                pe.wait_ge(copied, i + 1)
                pe.wait_ge(copied_end, i + 1)
                if h == 0 and t >= 1:
                    pe.wait_ge(o_ready, t)
                for b, (b0, br) in enumerate(TOK):
                    last = pe.matmul(E.PS[0:rows, 7, h * P:(h + 1) * P], E.probT2[0:br, i % 2, b, 0:rows],
                                     E.vn2[0:br, b, h * P:(h + 1) * P], start=(b == 0), stop=(b == nt - 1))
                last.then_inc(pv_done, 1)

            logits(0)
            for i in range(n + 1):
                if i + 1 < n:
                    logits(i + 1)
                if i < n:
                    turn(i)
                if i >= 1:
                    values(i - 1)

        @block.vector
        def _(dve):
            def top(i):
                t, h = units[i]
                rows = TOK[t][1]
                dve.wait_ge(logit_done, i + 1)
                dve.tensor_reduce(E.mx2[0:rows, i:i + 1], E.PS[0:rows, 2 * (i % 2):2 * (i % 2) + 2, 0:HALF],
                                  mybir.AxisListType.XY, ALU.max).then_inc(max_steps, 1)
                dve.wait_ge(max_steps, i + 1)
                dve.tensor_scalar(E.mx2[0:rows, i:i + 1], E.mx2[0:rows, i:i + 1], -MLA_SCALE, None,
                                  ALU.mult).then_inc(neg_max, 1)

            def copy(i):
                t, h = units[i]
                rows = TOK[t][1]
                dve.wait_ge(turned, i + 1)
                if i >= 2:
                    dve.wait_ge(pv_done, i - 1)
                dve.tensor_copy(E.probT2[:, i % 2, 0:4, 0:rows],
                                E.PS[:, 4 + i % 2, :].rearrange("p (b n) -> p b n", b=4)[:, :, 0:rows]).then_inc(copied, 1)

            def out(t):
                rows = TOK[t][1]
                s = E.sums2[0:rows, 4 * t:4 * t + 4]
                dve.wait_ge(exp_done, 4 * t + 4)
                dve.reciprocal(s, s).then_inc(inv_ready, 1)
                dve.wait_ge(pv_done, 4 * t + 4)
                dve.wait_ge(inv_ready, t + 1)
                if t == nt - 1:
                    dve.wait_ge(blank, 1)
                dve.tensor_tensor(E.on[0:rows, t, :].rearrange("p (h n) -> p h n", h=H_A),
                                  E.PS[0:rows, 7, :].rearrange("p (h n) -> p h n", h=H_A),
                                  s.unsqueeze(2).broadcast_to([rows, H_A, P]), ALU.mult).then_inc(o_ready, 1)

            top(0)
            for i in range(n + 2):
                if i + 1 < n:
                    top(i + 1)
                if i < n:
                    copy(i)
                if i >= 4 and i % 4 == 0:
                    out(i // 4 - 1)

        @block.scalar
        def _(act):
            for i, (t, h) in enumerate(units):
                rows = TOK[t][1]
                act.wait_ge(neg_max, i + 1)
                if i >= 2:
                    act.wait_ge(turned, i - 1)
                act.activation(halves(E.prob2[0:rows, i % 2, :], 2), E.PS[0:rows, 2 * (i % 2):2 * (i % 2) + 2, 0:HALF],
                               ACT.Exp, bias=E.mx2[0:rows, i:i + 1], scale=MLA_SCALE,
                               accum_out=E.sums2[0:rows, i:i + 1]).then_inc(exp_done, 1)
                act.wait_ge(turned, i + 1)
                if i >= 2:
                    act.wait_ge(pv_done, i - 1)
                act.copy(E.probT2[0:N_META, i % 2, 4, 0:rows],
                         E.PS[0:N_META, 6, (i % 2) * P:(i % 2) * P + rows]).then_inc(copied_end, 1)


def mla_out(nc, S, E):
    S.open()
    loaded = S.take("g_loaded")
    own = S.take("norm_steps")
    sq_ready = S.take("sq_ready")
    var_ready = S.take("var_ready")
    std_ready = S.take("std_ready")
    o_ready = S.take("o_ready")
    turned = S.take("turned")
    copied = S.take("copied")
    nt = len(TOK)
    with nc.Block() as block:
        @block.gpsimd
        def _(pool):
            S.clear_old(pool)

        @block.sync
        def _(sp):
            sp.dma_start(E.onorm[:, :], E.A["mla_out_norm_2"][E.li].partition_broadcast(P)).then_inc(loaded, 16)
            sp.wait_ge(loaded, 16)

        @block.scalar
        def _(act):
            act.activation(E.osq[:, :, :], E.on[:, :, :], ACT.Square).then_inc(sq_ready, 1)
            act.wait_ge(var_ready, 1)
            act.activation(E.ovar[:, :], E.ovar[:, :], ACT.Sqrt).then_inc(std_ready, 1)
            for m in range(4):
                act.wait_ge(turned, m + 1)
                act.copy(E.y[:, m, 0:512], E.PS[:, 2 * (m % 2), :])
                act.copy(E.y[:, m, 512:L], E.PS[:, 2 * (m % 2) + 1, 0:N_META]).then_inc(copied, 1)

        @block.vector
        def _(dve):
            c = Chain(dve, own)
            dve.wait_ge(sq_ready, 1)
            c.link(dve.tensor_reduce(E.ovar[:, :], E.osq[:, :, :].rearrange("p t (h n) -> p (t h) n", h=H_A), AX, ALU.add))
            dve.tensor_scalar(E.ovar[:, :], E.ovar[:, :], 1.0 / P, 1e-6, ALU.mult, ALU.add).then_inc(var_ready, 1)
            dve.wait_ge(std_ready, 1)
            c.link(dve.reciprocal(E.ovar[:, :], E.ovar[:, :]))
            v = E.on[:, :, :].rearrange("p t (h n) -> p (t h) n", h=H_A)
            c.link(dve.tensor_tensor(v, v, E.ovar[:, :].unsqueeze(2).broadcast_to([P, nt * H_A, P]), ALU.mult))
            dve.wait_ge(loaded, 16)
            dve.tensor_tensor(E.on[:, :, :], E.on[:, :, :], E.onorm[:, :].unsqueeze(1).broadcast_to([P, nt, 512]),
                              ALU.mult).then_inc(o_ready, 1)

        @block.tensor
        def _(pe):
            pe.wait_ge(o_ready, 1)
            for m in range(4):
                if m >= 2:
                    pe.wait_ge(copied, m - 1)
                for t, (t0, rows) in enumerate(TOK):
                    dst = E.PS[:, 2 * (m % 2) + t // 4, (t % 4) * P:(t % 4) * P + rows]
                    last = pe.transpose(dst, E.on[0:rows, t, m * P:(m + 1) * P], E.ident[0:rows, 0:rows])
                last.then_inc(turned, 1)


def lora_loads(E):
    A, li = E.A, E.li
    flat = E.wring[:, :, :, :].rearrange("p s k m -> p (s k m)")
    E.g2, E.w2, E.a2 = flat[:, 0:512], flat[:, 512:1024], flat[:, 1024:1536]
    E.v1 = flat[:, 1536:1664].rearrange("p (k m) -> p k m", k=4)
    E.v2 = flat[0:32, 1664:2176]
    return [(E.w2, A["rwkv_w2_2"][li].rearrange("d j m -> (d j) m")),
            (E.a2, A["rwkv_a2_2"][li].rearrange("d j m -> (d j) m")),
            (E.g2, A["rwkv_g2_2"][li]),
            (E.v1, A["rwkv_v1_2"][0].rearrange("(k p) m -> p k m", p=P)),
            (E.v2, A["rwkv_v2_2"][0])]


def value_mix(nc, S, E):
    S.open()
    own = S.take("mix_steps")
    low_done = S.take("low_done")
    low_ready = S.take("low_ready")
    up_done = S.take("up_done")
    sig = S.take("sig_ready")
    v, vf, d = E.zr[:, T_V - T_R:T_V - T_R + 4, 0:L], E.vfirst[:, :, :], E.tmp4
    with nc.Block() as block:
        @block.gpsimd
        def _(pool):
            S.clear_old(pool)

        @block.tensor
        def _(pe):
            for k in range(4):
                for a in range(2):
                    last = pe.matmul(E.PS[0:32, a, 0:HALF], E.v1[:, k, :], halves(v[:, k, :], 2)[:, a, :],
                                     start=(k == 0), stop=(k == 3))
            last.then_inc(low_done, 1)
            pe.wait_ge(low_ready, 1)
            for m in range(4):
                if m >= 3:
                    pe.wait_ge(sig, m - 2)
                for a in range(2):
                    last = pe.matmul(E.PS[:, 2 + 2 * (m % 3) + a, 0:HALF], E.v2[:, m * P:(m + 1) * P],
                                     halves(E.low[:, :], 2)[:, a, :], start=True, stop=True)
                last.then_inc(up_done, 1)

        @block.scalar
        def _(act):
            act.wait_ge(low_done, 1)
            act.copy(halves(E.low[:, :], 2), E.PS[0:32, 0:2, 0:HALF]).then_inc(low_ready, 1)
            for m in range(4):
                act.wait_ge(up_done, m + 1)
                b = 2 + 2 * (m % 3)
                act.activation(halves(E.tmp4b[:, m, :], 2), E.PS[:, b:b + 2, 0:HALF], ACT.Sigmoid,
                               bias=E.par[:, Q_V0 + m:Q_V0 + m + 1]).then_inc(sig, 1)

        @block.vector
        def _(dve):
            c = Chain(dve, own)
            c.link(dve.tensor_tensor(d, v, vf, ALU.subtract))
            c.link(dve.scalar_tensor_tensor(vf, d, E.par[:, Q_FIRST:Q_FIRST + 1], vf, ALU.mult, ALU.add))
            c.link(dve.tensor_tensor(d, vf, v, ALU.subtract))
            dve.wait_ge(sig, 4)
            dve.wait_ge(low_done, 1)
            c.link(dve.tensor_tensor(d, d, E.tmp4b, ALU.mult))
            dve.tensor_tensor(v, v, d, ALU.add)


def removal_keys(nc, S, E):
    S.open()
    raw = S.take("raw_ready")
    sq = S.take("sq_ready")
    ssq = S.take("ssq_ready")
    var = S.take("var_ready")
    std = S.take("std_ready")
    inv = S.take("inverse_ready")
    k = E.zr[:, T_K - T_R:T_K - T_R + 4, 0:L]
    with nc.Block() as block:
        @block.gpsimd
        def _(pool):
            S.clear_old(pool)
            pool.memset(E.kk[:, :, L:LP], 0.0)

        @block.tensor
        def _(pe):
            for m in range(4):
                pe.wait_ge(sq, m + 1)
                for a in range(2):
                    last = pe.matmul(E.PS[:, 2 * m + a, 0:HALF], E.head_ones[:, :], halves(E.tmp4[:, m, :], 2)[:, a, :],
                                     start=True, stop=True)
                last.then_inc(ssq, 1)

        @block.scalar
        def _(act):
            for m in range(4):
                act.wait_ge(raw, m + 1)
                act.activation(E.tmp4[:, m, :], E.kk[:, m, 0:L], ACT.Square).then_inc(sq, 1)
            act.wait_ge(var, 4)
            act.activation(E.tmp4, E.tmp4, ACT.Sqrt).then_inc(std, 1)

        @block.vector
        def _(dve):
            for m in range(4):
                dve.tensor_scalar(E.kk[:, m, 0:L], k[:, m, :], E.par[:, Q_KK + m:Q_KK + m + 1], None,
                                  ALU.mult).then_inc(raw, 1)
            for m in range(4):
                dve.wait_ge(ssq, m + 1)
                dve.tensor_scalar(halves(E.tmp4[:, m, :], 2), E.PS[:, 2 * m:2 * m + 2, 0:HALF], 1e-12, None,
                                  ALU.add).then_inc(var, 1)
            dve.wait_ge(std, 1)
            dve.reciprocal(E.tmp4, E.tmp4).then_inc(inv, 1)
            dve.wait_ge(inv, 1)
            dve.tensor_tensor(E.kk[:, :, 0:L], E.kk[:, :, 0:L], E.tmp4, ALU.mult)


def rates(nc, S, E, d):
    S.open()
    act_ready = S.take("tanh_ready")
    w_done = S.take("w_done")
    a_done = S.take("a_done")
    w_sig = S.take("w_sig")
    a_sig = S.take("a_sig")
    blank = S.take("blank")
    own = S.take("rate_steps")
    used = S.take("a_used")
    r = d * 64
    ld, cum, ba, kd = E.ld[d], E.cum[d], E.ba[d], E.kd[:, d]
    k = E.zr[:, T_K - T_R:T_K - T_R + 4, 0:L]
    with nc.Block() as block:
        @block.gpsimd
        def _(pool):
            S.clear_old(pool)
            for x in (ld, ba, kd):
                pool.memset(x[:, :, L:LP], 0.0).then_inc(blank, 1)

        @block.tensor
        def _(pe):
            pe.wait_ge(act_ready, 1)
            for m in range(4):
                if m >= 2:
                    pe.wait_ge(w_sig, m - 1)
                for a in range(2):
                    last = pe.matmul(E.PS[:, 4 * (m % 2) + a, 0:HALF], E.w2[r:r + 64, m * P:(m + 1) * P],
                                     halves(E.lora[:, 0, :], 2)[r:r + 64, a, :], start=True, stop=True)
                last.then_inc(w_done, 1)
                if m >= 2:
                    pe.wait_ge(a_sig, m - 1)
                for a in range(2):
                    last = pe.matmul(E.PS[:, 4 * (m % 2) + 2 + a, 0:HALF], E.a2[r:r + 64, m * P:(m + 1) * P],
                                     halves(E.zs[T_AD], 2)[r:r + 64, a, :], start=True, stop=True)
                last.then_inc(a_done, 1)

        @block.scalar
        def _(act):
            act.activation(E.lora[:, 0, :], E.zs[T_WD], ACT.Tanh).then_inc(act_ready, 1)
            for m in range(4):
                b = 4 * (m % 2)
                act.wait_ge(w_done, m + 1)
                act.activation(halves(ld[:, m, 0:L], 2), E.PS[:, b:b + 2, 0:HALF], ACT.Sigmoid,
                               bias=E.par[:, Q_W0 + 4 * d + m:Q_W0 + 4 * d + m + 1]).then_inc(w_sig, 1)
                act.wait_ge(a_done, m + 1)
                act.activation(halves(ba[:, m, 0:L], 2), E.PS[:, b + 2:b + 4, 0:HALF], ACT.Sigmoid,
                               bias=E.par[:, Q_A0 + 4 * d + m:Q_A0 + 4 * d + m + 1]).then_inc(a_sig, 1)

        @block.vector
        def _(dve):
            c = Chain(dve, own)
            dve.wait_ge(blank, 3)
            for m in range(4):
                dve.wait_ge(w_sig, m + 1)
                c.link(dve.tensor_scalar(ld[:, m, 0:L], ld[:, m, 0:L], -EXP_HALF, None, ALU.mult))
                c.add(dve.tensor_tensor_scan(cum[:, m, :], E.keep[:, :], ld[:, m, :], 0.0, ALU.mult, ALU.add))
                dve.wait_ge(a_sig, m + 1)
                ka = E.par[:, Q_KA + m:Q_KA + m + 1]
                c.link(dve.tensor_scalar(kd[:, m, 0:L], ba[:, m, 0:L], -1.0, ka, ALU.add, ALU.mult))
                c.add(dve.scalar_tensor_tensor(kd[:, m, 0:L], kd[:, m, 0:L], 1.0, k[:, m, :], ALU.add, ALU.mult))
                c.add(dve.tensor_tensor(ba[:, m, 0:L], ba[:, m, 0:L], E.kk[:, m, 0:L], ALU.mult))
            c.wait()
            if d == 1:
                x = cum.rearrange("p m (c n) -> p (m c) n", n=CH)
                c.link(dve.tensor_copy(E.total[:, :], x[:, :, CH - 1]))
                c.link(dve.tensor_tensor(x, E.total[:, :].unsqueeze(2).broadcast_to([P, 4 * N_CH, CH]), x, ALU.subtract))
                c.link(dve.tensor_tensor(cum, cum, ld, ALU.add))


def bonus(nc, S, E):
    S.open()
    own = S.take("bonus_steps")
    x_ready = S.take("x_ready")
    done = S.take("head_sum_done")
    r, v = E.zr[:, 0:4, 0:L], E.zr[:, T_V - T_R:T_V - T_R + 4, 0:L]
    with nc.Block() as block:
        @block.gpsimd
        def _(pool):
            S.clear_old(pool)
            pool.memset(E.zr[:, 0:12, L:LP], 0.0)
            pool.memset(E.state[:, :, :, :], 0.0)

        @block.vector
        def _(dve):
            c = Chain(dve, own)
            for m in range(4):
                c.link(dve.tensor_tensor(E.tmp4[:, m, :], E.kd[:, 0, m, 0:L], E.kd[:, 1, m, 0:L], ALU.add))
                dve.scalar_tensor_tensor(E.tmp4[:, m, :], E.tmp4[:, m, :], E.par[:, Q_RK + m:Q_RK + m + 1], r[:, m, :],
                                         ALU.mult, ALU.mult).then_inc(x_ready, 1)
            for m in range(4):
                dve.wait_ge(done, m + 1)
                dve.tensor_tensor(halves(E.bonus[:, m, :], 2), E.PS[:, 2 * m:2 * m + 2, 0:HALF],
                                  halves(v[:, m, :], 2), ALU.mult)

        @block.tensor
        def _(pe):
            for m in range(4):
                pe.wait_ge(x_ready, m + 1)
                for a in range(2):
                    last = pe.matmul(E.PS[:, 2 * m + a, 0:HALF], E.head_ones[:, :], halves(E.tmp4[:, m, :], 2)[:, a, :],
                                     start=True, stop=True)
                last.then_inc(done, 1)


def recurrence(nc, S, E):
    sweep(nc, S)
    names_a = ["before_ready", "exp_ready", "v_ready", "own_a", "ab_ready", "kr_ready", "products", "x_turned", "pair_copied", "end_ready"]
    names_b = ["f_done", "f_half", "f_ready", "y_half", "sa_done", "sa_ready", "u_done", "y_done", "t1_done", "t1_ready", "x_done", "x_ready", "own_b"]
    with ExitStack() as stack:
        a = {x: stack.enter_context(nc.semaphore("chunk_" + x)) for x in names_a}
        b = {x: stack.enter_context(nc.semaphore("chunk_" + x)) for x in names_b}
        with nc.Fori(0, N_CH) as c:
            _chunk_products(nc, E, c, a, b)
            _chunk_solve(nc, E, c, a, b)
        with nc.Block() as block:
            @block.gpsimd
            def _(pool):
                for s in [*a.values(), *b.values()]:
                    pool.sem_clear(s)


def _heads():
    return [(d, h, (h % 2) * 64, d * 64) for h in range(8) for d in range(2)]


def _by_parity(x):
    return x.rearrange("p (m q) n -> p q m n", q=2)


def _chunk_products(nc, E, c, a, b):
    at = [c * CH, (N_CH - 1 - c) * CH]

    def piece(x, d):
        return x[:, :, bass.ds(at[d], CH)]
    ar, bb, kb, vb = E.ar, E.bb, E.kb, E.vb
    with nc.Block() as block:
        @block.gpsimd
        def _(pool):
            for s in b.values():
                pool.sem_clear(s)
            pool.wait_ge(a["exp_ready"], 5)
            for d in range(2):
                pool.tensor_tensor(ar[:, :, d, 1, :], piece(E.zr[:, 0:4, :], d), E.ep[:, :, d, :],
                                   ALU.mult).then_inc(a["kr_ready"], 1)
            for d in range(2):
                pool.tensor_tensor(kb[:, :, d, :], piece(E.kd[:, d], d), E.en[:, :, d, :],
                                   ALU.mult).then_inc(a["kr_ready"], 1)

        @block.vector
        def _(dve):
            for d in range(2):
                dve.tensor_tensor(E.ex[:, :, d, :], piece(E.cum[d], d), piece(E.ld[d], d),
                                  ALU.subtract).then_inc(a["before_ready"], 1)
            dve.wait_ge(a["exp_ready"], 5)
            for d in range(2):
                dve.tensor_tensor(bb[:, :, d, :], piece(E.ba[d], d), E.en[:, :, d, :], ALU.mult).then_inc(a["ab_ready"], 1)
                dve.tensor_tensor(ar[:, :, d, 0, :], piece(E.kk, d), E.ex[:, :, d, :], ALU.mult).then_inc(a["ab_ready"], 1)
                dve.tensor_copy(E.pend[:, :, d], E.ep[:, :, d, CH - 1 if d == 0 else 0]).then_inc(a["end_ready"], 1)
            own = Chain(dve, a["own_a"])
            dve.wait_ge(a["products"], 1)
            eye = E.eye2[:, :].unsqueeze(1).broadcast_to([P, 8, CH])
            masks = E.pair[:, :, :].rearrange("p r n -> p (r n)").unsqueeze(1).unsqueeze(1).broadcast_to([P, 2, 4, 2 * CH])

            def banks(k):
                return E.PS[:, k:k + 2, :].rearrange("p q (m n) -> p q m n", m=4)

            def both(x):
                return _by_parity(x.rearrange("p h r n -> p h (r n)"))
            m0 = E.level[:, 0, 0, :].unsqueeze(1).broadcast_to([P, 8, CH])
            own.link(dve.tensor_tensor(_by_parity(E.x), E.PS[:, 0:2, 0:4 * CH].rearrange("p q (m n) -> p q m n", m=4),
                                       _by_parity(m0), ALU.mult))
            own.add(dve.tensor_tensor(E.x[:, :, :], eye, E.x[:, :, :], ALU.subtract))
            dve.wait_ge(a["products"], 2)
            own.link(dve.tensor_tensor(both(E.lb), banks(2), masks, ALU.mult))
            m0t = E.level[:, 1, 0, :].unsqueeze(1).broadcast_to([P, 8, CH])
            own.link(dve.tensor_tensor(E.xt[:, :, :], E.lb[:, :, 0, :], m0t, ALU.mult))
            own.add(dve.tensor_tensor(E.xt[:, :, :], eye, E.xt[:, :, :], ALU.subtract))
            dve.wait_ge(a["products"], 3)
            dve.tensor_tensor(both(E.mk), banks(4), masks, ALU.mult)
            for j in range(1, LEVELS):
                mj = E.level[:, 1, j, :].unsqueeze(1).broadcast_to([P, 8, CH])
                dve.tensor_tensor(E.mjt[j - 1], E.lb[:, :, 0, :], mj, ALU.mult)

        @block.scalar
        def _(act):
            for d in range(2):
                act.activation(E.ep[:, :, d, :], piece(E.cum[d], d), ACT.Exp).then_inc(a["exp_ready"], 1)
                act.activation(E.en[:, :, d, :], piece(E.cum[d], d), ACT.Exp, scale=-1.0).then_inc(a["exp_ready"], 1)
            act.wait_ge(a["before_ready"], 2)
            act.activation(E.ex[:, :, :, :], E.ex[:, :, :, :], ACT.Exp).then_inc(a["exp_ready"], 1)
            for d in range(2):
                act.copy(vb[:, :, d, :], piece(E.zr[:, T_V - T_R:T_V - T_R + 4, :], d)).then_inc(a["v_ready"], 1)
            for n, dst in enumerate((E.vtok, E.btok, E.ktok)):
                act.wait_ge(a["x_turned"], n + 1)
                act.copy(dst[:, :], E.PS[:, 6 + n % 2, :]).then_inc(a["pair_copied"], 1)

        @block.tensor
        def _(pe):
            def turn(src, bank):
                for hp in range(4):
                    last = pe.transpose(E.PS[:, bank, hp * P:(hp + 1) * P],
                                        src[:, hp, :, :].rearrange("p d n -> p (d n)"), E.ident[:, :])
                last.then_inc(a["x_turned"], 1)
            pe.wait_ge(a["v_ready"], 2)
            turn(vb, 6)
            pe.wait_ge(a["ab_ready"], 4)
            for d, h, hr, tr in _heads():
                last = pe.matmul(E.PS[tr:tr + CH, h % 2, (h // 2) * CH:(h // 2 + 1) * CH], ar[hr:hr + 64, h // 2, d, 0, :],
                                 bb[hr:hr + 64, h // 2, d, :], start=True, stop=True)
            last.then_inc(a["products"], 1)
            turn(bb, 7)
            pe.wait_ge(a["kr_ready"], 4)
            for bank, src in ((2, bb), (4, kb)):
                for d, h, hr, tr in _heads():
                    last = pe.matmul(E.PS[tr:tr + CH, bank + h % 2, (h // 2) * 2 * CH:(h // 2 + 1) * 2 * CH],
                                     src[hr:hr + 64, h // 2, d, :],
                                     ar[hr:hr + 64, h // 2, d, :, :].rearrange("p r n -> p (r n)"),
                                     start=True, stop=True)
                last.then_inc(a["products"], 1)
            pe.wait_ge(a["pair_copied"], 1)
            turn(kb, 6)


def _chunk_solve(nc, E, c, a, b):
    at = [c * CH, (N_CH - 1 - c) * CH]
    with nc.Block() as block:
        @block.gpsimd
        def _(pool):
            for s in a.values():
                pool.sem_clear(s)

        def by_head(x):
            return x.rearrange("p (h n) -> p h n", h=8)

        @block.tensor
        def _(pe):
            for d, h, hr, tr in _heads():
                pe.matmul(E.PS[tr:tr + CH, 3, h * CH:(h + 1) * CH], E.mk[tr:tr + CH, h, 0, :],
                          E.vtok[tr:tr + CH, h * CH:(h + 1) * CH], start=True, stop=True)
            for d, h, hr, tr in _heads():
                last = pe.matmul(E.PS[tr:tr + CH, 4 + h % 2, (h // 2) * CH:(h // 2 + 1) * CH],
                                 E.ar[hr:hr + 64, h // 2, d, 0, :], E.state[hr:hr + 64, h // 2, d, :],
                                 start=True, stop=True)
            last.then_inc(b["f_done"], 1)
            for j in range(1, LEVELS):
                if j > 1:
                    pe.wait_ge(b["x_ready"], 2 * (j - 1))
                for d, h, hr, tr in _heads():
                    last = pe.matmul(E.PS[tr:tr + CH, 0, h * CH:(h + 1) * CH], E.mjt[j - 1][tr:tr + CH, h, :],
                                     E.x[tr:tr + CH, h, :], start=True, stop=True)
                last.then_inc(b["t1_done"], 1)
                pe.wait_ge(b["t1_ready"], j)
                for d, h, hr, tr in _heads():
                    last = pe.matmul(E.PS[tr:tr + CH, 1, h * CH:(h + 1) * CH], E.t1[tr:tr + CH, h, :],
                                     E.xt[tr:tr + CH, h, :], start=True, stop=True)
                last.then_inc(b["x_done"], 1)
                if j < LEVELS - 1:
                    for d, h, hr, tr in _heads():
                        last = pe.matmul(E.PS[tr:tr + CH, 2, h * CH:(h + 1) * CH], E.xt[tr:tr + CH, h, :],
                                         E.t1[tr:tr + CH, h, :], start=True, stop=True)
                    last.then_inc(b["x_done"], 1)
            pe.wait_ge(b["f_ready"], 1)
            pe.wait_ge(b["x_ready"], 2 * (LEVELS - 1) - 1)
            for d, h, hr, tr in _heads():
                last = pe.matmul(E.PS[tr:tr + CH, 6, h * CH:(h + 1) * CH], E.xt[tr:tr + CH, h, :],
                                 E.f[tr:tr + CH, h, :], start=True, stop=True)
            last.then_inc(b["sa_done"], 1)
            pe.wait_ge(b["sa_ready"], 1)
            for d, h, hr, tr in _heads():
                dst = E.PS[hr:hr + 64, d, (h // 2) * CH:(h // 2 + 1) * CH]
                pe.matmul(dst, E.ktok[tr:tr + CH, h * CH:(h + 1) * CH], E.vtok[tr:tr + CH, h * CH:(h + 1) * CH],
                          start=True, stop=False)
                last = pe.matmul(dst, E.btok[tr:tr + CH, h * CH:(h + 1) * CH], E.sa[tr:tr + CH, h, :],
                                 start=False, stop=True)
            last.then_inc(b["u_done"], 1)
            for d, h, hr, tr in _heads():
                cols = ((h // 2) * 2 + d) * CH
                pe.matmul(E.PS[hr:hr + 64, 7, cols:cols + CH], E.state[hr:hr + 64, h // 2, d, :],
                          E.ar[hr:hr + 64, h // 2, d, 1, :], start=True, stop=True)
            for d, h, hr, tr in _heads():
                dst = E.PS[hr:hr + 64, 2 + d, (h // 2) * CH:(h // 2 + 1) * CH]
                pe.matmul(dst, E.vtok[tr:tr + CH, h * CH:(h + 1) * CH], E.mk[tr:tr + CH, h, 1, :], start=True, stop=False)
                last = pe.matmul(dst, E.sa[tr:tr + CH, h, :], E.lb[tr:tr + CH, h, 1, :], start=False, stop=True)
            last.then_inc(b["y_done"], 1)

        @block.scalar
        def _(act):
            act.wait_ge(b["f_done"], 1)
            act.copy(E.f[:, :, :], by_head(E.PS[:, 3, :])).then_inc(b["f_half"], 1)
            for j in range(1, LEVELS):
                act.wait_ge(b["t1_done"], j)
                act.copy(E.t1[:, :, :], by_head(E.PS[:, 0, :])).then_inc(b["t1_ready"], 1)
            act.wait_ge(b["sa_done"], 1)
            act.mul(E.sa[:, :, :], by_head(E.PS[:, 6, :]), -1.0).then_inc(b["sa_ready"], 1)
            act.wait_ge(b["y_done"], 1)
            y = E.PS[:, 7, :].rearrange("p (m d n) -> p m d n", m=4, d=2)
            for d in range(2):
                act.copy(E.ba[d][:, :, bass.ds(at[d], CH)], y[:, :, d, :]).then_inc(b["y_half"], 1)

        @block.vector
        def _(dve):
            dve.wait_ge(b["f_half"], 1)
            dve.tensor_tensor(_by_parity(E.f), _by_parity(E.f),
                              E.PS[:, 4:6, 0:4 * CH].rearrange("p q (m n) -> p q m n", m=4), ALU.add).then_inc(b["f_ready"], 1)
            for j in range(1, LEVELS):
                last_level = j == LEVELS - 1
                dve.wait_ge(b["x_done"], 2 * j - (1 if last_level else 0))
                dve.tensor_tensor(E.xt[:, :, :], E.xt[:, :, :], by_head(E.PS[:, 1, :]), ALU.subtract).then_inc(b["x_ready"], 1)
                if not last_level:
                    dve.tensor_tensor(E.x[:, :, :], E.x[:, :, :], by_head(E.PS[:, 2, :]), ALU.subtract).then_inc(b["x_ready"], 1)
            dve.wait_ge(b["y_done"], 1)
            own = Chain(dve, b["own_b"])
            st = E.state[:, :, :, :]
            own.link(dve.tensor_tensor(st, st, E.PS[:, 0:2, 0:4 * CH].rearrange("p d (m n) -> p m d n", m=4), ALU.add))
            dve.tensor_tensor(st, st, E.pend[:, :, :].unsqueeze(3).broadcast_to([P, 4, 2, CH]), ALU.mult)
            for d in range(2):
                dve.wait_ge(b["y_half"], d + 1)
                y = E.ba[d][:, :, bass.ds(at[d], CH)]
                dve.tensor_tensor(y, y, E.PS[:, 2 + d, 0:4 * CH].rearrange("p (m n) -> p m n", m=4), ALU.add)


def head_norm(nc, S, E):
    S.open()
    y_ready = S.take("y_ready")
    mean_done = S.take("mean_done")
    xc_ready = S.take("xc_ready")
    sq_ready = S.take("sq_ready")
    var_done = S.take("var_done")
    var_ready = S.take("var_ready")
    std_ready = S.take("std_ready")
    inv = S.take("inverse_ready")
    own = S.take("norm_steps")
    g_in = S.take("g_in_ready")
    g_done = S.take("g_done")
    biased = S.take("biased")
    yf, yb = E.ba
    out = E.y[:, 4:8, :]
    x = E.tmp8a
    sq = E.tmp8b
    with nc.Block() as block:
        @block.gpsimd
        def _(pool):
            S.clear_old(pool)
            for m in range(4):
                pool.tensor_tensor(x[:, m, :], yf[:, m, 0:L], yb[:, m, 0:L], ALU.add).then_inc(y_ready, 1)

        @block.tensor
        def _(pe):
            for m in range(4):
                pe.wait_ge(y_ready, m + 1)
                for a in range(2):
                    last = pe.matmul(E.PS[:, 2 * m + a, 0:HALF], E.head_mean[:, :], halves(x[:, m, :], 2)[:, a, :],
                                     start=True, stop=True)
                last.then_inc(mean_done, 1)
            for m in range(4):
                pe.wait_ge(sq_ready, m + 1)
                for a in range(2):
                    last = pe.matmul(E.PS[:, 2 * m + a, 0:HALF], E.head_mean[:, :], halves(sq[:, m, :], 2)[:, a, :],
                                     start=True, stop=True)
                last.then_inc(var_done, 1)
            pe.wait_ge(g_in, 1)
            for m in range(4):
                pe.wait_ge(var_ready, m + 1)
                for a in range(2):
                    last = pe.matmul(E.PS[:, 2 * m + a, 0:HALF], E.g2[:, m * P:(m + 1) * P],
                                     halves(E.lora[:, 1, :], 2)[:, a, :], start=True, stop=True)
                last.then_inc(g_done, 1)

        @block.scalar
        def _(act):
            act.activation(E.lora[:, 1, :], E.zs[T_GD], ACT.Sigmoid).then_inc(g_in, 1)
            for m in range(4):
                act.wait_ge(xc_ready, m + 1)
                act.activation(sq[:, m, :], x[:, m, :], ACT.Square).then_inc(sq_ready, 1)
            act.wait_ge(var_ready, 4)
            act.activation(sq, sq, ACT.Sqrt).then_inc(std_ready, 1)

        @block.vector
        def _(dve):
            c = Chain(dve, own)
            for m in range(4):
                dve.wait_ge(mean_done, m + 1)
                dve.tensor_tensor(halves(x[:, m, :], 2), halves(x[:, m, :], 2), E.PS[:, 2 * m:2 * m + 2, 0:HALF],
                                  ALU.subtract).then_inc(xc_ready, 1)
            for m in range(4):
                dve.wait_ge(var_done, m + 1)
                dve.tensor_scalar(halves(sq[:, m, :], 2), E.PS[:, 2 * m:2 * m + 2, 0:HALF], 64e-5, None,
                                  ALU.add).then_inc(var_ready, 1)
            dve.wait_ge(std_ready, 1)
            dve.reciprocal(sq, sq).then_inc(inv, 1)
            dve.wait_ge(inv, 1)
            for m in range(4):
                c.link(dve.scalar_tensor_tensor(x[:, m, :], x[:, m, :], E.par[:, Q_GG + m:Q_GG + m + 1], sq[:, m, :],
                                                ALU.mult, ALU.mult))
                c.link(dve.scalar_tensor_tensor(x[:, m, :], x[:, m, :], E.par[:, Q_GB + m:Q_GB + m + 1],
                                                E.bonus[:, m, :], ALU.add, ALU.add))
                dve.wait_ge(g_done, m + 1)
                dve.tensor_tensor(halves(out[:, m, :], 2), halves(x[:, m, :], 2), E.PS[:, 2 * m:2 * m + 2, 0:HALF],
                                  ALU.mult)


def route(nc, S, E):
    S.open()
    loaded = S.take("w_loaded")
    blank = S.take("blank")
    done = S.take("logits_done")
    own = S.take("route_steps")
    e_in = S.take("exp_in")
    e_out = S.take("exp_out")
    g_ready = S.take("gates_ready")
    turned = S.take("turned")
    copied = S.take("copied")
    stored = S.take("stored")
    nt = len(TOK)
    R = E.router
    wr = R[:, 0:288].rearrange("p (k m) -> p k m", k=KT)
    bias = R[:, 288:324]
    at = [324]

    def buf(*shape):
        n = int(np.prod(shape))
        x = R[:, at[0]:at[0] + n]
        at[0] += n
        if len(shape) == 2:
            return x.rearrange("p (a b) -> p a b", a=shape[0])
        return x
    lg = buf(nt, 36)
    gl, gx, gs, gc = (buf(nt, 4) for _ in range(4))
    el, ex, s1, s2, cum = (buf(nt, 32) for _ in range(5))
    gm, gsum, m1, m2, z = (buf(nt) for _ in range(5))
    keep_g, keep_e = buf(20), buf(160)

    def over(x, n):
        return x.unsqueeze(2).broadcast_to([P, nt, n])

    def flat(x):
        return x.rearrange("p a b -> p (a b)")
    with nc.Block() as block:
        @block.gpsimd
        def _(pool):
            S.clear_old(pool)
            pool.memset(lg, 0.0).then_inc(blank, 1)

        @block.sync
        def _(sp):
            A, li = E.A, E.li
            sp.dma_start(wr[:, :, 0:4], A["moe_w_group_2"][li].rearrange("(k p) m -> p k m", p=P)).then_inc(loaded, 16)
            sp.dma_start(wr[:, :, 4:36], A["moe_w_expert_2"][li].rearrange("(k p) m -> p k m", p=P)).then_inc(loaded, 16)
            sp.dma_start(bias[:, 0:4], A["moe_b_group_2"][li].partition_broadcast(P)).then_inc(loaded, 16)
            sp.dma_start(bias[:, 4:36], A["moe_b_expert_2"][li].partition_broadcast(P)).then_inc(loaded, 16)
            sp.dma_start(keep_g, A["keep_group"]).then_inc(loaded, 16)
            sp.dma_start(keep_e, A["keep_expert"]).then_inc(loaded, 16)
            sp.wait_ge(copied, 2)
            sp.dma_start(E.gates_dram, E.gT[:, :]).then_inc(stored, 16)
            sp.wait_ge(stored, 16)

        @block.tensor
        def _(pe):
            pe.wait_ge(loaded, 96)
            for t, (t0, rows) in enumerate(TOK):
                for k in range(KT):
                    last = pe.matmul(E.PS[0:rows, 0, t * 36:(t + 1) * 36], E.h[:, k, t0:t0 + rows], wr[:, k, :],
                                     start=(k == 0), stop=(k == KT - 1))
            last.then_inc(done, 1)
            pe.wait_ge(g_ready, 1)
            for t, (t0, rows) in enumerate(TOK):
                last = pe.transpose(E.PS[0:32, 1 + t // 4, (t % 4) * P:(t % 4) * P + rows], ex[0:rows, t, :],
                                    E.ident[0:rows, 0:rows])
            last.then_inc(turned, 1)

        @block.scalar
        def _(act):
            act.wait_ge(e_in, 1)
            act.activation(gx, gx, ACT.Exp).then_inc(e_out, 1)
            act.wait_ge(e_in, 2)
            act.activation(ex, ex, ACT.Exp).then_inc(e_out, 1)
            act.wait_ge(e_in, 3)
            act.activation(m2, m2, ACT.Exp).then_inc(e_out, 1)
            act.wait_ge(turned, 1)
            act.copy(E.gT[:, 0:512], E.PS[0:32, 1, :]).then_inc(copied, 1)
            act.copy(E.gT[:, 512:L], E.PS[0:32, 2, 0:N_META]).then_inc(copied, 1)

        @block.vector
        def _(dve):
            c = Chain(dve, own)
            tt, ts, stt = dve.tensor_tensor, dve.tensor_scalar, dve.scalar_tensor_tensor
            dve.wait_ge(blank, 1)
            dve.wait_ge(loaded, 96)
            dve.wait_ge(done, 1)
            for t, (_, rows) in enumerate(TOK):
                c.add(tt(lg[0:rows, t, :], E.PS[0:rows, 0, t * 36:(t + 1) * 36], bias[0:rows, :], ALU.add))
            c.wait()
            c.link(dve.tensor_copy(gl, lg[:, :, 0:4]))
            c.link(dve.tensor_reduce(gm, gl, AX, ALU.max))
            tt(gx, gl, over(gm, 4), ALU.subtract).then_inc(e_in, 1)
            c.link(tt(gs, gl, over(gm, 4), ALU.is_equal))
            c.link(dve.tensor_tensor_scan(flat(gc), keep_g, flat(gs), 0.0, ALU.mult, ALU.add))
            c.link(stt(gs, gc, 1.0, gs, ALU.is_le, ALU.mult))
            c.link(ts(gs, gs, BIG, -BIG, ALU.mult, ALU.add))
            c.link(tt(el.rearrange("p a (g n) -> p a g n", g=4), lg[:, :, 4:36].rearrange("p a (g n) -> p a g n", g=4),
                      gs.unsqueeze(3).broadcast_to([P, nt, 4, 8]), ALU.add))
            c.link(dve.tensor_reduce(m1, el, AX, ALU.max))
            tt(ex, el, over(m1, 32), ALU.subtract).then_inc(e_in, 1)

            def first_of(sel, top):
                c.link(tt(sel, el, over(top, 32), ALU.is_equal))
                c.link(dve.tensor_tensor_scan(flat(cum), keep_e, flat(sel), 0.0, ALU.mult, ALU.add))
                c.link(stt(sel, cum, 1.0, sel, ALU.is_le, ALU.mult))
            first_of(s1, m1)
            c.link(stt(el, s1, -3 * BIG, el, ALU.mult, ALU.add))
            c.link(dve.tensor_reduce(m2, el, AX, ALU.max))
            first_of(s2, m2)
            tt(m2, m2, m1, ALU.subtract).then_inc(e_in, 1)
            dve.wait_ge(e_out, 2)
            c.add(dve.tensor_reduce(gsum, gx, AX, ALU.add))
            c.link(dve.tensor_reduce(z, ex, AX, ALU.add))
            c.link(tt(z, z, gsum, ALU.mult))
            c.link(dve.reciprocal(z, z))
            dve.wait_ge(e_out, 3)
            c.link(tt(s2, s2, over(m2, 32), ALU.mult))
            c.link(tt(s1, s1, s2, ALU.add))
            tt(ex, s1, over(z, 32), ALU.mult).then_inc(g_ready, 1)


def scale_residual(nc, S, E):
    S.open()
    with nc.Block() as block:
        @block.gpsimd
        def _(pool):
            S.clear_old(pool)

        @block.vector
        def _(dve):
            dve.tensor_scalar(E.h1[:, :, :], E.h[:, :, :], ALPHA, None, ALU.mult)


def experts(nc, S, E):
    S.open()
    loaded = [S.take("w_loaded_0"), S.take("w_loaded_1")]
    read_in = S.take("w13_read")
    read_out = S.take("w2_read")
    done = S.take("tile_done")
    act_out = S.take("silu_out")
    dve_out = S.take("dve_out")
    own = S.take("hidden_steps")
    A, li = E.A, E.li
    w1 = A["moe_w1_2"][li].rearrange("e (k p) m -> e p k m", p=P)
    w3 = A["moe_w3_2"][li].rearrange("e (k p) m -> e p k m", p=P)
    w2 = A["moe_w2_2"][li].rearrange("e (k p) m -> e p k m", p=P)
    with nc.Block() as block:
        @block.gpsimd
        def _(pool):
            S.clear_old(pool)

        @block.sync
        def _(sp):
            def load(j, slot, turn):
                sp.wait_ge(dve_out, j * 10 + 10)
                for dst, src in ((E.w1s[:, slot], w1[j]), (E.w3s[:, slot], w3[j]), (E.w2s[:, slot], w2[j]),
                                 (E.gate_row[:, slot, :], E.gates_dram[j].partition_broadcast(P))):
                    sp.dma_start(dst, src).then_inc(loaded[slot], 16)
            in_pairs(sp, N_EXP, load)

        @block.tensor
        def _(pe):
            def body(j, slot, turn):
                def tile(q, w, rhs, nk):
                    s = 2 * (q % 4)
                    for k in range(nk):
                        for a in range(2):
                            last = pe.matmul(E.PS[:, s + a, 0:HALF], w(k), halves(rhs(k), 2)[:, a, :],
                                             start=(k == 0), stop=(k == nk - 1))
                    last.then_inc(done, 1)
                pe.wait_ge(loaded[slot], turn * 64 + 64)
                for m in range(2):
                    for n, w in enumerate((E.w1s, E.w3s)):
                        pe.wait_ge(dve_out, j * 10 + (17 + 2 * m + n))
                        tile(2 * m + n, lambda k: w[:, slot, k, m * P:(m + 1) * P], lambda k: E.h[:, k, :], KT)
                pe.wait_ge(dve_out, j * 10 + 22)
                for m in range(KT):
                    if m >= 4:
                        pe.wait_ge(dve_out, j * 10 + (23 + m - 4))
                    tile(4 + m, lambda k: E.w2s[:, slot, k, m * P:(m + 1) * P], lambda k: E.hid[:, k, :], 2)
            in_pairs(pe, N_EXP, body)

        @block.scalar
        def _(act):
            def body(j, slot, turn):
                for m in range(2):
                    act.wait_ge(done, j * 12 + (2 * m + 1))
                    act.activation(halves(E.silu[:, m, :], 2), E.PS[:, 4 * m:4 * m + 2, 0:HALF],
                                   ACT.Silu).then_inc(act_out, 1)
            in_pairs(act, N_EXP, body)

        @block.vector
        def _(dve):
            dve.sem_inc(dve_out, 20)

            def body(j, slot, turn):
                dve.wait_ge(loaded[slot], turn * 64 + 64)
                for m in range(2):
                    dve.wait_ge(act_out, j * 2 + (m + 1))
                    dve.tensor_tensor(E.silu[:, m, :], E.silu[:, m, :], E.gate_row[:, slot, :],
                                      ALU.mult).then_inc(own, 1)
                    dve.wait_ge(done, j * 12 + (2 * m + 2))
                    dve.wait_ge(own, j * 2 + (m + 1))
                    dve.tensor_tensor(halves(E.hid[:, m, :], 2), halves(E.silu[:, m, :], 2),
                                      E.PS[:, 4 * m + 2:4 * m + 4, 0:HALF], ALU.mult).then_inc(dve_out, 1)
                for m in range(KT):
                    dve.wait_ge(done, j * 12 + (5 + m))
                    s = 2 * (m % 4)
                    dve.tensor_tensor(halves(E.h1[:, m, :], 2), halves(E.h1[:, m, :], 2), E.PS[:, s:s + 2, 0:HALF],
                                      ALU.add).then_inc(dve_out, 1)
            in_pairs(dve, N_EXP, body)


def store_output(nc, S, E):
    S.open()
    turned = S.take("turned")
    copied = S.take("copied")
    stored = S.take("output_stored")
    out = E.out[0].rearrange("(t p) d -> t p d", p=P)
    with nc.Block() as block:
        @block.gpsimd
        def _(pool):
            S.clear_old(pool)

        @block.tensor
        def _(pe):
            for t in range(4):
                if t >= 2:
                    pe.wait_ge(copied, t - 1)
                for k in range(KT):
                    last = pe.transpose(E.PS[:, 2 * (t % 2) + k // 4, (k % 4) * P:(k % 4 + 1) * P],
                                        E.h[:, k, N_META + t * P:N_META + (t + 1) * P], E.ident[:, :])
                last.then_inc(turned, 1)

        @block.scalar
        def _(act):
            for t in range(4):
                act.wait_ge(turned, t + 1)
                act.copy(E.outbuf[:, t, :].rearrange("p (b n) -> p b n", b=2),
                         E.PS[:, 2 * (t % 2):2 * (t % 2) + 2, :]).then_inc(copied, 1)

        @block.sync
        def _(sp):
            for t in range(4):
                sp.wait_ge(copied, t + 1)
                sp.dma_start(out[t], E.outbuf[:, t, :]).then_inc(stored, 16)
            sp.wait_ge(stored, 64)


def second_block(nc, S, E, scope):
    A = E.A

    def sb(name, shape, dt=F32):
        return scope.enter_context(nc.sbuf_tensor(name, shape, dt))
    E.zt = sb("zt", [P, 19 * LP])
    E.zs = [E.zt[:, i * LP:i * LP + L] for i in range(19)]
    E.zr = E.zt[:, T_R * LP:(T_R + 12) * LP].rearrange("p (a n) -> p a n", a=12)
    E.kdbuf = sb("kd", [P, WIDE])
    E.kd = E.kdbuf[:, :].rearrange("p (d m n) -> p d m n", d=2, m=4)
    E.vfirst = sb("vfirst", [P, 4, L])
    E.head_ones = sb("head_ones", [P, P])
    E.head_mean = sb("head_mean", [P, P])
    E.level = sb("level", [P, 2, LEVELS, CH])
    E.pair = sb("pair", [P, 2, CH])
    E.eye2 = sb("eye2", [P, CH])
    E.total = sb("total", [P, 4 * N_CH])
    E.state = sb("state", [P, 4, 2, CH])
    E.pend = sb("pend", [P, 4, 2])
    E.invf = sb("invf", [P, 1])
    E.mx2 = sb("mx2", [P, 20])
    E.sums2 = sb("sums2", [P, 20])
    E.ovar = sb("ovar", [P, 20])

    def four(x, i):
        return x[:, i * 4 * LP:(i + 1) * 4 * LP].rearrange("p (m n) -> p m n", m=4)
    E.cum = [four(E.n_flat, 0), four(E.n_flat, 1)]
    E.ld = [four(E.h1_flat, 0), four(E.h1_flat, 1)]
    E.ba = [four(E.norm_flat, 0), four(E.norm_flat, 1)]
    E.pos_int = E.n_flat[:, 0:SEQ].bitcast(I32)
    E.shifted = E.norm_flat[:, 0:4 * L].rearrange("p (a n) -> p a n", a=4)
    E.qn, E.kn = E.h1[:, 0:4, :], E.h1[:, 4:8, :]
    E.qp = E.norm_flat[:, 2560:2560 + 2 * L].rearrange("p (a n) -> p a n", a=2)
    E.vn2 = E.norm_flat[:, 0:2560].rearrange("p (t n) -> p t n", t=5)
    E.prob2 = E.n_flat[:, 0:2 * L].rearrange("p (a n) -> p a n", a=2)
    E.probT2 = E.n_flat[:, 2 * L:2 * L + 2 * 5 * P].rearrange("p (a b n) -> p a b n", a=2, b=5)
    flat = E.wring[:, :, :, :].rearrange("p s k m -> p (s k m)")
    E.on = flat[:, 0:2560].rearrange("p (t n) -> p t n", t=5)
    E.osq = E.norm_flat[:, 0:2560].rearrange("p (t n) -> p t n", t=5)
    E.onorm = flat[:, 2560:3072]
    tmp = E.y[:, 4:8, :].rearrange("p m n -> p (m n)")
    E.tmp4 = E.y[:, 4:8, :]
    E.tmp4b = E.rotbuf[:, :, :, :].rearrange("p a b n -> p (a b) n")
    E.lora = sb("lora", [P, 2, L])
    E.low = E.lora[0:32, 0, :]
    E.kk = E.zt[:, 0:4 * LP].rearrange("p (m n) -> p m n", m=4)
    E.tmp8a = E.h1[:, 0:4, :]
    E.tmp8b = E.h1[:, 4:8, :]

    rot = E.rotbuf[:, :, :, :].rearrange("p a b n -> p (a b n)")
    spare = [(flat, 512, 4096), (rot, 0, 2112), (tmp, 0, 2112), (E.zt, T_WD * LP, T_GD * LP), (E.stat, 0, L),
             (E.lora[:, 0, :], 0, L)]

    def cut(n, name):
        for i, (x, a, z) in enumerate(spare):
            if z - a >= n:
                spare[i] = (x, a + n, z)
                return x[:, a:a + n]
        return sb(name, [P, n])[:, :]
    N = 8 * CH
    E.ex, E.ep, E.en, E.bb, E.kb, E.vb = (cut(N, x).rearrange("p (m d n) -> p m d n", m=4, d=2)
                                          for x in ("ex", "ep", "en", "bb", "kb", "vb"))
    E.ar = cut(2 * N, "ar").rearrange("p (m d r n) -> p m d r n", m=4, d=2, r=2)
    E.lb, E.mk = (cut(2 * N, x).rearrange("p (h r n) -> p h r n", h=8, r=2) for x in ("lb", "mk"))
    E.vtok, E.btok, E.ktok = (cut(N, x) for x in ("vtok", "btok", "ktok"))
    E.x, E.xt = (cut(N, x).rearrange("p (h n) -> p h n", h=8) for x in ("x", "xt"))
    E.mjt = [cut(N, f"mjt{j}").rearrange("p (h n) -> p h n", h=8) for j in range(1, LEVELS)]
    E.t1 = E.ex.rearrange("p m d n -> p (m d n)").rearrange("p (h n) -> p h n", h=8)
    E.f = E.ep.rearrange("p m d n -> p (m d n)").rearrange("p (h n) -> p h n", h=8)
    E.sa = E.en.rearrange("p m d n -> p (m d n)").rearrange("p (h n) -> p h n", h=8)
    E.keep = flat[:, 2176:2176 + LP]
    E.bonus = E.zr[:, T_K - T_R:T_K - T_R + 4, 0:L]

    E.w1s, E.w3s = (E.zt[:, i * 4096:(i + 1) * 4096].rearrange("p (s k m) -> p s k m", s=2, k=KT) for i in range(2))
    E.w2s = flat.rearrange("p (s k m) -> p s k m", s=2, k=2)
    E.router = E.norm_flat
    E.gT = E.n_flat[0:32, 0:L]
    E.silu = E.n[:, 0:2, :]
    E.hid = E.n[:, 2:4, :]
    E.gate_row = E.n[:, 4:6, :]
    E.outbuf = E.n_flat[:, 0:4096].rearrange("p (t d) -> p t d", t=4)
    E.gates_dram = nc.dram_tensor("gates", (N_EXP, L), F32, kind="Internal").ap()

    meta = E.norm_flat[0:N_META, 0:D]
    load_constants(nc, S, [(E.head_ones[:, :], A["head_ones"]), (E.head_mean[:, :], A["head_mean"]),
                           (E.level[:, :, :, :], A["level_masks"]), (E.pair[:, :, :], A["pair_masks"]),
                           (E.eye2[:, :], A["eye2"]), (meta, A["meta_tokens_2"])])
    transpose_rows(nc, S, E, lambda k: E.h1[:, k, 0:N_META], KT, parts=[(meta, 0, N_META)])
    norm(nc, S, E, lambda k: E.h1[:, k, :], lambda k: E.h[:, k, :], KT, 2, HALF, lambda k: E.par[:, 8 + k:9 + k], 1e-5,
         b=lambda k: E.par[:, 16 + k:17 + k])
    angles(nc, S, E)
    clear_vfirst(nc, S, E)
    sweep(nc, S)
    with nc.Fori(0, E.depth) as li:
        E.li = li

        def rows(name, n, *ix):
            x = A[name][li]
            for i in ix:
                x = x[i]
            return x.rearrange("(t p) -> t p", p=P)[0:n]

        def par(r):
            return lambda k: E.par[:, r + k:r + k + 1]
        load_params(nc, S, E, [
            (Q_QN, 2, rows("mla_q_norm_2", 2), 0, P), (Q_KVN, 1, rows("mla_kv_norm_2", 1), 0, P),
            (Q_MP, 15, rows("rwkv_mu_prev_2", 15), 0, P), (Q_MN, 15, rows("rwkv_mu_next_2", 15), 0, P),
            (Q_W0, 8, A["rwkv_w0_2"][li].rearrange("d (t p) -> (d t) p", p=P), 0, P),
            (Q_A0, 8, A["rwkv_a0_2"][li].rearrange("d (t p) -> (d t) p", p=P), 0, P),
            (Q_KK, 4, rows("rwkv_k_k_2", 4), 0, P), (Q_KA, 4, rows("rwkv_k_a_2", 4), 0, P),
            (Q_RK, 4, A["rwkv_r_k_2"][li].rearrange("(t h) n -> t (h n)", h=2), 0, P),
            (Q_GG, 4, rows("rwkv_gn_g_2", 4), 0, P), (Q_GB, 4, rows("rwkv_gn_b_2", 4), 0, P),
            (Q_V0, 4, A["rwkv_v0_2"][0].rearrange("(t p) -> t p", p=P), 0, P),
            (Q_L1G, 8, rows("ln1_g_2", 8), 0, P), (Q_L1B, 8, rows("ln1_b_2", 8), 0, P),
            (Q_L2G, 8, rows("ln2_g_2", 8), 0, P), (Q_L2B, 8, rows("ln2_b_2", 8), 0, P),
            (Q_FIRST, 1, A["is_first"][li].unsqueeze(0), 0, P)])
        project_tail(nc, S, E)
        w_in = A["w_in_2"][li].rearrange("(k p) m -> p k m", p=P)
        zall = E.zt[:, :].rearrange("p (a n) -> p a n", n=LP)

        def to_z(eng, j, t, psum):
            q = j * 2 + (t + T_R)
            return eng.activation(zall[:, bass.ds(q, 1), 0:L].rearrange("p o (a n) -> p (o a) n", a=2), psum, ACT.Identity)
        project(nc, S, E, lambda j: w_in[:, :, bass.ds(j * 256 + 448, 256)], lambda k: E.h[:, k, :], KT, 7, 2, HALF, to_z)
        norm(nc, S, E, lambda k: E.zs[T_CQ + k], lambda k: E.n[:, k, :], 2, 2, HALF, par(Q_QN), 1e-6)
        norm(nc, S, E, lambda k: E.zs[T_CKV], lambda k: E.n[:, 2, :], 1, 2, HALF, par(Q_KVN), 1e-6)
        mla_project(nc, S, E)
        rotate(nc, S, E, [E.qp[:, 0, :], E.qp[:, 1, :], E.zs[T_KPE]], L, 2)
        mla_attend(nc, S, E)
        mla_out(nc, S, E)
        shift(nc, S, E)
        load_constants(nc, S, [*lora_loads(E), (E.keep, A["keep"])])
        value_mix(nc, S, E)
        removal_keys(nc, S, E)
        rates(nc, S, E, 0)
        rates(nc, S, E, 1)
        bonus(nc, S, E)
        recurrence(nc, S, E)
        head_norm(nc, S, E)
        w_out = A["w_out_2"][li].rearrange("(k p) m -> p k m", p=P)

        def add_h(eng, j, t, psum):
            q = j * 2 + t

            def tile(x):
                return x[:, bass.ds(q, 1), :].rearrange("p o (a n) -> p (o a) n", a=2)
            return eng.scalar_tensor_tensor(tile(E.h1), tile(E.h), ALPHA, psum, ALU.mult, ALU.add)
        project(nc, S, E, lambda j: w_out[:, :, bass.ds(j * 256, 256)], lambda k: E.y[:, k, :], KT, KT // 2,
                2, HALF, add_h, on="vector")
        norm(nc, S, E, lambda k: E.h1[:, k, :], lambda k: E.h[:, k, :], KT, 2, HALF, par(Q_L1G), 1e-5, b=par(Q_L1B))
        route(nc, S, E)
        scale_residual(nc, S, E)
        experts(nc, S, E)
        norm(nc, S, E, lambda k: E.h1[:, k, :], lambda k: E.h[:, k, :], KT, 2, HALF, par(Q_L2G), 1e-5, b=par(Q_L2B))
        sweep(nc, S)
    store_output(nc, S, E)


def clear_vfirst(nc, S, E):
    S.open()
    with nc.Block() as block:
        @block.gpsimd
        def _(pool):
            S.clear_old(pool)
            pool.memset(E.vfirst[:, :, :], 0.0)


def program(nc, A, out):
    E = Env()
    E.A, E.out = A, out
    E.depth = DEPTH
    S = Sems(nc)
    with ExitStack() as ctx:
        def sb(name, shape, dt=F32):
            return ctx.enter_context(nc.sbuf_tensor(name, shape, dt))
        E.PS = ctx.enter_context(nc.psum_tensor("PS", [P, 8, 512], F32))
        E.ident = sb("ident", [P, P])
        E.ones = sb("ones", [P, P])
        E.rot = sb("rot", [P, P])
        E.cos = sb("cos", [P, L])
        E.sin = sb("sin", [P, L])
        E.praw = sb("praw", [P, P])
        E.par = sb("par", [P, P])
        E.stat = sb("stat", [P, L])
        E.rotbuf = sb("rotbuf", [P, 2, 2, L])
        E.h = sb("h", [P, KT, L])
        E.h1_flat = sb("h1", [P, WIDE])
        E.n_flat = sb("n", [P, WIDE])
        E.norm_flat = sb("normbuf", [P, WIDE])
        E.h1, E.n, E.normbuf = (x[:, 0:KT * L].rearrange("p (k n) -> p k n", k=KT)
                                for x in (E.h1_flat, E.n_flat, E.norm_flat))
        E.y = sb("y", [P, KT, L])
        E.wring = sb("wring", [P, 2, KT, 256])
        load_constants(nc, S, [(E.ident[:, :], A["ident"]), (E.ones[:, :], A["ones"]), (E.rot[:, :], A["rot"])])
        with ExitStack() as scope:
            first_block(nc, S, E, scope)
        with ExitStack() as scope:
            second_block(nc, S, E, scope)
        sweep(nc, S)


def shape_constants():
    f = np.float32
    rot = np.zeros((P, P), f)
    for m in range(P):
        if m % 64 < 32:
            rot[m + 32, m] = -1.0
        else:
            rot[m - 32, m] = 1.0
    half = 32
    inv = (f(10000.0) ** (-np.arange(half, dtype=f) / f(half))).astype(f)
    ang = (np.arange(SEQ, dtype=f)[None, :] * inv[:, None]).astype(f)
    t = np.arange(SEQ)
    cnt = np.zeros((P, 2, SEQ), f)
    for g, win in enumerate((2, 4, 8, 16)):
        cnt[(g % 2) * 64:(g % 2) * 64 + 64, g // 2] = 1.0 / np.minimum(t + 1, win)
    inv2 = (f(10000.0) ** (-np.arange(0, 64, 2, dtype=f) / f(64))).astype(f)
    s_, t_ = np.arange(CH)[:, None], np.arange(CH)[None, :]
    strict = (t_ < s_).astype(f)
    level = np.zeros((P, 2, LEVELS, CH), f)
    for j in range(LEVELS):
        b = 1 << j
        m = ((s_ // (2 * b) == t_ // (2 * b)) & (s_ // b > t_ // b)).astype(f)
        level[:CH, 0, j], level[CH:, 0, j] = m, m.T
        level[:CH, 1, j], level[CH:, 1, j] = m.T, m
    pair = np.zeros((P, 2, CH), f)
    pair[:CH, 0], pair[CH:, 0] = strict.T, strict
    pair[:CH, 1], pair[CH:, 1] = strict.T + np.eye(CH, dtype=f), strict + np.eye(CH, dtype=f)
    keep = np.ones((P, LP), f)
    keep[:, ::CH] = 0.0
    keep_group = np.tile((np.arange(20) % 4 != 0).astype(f), (P, 1))
    keep_expert = np.tile((np.arange(160) % 32 != 0).astype(f), (P, 1))
    heads = np.zeros((P, P), f)
    heads[:64, :64] = heads[64:, 64:] = 1.0
    return {
        "ident": np.eye(P, dtype=f), "ones": np.ones((P, P), f), "rot": rot,
        "cos1": np.tile(np.cos(ang), (4, 1)).astype(f), "sin1": np.tile(np.sin(ang), (4, 1)).astype(f),
        "invcnt": cnt, "onesrow": np.ones((P, SEQ), f),
        "inv_freq": np.tile(inv2, 4)[:, None].copy(), "meta_pos": np.tile(np.arange(N_META, dtype=f), (P, 1)),
        "level_masks": level, "pair_masks": pair, "eye2": np.tile(np.eye(CH, dtype=f), (2, 1)),
        "keep": keep, "keep_group": keep_group, "keep_expert": keep_expert, "head_ones": heads, "head_mean": heads / f(64),
        "is_first": np.repeat(np.arange(DEPTH)[:, None] == 0, P, axis=1).astype(f),
    }


def kernel(**inputs):
    import concourse.bacc as bacc
    from concourse.bass_utils import run_bass_kernel_spmd

    nc = bacc.Bacc("TRN2", target_bir_lowering=False, num_devices=1)
    arrays, aps = {}, {}
    for name, a in {**inputs, **shape_constants()}.items():
        a = np.ascontiguousarray(a)
        arrays[f"in_{name}"] = a
        aps[name] = nc.dram_tensor(f"in_{name}", a.shape, mybir.dt.from_np(a.dtype), kind="ExternalInput").ap()
    out = nc.dram_tensor("out", (1, SEQ, D), F32, kind="ExternalOutput").ap()
    program(nc, aps, out)
    r = run_bass_kernel_spmd(nc, [arrays], core_ids=[0])
    return r.results[0]["out"]
```

```python
from contextlib import ExitStack

import numpy as np

import concourse.bass as bass
from concourse import mybir

F32 = mybir.dt.float32
I32 = mybir.dt.int32
ALU = mybir.AluOpType
ACT = mybir.ActivationFunctionType
AX = mybir.AxisListType.X

P = 128
D = 1024
KT = D // P
SEQ = 512
DEPTH = 2
BIG = 1e30

CONV_K = 31
TOPK = 128
IDX_HEADS = 4
Z_TILES = 30
Z_VAL, Z_GLU, Z_CGATE, Z_PIN, Z_PGATE, Z_Q, Z_K, Z_V, Z_AGATE, Z_QI, Z_KI, Z_WI = (
    0, 2, 4, 6, 8, 10, 14, 18, 22, 26, 28, 29)
PAIRS1 = 14

N_META = 16
L = SEQ + N_META
HALF = L // 2
H_A = 4
MLA_SCALE = 192 ** -0.5
RW_TILES = 4
CH = 64
N_CH = -(-L // CH)
LP = N_CH * CH
WIDE = 2 * RW_TILES * LP
LEVELS = 6
N_EXP = 32
E_HID = 256
CAP = 128
ALPHA = (2 * DEPTH) ** 0.25
EXP_HALF = float(np.exp(-0.5))
T_CQ, T_CKV, T_KPE, T_R, T_K, T_V, T_WD, T_AD, T_GD = 0, 2, 3, 4, 8, 12, 16, 17, 18
TOK = [(t * P, min(P, L - t * P)) for t in range(-(-L // P))]


POOL_DMA_SEMS = ("choices_listed", "lists_fetched", "x_gathered_0", "x_gathered_1", "y_stored_0", "y_stored_1")


class Sems:

    def __init__(self, nc):
        self.nc = nc
        self.old = []
        self.new = []
        self.stack = ExitStack()
        self.last = ExitStack()
        self.forever = ExitStack()
        self.own = {name: self.forever.enter_context(nc.semaphore(name)) for name in POOL_DMA_SEMS}
        self.stage = 0

    def open(self):
        self.last.close()
        self.stage += 1
        self.old, self.new = self.new, []
        self.last, self.stack = self.stack, ExitStack()

    def take(self, name):
        s = self.stack.enter_context(self.nc.semaphore(f"{name}_{self.stage}"))
        self.new.append(s)
        return s

    def take_own(self, name):
        self.new.append(self.own[name])
        return self.own[name]

    def clear_old(self, pool):
        if any(s in self.own.values() for s in self.old):
            pool.dma_reset()
        for s in self.old:
            pool.sem_clear(s)


class Chain:

    def __init__(self, eng, sem):
        self.eng, self.sem, self.n = eng, sem, 0

    def add(self, ins):
        ins.then_inc(self.sem, 1)
        self.n += 1
        return self.n

    def wait(self, n=None):
        self.eng.wait_ge(self.sem, self.n if n is None else n)

    def link(self, ins):
        self.add(ins)
        self.wait()


def in_pairs(eng, n, body):
    if n >= 2:
        with eng.Fori(0, n // 2) as i:
            body(i * 2, 0, i)
            body(i * 2 + 1, 1, i)
    if n % 2:
        body(n - 1, 0, n // 2)


def halves(ap, nh):
    return ap.rearrange("p (a n) -> p a n", a=nh)


class Env:
    pass


def sweep(nc, S):
    S.open()
    with nc.Block() as block:
        @block.gpsimd
        def _(pool):
            S.clear_old(pool)
    S.open()


def load_constants(nc, S, pairs):
    S.open()
    loaded = S.take("constants_loaded")
    with nc.Block() as block:
        @block.gpsimd
        def _(pool):
            S.clear_old(pool)

        @block.sync
        def _(sp):
            for dst, src in pairs:
                sp.dma_start(dst, src).then_inc(loaded, 16)
            sp.wait_ge(loaded, 16 * len(pairs))


def transpose_rows(nc, S, E, dst, ntiles, parts):
    S.open()
    turned = S.take("turned")
    copied = S.take("copied")
    with nc.Block() as block:
        @block.gpsimd
        def _(pool):
            S.clear_old(pool)

        @block.tensor
        def _(pe):
            for k in range(ntiles):
                if k >= 8:
                    pe.wait_ge(copied, k - 7)
                for n, (tile_ap, c0, rows_n) in enumerate(parts):
                    last = pe.transpose(E.PS[:, k % 8, c0:c0 + rows_n], tile_ap[:, k * P:(k + 1) * P],
                                        E.ident[0:rows_n, 0:rows_n])
                last.then_inc(turned, 1)

        @block.scalar
        def _(act):
            w = parts[-1][1] + parts[-1][2]
            for k in range(ntiles):
                act.wait_ge(turned, k + 1)
                act.copy(dst(k), E.PS[:, k % 8, 0:w]).then_inc(copied, 1)


def load_params(nc, S, E, rows):
    S.open()
    blank = S.take("blank")
    loaded = S.take("rows_loaded")
    turned = S.take("turned")
    with nc.Block() as block:
        @block.gpsimd
        def _(pool):
            S.clear_old(pool)

        @block.vector
        def _(dve):
            dve.memset(E.praw[:, :], 0.0).then_inc(blank, 1)

        @block.sync
        def _(sp):
            sp.wait_ge(blank, 1)
            for r, n, src, c0, w in rows:
                sp.dma_start(E.praw[r:r + n, c0:c0 + w], src).then_inc(loaded, 16)

        @block.tensor
        def _(pe):
            pe.wait_ge(loaded, 16 * len(rows))
            pe.transpose(E.PS[:, 0, 0:P], E.praw[:, :], E.ident[:, :]).then_inc(turned, 1)

        @block.scalar
        def _(act):
            act.wait_ge(turned, 1)
            act.copy(E.par[:, :], E.PS[:, 0, 0:P])


def norm(nc, S, E, src, dst, nk, nh, nw, g, eps, b=None, func=None):
    S.open()
    centred = b is not None
    sum_ready = S.take("sum_ready")
    xc_ready = S.take("xc_ready")
    sq_ready = S.take("sq_ready")
    ssq_ready = S.take("ssq_ready")
    var_ready = S.take("var_ready")
    std_ready = S.take("std_ready")
    scaled = S.take("scaled")
    own = S.take("dve_steps")
    width = nk * P
    bank_sum = E.PS[:, 0:nh, 0:nw]
    bank_sq = E.PS[:, 2:2 + nh, 0:nw]
    sq = E.normbuf
    stat = halves(E.stat[:, 0:nh * nw], nh)

    with nc.Block() as block:
        @block.gpsimd
        def _(pool):
            S.clear_old(pool)

        @block.tensor
        def _(pe):
            if centred:
                for k in range(nk):
                    for a in range(nh):
                        last = pe.matmul(E.PS[:, a, 0:nw], E.ones[:, :], halves(src(k), nh)[:, a, :],
                                         start=(k == 0), stop=(k == nk - 1))
                last.then_inc(sum_ready, 1)
            for k in range(nk):
                pe.wait_ge(sq_ready, k + 1)
                for a in range(nh):
                    last = pe.matmul(E.PS[:, 2 + a, 0:nw], E.ones[:, :],
                                     halves(sq[:, k, 0:nh * nw], nh)[:, a, :],
                                     start=(k == 0), stop=(k == nk - 1))
            last.then_inc(ssq_ready, 1)

        @block.scalar
        def _(act):
            for k in range(nk):
                if centred:
                    act.wait_ge(xc_ready, k + 1)
                act.activation(sq[:, k, 0:nh * nw], dst(k) if centred else src(k),
                               ACT.Square).then_inc(sq_ready, 1)
            act.wait_ge(var_ready, 1)
            act.activation(stat, stat, ACT.Sqrt).then_inc(std_ready, 1)
            if centred:
                for k in range(nk):
                    act.wait_ge(scaled, k + 1)
                    act.activation(dst(k), dst(k), func or ACT.Identity, bias=b(k))

        @block.vector
        def _(dve):
            c = Chain(dve, own)
            if centred:
                dve.wait_ge(sum_ready, 1)
                c.link(dve.tensor_scalar(stat, bank_sum, 1.0 / width, None, ALU.mult))
                for k in range(nk):
                    dve.tensor_tensor(dst(k), src(k), E.stat[:, 0:nh * nw], ALU.subtract).then_inc(xc_ready, 1)
                dve.wait_ge(xc_ready, nk)
            dve.wait_ge(ssq_ready, 1)
            dve.tensor_scalar(stat, bank_sq, 1.0 / width, eps, ALU.mult, ALU.add).then_inc(var_ready, 1)
            dve.wait_ge(std_ready, 1)
            c.link(dve.reciprocal(E.stat[:, 0:nh * nw], E.stat[:, 0:nh * nw]))
            for k in range(nk):
                dve.scalar_tensor_tensor(dst(k), dst(k) if centred else src(k), g(k), E.stat[:, 0:nh * nw],
                                         ALU.mult, ALU.mult).then_inc(scaled, 1)


def project(nc, S, E, w_of, rhs, nk, npairs, nh, nw, evac, on="scalar", beside=None):
    S.open()
    steps = S.take("beside_steps")
    loaded = [S.take("w_loaded_0"), S.take("w_loaded_1")]
    done = S.take("tile_done")
    freed = S.take("tile_out")
    with nc.Block() as block:
        @block.gpsimd
        def _(pool):
            S.clear_old(pool)

        @block.sync
        def _(sp):
            def load(j, slot, turn):
                sp.wait_ge(done, j * 2 + 1)
                sp.dma_start(E.wring[:, slot, 0:nk, :], w_of(j)).then_inc(loaded[slot], 16)
            in_pairs(sp, npairs, load)

        @block.tensor
        def _(pe):
            pe.sem_inc(done, 3)

            def multiply(j, slot, turn):
                pe.wait_ge(loaded[slot], turn * 16 + 16)
                for t in range(2):
                    pe.wait_ge(freed, j * 2 + (t + 1))
                    for k in range(nk):
                        for a in range(nh):
                            last = pe.matmul(E.PS[:, 4 * slot + 2 * t + a, 0:nw],
                                             E.wring[:, slot, k, t * P:(t + 1) * P],
                                             halves(rhs(k), nh)[:, a, :], start=(k == 0), stop=(k == nk - 1))
                    last.then_inc(done, 1)
            in_pairs(pe, npairs, multiply)

        def take_out(eng):
            eng.sem_inc(freed, 4)

            def body(j, slot, turn):
                for t in range(2):
                    eng.wait_ge(done, j * 2 + (t + 4))
                    b = 4 * slot + 2 * t
                    evac(eng, j, t, E.PS[:, b:b + nh, 0:nw]).then_inc(freed, 1)
            in_pairs(eng, npairs, body)

        if on == "scalar":
            @block.scalar
            def _(act):
                take_out(act)
            if beside:
                @block.vector
                def _(dve):
                    beside(dve, steps)
        else:
            @block.vector
            def _(dve):
                take_out(dve)


def conv_gate(nc, S, E):
    S.open()
    sig_ready = S.take("sig_ready")
    pad = CONV_K - 1
    with nc.Block() as block:
        @block.gpsimd
        def _(pool):
            S.clear_old(pool)

        @block.scalar
        def _(act):
            act.activation(E.z[:, Z_GLU:Z_GLU + 2, :], E.z[:, Z_GLU:Z_GLU + 2, :],
                           ACT.Sigmoid).then_inc(sig_ready, 1)

        @block.vector
        def _(dve):
            dve.memset(E.upad[:, :, 0:pad], 0.0)
            dve.wait_ge(sig_ready, 1)
            dve.tensor_tensor(E.upad[:, :, pad:pad + SEQ], E.z[:, Z_VAL:Z_VAL + 2, :],
                              E.z[:, Z_GLU:Z_GLU + 2, :], ALU.mult)


def conv_taps(E, dve, steps):
    c = Chain(dve, steps)
    for tap in range(CONV_K):
        for t in range(2):
            acc, u = E.conv[:, t, :], E.upad[:, t, tap:tap + SEQ]
            w = E.par[:, R_DW + 2 * tap + t:R_DW + 2 * tap + t + 1]
            if tap == 0:
                c.add(dve.tensor_scalar(acc, u, w, E.par[:, R_DWB + t:R_DWB + t + 1], ALU.mult, ALU.add))
            else:
                c.wait(2 * tap - 1 + t)
                c.add(dve.scalar_tensor_tensor(acc, u, w, acc, ALU.mult, ALU.add))


def conv_point(nc, S, E):
    S.open()
    loaded = S.take("pw_loaded")
    silu_ready = S.take("silu_ready")
    done = S.take("point_done")
    with nc.Block() as block:
        @block.gpsimd
        def _(pool):
            S.clear_old(pool)

        @block.sync
        def _(sp):
            sp.dma_start(E.wring[:, 0, 0:2, :],
                         E.A["conv_pw_w"][E.li].rearrange("(k p) m -> p k m", p=P)).then_inc(loaded, 16)
            sp.wait_ge(loaded, 16)

        @block.scalar
        def _(act):
            act.activation(E.z[:, Z_CGATE:Z_CGATE + 2, :], E.z[:, Z_CGATE:Z_CGATE + 2, :],
                           ACT.Silu).then_inc(silu_ready, 1)

        @block.tensor
        def _(pe):
            pe.wait_ge(loaded, 16)
            for m in range(2):
                for k in range(2):
                    last = pe.matmul(E.PS[:, m, :], E.wring[:, 0, k, m * P:(m + 1) * P], E.conv[:, k, :],
                                     start=(k == 0), stop=(k == 1))
                last.then_inc(done, 1)

        @block.vector
        def _(dve):
            dve.wait_ge(silu_ready, 1)
            for m in range(2):
                dve.wait_ge(done, m + 1)
                dve.scalar_tensor_tensor(E.y[:, m, 0:SEQ], E.PS[:, m, :], E.par[:, R_PWB + m:R_PWB + m + 1],
                                         E.z[:, Z_CGATE + m, :], ALU.add, ALU.mult)


def pool_windows(E, dve, steps):
    c = Chain(dve, steps)
    G = 64
    x = E.z[:, Z_PIN:Z_PIN + 2, :]
    a, b = E.win[:, 0, :, :], E.win[:, 1, :, :]
    c.add(dve.memset(E.win[:, :, :, 0:16], 0.0))
    c.link(dve.tensor_copy(a[:, :, 16:16 + SEQ], x))

    def double(dst, src, by):
        c.link(dve.tensor_tensor(dst[:, :, 16:16 + SEQ], src[:, :, 16:16 + SEQ],
                                 src[:, :, 16 - by:16 - by + SEQ], ALU.add))

    def use(src, g):
        r, t = (g % 2) * G, g // 2
        c.add(dve.tensor_copy(E.avg[r:r + G, t, :], src[r:r + G, t, 16:16 + SEQ]))
    double(b, a, 1)
    use(b, 0)
    double(a, b, 2)
    use(a, 1)
    double(b, a, 4)
    use(b, 2)
    double(a, b, 8)
    use(a, 3)
    c.wait()
    c.link(dve.tensor_tensor(E.avg, E.avg, E.invcnt[:, :, :], ALU.mult))
    dve.tensor_tensor(E.avg, E.avg, x, ALU.subtract)


def pool_mix(nc, S, E):
    S.open()
    loaded = S.take("pool_w_loaded")
    scaled = S.take("scaled")
    silu_ready = S.take("silu_ready")
    done = S.take("pool_done")
    G = 64
    with nc.Block() as block:
        @block.gpsimd
        def _(pool):
            S.clear_old(pool)

        @block.sync
        def _(sp):
            for g in range(4):
                r = (g % 2) * G
                sp.dma_start(E.wring[r:r + G, 0, 0, (g // 2) * G:(g // 2) * G + G],
                             E.A["pool_w"][E.li, g]).then_inc(loaded, 16)
            sp.wait_ge(loaded, 64)

        @block.scalar
        def _(act):
            act.activation(E.z[:, Z_PGATE:Z_PGATE + 2, :], E.z[:, Z_PGATE:Z_PGATE + 2, :],
                           ACT.Silu).then_inc(silu_ready, 1)

        @block.vector
        def _(dve):
            dve.wait_ge(done, 1)
            for t in range(2):
                dve.tensor_scalar(E.avg[:, t, :], E.PS[:, t, :], E.par[:, R_PB + t:R_PB + t + 1],
                                  E.par[:, R_PS + t:R_PS + t + 1], ALU.add, ALU.mult).then_inc(scaled, 1)
            dve.wait_ge(silu_ready, 1)
            dve.wait_ge(scaled, 2)
            dve.tensor_tensor(E.y[:, 2:4, 0:SEQ], E.avg, E.z[:, Z_PGATE:Z_PGATE + 2, :], ALU.mult)

        @block.tensor
        def _(pe):
            pe.wait_ge(loaded, 64)
            for g in range(4):
                r, t = (g % 2) * G, g // 2
                last = pe.matmul(E.PS[r:r + G, t, :], E.wring[r:r + G, 0, 0, t * G:t * G + G],
                                 E.avg[r:r + G, t, :], start=True, stop=True)
            last.then_inc(done, 1)


def rotate(nc, S, E, tiles, n_tokens, nh):
    S.open()
    turned = S.take("turned")
    cos_done = S.take("cos_done")
    sin_done = S.take("sin_done")
    added = S.take("added")
    nw = n_tokens // nh
    with nc.Block() as block:
        @block.gpsimd
        def _(pool):
            S.clear_old(pool)
            for i, x in enumerate(tiles):
                pool.wait_ge(cos_done, i + 1)
                pool.wait_ge(sin_done, i + 1)
                pool.tensor_tensor(x, E.rotbuf[:, 0, i % 2, 0:n_tokens], E.rotbuf[:, 1, i % 2, 0:n_tokens],
                                   ALU.add).then_inc(added, 1)

        @block.tensor
        def _(pe):
            for i, x in enumerate(tiles):
                if i >= 4:
                    pe.wait_ge(sin_done, i - 3)
                for a in range(nh):
                    last = pe.matmul(E.PS[:, 2 * (i % 4) + a, 0:nw], E.rot[:, :], halves(x, nh)[:, a, :],
                                     start=True, stop=True)
                last.then_inc(turned, 1)

        @block.vector
        def _(dve):
            for i, x in enumerate(tiles):
                if i >= 2:
                    dve.wait_ge(added, i - 1)
                dve.tensor_tensor(E.rotbuf[:, 0, i % 2, 0:n_tokens], x, E.cos[:, 0:n_tokens],
                                  ALU.mult).then_inc(cos_done, 1)
                dve.wait_ge(turned, i + 1)
                b = 2 * (i % 4)
                dve.tensor_tensor(halves(E.rotbuf[:, 1, i % 2, 0:n_tokens], nh), E.PS[:, b:b + nh, 0:nw],
                                  halves(E.sin[:, 0:n_tokens], nh), ALU.mult).then_inc(sin_done, 1)


def turn_values(nc, S, E):
    S.open()
    turned = S.take("turned")
    with nc.Block() as block:
        @block.gpsimd
        def _(pool):
            S.clear_old(pool)

        @block.tensor
        def _(pe):
            for t in range(4):
                for m in range(4):
                    last = pe.transpose(E.PS[:, t, m * P:(m + 1) * P], E.z[:, Z_V + m, t * P:(t + 1) * P],
                                        E.ident[:, :])
                last.then_inc(turned, 1)

        @block.scalar
        def _(act):
            for t in range(4):
                act.wait_ge(turned, t + 1)
                act.copy(E.vn[:, t, :], E.PS[:, t, :])


def index_scores(nc, S, E):
    S.open()
    s_done = S.take("s_done")
    relu_done = S.take("relu_done")
    score_done = S.take("score_done")
    causal = S.take("causal")
    own = S.take("select_steps")
    blank = S.take("blank")
    turned = S.take("weights_turned")
    copied = S.take("weights_copied")
    units = [(qb, h) for qb in (1, 2, 3) for h in range(IDX_HEADS)]
    with nc.Block() as block:
        @block.tensor
        def _(pe):
            for t in range(4):
                last = pe.transpose(E.PS[:, 7, 4 * t:4 * t + 4], E.z[0:4, Z_WI, t * P:(t + 1) * P],
                                    E.ident[0:4, 0:4])
            last.then_inc(turned, 1)
            for i, (qb, h) in enumerate(units):
                if i >= 7:
                    pe.wait_ge(relu_done, i - 6)
                r, nk = (h % 2) * 64, (qb + 1) * P
                pe.matmul(E.PS[:, i % 7, 0:nk], E.z[r:r + 64, Z_QI + h // 2, qb * P:(qb + 1) * P],
                          E.z[r:r + 64, Z_KI, 0:nk], start=True, stop=True).then_inc(s_done, 1)

        @block.scalar
        def _(act):
            act.wait_ge(turned, 1)
            act.copy(E.wi[:, :], E.PS[:, 7, 0:16]).then_inc(copied, 1)
            for i, (qb, h) in enumerate(units):
                act.wait_ge(s_done, i + 1)
                if i >= 4:
                    act.wait_ge(own, i - 3)
                nk = (qb + 1) * P
                act.activation(E.index_relu[:, i % 4, 0:nk], E.PS[:, i % 7, 0:nk], ACT.Relu,
                               scale=0.125).then_inc(relu_done, 1)

        @block.gpsimd
        def _(pool):
            S.clear_old(pool)
            pool.memset(E.mask[:, 0, 0:P], 0.0).then_inc(blank, 1)
            pool.wait_ge(blank, 1)
            pool.affine_select(out=E.mask[:, 0, 0:P], in_=E.mask[:, 0, 0:P], compare_op=ALU.is_ge, fill=-BIG,
                               base=0, pattern=[[-1, P]], channel_multiplier=1)
            for n, qb in enumerate((1, 2, 3)):
                pool.wait_ge(score_done, n + 1)
                x = E.score[:, qb, qb * P:(qb + 1) * P]
                pool.affine_select(out=x, in_=x, compare_op=ALU.is_ge, fill=-3e38, base=0,
                                   pattern=[[-1, P]], channel_multiplier=1).then_inc(causal, 1)

        @block.vector
        def _(dve):
            c = Chain(dve, own)
            dve.wait_ge(copied, 1)
            for i, (qb, h) in enumerate(units):
                dve.wait_ge(relu_done, i + 1)
                nk = (qb + 1) * P
                acc, w = E.score[:, qb, 0:nk], E.wi[:, 4 * qb + h:4 * qb + h + 1]
                if h == 0:
                    c.link(dve.tensor_scalar(acc, E.index_relu[:, i % 4, 0:nk], w, None, ALU.mult))
                else:
                    c.link(dve.scalar_tensor_tensor(acc, E.index_relu[:, i % 4, 0:nk], w, acc, ALU.mult, ALU.add))
                if h == IDX_HEADS - 1:
                    dve.sem_inc(score_done, 1)


def select_keys(E, dve, steps):
    c = Chain(dve, steps)
    ROUNDS = TOPK // 8
    for r in range(ROUNDS):
        for qb in (1, 2, 3):
            nk = (qb + 1) * P
            if r:
                c.wait(last_rep[qb])
            src = E.work[:, qb, 0:nk] if r else E.score[:, qb, 0:nk]
            c.add(dve.max(out=E.best[:, qb, :], in_=src))
        top = c.n
        last_rep = {}
        for qb in (1, 2, 3):
            nk = (qb + 1) * P
            c.wait(top)
            src = E.work[:, qb, 0:nk] if r else E.score[:, qb, 0:nk]
            if r < ROUNDS - 1:
                last_rep[qb] = c.add(dve.match_replace(out=E.work[:, qb, 0:nk], in_to_replace=E.best[:, qb, :],
                                                       in_values=src, imm_value=-3e38))
    for qb in (1, 2, 3):
        nk = (qb + 1) * P
        s, m = E.score[:, qb, 0:nk], E.mask[:, qb, 0:nk]
        eq, cum = E.work[:, qb, 0:nk], E.index_relu[:, qb, 0:nk]
        thr, need = E.best[:, qb, 7:8], E.count[:, qb:qb + 1]
        c.add(dve.tensor_scalar(eq, s, thr, None, ALU.is_equal))
        c.link(dve.tensor_scalar(m, s, thr, 0.0, ALU.is_gt, ALU.add, accum_out=need))
        c.add(dve.tensor_scalar(need, need, -1.0, float(TOPK), ALU.mult, ALU.add))
        c.link(dve.tensor_tensor_scan(cum, E.onesrow[:, 0:nk], eq, 0.0, ALU.mult, ALU.add))
        c.link(dve.scalar_tensor_tensor(eq, cum, need, eq, ALU.is_le, ALU.mult))
        c.link(dve.tensor_tensor(m, m, eq, ALU.add))
        c.add(dve.tensor_scalar(m, m, BIG, -BIG, ALU.mult, ALU.add))
    c.wait()


def attend(nc, S, E):
    S.open()
    logit_done = S.take("logit_done")
    masked = S.take("masked")
    neg_max = S.take("neg_max")
    exp_done = S.take("exp_done")
    turned = S.take("probs_turned")
    copied = S.take("probs_copied")
    pv_done = S.take("pv_done")
    rsum = S.take("sum_inverse")
    o_ready = S.take("o_ready")
    o_turned = S.take("o_turned")
    gate = S.take("gate_ready")
    used = S.take("o_used")
    units = [(qb, h) for qb in range(4) for h in range(8)]
    SCALE = 0.125
    with nc.Block() as block:
        @block.gpsimd
        def _(pool):
            S.clear_old(pool)

        @block.tensor
        def _(pe):
            def logits(i):
                qb, h = units[i]
                r, nk = (h % 2) * 64, (qb + 1) * P
                if i >= 2:
                    pe.wait_ge(masked, i - 1)
                pe.matmul(E.PS[:, i % 2, 0:nk], E.z[r:r + 64, Z_Q + h // 2, qb * P:(qb + 1) * P],
                          E.z[r:r + 64, Z_K + h // 2, 0:nk], start=True, stop=True).then_inc(logit_done, 1)

            def turn(i):
                qb, h = units[i]
                pe.wait_ge(exp_done, i + 1)
                if i >= 2:
                    pe.wait_ge(copied, i - 1)
                for kb in range(qb + 1):
                    last = pe.transpose(E.PS[:, 2 + i % 2, kb * P:(kb + 1) * P],
                                        E.prob[:, i % 2, kb * P:(kb + 1) * P], E.ident[:, :])
                last.then_inc(turned, 1)

            def values(i):
                qb, h = units[i]
                pe.wait_ge(copied, i + 1)
                if h == 0 and qb >= 2:
                    pe.wait_ge(o_ready, qb - 1)
                for kb in range(qb + 1):
                    last = pe.matmul(E.PS[:, 4 + qb % 2, h * 64:h * 64 + 64],
                                     E.probT[:, i % 2, kb * P:(kb + 1) * P],
                                     E.vn[:, kb, h * 64:h * 64 + 64], start=(kb == 0), stop=(kb == qb))
                last.then_inc(pv_done, 1)

            def turn_out(qb):
                pe.wait_ge(o_ready, qb + 1)
                if qb >= 2:
                    pe.wait_ge(used, qb - 1)
                for m in range(4):
                    last = pe.transpose(E.PS[:, 6 + qb % 2, m * P:(m + 1) * P], E.o[:, qb % 2, m * P:(m + 1) * P],
                                        E.ident[:, :])
                last.then_inc(o_turned, 1)

            n = len(units)
            logits(0)
            for i in range(n + 2):
                if i + 1 < n:
                    logits(i + 1)
                if i < n:
                    turn(i)
                if 1 <= i <= n:
                    values(i - 1)
                if i >= 9 and (i - 9) % 8 == 0:
                    turn_out((i - 9) // 8)

        @block.vector
        def _(dve):
            def mask(i):
                qb, h = units[i]
                nk = (qb + 1) * P
                dve.wait_ge(logit_done, i + 1)
                if i >= 2:
                    dve.wait_ge(exp_done, i - 1)
                dve.tensor_tensor_reduce(E.logit[:, i % 2, 0:nk], E.PS[:, i % 2, 0:nk], E.mask[:, qb, 0:nk],
                                         1.0, -3e38, ALU.add, ALU.max, E.mx[:, i:i + 1]).then_inc(masked, 1)
                dve.wait_ge(masked, i + 1)
                dve.tensor_scalar(E.mx[:, i:i + 1], E.mx[:, i:i + 1], -SCALE, None, ALU.mult).then_inc(neg_max, 1)

            def copy(i):
                qb, h = units[i]
                nk = (qb + 1) * P
                dve.wait_ge(turned, i + 1)
                if i >= 2:
                    dve.wait_ge(pv_done, i - 1)
                dve.tensor_copy(E.probT[:, i % 2, 0:nk], E.PS[:, 2 + i % 2, 0:nk]).then_inc(copied, 1)

            def out(qb):
                dve.wait_ge(exp_done, 8 * qb + 8)
                dve.reciprocal(E.sums[:, 8 * qb:8 * qb + 8], E.sums[:, 8 * qb:8 * qb + 8]).then_inc(rsum, 1)
                dve.wait_ge(pv_done, 8 * qb + 8)
                dve.wait_ge(rsum, qb + 1)
                if qb >= 2:
                    dve.wait_ge(o_turned, qb - 1)
                dve.tensor_tensor(E.o[:, qb % 2, :].rearrange("p (h n) -> p h n", h=8),
                                  E.PS[:, 4 + qb % 2, :].rearrange("p (h n) -> p h n", h=8),
                                  E.sums[:, 8 * qb:8 * qb + 8].unsqueeze(2).broadcast_to([P, 8, 64]),
                                  ALU.mult).then_inc(o_ready, 1)

            def store(qb):
                dve.wait_ge(o_turned, qb + 1)
                dve.wait_ge(gate, 1)
                dve.tensor_tensor(E.y[:, 4:8, qb * P:(qb + 1) * P],
                                  E.PS[:, 6 + qb % 2, :].rearrange("p (m n) -> p m n", m=4),
                                  E.z[:, Z_AGATE:Z_AGATE + 4, qb * P:(qb + 1) * P], ALU.mult).then_inc(used, 1)

            n = len(units)
            mask(0)
            for i in range(n + 3):
                if i + 1 < n:
                    mask(i + 1)
                if i < n:
                    copy(i)
                if i >= 8 and (i - 8) % 8 == 0 and i <= n:
                    out(i // 8 - 1)
                if i >= 10 and (i - 10) % 8 == 0:
                    store((i - 10) // 8)

        @block.scalar
        def _(act):
            act.activation(E.z[:, Z_AGATE:Z_AGATE + 4, :], E.z[:, Z_AGATE:Z_AGATE + 4, :],
                           ACT.Silu).then_inc(gate, 1)
            for i, (qb, h) in enumerate(units):
                nk = (qb + 1) * P
                act.wait_ge(neg_max, i + 1)
                if i >= 2:
                    act.wait_ge(turned, i - 1)
                act.activation(E.prob[:, i % 2, 0:nk], E.logit[:, i % 2, 0:nk], ACT.Exp, bias=E.mx[:, i:i + 1],
                               scale=SCALE, accum_out=E.sums[:, i:i + 1]).then_inc(exp_done, 1)


def index_weights(nc, S, E, beside):
    S.open()
    steps = S.take("beside_steps")
    loaded = S.take("w_loaded")
    done = S.take("tile_done")
    ki0 = Z_KI * P
    w = E.A["w_in"][E.li].rearrange("(k p) m -> p k m", p=P)
    with nc.Block() as block:
        @block.gpsimd
        def _(pool):
            S.clear_old(pool)

        @block.sync
        def _(sp):
            sp.dma_start(E.wring[:, 0, :, 0:64], w[:, :, ki0:ki0 + 64]).then_inc(loaded, 16)
            sp.dma_start(E.wring[:, 0, :, 64:128], w[:, :, ki0:ki0 + 64]).then_inc(loaded, 16)
            sp.dma_start(E.wring[:, 0, :, 128:132], w[:, :, ki0 + 64:ki0 + 68]).then_inc(loaded, 16)
            sp.wait_ge(loaded, 48)

        @block.vector
        def _(dve):
            beside(dve, steps)

        @block.tensor
        def _(pe):
            pe.wait_ge(loaded, 48)
            for n, (c0, m) in enumerate(((0, P), (P, 4))):
                for k in range(KT):
                    last = pe.matmul(E.PS[0:m, n, :], E.wring[:, 0, k, c0:c0 + m], E.n[:, k, 0:SEQ],
                                     start=(k == 0), stop=(k == KT - 1))
                last.then_inc(done, 1)

        @block.scalar
        def _(act):
            for n, m in enumerate((P, 4)):
                act.wait_ge(done, n + 1)
                act.activation(E.z[0:m, Z_KI + n, :], E.PS[0:m, n, :], ACT.Identity,
                               bias=E.par[0:m, R_B + Z_KI + n:R_B + Z_KI + n + 1])


def gated_skip(nc, S, E):
    S.open()
    loaded = S.take("ple_loaded")
    done = S.take("tile_done")
    times = S.take("times_gate")
    freed = S.take("bank_out")
    with nc.Block() as block:
        @block.gpsimd
        def _(pool):
            S.clear_old(pool)
            for m in range(KT):
                pool.wait_ge(times, m + 1)
                pool.tensor_tensor(E.h[:, m, 0:SEQ], E.h1[:, m, 0:SEQ], E.n[:, m, 0:SEQ], ALU.add)

        @block.sync
        def _(sp):
            sp.dma_start(E.plew[:, :, :], E.A["ple_w"][E.li].rearrange("(k p) m -> p k m", p=P)).then_inc(loaded, 16)
            sp.wait_ge(loaded, 16)

        @block.tensor
        def _(pe):
            pe.wait_ge(loaded, 16)
            for m in range(KT):
                for k in range(2):
                    last = pe.matmul(E.PS[:, m, :], E.plew[:, k, m * P:(m + 1) * P], E.pT[:, k, :],
                                     start=(k == 0), stop=(k == 1))
                last.then_inc(done, 1)

        @block.vector
        def _(dve):
            for m in range(KT):
                dve.wait_ge(done, m + 1)
                dve.tensor_tensor(E.n[:, m, 0:SEQ], E.PS[:, m, :], E.n[:, m, 0:SEQ], ALU.mult).then_inc(times, 1)


R_NG, R_B, R_DW, R_DWB, R_LG, R_LB, R_PWB, R_PB, R_PS = 0, 8, 38, 100, 102, 104, 106, 108, 110


def first_block(nc, S, E, scope):
    A = E.A

    def sb(name, shape):
        return scope.enter_context(nc.sbuf_tensor(name, shape, F32))
    E.z = sb("z", [P, Z_TILES, SEQ])
    h1 = E.h1_flat
    padded = SEQ + CONV_K - 1
    E.upad = h1[:, 0:2 * padded].rearrange("p (a n) -> p a n", a=2)
    at = 2 * padded
    E.conv = h1[:, at:at + 2 * SEQ].rearrange("p (a n) -> p a n", a=2)
    at += 2 * SEQ
    E.win = h1[:, at:at + 4 * (SEQ + 16)].rearrange("p (b a n) -> p b a n", b=2, a=2)
    E.avg = E.y[:, 2:4, 0:SEQ]
    E.index_relu = E.y[:, 4:8, 0:SEQ]
    n = E.n_flat
    E.vn = n[:, 0:4 * SEQ].rearrange("p (a n) -> p a n", a=4)
    E.relu = n[:, 4 * SEQ:8 * SEQ].rearrange("p (a n) -> p a n", a=4)
    E.invcnt = sb("invcnt", [P, 2, SEQ])
    E.wi = sb("wi", [P, 16])
    E.score = sb("score", [P, 4, SEQ])
    E.work = E.normbuf[:, 0:4, 0:SEQ]
    E.mask = E.normbuf[:, 4:8, 0:SEQ]
    E.best = sb("best", [P, 4, 8])
    E.count = sb("count", [P, 4])
    E.onesrow = sb("onesrow", [P, SEQ])
    E.logit = E.relu[:, 0:2, :]
    E.prob = E.relu[:, 2:4, :]
    E.probT = E.score[:, 0:2, :]
    E.o = E.score[:, 2:4, :]
    E.mx = sb("mx", [P, 32])
    E.sums = sb("sums", [P, 32])
    E.plew = E.z[:, 0:4, :].rearrange("p a n -> p (a n)").rearrange("p (k m) -> p k m", k=2)
    E.pT = E.z[:, 4:6, :]
    xn = E.z[:, 0:8, :].rearrange("p a n -> p (a n)").rearrange("p (t d) -> p t d", t=4)
    pn = E.z[:, 8:10, :].rearrange("p a n -> p (a n)").rearrange("p (t d) -> p t d", t=4)

    load_constants(nc, S, [(E.invcnt[:, :, :], A["invcnt"]), (E.cos[:, 0:SEQ], A["cos1"]), (E.sin[:, 0:SEQ], A["sin1"]),
                           (E.onesrow[:, :], A["onesrow"]),
                           (xn, A["x"][0].rearrange("(t p) d -> p t d", p=P))])
    transpose_rows(nc, S, E, lambda k: E.h[:, k, 0:SEQ], KT,
                   parts=[(xn[:, t, :], t * P, P) for t in range(4)])
    sweep(nc, S)
    with nc.Fori(0, E.depth) as li:
        E.li = li

        def rows(name, n):
            return A[name][li].rearrange("(t p) -> t p", p=P)[0:n]
        b = A["b_in"][li]
        ki0 = Z_KI * P
        load_params(nc, S, E, [
            (R_NG, 8, rows("norm_g", 8), 0, P),
            (R_B, 28, b[0:28 * P].rearrange("(t p) -> t p", p=P), 0, P),
            (R_B + 28, 1, b[ki0:ki0 + 64].unsqueeze(0), 0, 64),
            (R_B + 28, 1, b[ki0:ki0 + 64].unsqueeze(0), 64, 64),
            (R_B + 29, 1, b[ki0 + 64:ki0 + 68].unsqueeze(0), 0, 4),
            (R_DW, 62, A["conv_dw_w"][li].rearrange("k (t p) -> (k t) p", p=P), 0, P),
            (R_DWB, 2, rows("conv_dw_b", 2), 0, P), (R_LG, 2, rows("conv_ln_g", 2), 0, P),
            (R_LB, 2, rows("conv_ln_b", 2), 0, P), (R_PWB, 2, rows("conv_pw_b", 2), 0, P),
            (R_PB, 2, rows("pool_b", 2), 0, P), (R_PS, 2, rows("pool_scale", 2), 0, P)])

        def par(r):
            return lambda k: E.par[:, r + k:r + k + 1]
        norm(nc, S, E, lambda k: E.h[:, k, 0:SEQ], lambda k: E.n[:, k, 0:SEQ], KT, 1, SEQ, par(R_NG), 1e-6)
        w_in = A["w_in"][li].rearrange("(k p) m -> p k m", p=P)
        par_b = E.par[:, R_B:R_B + 30]

        def to_z(eng, j, t, psum):
            q = j * 2 + t
            return eng.activation(E.z[:, bass.ds(q, 1), :], psum, ACT.Identity, bias=par_b[:, bass.ds(q, 1)])

        def project_in(first, count, beside=None):
            def evac(eng, j, t, psum):
                return to_z(eng, j + first, t, psum)
            project(nc, S, E, lambda j: w_in[:, :, bass.ds((j + first) * 256, 256)], lambda k: E.n[:, k, 0:SEQ], KT,
                    count, 1, SEQ, evac, beside=beside)
        project_in(0, Z_Q // 2)
        conv_gate(nc, S, E)
        split = (Z_V + 2) // 2
        project_in(split, PAIRS1 - split, beside=lambda dve, steps: conv_taps(E, dve, steps))
        index_weights(nc, S, E, lambda dve, steps: pool_windows(E, dve, steps))
        norm(nc, S, E, lambda k: E.conv[:, k, :], lambda k: E.conv[:, k, :], 2, 1, SEQ, par(R_LG), 1e-6,
             b=par(R_LB), func=ACT.Silu)
        conv_point(nc, S, E)
        pool_mix(nc, S, E)
        rotate(nc, S, E, [E.z[:, m, :] for m in (Z_QI, Z_QI + 1, Z_KI)], SEQ, 1)
        index_scores(nc, S, E)
        project_in(Z_Q // 2, split - Z_Q // 2, beside=lambda dve, steps: select_keys(E, dve, steps))
        rotate(nc, S, E, [E.z[:, m, :] for m in range(Z_Q, Z_V)], SEQ, 1)
        turn_values(nc, S, E)
        attend(nc, S, E)
        w_out = A["w_out"][li].rearrange("(k p) m -> p k m", p=P)

        def add_h(eng, j, t, psum):
            q = j * 2 + t
            return eng.tensor_tensor(E.h1[:, bass.ds(q, 1), 0:SEQ], psum, E.h[:, bass.ds(q, 1), 0:SEQ], ALU.add)
        project(nc, S, E, lambda j: w_out[:, :, bass.ds(j * 256, 256)], lambda k: E.y[:, k, 0:SEQ], KT, KT // 2,
                1, SEQ, add_h, on="vector")
        ple_gate = A["ple_gate_w"][li].rearrange("(k p) m -> p k m", p=P)

        def sigmoids(eng, j, t, psum):
            return eng.activation(E.n[:, bass.ds(j * 2 + t, 1), 0:SEQ], psum, ACT.Sigmoid)
        project(nc, S, E, lambda j: ple_gate[:, :, bass.ds(j * 256, 256)], lambda k: E.h1[:, k, 0:SEQ], KT, KT // 2,
                1, SEQ, sigmoids)
        load_constants(nc, S, [(pn, A["p"][li, 0].rearrange("(t p) d -> p t d", p=P))])
        transpose_rows(nc, S, E, lambda k: E.pT[:, k, :], 2, parts=[(pn[:, t, :], t * P, P) for t in range(4)])
        gated_skip(nc, S, E)
        sweep(nc, S)
    load_params(nc, S, E, [(0, 8, A["final_norm_g"].rearrange("(t p) -> t p", p=P), 0, P),
                           (8, 8, A["emb_ln_g_2"].rearrange("(t p) -> t p", p=P), 0, P),
                           (16, 8, A["emb_ln_b_2"].rearrange("(t p) -> t p", p=P), 0, P)])
    norm(nc, S, E, lambda k: E.h[:, k, 0:SEQ], lambda k: E.h1[:, k, N_META:L], KT, 1, SEQ,
         lambda k: E.par[:, k:k + 1], 1e-6)


(Q_QN, Q_KVN, Q_MP, Q_MN, Q_W0, Q_A0, Q_KK, Q_KA, Q_RK, Q_GG, Q_GB, Q_V0, Q_L1G, Q_L1B, Q_L2G, Q_L2B, Q_FIRST,
 Q_C0) = (0, 2, 3, 18, 33, 41, 49, 53, 57, 61, 65, 69, 73, 81, 89, 97, 105, 106)


def angles(nc, S, E):
    S.open()
    loaded = S.take("positions_loaded")
    own = S.take("angle_steps")
    r_ready = S.take("r_ready")
    TURN = 2 * np.pi
    C1 = 6.28125
    C2 = float(np.float32(np.round((TURN - C1) * 2 ** 21) / 2 ** 21))
    C3 = TURN - C1 - C2
    MAGIC = 1.5 * 2 ** 23
    with nc.Block() as block:
        @block.gpsimd
        def _(pool):
            S.clear_old(pool)

        @block.sync
        def _(sp):
            sp.dma_start(E.pos_int[:, :], E.A["positions_2"][0].partition_broadcast(P)).then_inc(loaded, 16)
            sp.dma_start(E.cos[:, 0:N_META], E.A["meta_pos"]).then_inc(loaded, 16)
            sp.dma_start(E.invf[:, :], E.A["inv_freq"]).then_inc(loaded, 16)
            sp.wait_ge(loaded, 48)

        @block.vector
        def _(dve):
            c = Chain(dve, own)
            dve.wait_ge(loaded, 48)
            c.link(dve.tensor_copy(E.cos[:, N_META:L], E.pos_int[:, :]))
            c.link(dve.tensor_scalar(E.cos[:, N_META:L], E.cos[:, N_META:L], float(N_META), None, ALU.add))
            c.link(dve.tensor_scalar(E.cos[:, :], E.cos[:, :], E.invf[:, 0:1], None, ALU.mult))
            turns = E.stat[:, 0:L]
            c.link(dve.tensor_scalar(turns, E.cos[:, :], 1.0 / TURN, MAGIC, ALU.mult, ALU.add))
            c.link(dve.tensor_scalar(turns, turns, -MAGIC, None, ALU.add))
            for part in (C1, C2, C3):
                c.link(dve.scalar_tensor_tensor(E.cos[:, :], turns, -part, E.cos[:, :], ALU.mult, ALU.add))
            PI = 3.1415925
            c.link(dve.tensor_scalar(E.cos[:, :], E.cos[:, :], PI, -PI, ALU.min, ALU.max))
            c.link(dve.tensor_scalar(E.stat[:, 0:L], E.cos[:, :], -1.0, None, ALU.mult))
            c.link(dve.tensor_tensor(E.stat[:, 0:L], E.stat[:, 0:L], E.cos[:, :], ALU.max))
            dve.tensor_scalar(E.stat[:, 0:L], E.stat[:, 0:L], -1.0, float(np.pi / 2), ALU.mult,
                              ALU.add).then_inc(r_ready, 1)

        @block.scalar
        def _(act):
            act.wait_ge(r_ready, 1)
            act.activation(E.sin[:, :], E.cos[:, :], ACT.Sin).then_inc(r_ready, 1)
            act.wait_ge(r_ready, 2)
            act.activation(E.cos[:, :], E.stat[:, 0:L], ACT.Sin)


def project_tail(nc, S, E):
    S.open()
    loaded = S.take("w_loaded")
    done = S.take("tile_done")
    w = E.A["w_in_2"][E.li].rearrange("(k p) m -> p k m", p=P)
    first_rw = 3 * P + 64
    out = S.take("tile_out")
    tiles = (0, 1, 2, 3, T_GD)
    wt = E.norm_flat[:, 0:KT * 512].rearrange("p (k m) -> p k m", k=KT)
    w_gd = E.wring[:, 0, :, 0:P]
    with nc.Block() as block:
        @block.gpsimd
        def _(pool):
            S.clear_old(pool)

        @block.sync
        def _(sp):
            sp.dma_start(wt[:, :, 0:448], w[:, :, 0:448]).then_inc(loaded, 16)
            sp.dma_start(wt[:, :, 448:512], w[:, :, 384:448]).then_inc(loaded, 16)
            c0 = first_rw + 14 * P
            sp.dma_start(w_gd, w[:, :, c0:c0 + P]).then_inc(loaded, 16)
            sp.wait_ge(loaded, 48)

        @block.tensor
        def _(pe):
            pe.wait_ge(loaded, 48)
            for i, m in enumerate(tiles):
                if i == 4:
                    pe.wait_ge(out, 1)
                for k in range(KT):
                    wk = wt[:, k, i * P:(i + 1) * P] if i < 4 else w_gd[:, k, :]
                    for a in range(2):
                        last = pe.matmul(E.PS[:, 2 * (i % 4) + a, 0:HALF], wk,
                                         halves(E.h[:, k, :], 2)[:, a, :], start=(k == 0), stop=(k == KT - 1))
                last.then_inc(done, 1)

        @block.scalar
        def _(act):
            for i, m in enumerate(tiles):
                act.wait_ge(done, i + 1)
                act.activation(halves(E.zs[m], 2), E.PS[:, 2 * (i % 4):2 * (i % 4) + 2, 0:HALF],
                               ACT.Identity).then_inc(out, 1)


def shift(nc, S, E):
    S.open()
    c0_ready = S.take("c0_ready")
    own = S.take("shift_steps")
    centre = S.take("centre_ready")
    both = S.take("neighbours_added")
    back = S.take("copied_back")
    n_t = 15
    with nc.Block() as block:
        @block.gpsimd
        def _(pool):
            S.clear_old(pool)

        @block.scalar
        def _(act):
            act.wait_ge(c0_ready, 1)

            def return_tile(i):
                act.wait_ge(both, i + 1)
                act.copy(E.zs[T_R + i], E.shifted[:, i % 4, :]).then_inc(back, 1)
            for i in range(n_t):
                if i >= 4:
                    act.wait_ge(back, i - 3)
                act.mul(E.shifted[:, i % 4, :], E.zs[T_R + i], E.par[:, Q_C0 + i:Q_C0 + i + 1]).then_inc(centre, 1)
                if i >= 2:
                    return_tile(i - 2)
            for i in (n_t - 2, n_t - 1):
                return_tile(i)

        @block.vector
        def _(dve):
            c = Chain(dve, own)
            c0 = E.par[:, Q_C0:Q_C0 + n_t]
            c.link(dve.tensor_tensor(c0, E.par[:, Q_MP:Q_MP + n_t], E.par[:, Q_MN:Q_MN + n_t], ALU.add))
            dve.tensor_scalar(c0, c0, -1.0, 1.0, ALU.mult, ALU.add).then_inc(c0_ready, 1)
            for i in range(n_t):
                x, u = E.zs[T_R + i], E.shifted[:, i % 4, :]
                dve.wait_ge(centre, i + 1)
                c.link(dve.scalar_tensor_tensor(u[:, 1:L], x[:, 0:L - 1], E.par[:, Q_MP + i:Q_MP + i + 1],
                                                u[:, 1:L], ALU.mult, ALU.add))
                dve.scalar_tensor_tensor(u[:, 0:L - 1], x[:, 1:L], E.par[:, Q_MN + i:Q_MN + i + 1],
                                         u[:, 0:L - 1], ALU.mult, ALU.add).then_inc(both, 1)


def mla_project(nc, S, E):
    S.open()
    loaded = S.take("w_loaded")
    done = S.take("tile_done")
    out = S.take("tile_out")
    flat = E.wring[:, :, :, :].rearrange("p s k m -> p (s k m)")
    uq = flat[:, 0:1536].rearrange("p (k h c) -> p k h c", k=2, h=H_A)
    ukv = flat[:, 1536:2560].rearrange("p (h c) -> p h c", h=H_A)
    pe_w = flat[:, 2560:3072].rearrange("p (k h c) -> p k h c", k=2, h=H_A)
    tiles = [([uq[:, k, h, 0:P] for k in range(2)], 0, E.qn[:, h, :]) for h in range(H_A)]
    tiles += [([pe_w[:, k, 2 * j:2 * j + 2, :].rearrange("p h c -> p (h c)") for k in range(2)], 0, E.qp[:, j, :])
              for j in range(2)]
    tiles += [([ukv[:, h, 0:P]], 2, E.kn[:, h, :]) for h in range(H_A)]
    with nc.Block() as block:
        @block.gpsimd
        def _(pool):
            S.clear_old(pool)

        @block.sync
        def _(sp):
            w = E.A["mla_w_uq_2"][E.li].rearrange("(k p) (h c) -> p k h c", p=P, h=H_A)
            for k in range(2):
                sp.dma_start(uq[:, k], w[:, k]).then_inc(loaded, 16)
                sp.dma_start(pe_w[:, k], w[:, k, :, P:192]).then_inc(loaded, 16)
            sp.dma_start(ukv, E.A["mla_w_ukv_2"][E.li].rearrange("p (h c) -> p h c", h=H_A)).then_inc(loaded, 16)
            sp.wait_ge(loaded, 80)

        @block.tensor
        def _(pe):
            pe.wait_ge(loaded, 80)
            for i, (w, k0, _) in enumerate(tiles):
                if i >= 4:
                    pe.wait_ge(out, i - 3)
                for k in range(len(w)):
                    for a in range(2):
                        last = pe.matmul(E.PS[:, 2 * (i % 4) + a, 0:HALF], w[k],
                                         halves(E.n[:, k0 + k, :], 2)[:, a, :], start=(k == 0), stop=(k == len(w) - 1))
                last.then_inc(done, 1)
            pe.wait_ge(out, 10)
            for t, (t0, rows) in enumerate(TOK):
                last = pe.matmul(E.PS[0:rows, t, :], E.n[:, 2, t0:t0 + rows], ukv[:, :, P:2 * P], start=True, stop=True)
                last.then_inc(done, 1)

        @block.scalar
        def _(act):
            for i, (_, _, dst) in enumerate(tiles):
                act.wait_ge(done, i + 1)
                act.activation(halves(dst, 2), E.PS[:, 2 * (i % 4):2 * (i % 4) + 2, 0:HALF],
                               ACT.Identity).then_inc(out, 1)
            for t, (t0, rows) in enumerate(TOK):
                act.wait_ge(done, 11 + t)
                act.copy(E.vn2[0:rows, t, :], E.PS[0:rows, t, :])


def mla_attend(nc, S, E):
    S.open()
    logit_done = S.take("logit_done")
    neg_max = S.take("neg_max")
    max_steps = S.take("max_steps")
    exp_done = S.take("exp_done")
    turned = S.take("probs_turned")
    copied = S.take("probs_copied")
    copied_end = S.take("probs_end_copied")
    pv_done = S.take("pv_done")
    inv_ready = S.take("sum_inverse")
    o_ready = S.take("o_ready")
    blank = S.take("blank")
    units = [(t, h) for t in range(len(TOK)) for h in range(H_A)]
    n = len(units)
    nt = len(TOK)
    with nc.Block() as block:
        @block.gpsimd
        def _(pool):
            S.clear_old(pool)
            pool.memset(E.on[:, nt - 1, :], 1.0).then_inc(blank, 1)

        @block.tensor
        def _(pe):
            def logits(i):
                t, h = units[i]
                t0, rows = TOK[t]
                r = (h % 2) * 64
                if i >= 2:
                    pe.wait_ge(exp_done, i - 1)
                for a in range(2):
                    dst = E.PS[0:rows, 2 * (i % 2) + a, 0:HALF]
                    pe.matmul(dst, E.qn[:, h, t0:t0 + rows], halves(E.kn[:, h, :], 2)[:, a, :], start=True, stop=False)
                    last = pe.matmul(dst, E.qp[r:r + 64, h // 2, t0:t0 + rows],
                                     halves(E.zs[T_KPE], 2)[r:r + 64, a, :], start=False, stop=True)
                last.then_inc(logit_done, 1)

            def turn(i):
                t, h = units[i]
                rows = TOK[t][1]
                pe.wait_ge(exp_done, i + 1)
                if i >= 2:
                    pe.wait_ge(copied, i - 1)
                    pe.wait_ge(copied_end, i - 1)
                for b, (b0, br) in enumerate(TOK):
                    dst = (E.PS[0:br, 4 + i % 2, b * P:b * P + rows] if b < 4 else
                           E.PS[0:br, 6, (i % 2) * P:(i % 2) * P + rows])
                    last = pe.transpose(dst, E.prob2[0:rows, i % 2, b0:b0 + br], E.ident[0:rows, 0:rows])
                last.then_inc(turned, 1)

            def values(i):
                t, h = units[i]
                rows = TOK[t][1]
                pe.wait_ge(copied, i + 1)
                pe.wait_ge(copied_end, i + 1)
                if h == 0 and t >= 1:
                    pe.wait_ge(o_ready, t)
                for b, (b0, br) in enumerate(TOK):
                    last = pe.matmul(E.PS[0:rows, 7, h * P:(h + 1) * P], E.probT2[0:br, i % 2, b, 0:rows],
                                     E.vn2[0:br, b, h * P:(h + 1) * P], start=(b == 0), stop=(b == nt - 1))
                last.then_inc(pv_done, 1)

            logits(0)
            for i in range(n + 1):
                if i + 1 < n:
                    logits(i + 1)
                if i < n:
                    turn(i)
                if i >= 1:
                    values(i - 1)

        @block.vector
        def _(dve):
            def top(i):
                t, h = units[i]
                rows = TOK[t][1]
                dve.wait_ge(logit_done, i + 1)
                dve.tensor_reduce(E.mx2[0:rows, i:i + 1], E.PS[0:rows, 2 * (i % 2):2 * (i % 2) + 2, 0:HALF],
                                  mybir.AxisListType.XY, ALU.max).then_inc(max_steps, 1)
                dve.wait_ge(max_steps, i + 1)
                dve.tensor_scalar(E.mx2[0:rows, i:i + 1], E.mx2[0:rows, i:i + 1], -MLA_SCALE, None,
                                  ALU.mult).then_inc(neg_max, 1)

            def copy(i):
                t, h = units[i]
                rows = TOK[t][1]
                dve.wait_ge(turned, i + 1)
                if i >= 2:
                    dve.wait_ge(pv_done, i - 1)
                dve.tensor_copy(E.probT2[:, i % 2, 0:4, 0:rows],
                                E.PS[:, 4 + i % 2, :].rearrange("p (b n) -> p b n", b=4)[:, :, 0:rows]).then_inc(copied, 1)

            def out(t):
                rows = TOK[t][1]
                s = E.sums2[0:rows, 4 * t:4 * t + 4]
                dve.wait_ge(exp_done, 4 * t + 4)
                dve.reciprocal(s, s).then_inc(inv_ready, 1)
                dve.wait_ge(pv_done, 4 * t + 4)
                dve.wait_ge(inv_ready, t + 1)
                if t == nt - 1:
                    dve.wait_ge(blank, 1)
                dve.tensor_tensor(E.on[0:rows, t, :].rearrange("p (h n) -> p h n", h=H_A),
                                  E.PS[0:rows, 7, :].rearrange("p (h n) -> p h n", h=H_A),
                                  s.unsqueeze(2).broadcast_to([rows, H_A, P]), ALU.mult).then_inc(o_ready, 1)

            top(0)
            for i in range(n + 2):
                if i + 1 < n:
                    top(i + 1)
                if i < n:
                    copy(i)
                if i >= 4 and i % 4 == 0:
                    out(i // 4 - 1)

        @block.scalar
        def _(act):
            for i, (t, h) in enumerate(units):
                rows = TOK[t][1]
                act.wait_ge(neg_max, i + 1)
                if i >= 2:
                    act.wait_ge(turned, i - 1)
                act.activation(halves(E.prob2[0:rows, i % 2, :], 2), E.PS[0:rows, 2 * (i % 2):2 * (i % 2) + 2, 0:HALF],
                               ACT.Exp, bias=E.mx2[0:rows, i:i + 1], scale=MLA_SCALE,
                               accum_out=E.sums2[0:rows, i:i + 1]).then_inc(exp_done, 1)
                act.wait_ge(turned, i + 1)
                if i >= 2:
                    act.wait_ge(pv_done, i - 1)
                act.copy(E.probT2[0:N_META, i % 2, 4, 0:rows],
                         E.PS[0:N_META, 6, (i % 2) * P:(i % 2) * P + rows]).then_inc(copied_end, 1)


def mla_out(nc, S, E):
    S.open()
    loaded = S.take("g_loaded")
    own = S.take("norm_steps")
    sq_ready = S.take("sq_ready")
    var_ready = S.take("var_ready")
    std_ready = S.take("std_ready")
    o_ready = S.take("o_ready")
    turned = S.take("turned")
    copied = S.take("copied")
    nt = len(TOK)
    with nc.Block() as block:
        @block.gpsimd
        def _(pool):
            S.clear_old(pool)

        @block.sync
        def _(sp):
            sp.dma_start(E.onorm[:, :], E.A["mla_out_norm_2"][E.li].partition_broadcast(P)).then_inc(loaded, 16)
            sp.wait_ge(loaded, 16)

        @block.scalar
        def _(act):
            act.activation(E.osq[:, :, :], E.on[:, :, :], ACT.Square).then_inc(sq_ready, 1)
            act.wait_ge(var_ready, 1)
            act.activation(E.ovar[:, :], E.ovar[:, :], ACT.Sqrt).then_inc(std_ready, 1)
            for m in range(4):
                act.wait_ge(turned, m + 1)
                act.copy(E.y[:, m, 0:512], E.PS[:, 2 * (m % 2), :])
                act.copy(E.y[:, m, 512:L], E.PS[:, 2 * (m % 2) + 1, 0:N_META]).then_inc(copied, 1)

        @block.vector
        def _(dve):
            c = Chain(dve, own)
            dve.wait_ge(sq_ready, 1)
            c.link(dve.tensor_reduce(E.ovar[:, :], E.osq[:, :, :].rearrange("p t (h n) -> p (t h) n", h=H_A), AX, ALU.add))
            dve.tensor_scalar(E.ovar[:, :], E.ovar[:, :], 1.0 / P, 1e-6, ALU.mult, ALU.add).then_inc(var_ready, 1)
            dve.wait_ge(std_ready, 1)
            c.link(dve.reciprocal(E.ovar[:, :], E.ovar[:, :]))
            v = E.on[:, :, :].rearrange("p t (h n) -> p (t h) n", h=H_A)
            c.link(dve.tensor_tensor(v, v, E.ovar[:, :].unsqueeze(2).broadcast_to([P, nt * H_A, P]), ALU.mult))
            dve.wait_ge(loaded, 16)
            dve.tensor_tensor(E.on[:, :, :], E.on[:, :, :], E.onorm[:, :].unsqueeze(1).broadcast_to([P, nt, 512]),
                              ALU.mult).then_inc(o_ready, 1)

        @block.tensor
        def _(pe):
            pe.wait_ge(o_ready, 1)
            for m in range(4):
                if m >= 2:
                    pe.wait_ge(copied, m - 1)
                for t, (t0, rows) in enumerate(TOK):
                    dst = E.PS[:, 2 * (m % 2) + t // 4, (t % 4) * P:(t % 4) * P + rows]
                    last = pe.transpose(dst, E.on[0:rows, t, m * P:(m + 1) * P], E.ident[0:rows, 0:rows])
                last.then_inc(turned, 1)


def lora_loads(E):
    A, li = E.A, E.li
    flat = E.wring[:, :, :, :].rearrange("p s k m -> p (s k m)")
    E.g2, E.w2, E.a2 = flat[:, 0:512], flat[:, 512:1024], flat[:, 1024:1536]
    E.v1 = flat[:, 1536:1664].rearrange("p (k m) -> p k m", k=4)
    E.v2 = flat[0:32, 1664:2176]
    return [(E.w2, A["rwkv_w2_2"][li].rearrange("d j m -> (d j) m")),
            (E.a2, A["rwkv_a2_2"][li].rearrange("d j m -> (d j) m")),
            (E.g2, A["rwkv_g2_2"][li]),
            (E.v1, A["rwkv_v1_2"][0].rearrange("(k p) m -> p k m", p=P)),
            (E.v2, A["rwkv_v2_2"][0])]


def value_mix(nc, S, E):
    S.open()
    own = S.take("mix_steps")
    low_done = S.take("low_done")
    low_ready = S.take("low_ready")
    up_done = S.take("up_done")
    sig = S.take("sig_ready")
    v, vf, d = E.zr[:, T_V - T_R:T_V - T_R + 4, 0:L], E.vfirst[:, :, :], E.tmp4
    with nc.Block() as block:
        @block.gpsimd
        def _(pool):
            S.clear_old(pool)

        @block.tensor
        def _(pe):
            for k in range(4):
                for a in range(2):
                    last = pe.matmul(E.PS[0:32, a, 0:HALF], E.v1[:, k, :], halves(v[:, k, :], 2)[:, a, :],
                                     start=(k == 0), stop=(k == 3))
            last.then_inc(low_done, 1)
            pe.wait_ge(low_ready, 1)
            for m in range(4):
                if m >= 3:
                    pe.wait_ge(sig, m - 2)
                for a in range(2):
                    last = pe.matmul(E.PS[:, 2 + 2 * (m % 3) + a, 0:HALF], E.v2[:, m * P:(m + 1) * P],
                                     halves(E.low[:, :], 2)[:, a, :], start=True, stop=True)
                last.then_inc(up_done, 1)

        @block.scalar
        def _(act):
            act.wait_ge(low_done, 1)
            act.copy(halves(E.low[:, :], 2), E.PS[0:32, 0:2, 0:HALF]).then_inc(low_ready, 1)
            for m in range(4):
                act.wait_ge(up_done, m + 1)
                b = 2 + 2 * (m % 3)
                act.activation(halves(E.tmp4b[:, m, :], 2), E.PS[:, b:b + 2, 0:HALF], ACT.Sigmoid,
                               bias=E.par[:, Q_V0 + m:Q_V0 + m + 1]).then_inc(sig, 1)

        @block.vector
        def _(dve):
            c = Chain(dve, own)
            c.link(dve.tensor_tensor(d, v, vf, ALU.subtract))
            c.link(dve.scalar_tensor_tensor(vf, d, E.par[:, Q_FIRST:Q_FIRST + 1], vf, ALU.mult, ALU.add))
            c.link(dve.tensor_tensor(d, vf, v, ALU.subtract))
            dve.wait_ge(sig, 4)
            dve.wait_ge(low_done, 1)
            c.link(dve.tensor_tensor(d, d, E.tmp4b, ALU.mult))
            dve.tensor_tensor(v, v, d, ALU.add)


def removal_keys(nc, S, E):
    S.open()
    raw = S.take("raw_ready")
    sq = S.take("sq_ready")
    ssq = S.take("ssq_ready")
    var = S.take("var_ready")
    std = S.take("std_ready")
    inv = S.take("inverse_ready")
    k = E.zr[:, T_K - T_R:T_K - T_R + 4, 0:L]
    with nc.Block() as block:
        @block.gpsimd
        def _(pool):
            S.clear_old(pool)
            pool.memset(E.kk[:, :, L:LP], 0.0)

        @block.tensor
        def _(pe):
            for m in range(4):
                pe.wait_ge(sq, m + 1)
                for a in range(2):
                    last = pe.matmul(E.PS[:, 2 * m + a, 0:HALF], E.head_ones[:, :], halves(E.tmp4[:, m, :], 2)[:, a, :],
                                     start=True, stop=True)
                last.then_inc(ssq, 1)

        @block.scalar
        def _(act):
            for m in range(4):
                act.wait_ge(raw, m + 1)
                act.activation(E.tmp4[:, m, :], E.kk[:, m, 0:L], ACT.Square).then_inc(sq, 1)
            act.wait_ge(var, 4)
            act.activation(E.tmp4, E.tmp4, ACT.Sqrt).then_inc(std, 1)

        @block.vector
        def _(dve):
            for m in range(4):
                dve.tensor_scalar(E.kk[:, m, 0:L], k[:, m, :], E.par[:, Q_KK + m:Q_KK + m + 1], None,
                                  ALU.mult).then_inc(raw, 1)
            for m in range(4):
                dve.wait_ge(ssq, m + 1)
                dve.tensor_scalar(halves(E.tmp4[:, m, :], 2), E.PS[:, 2 * m:2 * m + 2, 0:HALF], 1e-12, None,
                                  ALU.add).then_inc(var, 1)
            dve.wait_ge(std, 1)
            dve.reciprocal(E.tmp4, E.tmp4).then_inc(inv, 1)
            dve.wait_ge(inv, 1)
            dve.tensor_tensor(E.kk[:, :, 0:L], E.kk[:, :, 0:L], E.tmp4, ALU.mult)


def rates(nc, S, E, d):
    S.open()
    act_ready = S.take("tanh_ready")
    w_done = S.take("w_done")
    a_done = S.take("a_done")
    w_sig = S.take("w_sig")
    a_sig = S.take("a_sig")
    blank = S.take("blank")
    own = S.take("rate_steps")
    used = S.take("a_used")
    r = d * 64
    ld, cum, ba, kd = E.ld[d], E.cum[d], E.ba[d], E.kd[:, d]
    k = E.zr[:, T_K - T_R:T_K - T_R + 4, 0:L]
    with nc.Block() as block:
        @block.gpsimd
        def _(pool):
            S.clear_old(pool)
            for x in (ld, ba, kd):
                pool.memset(x[:, :, L:LP], 0.0).then_inc(blank, 1)

        @block.tensor
        def _(pe):
            pe.wait_ge(act_ready, 1)
            for m in range(4):
                if m >= 2:
                    pe.wait_ge(w_sig, m - 1)
                for a in range(2):
                    last = pe.matmul(E.PS[:, 4 * (m % 2) + a, 0:HALF], E.w2[r:r + 64, m * P:(m + 1) * P],
                                     halves(E.lora[:, 0, :], 2)[r:r + 64, a, :], start=True, stop=True)
                last.then_inc(w_done, 1)
                if m >= 2:
                    pe.wait_ge(a_sig, m - 1)
                for a in range(2):
                    last = pe.matmul(E.PS[:, 4 * (m % 2) + 2 + a, 0:HALF], E.a2[r:r + 64, m * P:(m + 1) * P],
                                     halves(E.zs[T_AD], 2)[r:r + 64, a, :], start=True, stop=True)
                last.then_inc(a_done, 1)

        @block.scalar
        def _(act):
            act.activation(E.lora[:, 0, :], E.zs[T_WD], ACT.Tanh).then_inc(act_ready, 1)
            for m in range(4):
                b = 4 * (m % 2)
                act.wait_ge(w_done, m + 1)
                act.activation(halves(ld[:, m, 0:L], 2), E.PS[:, b:b + 2, 0:HALF], ACT.Sigmoid,
                               bias=E.par[:, Q_W0 + 4 * d + m:Q_W0 + 4 * d + m + 1]).then_inc(w_sig, 1)
                act.wait_ge(a_done, m + 1)
                act.activation(halves(ba[:, m, 0:L], 2), E.PS[:, b + 2:b + 4, 0:HALF], ACT.Sigmoid,
                               bias=E.par[:, Q_A0 + 4 * d + m:Q_A0 + 4 * d + m + 1]).then_inc(a_sig, 1)

        @block.vector
        def _(dve):
            c = Chain(dve, own)
            dve.wait_ge(blank, 3)
            for m in range(4):
                dve.wait_ge(w_sig, m + 1)
                c.link(dve.tensor_scalar(ld[:, m, 0:L], ld[:, m, 0:L], -EXP_HALF, None, ALU.mult))
                c.add(dve.tensor_tensor_scan(cum[:, m, :], E.keep[:, :], ld[:, m, :], 0.0, ALU.mult, ALU.add))
                dve.wait_ge(a_sig, m + 1)
                ka = E.par[:, Q_KA + m:Q_KA + m + 1]
                c.link(dve.tensor_scalar(kd[:, m, 0:L], ba[:, m, 0:L], -1.0, ka, ALU.add, ALU.mult))
                c.add(dve.scalar_tensor_tensor(kd[:, m, 0:L], kd[:, m, 0:L], 1.0, k[:, m, :], ALU.add, ALU.mult))
                c.add(dve.tensor_tensor(ba[:, m, 0:L], ba[:, m, 0:L], E.kk[:, m, 0:L], ALU.mult))
            c.wait()
            if d == 1:
                x = cum.rearrange("p m (c n) -> p (m c) n", n=CH)
                c.link(dve.tensor_copy(E.total[:, :], x[:, :, CH - 1]))
                c.link(dve.tensor_tensor(x, E.total[:, :].unsqueeze(2).broadcast_to([P, 4 * N_CH, CH]), x, ALU.subtract))
                c.link(dve.tensor_tensor(cum, cum, ld, ALU.add))


def bonus(nc, S, E):
    S.open()
    own = S.take("bonus_steps")
    x_ready = S.take("x_ready")
    done = S.take("head_sum_done")
    r, v = E.zr[:, 0:4, 0:L], E.zr[:, T_V - T_R:T_V - T_R + 4, 0:L]
    with nc.Block() as block:
        @block.gpsimd
        def _(pool):
            S.clear_old(pool)
            pool.memset(E.zr[:, 0:12, L:LP], 0.0)
            pool.memset(E.state[:, :, :, :], 0.0)

        @block.vector
        def _(dve):
            c = Chain(dve, own)
            for m in range(4):
                c.link(dve.tensor_tensor(E.tmp4[:, m, :], E.kd[:, 0, m, 0:L], E.kd[:, 1, m, 0:L], ALU.add))
                dve.scalar_tensor_tensor(E.tmp4[:, m, :], E.tmp4[:, m, :], E.par[:, Q_RK + m:Q_RK + m + 1], r[:, m, :],
                                         ALU.mult, ALU.mult).then_inc(x_ready, 1)
            for m in range(4):
                dve.wait_ge(done, m + 1)
                dve.tensor_tensor(halves(E.bonus[:, m, :], 2), E.PS[:, 2 * m:2 * m + 2, 0:HALF],
                                  halves(v[:, m, :], 2), ALU.mult)

        @block.tensor
        def _(pe):
            for m in range(4):
                pe.wait_ge(x_ready, m + 1)
                for a in range(2):
                    last = pe.matmul(E.PS[:, 2 * m + a, 0:HALF], E.head_ones[:, :], halves(E.tmp4[:, m, :], 2)[:, a, :],
                                     start=True, stop=True)
                last.then_inc(done, 1)


def recurrence(nc, S, E):
    sweep(nc, S)
    names_a = ["end_ready", "products", "x_turned", "pair_copied", "own_a"]
    names_b = ["before_ready", "exp_ready", "levels_ready", "mk_ready", "own_b"] + [f"{x}_{g}" for g in range(2) for x in (
        "f_done", "f_half", "f_ready", "t1_done", "t1_ready", "x_done", "x_ready", "xt_done", "xt_ready",
        "sa_done", "sa_ready", "y_state", "y_half", "y_done")]
    with ExitStack() as stack:
        a = {x: stack.enter_context(nc.semaphore("chunk_" + x)) for x in names_a}
        b = {x: stack.enter_context(nc.semaphore("chunk_" + x)) for x in names_b}
        prep = Preparation(E, 0, b)
        with nc.Block() as block:
            @block.scalar
            def _(act):
                prep.decays(act, 0)
                prep.decays(act, 1)
                prep.before(act)
                prep.values(act)

            @block.vector
            def _(dve):
                prep.differences(dve)
                prep.removals(dve)

            @block.gpsimd
            def _(pool):
                prep.keys(pool)
        with nc.Fori(0, N_CH - 1) as c:
            _chunk_products(nc, E, a, b)
            _chunk_solve(nc, E, c, a, b, Preparation(E, c + 1, b))
        _chunk_products(nc, E, a, b)
        _chunk_solve(nc, E, N_CH - 1, a, b, None)
        with nc.Block() as block:
            @block.gpsimd
            def _(pool):
                for s in [*a.values(), *b.values()]:
                    pool.sem_clear(s)


class Preparation:

    def __init__(self, E, c, b):
        self.E, self.b = E, b
        self.at = [c * CH, (N_CH - 1 - c) * CH]

    def piece(self, x, d):
        return x[:, :, bass.ds(self.at[d], CH)]

    def decays(self, act, d):
        E = self.E
        act.activation(E.ep[:, :, d, :], self.piece(E.cum[d], d), ACT.Exp).then_inc(self.b["exp_ready"], 1)
        act.activation(E.en[:, :, d, :], self.piece(E.cum[d], d), ACT.Exp, scale=-1.0).then_inc(self.b["exp_ready"], 1)

    def differences(self, dve):
        E = self.E
        for d in range(2):
            dve.tensor_tensor(E.ex[:, :, d, :], self.piece(E.cum[d], d), self.piece(E.ld[d], d),
                              ALU.subtract).then_inc(self.b["before_ready"], 1)

    def before(self, act):
        act.wait_ge(self.b["before_ready"], 2)
        act.activation(self.E.ex, self.E.ex, ACT.Exp).then_inc(self.b["exp_ready"], 1)

    def values(self, act):
        E = self.E
        for d in range(2):
            act.copy(E.vb[:, :, d, :], self.piece(E.zr[:, T_V - T_R:T_V - T_R + 4, :], d))

    def removals(self, dve):
        E = self.E
        dve.wait_ge(self.b["exp_ready"], 5)
        for d in range(2):
            dve.tensor_tensor(E.bb[:, :, d, :], self.piece(E.ba[d], d), E.en[:, :, d, :], ALU.mult)
            dve.tensor_tensor(E.ar[:, :, d, 0, :], self.piece(E.kk, d), E.ex[:, :, d, :], ALU.mult)

    def keys(self, pool):
        E = self.E
        pool.wait_ge(self.b["exp_ready"], 5)
        for d in range(2):
            pool.tensor_tensor(E.ar[:, :, d, 1, :], self.piece(E.zr[:, 0:4, :], d), E.ep[:, :, d, :], ALU.mult)
            pool.tensor_tensor(E.kb[:, :, d, :], self.piece(E.kd[:, d], d), E.en[:, :, d, :], ALU.mult)


def _heads():
    return [(d, h, (h % 2) * 64, d * 64) for h in range(8) for d in range(2)]


def _by_parity(x):
    return x.rearrange("p (m q) n -> p q m n", q=2)


def _pair_masks(E):
    return E.pair[:, :, :].rearrange("p r n -> p (r n)").unsqueeze(1).unsqueeze(1).broadcast_to([P, 2, 4, 2 * CH])


def _both(x):
    return _by_parity(x.rearrange("p h r n -> p h (r n)"))


MK_BANKS = (3, 7)


def _chunk_products(nc, E, a, b):
    ar, bb, kb, vb = E.ar, E.bb, E.kb, E.vb
    with nc.Block() as block:
        @block.gpsimd
        def _(pool):
            for s in b.values():
                pool.sem_clear(s)

        @block.vector
        def _(dve):
            for d in range(2):
                dve.tensor_copy(E.pend[:, :, d], E.ep[:, :, d, CH - 1 if d == 0 else 0])
            own = Chain(dve, a["own_a"])
            eye = E.eye2[:, :].unsqueeze(1).broadcast_to([P, 8, CH])
            m0 = E.level[:, 0, 0, :].unsqueeze(1).broadcast_to([P, 8, CH])
            dve.wait_ge(a["products"], 1)
            own.link(dve.tensor_tensor(_by_parity(E.x), E.PS[:, 0:2, 0:4 * CH].rearrange("p q (m n) -> p q m n", m=4),
                                       _by_parity(m0), ALU.mult))
            own.add(dve.tensor_tensor(E.x[:, :, :], eye, E.x[:, :, :], ALU.subtract))
            dve.wait_ge(a["products"], 2)
            own.link(dve.tensor_tensor(_both(E.lb), E.PS[:, 4:6, :].rearrange("p q (m n) -> p q m n", m=4),
                                       _pair_masks(E), ALU.mult))
            m0t = E.level[:, 1, 0, :].unsqueeze(1).broadcast_to([P, 8, CH])
            m1t = E.level[:, 1, 1, :].unsqueeze(1).broadcast_to([P, 8, CH])
            own.add(dve.tensor_tensor(E.mjt[0], E.lb[:, :, 0, :], m1t, ALU.mult))
            own.link(dve.tensor_tensor(E.xt[:, :, :], E.lb[:, :, 0, :], m0t, ALU.mult))
            dve.tensor_tensor(E.xt[:, :, :], eye, E.xt[:, :, :], ALU.subtract)

        @block.scalar
        def _(act):
            for n, dst in enumerate((E.vtok, E.btok, E.ktok)):
                act.wait_ge(a["x_turned"], n + 1)
                act.copy(dst[:, :], E.PS[:, (6, 2, 6)[n], :]).then_inc(a["pair_copied"], 1)

        @block.tensor
        def _(pe):
            def turn(src, bank):
                for hp in range(4):
                    last = pe.transpose(E.PS[:, bank, hp * P:(hp + 1) * P],
                                        src[:, hp, :, :].rearrange("p d n -> p (d n)"), E.ident[:, :])
                last.then_inc(a["x_turned"], 1)
            for d, h, hr, tr in _heads():
                last = pe.matmul(E.PS[tr:tr + CH, h % 2, (h // 2) * CH:(h // 2 + 1) * CH], ar[hr:hr + 64, h // 2, d, 0, :],
                                 bb[hr:hr + 64, h // 2, d, :], start=True, stop=True)
            last.then_inc(a["products"], 1)

            def pairs(src, banks):
                for d, h, hr, tr in _heads():
                    last = pe.matmul(E.PS[tr:tr + CH, banks[h % 2], (h // 2) * 2 * CH:(h // 2 + 1) * 2 * CH],
                                     src[hr:hr + 64, h // 2, d, :],
                                     ar[hr:hr + 64, h // 2, d, :, :].rearrange("p r n -> p (r n)"),
                                     start=True, stop=True)
                return last
            pairs(bb, (4, 5)).then_inc(a["products"], 1)
            turn(vb, 6)
            turn(bb, 2)
            pairs(kb, MK_BANKS)
            pe.wait_ge(a["pair_copied"], 1)
            turn(kb, 6)


def _chunk_solve(nc, E, c, a, b, prep):
    at = [c * CH, (N_CH - 1 - c) * CH]

    def group(x, g):
        return _by_parity(x)[:, g]

    def psum(g, bank):
        return E.PS[:, 4 * g + bank, 0:256].rearrange("p (m n) -> p m n", m=4)
    with nc.Block() as block:
        @block.gpsimd
        def _(pool):
            for s in a.values():
                pool.sem_clear(s)
            for j in range(2, LEVELS):
                mj = E.level[:, 1, j, :].unsqueeze(1).broadcast_to([P, 8, CH])
                pool.tensor_tensor(E.mjt[j - 1], E.lb[:, :, 0, :], mj, ALU.mult).then_inc(b["levels_ready"], 1)
            if prep:
                for g in range(2):
                    pool.wait_ge(b[f"f_done_{g}"], 1)
                prep.keys(pool)

        @block.tensor
        def _(pe):
            def tokens_product(g, bank, left, right):
                for m in range(4):
                    for d in range(2):
                        tr, h, col = d * CH, 2 * m + g, m * CH
                        last = pe.matmul(E.PS[tr:tr + CH, 4 * g + bank, col:col + CH], left[tr:tr + CH, h, :],
                                         right[tr:tr + CH, h, :], start=True, stop=True)
                return last

            def by_head(x):
                return x.rearrange("p (h n) -> p h n", h=8)

            def old_state():
                for g in range(2):
                    hr = g * 64
                    for m in range(4):
                        for d in range(2):
                            cols = (m * 2 + d) * CH
                            last = pe.matmul(E.PS[hr:hr + 64, 4 * g + 2, cols:cols + CH], E.state[hr:hr + 64, m, d, :],
                                             E.ar[hr:hr + 64, m, d, 1, :], start=True, stop=True)
                    last.then_inc(b[f"y_state_{g}"], 1)
                for g in range(2):
                    pe.wait_ge(b["mk_ready"], g + 1)
                    hr = g * 64
                    for m in range(4):
                        for d in range(2):
                            pe.matmul(E.PS[d * CH:d * CH + CH, 4 * g + 3, m * CH:(m + 1) * CH],
                                      E.ar[hr:hr + 64, m, d, 0, :], E.state[hr:hr + 64, m, d, :],
                                      start=True, stop=True)
                    tokens_product(g, 1, E.mk[:, :, 0, :], by_head(E.vtok)).then_inc(b[f"f_done_{g}"], 1)

            for j in range(1, LEVELS):
                if j > 1:
                    pe.wait_ge(b["levels_ready"], j - 1)
                for g in range(2):
                    if j > 1:
                        pe.wait_ge(b[f"x_ready_{g}"], j - 1)
                    tokens_product(g, 0, E.mjt[j - 1], E.x).then_inc(b[f"t1_done_{g}"], 1)
                if j == 1:
                    old_state()
                for g in range(2):
                    pe.wait_ge(b[f"t1_ready_{g}"], j)
                    if j > 1:
                        pe.wait_ge(b[f"xt_ready_{g}"], j - 1)
                    else:
                        pe.wait_ge(b[f"f_half_{g}"], 1)
                        pe.wait_ge(b[f"y_half_{g}"], 2)
                    if j < LEVELS - 1:
                        tokens_product(g, 1, E.xt, E.t1).then_inc(b[f"x_done_{g}"], 1)
                    tokens_product(g, 2, E.t1, E.xt).then_inc(b[f"xt_done_{g}"], 1)
            for g in range(2):
                pe.wait_ge(b[f"f_ready_{g}"], 1)
                pe.wait_ge(b[f"xt_ready_{g}"], LEVELS - 1)
                tokens_product(g, 0, E.xt, E.f).then_inc(b[f"sa_done_{g}"], 1)
            for g in range(2):
                hr = g * 64
                pe.wait_ge(b[f"sa_ready_{g}"], 1)
                for m in range(4):
                    for d in range(2):
                        tr, h = d * CH, 2 * m + g
                        dst = E.PS[hr:hr + 64, 4 * g + 1 + d, m * CH:(m + 1) * CH]
                        pe.matmul(dst, E.ktok[tr:tr + CH, h * CH:(h + 1) * CH], E.vtok[tr:tr + CH, h * CH:(h + 1) * CH],
                                  start=True, stop=False)
                        pe.matmul(dst, E.btok[tr:tr + CH, h * CH:(h + 1) * CH], E.sa[tr:tr + CH, h, :],
                                  start=False, stop=True)
                for m in range(4):
                    for d in range(2):
                        tr, h = d * CH, 2 * m + g
                        dst = E.PS[hr:hr + 64, 4 * g + 1 + d, 256 + m * CH:256 + (m + 1) * CH]
                        pe.matmul(dst, E.vtok[tr:tr + CH, h * CH:(h + 1) * CH], E.mk[tr:tr + CH, h, 1, :],
                                  start=True, stop=False)
                        last = pe.matmul(dst, E.sa[tr:tr + CH, h, :], E.lb[tr:tr + CH, h, 1, :], start=False, stop=True)
                last.then_inc(b[f"y_done_{g}"], 1)

        @block.scalar
        def _(act):
            for j in range(1, LEVELS):
                for g in range(2):
                    act.wait_ge(b[f"t1_done_{g}"], j)
                    act.copy(group(E.t1, g), psum(g, 0)).then_inc(b[f"t1_ready_{g}"], 1)
                if j == 1:
                    for g in range(2):
                        hr = slice(g * 64, g * 64 + 64)
                        act.wait_ge(b[f"y_state_{g}"], 1)
                        y = E.PS[hr, 4 * g + 2, :].rearrange("p (m d n) -> p m d n", m=4, d=2)
                        for d in range(2):
                            act.copy(E.ba[d][hr, :, bass.ds(at[d], CH)], y[:, :, d, :]).then_inc(b[f"y_half_{g}"], 1)
                    for g in range(2):
                        act.wait_ge(b[f"f_done_{g}"], 1)
                        act.copy(group(E.f, g), psum(g, 1)).then_inc(b[f"f_half_{g}"], 1)
                if prep and j == 2:
                    prep.decays(act, 0)
                if prep and j == 3:
                    prep.decays(act, 1)
                if prep and j == 4:
                    prep.before(act)
                    prep.values(act)
            for g in range(2):
                act.wait_ge(b[f"sa_done_{g}"], 1)
                act.mul(group(E.sa, g), psum(g, 0), -1.0).then_inc(b[f"sa_ready_{g}"], 1)

        @block.vector
        def _(dve):
            def subtract(x, g, bank, ready):
                dve.tensor_tensor(group(x, g), group(x, g), psum(g, bank), ALU.subtract).then_inc(ready, 1)
            for q, bank in enumerate(MK_BANKS):
                dve.tensor_tensor(_both(E.mk)[:, q], E.PS[:, bank, :].rearrange("p (m n) -> p m n", m=4),
                                  _pair_masks(E)[:, q], ALU.mult).then_inc(b["mk_ready"], 1)
            for g in range(2):
                dve.wait_ge(b[f"f_half_{g}"], 1)
                dve.tensor_tensor(group(E.f, g), group(E.f, g), psum(g, 3), ALU.add).then_inc(b[f"f_ready_{g}"], 1)
            for j in range(1, LEVELS):
                for g in range(2):
                    if j < LEVELS - 1:
                        dve.wait_ge(b[f"x_done_{g}"], j)
                        subtract(E.x, g, 1, b[f"x_ready_{g}"])
                    dve.wait_ge(b[f"xt_done_{g}"], j)
                    subtract(E.xt, g, 2, b[f"xt_ready_{g}"])
                if prep and j == 2:
                    prep.differences(dve)
            if prep:
                prep.removals(dve)
            for g in range(2):
                hr = slice(g * 64, g * 64 + 64)
                st = E.state[hr, :, :, :]
                dve.wait_ge(b[f"y_done_{g}"], 1)
                dve.tensor_tensor(st, st, E.PS[hr, 4 * g + 1:4 * g + 3, 0:256].rearrange("p d (m n) -> p m d n", m=4),
                                  ALU.add).then_inc(b["own_b"], 1)
                for d in range(2):
                    y = E.ba[d][hr, :, bass.ds(at[d], CH)]
                    dve.tensor_tensor(y, y, E.PS[hr, 4 * g + 1 + d, 256:512].rearrange("p (m n) -> p m n", m=4), ALU.add)
                dve.wait_ge(b["own_b"], g + 1)
                dve.tensor_tensor(st, st, E.pend[hr, :, :].unsqueeze(3).broadcast_to([64, 4, 2, CH]), ALU.mult)


def head_norm(nc, S, E):
    S.open()
    y_ready = S.take("y_ready")
    mean_done = S.take("mean_done")
    xc_ready = S.take("xc_ready")
    sq_ready = S.take("sq_ready")
    var_done = S.take("var_done")
    var_ready = S.take("var_ready")
    std_ready = S.take("std_ready")
    inv = S.take("inverse_ready")
    own = S.take("norm_steps")
    g_in = S.take("g_in_ready")
    g_done = S.take("g_done")
    biased = S.take("biased")
    yf, yb = E.ba
    out = E.y[:, 4:8, :]
    x = E.tmp8a
    sq = E.tmp8b
    with nc.Block() as block:
        @block.gpsimd
        def _(pool):
            S.clear_old(pool)
            for m in range(4):
                pool.tensor_tensor(x[:, m, :], yf[:, m, 0:L], yb[:, m, 0:L], ALU.add).then_inc(y_ready, 1)

        @block.tensor
        def _(pe):
            for m in range(4):
                pe.wait_ge(y_ready, m + 1)
                for a in range(2):
                    last = pe.matmul(E.PS[:, 2 * m + a, 0:HALF], E.head_mean[:, :], halves(x[:, m, :], 2)[:, a, :],
                                     start=True, stop=True)
                last.then_inc(mean_done, 1)
            for m in range(4):
                pe.wait_ge(sq_ready, m + 1)
                for a in range(2):
                    last = pe.matmul(E.PS[:, 2 * m + a, 0:HALF], E.head_mean[:, :], halves(sq[:, m, :], 2)[:, a, :],
                                     start=True, stop=True)
                last.then_inc(var_done, 1)
            pe.wait_ge(g_in, 1)
            for m in range(4):
                pe.wait_ge(var_ready, m + 1)
                for a in range(2):
                    last = pe.matmul(E.PS[:, 2 * m + a, 0:HALF], E.g2[:, m * P:(m + 1) * P],
                                     halves(E.lora[:, 1, :], 2)[:, a, :], start=True, stop=True)
                last.then_inc(g_done, 1)

        @block.scalar
        def _(act):
            act.activation(E.lora[:, 1, :], E.zs[T_GD], ACT.Sigmoid).then_inc(g_in, 1)
            for m in range(4):
                act.wait_ge(xc_ready, m + 1)
                act.activation(sq[:, m, :], x[:, m, :], ACT.Square).then_inc(sq_ready, 1)
            act.wait_ge(var_ready, 4)
            act.activation(sq, sq, ACT.Sqrt).then_inc(std_ready, 1)

        @block.vector
        def _(dve):
            c = Chain(dve, own)
            for m in range(4):
                dve.wait_ge(mean_done, m + 1)
                dve.tensor_tensor(halves(x[:, m, :], 2), halves(x[:, m, :], 2), E.PS[:, 2 * m:2 * m + 2, 0:HALF],
                                  ALU.subtract).then_inc(xc_ready, 1)
            for m in range(4):
                dve.wait_ge(var_done, m + 1)
                dve.tensor_scalar(halves(sq[:, m, :], 2), E.PS[:, 2 * m:2 * m + 2, 0:HALF], 64e-5, None,
                                  ALU.add).then_inc(var_ready, 1)
            dve.wait_ge(std_ready, 1)
            dve.reciprocal(sq, sq).then_inc(inv, 1)
            dve.wait_ge(inv, 1)
            for m in range(4):
                c.link(dve.scalar_tensor_tensor(x[:, m, :], x[:, m, :], E.par[:, Q_GG + m:Q_GG + m + 1], sq[:, m, :],
                                                ALU.mult, ALU.mult))
                c.link(dve.scalar_tensor_tensor(x[:, m, :], x[:, m, :], E.par[:, Q_GB + m:Q_GB + m + 1],
                                                E.bonus[:, m, :], ALU.add, ALU.add))
                dve.wait_ge(g_done, m + 1)
                dve.tensor_tensor(halves(out[:, m, :], 2), halves(x[:, m, :], 2), E.PS[:, 2 * m:2 * m + 2, 0:HALF],
                                  ALU.mult)


def route(nc, S, E):
    S.open()
    loaded = S.take("w_loaded")
    blank = S.take("blank")
    done = S.take("logits_done")
    own = S.take("route_steps")
    e_in = S.take("exp_in")
    e_out = S.take("exp_out")
    g_ready = S.take("gates_ready")
    turned = S.take("turned")
    copied = S.take("copied")
    stored = S.take("stored")
    nt = len(TOK)
    R = E.router
    wr = R[:, 0:288].rearrange("p (k m) -> p k m", k=KT)
    bias = R[:, 288:324]
    at = [324]

    def buf(*shape):
        n = int(np.prod(shape))
        x = R[:, at[0]:at[0] + n]
        at[0] += n
        if len(shape) == 2:
            return x.rearrange("p (a b) -> p a b", a=shape[0])
        return x
    lg = buf(nt, 36)
    gl, gx, gs, gc = (buf(nt, 4) for _ in range(4))
    el, ex, s1, s2, cum = (buf(nt, 32) for _ in range(5))
    gm, gsum, m1, m2, z = (buf(nt) for _ in range(5))
    keep_g, keep_e = buf(20), buf(160)
    E.sel = [buf(nt, 32), buf(nt, 32)]
    E.gates = [buf(nt), buf(nt)]
    valid = buf(nt)
    E.router_used = at[0]

    def over(x, n):
        return x.unsqueeze(2).broadcast_to([P, nt, n])

    def flat(x):
        return x.rearrange("p a b -> p (a b)")
    with nc.Block() as block:
        @block.gpsimd
        def _(pool):
            S.clear_old(pool)
            pool.memset(lg, 0.0).then_inc(blank, 1)

        @block.sync
        def _(sp):
            A, li = E.A, E.li
            sp.dma_start(wr[:, :, 0:4], A["moe_w_group_2"][li].rearrange("(k p) m -> p k m", p=P)).then_inc(loaded, 16)
            sp.dma_start(wr[:, :, 4:36], A["moe_w_expert_2"][li].rearrange("(k p) m -> p k m", p=P)).then_inc(loaded, 16)
            sp.dma_start(bias[:, 0:4], A["moe_b_group_2"][li].partition_broadcast(P)).then_inc(loaded, 16)
            sp.dma_start(bias[:, 4:36], A["moe_b_expert_2"][li].partition_broadcast(P)).then_inc(loaded, 16)
            sp.dma_start(keep_g, A["keep_group"]).then_inc(loaded, 16)
            sp.dma_start(keep_e, A["keep_expert"]).then_inc(loaded, 16)
            sp.dma_start(valid, A["valid_token"]).then_inc(loaded, 16)
            sp.wait_ge(copied, 2)
            sp.dma_start(E.gates_dram, E.gT[:, :]).then_inc(stored, 16)
            sp.wait_ge(stored, 16)

        @block.tensor
        def _(pe):
            pe.wait_ge(loaded, 112)
            for t, (t0, rows) in enumerate(TOK):
                for k in range(KT):
                    last = pe.matmul(E.PS[0:rows, 0, t * 36:(t + 1) * 36], E.h[:, k, t0:t0 + rows], wr[:, k, :],
                                     start=(k == 0), stop=(k == KT - 1))
            last.then_inc(done, 1)
            pe.wait_ge(g_ready, 1)
            for t, (t0, rows) in enumerate(TOK):
                last = pe.transpose(E.PS[0:32, 1 + t // 4, (t % 4) * P:(t % 4) * P + rows], ex[0:rows, t, :],
                                    E.ident[0:rows, 0:rows])
            last.then_inc(turned, 1)

        @block.scalar
        def _(act):
            act.wait_ge(e_in, 1)
            act.activation(gx, gx, ACT.Exp).then_inc(e_out, 1)
            act.wait_ge(e_in, 2)
            act.activation(ex, ex, ACT.Exp).then_inc(e_out, 1)
            act.wait_ge(e_in, 3)
            act.activation(m2, m2, ACT.Exp).then_inc(e_out, 1)
            act.wait_ge(turned, 1)
            act.copy(E.gT[:, 0:512], E.PS[0:32, 1, :]).then_inc(copied, 1)
            act.copy(E.gT[:, 512:L], E.PS[0:32, 2, 0:N_META]).then_inc(copied, 1)

        @block.vector
        def _(dve):
            c = Chain(dve, own)
            tt, ts, stt = dve.tensor_tensor, dve.tensor_scalar, dve.scalar_tensor_tensor
            dve.wait_ge(blank, 1)
            dve.wait_ge(loaded, 112)
            dve.wait_ge(done, 1)
            for t, (_, rows) in enumerate(TOK):
                c.add(tt(lg[0:rows, t, :], E.PS[0:rows, 0, t * 36:(t + 1) * 36], bias[0:rows, :], ALU.add))
            c.wait()
            c.link(dve.tensor_copy(gl, lg[:, :, 0:4]))
            c.link(dve.tensor_reduce(gm, gl, AX, ALU.max))
            tt(gx, gl, over(gm, 4), ALU.subtract).then_inc(e_in, 1)
            c.link(tt(gs, gl, over(gm, 4), ALU.is_equal))
            c.link(dve.tensor_tensor_scan(flat(gc), keep_g, flat(gs), 0.0, ALU.mult, ALU.add))
            c.link(stt(gs, gc, 1.0, gs, ALU.is_le, ALU.mult))
            c.link(ts(gs, gs, BIG, -BIG, ALU.mult, ALU.add))
            c.link(tt(el.rearrange("p a (g n) -> p a g n", g=4), lg[:, :, 4:36].rearrange("p a (g n) -> p a g n", g=4),
                      gs.unsqueeze(3).broadcast_to([P, nt, 4, 8]), ALU.add))
            c.link(dve.tensor_reduce(m1, el, AX, ALU.max))
            tt(ex, el, over(m1, 32), ALU.subtract).then_inc(e_in, 1)

            def first_of(sel, top):
                c.link(tt(sel, el, over(top, 32), ALU.is_equal))
                c.link(dve.tensor_tensor_scan(flat(cum), keep_e, flat(sel), 0.0, ALU.mult, ALU.add))
                c.link(stt(sel, cum, 1.0, sel, ALU.is_le, ALU.mult))
            first_of(s1, m1)
            c.link(stt(el, s1, -3 * BIG, el, ALU.mult, ALU.add))
            c.link(dve.tensor_reduce(m2, el, AX, ALU.max))
            first_of(s2, m2)
            c.add(tt(E.sel[0], s1, over(valid, 32), ALU.mult))
            c.link(tt(E.sel[1], s2, over(valid, 32), ALU.mult))
            tt(m2, m2, m1, ALU.subtract).then_inc(e_in, 1)
            dve.wait_ge(e_out, 2)
            c.add(dve.tensor_reduce(gsum, gx, AX, ALU.add))
            c.link(dve.tensor_reduce(z, ex, AX, ALU.add))
            c.link(tt(z, z, gsum, ALU.mult))
            c.link(dve.reciprocal(z, z))
            dve.wait_ge(e_out, 3)
            c.add(dve.tensor_copy(E.gates[0], z))
            c.add(tt(E.gates[1], z, m2, ALU.mult))
            c.link(tt(s2, s2, over(m2, 32), ALU.mult))
            c.link(tt(s1, s1, s2, ALU.add))
            tt(ex, s1, over(z, 32), ALU.mult).then_inc(g_ready, 1)


def dispatch(nc, S, E):
    S.open()
    loaded = S.take("tables_loaded")
    blank = S.take("none_ready")
    both = S.take("both_ready")
    counted = S.take("counted")
    own = S.take("place_steps")
    placed = S.take("places_ready")
    cleared = S.take("lists_cleared")
    listed = S.take_own("choices_listed")
    fetched = S.take_own("lists_fetched")
    turned = S.take("tokens_turned")
    copied = S.take("tokens_copied")
    stored = S.take("tokens_stored")
    nt = len(TOK)
    R = E.router
    at = [E.router_used]

    def buf(n):
        at[0] += n
        return R[:, at[0] - n:at[0]]
    before, expert, beyond, choice = buf(P), buf(160), buf(10), buf(10)
    both_sel, within, at_place, earlier, total = buf(160), buf(160), buf(160), buf(160), buf(160)
    dest_f, top = buf(10), buf(1)
    dest = buf(10).bitcast(I32)
    none, lists, over_l = buf(32), buf(32), buf(32)
    E.choice_list, E.token_list = (buf(32).bitcast(I32) for _ in range(2))

    def by_tile(x):
        return x.rearrange("p (t e) -> p t e", t=nt)
    flat_sel = [x.rearrange("p t e -> p (t e)") for x in E.sel]
    lists_dram = E.list_dram.rearrange("(s e) o -> s (e o)", e=N_EXP)
    with nc.Block() as block:
        @block.sync
        def _(sp):
            A = E.A
            for dst, name in ((before, "before"), (expert, "expert_index"), (beyond, "beyond"), (choice, "choice")):
                sp.dma_start(dst, A[name]).then_inc(loaded, 16)
            sp.wait_ge(blank, 1)
            sp.dma_start(lists_dram, none[0:CAP, :]).then_inc(cleared, 16)
            for t, (t0, rows) in enumerate(TOK):
                sp.wait_ge(copied, 2 * t + 2)
                sp.dma_start(E.h_dram[t0:t0 + rows, :], E.natural[0:rows, t, :]).then_inc(stored, 16)
            sp.wait_ge(stored, 16 * nt)

        @block.gpsimd
        def _(pool):
            S.clear_old(pool)
            pool.memset(none, float(16 * L)).then_inc(blank, 1)
            pool.wait_ge(cleared, 16)
            pool.wait_ge(placed, 1)
            for q in range(2 * nt):
                pool.indirect_dma_start(
                    out=E.list_dram[:, :], out_offset=bass.IndirectOffsetOnAxis(ap=dest[:, q:q + 1], axis=0),
                    in_=choice[:, q:q + 1], in_offset=None, bounds_check=CAP * N_EXP - 1,
                    oob_is_err=False).then_inc(listed, 16)
            pool.wait_ge(listed, 16 * 2 * nt)
            pool.dma_start(lists[0:CAP, :], lists_dram).then_inc(fetched, 16)
            pool.wait_ge(fetched, 16)

        @block.tensor
        def _(pe):
            pe.wait_ge(loaded, 64)
            pe.wait_ge(both, 1)
            pe.matmul(E.PS[:, 0, 0:160], before, both_sel, start=True, stop=True)
            pe.matmul(E.PS[:, 1, 0:160], E.ones[:, :], both_sel, start=True, stop=True).then_inc(counted, 1)
            for t, (t0, rows) in enumerate(TOK):
                b = 2 + 2 * (t % 3)
                if t >= 3:
                    pe.wait_ge(copied, 2 * t - 4)
                for k in range(KT):
                    last = pe.transpose(E.PS[0:rows, b + k // 4, (k % 4) * P:(k % 4 + 1) * P], E.h[:, k, t0:t0 + rows],
                                        E.ident[:, :])
                last.then_inc(turned, 1)

        @block.scalar
        def _(act):
            for t, (t0, rows) in enumerate(TOK):
                b = 2 + 2 * (t % 3)
                act.wait_ge(turned, t + 1)
                for a in range(2):
                    act.copy(E.natural[0:rows, t, a * 512:(a + 1) * 512], E.PS[0:rows, b + a, :]).then_inc(copied, 1)

        @block.vector
        def _(dve):
            c = Chain(dve, own)
            dve.tensor_tensor(both_sel, flat_sel[0], flat_sel[1], ALU.add).then_inc(both, 1)
            dve.wait_ge(counted, 1)
            c.add(dve.tensor_copy(total, E.PS[:, 1, 0:160]))
            c.link(dve.memset(earlier[:, 0:32], 0.0))
            for t in range(1, nt):
                c.link(dve.tensor_tensor(by_tile(earlier)[:, t, :], by_tile(earlier)[:, t - 1, :],
                                         by_tile(total)[:, t - 1, :], ALU.add))
            c.link(dve.tensor_tensor(within, E.PS[:, 0, 0:160], earlier, ALU.add))
            dve.wait_ge(loaded, 64)
            c.link(dve.scalar_tensor_tensor(within, within, float(N_EXP), expert, ALU.mult, ALU.add))
            for w in range(2):
                c.link(dve.tensor_tensor(at_place, within, flat_sel[w], ALU.mult))
                c.link(dve.tensor_reduce(dest_f[:, w * nt:(w + 1) * nt], by_tile(at_place), AX, ALU.add))
            c.link(dve.tensor_tensor(dest_f, dest_f, beyond, ALU.add))
            dve.tensor_copy(dest, dest_f).then_inc(placed, 1)
            c.link(dve.tensor_tensor(total[:, 0:32], by_tile(earlier)[:, nt - 1, :], by_tile(total)[:, nt - 1, :],
                                     ALU.add))
            c.link(dve.tensor_reduce(top, total[:, 0:32], AX, ALU.max))
            c.link(dve.tensor_copy(E.most[:, :], top))
            dve.wait_ge(fetched, 16)
            c.link(dve.tensor_scalar(over_l[0:CAP], lists[0:CAP], float(L), float(-L), ALU.is_ge, ALU.mult))
            c.add(dve.tensor_copy(E.choice_list[0:CAP], lists[0:CAP]))
            c.link(dve.tensor_tensor(over_l[0:CAP], over_l[0:CAP], lists[0:CAP], ALU.add))
            dve.tensor_copy(E.token_list[0:CAP], over_l[0:CAP])


def experts(nc, S, E):
    S.open()
    sparse, dense = SparseExperts(S, E), DenseExperts(S, E)
    with nc.Block() as block:
        @block.gpsimd
        def _(pool):
            S.clear_old(pool)
            most = pool.value_load(E.most[0:1, 0:1])
            with pool.If(most > CAP):
                pass
            with pool.Else():
                sparse.pool(pool)

        @block.sync
        def _(sp):
            most = sp.value_load(E.most[0:1, 0:1])
            with sp.If(most > CAP):
                dense.sync(sp)
            with sp.Else():
                sparse.sync(sp)

        @block.tensor
        def _(pe):
            most = pe.value_load(E.most[0:1, 0:1])
            with pe.If(most > CAP):
                dense.tensor(pe)
            with pe.Else():
                sparse.tensor(pe)

        @block.scalar
        def _(act):
            most = act.value_load(E.most[0:1, 0:1])
            with act.If(most > CAP):
                dense.scalar(act)
            with act.Else():
                sparse.scalar(act)

        @block.vector
        def _(dve):
            most = dve.value_load(E.most[0:1, 0:1])
            with dve.If(most > CAP):
                dense.vector(dve)
            with dve.Else():
                sparse.vector(dve)


class SparseExperts:

    def __init__(self, S, E):
        self.E = E
        self.w13_loaded = [S.take("w13_loaded_0"), S.take("w13_loaded_1")]
        self.w2_loaded = [S.take("w2_loaded_0"), S.take("w2_loaded_1")]
        self.x_blank = S.take("x_blank")
        self.x_indexed, self.y_indexed = S.take("x_indexed"), S.take("y_indexed")
        self.x_gathered = [S.take_own("x_gathered_0"), S.take_own("x_gathered_1")]
        self.x_turned = S.take("x_turned")
        self.x_act = S.take("x_copied_act")
        self.x_dve = S.take("x_copied_dve")
        self.h_done = S.take("h_done")
        self.silu_done = S.take("h_silu")
        self.hid_done = S.take("hid_done")
        self.hid_turned = S.take("hid_turned")
        self.hid_copied = S.take("hid_copied")
        self.y_done = S.take("y_done")
        self.y_act = S.take("y_copied_act")
        self.y_dve = S.take("y_copied_dve")
        self.y_stored = [S.take_own("y_stored_0"), S.take_own("y_stored_1")]
        A, li = E.A, E.li
        self.w1 = A["moe_w1_2"][li].rearrange("e (p k) m -> e p k m", p=P)
        self.w3 = A["moe_w3_2"][li].rearrange("e (p k) m -> e p k m", p=P)
        self.w2 = A["moe_w2_2"][li].rearrange("e (p k) m -> e p k m", p=P)
        self.w2s = E.wring[:, :, :, :].rearrange("p s k m -> p s (k m)").rearrange("p s (k m) -> p s k m", k=2)

    @staticmethod
    def in_turn(eng, body):
        body(0, 0, 0)
        with eng.Fori(0, N_EXP // 2 - 1) as i:
            body(i * 2 + 1, 1, i)
            body(i * 2 + 2, 0, i + 1)
        body(N_EXP - 1, 1, N_EXP // 2 - 1)

    @staticmethod
    def neighbours(j, slot, turn):
        first = isinstance(j, int) and j == 0
        last = isinstance(j, int) and j == N_EXP - 1
        before = None if first else (1 - slot, turn if slot else turn - 1)
        after = None if last else (1 - slot, turn + 1 if slot else turn)
        return before, after

    def sync(self, sp):
        E = self.E

        def load_13(j, slot):
            sp.dma_start(E.w13[:, slot, 0], self.w1[j]).then_inc(self.w13_loaded[slot], 16)
            sp.dma_start(E.w13[:, slot, 1], self.w3[j]).then_inc(self.w13_loaded[slot], 16)

        def load_2(j, slot):
            sp.dma_start(self.w2s[:, slot], self.w2[j]).then_inc(self.w2_loaded[slot], 16)
        for j in range(2):
            load_13(j, j)
            load_2(j, j)
        with sp.Fori(0, N_EXP // 2 - 1) as i:
            for slot in range(2):
                sp.wait_ge(self.h_done, i * 2 + (slot + 1))
                load_13(i * 2 + (slot + 2), slot)
                sp.wait_ge(self.y_done, i * 2 + (slot + 1))
                load_2(i * 2 + (slot + 2), slot)

    def pool(self, pool):
        E = self.E

        def gather(j, slot):
            pool.tensor_copy(E.x_index[:, slot:slot + 1], E.token_list[:, bass.ds(j, 1)]).then_inc(self.x_indexed, 1)
            pool.wait_ge(self.x_indexed, 1)
            pool.sem_clear(self.x_indexed)
            pool.indirect_dma_start(
                out=E.xg[:, slot, :], out_offset=None, in_=E.h_dram[:, :],
                in_offset=bass.IndirectOffsetOnAxis(ap=E.x_index[:, slot:slot + 1], axis=0),
                bounds_check=L - 1, oob_is_err=False).then_inc(self.x_gathered[slot], 16)

        def scatter(j, slot):
            pool.wait_ge(self.y_act, j + 2)
            pool.wait_ge(self.y_dve, j + 2)
            pool.tensor_copy(E.y_index[:, slot:slot + 1], E.choice_list[:, bass.ds(j, 1)]).then_inc(self.y_indexed, 1)
            pool.wait_ge(self.y_indexed, 1)
            pool.sem_clear(self.y_indexed)
            pool.indirect_dma_start(
                out=E.out_dram[:, :], out_offset=bass.IndirectOffsetOnAxis(ap=E.y_index[:, slot:slot + 1], axis=0),
                in_=E.yo[:, slot, :], in_offset=None,
                bounds_check=2 * L - 1, oob_is_err=False).then_inc(self.y_stored[slot], 16)
        pool.memset(E.xg, 0.0).then_inc(self.x_blank, 1)
        pool.wait_ge(self.x_blank, 1)
        gather(0, 0)

        def body(j, slot, turn):
            before, after = self.neighbours(j, slot, turn)
            if after:
                if before:
                    pool.wait_ge(self.x_turned, j)
                gather(j + 1, after[0])
            if before:
                scatter(j - 1, before[0])
        self.in_turn(pool, body)
        scatter(N_EXP - 1, 1)
        for slot in range(2):
            pool.wait_ge(self.y_stored[slot], 16 * (N_EXP // 2))

    def tensor(self, pe):
        E = self.E

        def turn_x(j, slot, turn):
            pe.wait_ge(self.x_gathered[slot], turn * 16 + 16)
            x = E.xg[:, slot, :].rearrange("s (p k) -> s k p", k=KT)
            for k in range(KT):
                last = pe.transpose(E.PS[:, k // 4, (k % 4) * P:(k % 4 + 1) * P], x[:, k, :], E.ident[:, :])
            last.then_inc(self.x_turned, 1)

        def hidden(j, slot, turn):
            pe.wait_ge(self.w13_loaded[slot], turn * 32 + 32)
            pe.wait_ge(self.x_act, j + 1)
            pe.wait_ge(self.x_dve, j + 1)
            for k in range(KT):
                last = pe.matmul(E.PS[:, 2 + slot, :].rearrange("p (w m) -> p w m", w=2), E.xT[:, k * P:(k + 1) * P],
                                 E.w13[:, slot, :, k, :], start=(k == 0), stop=(k == KT - 1))
            last.then_inc(self.h_done, 1)

        def turn_hidden(j):
            pe.wait_ge(self.hid_done, j + 1)
            hid = E.hg.rearrange("s (p k) -> s k p", k=2)
            for k in range(2):
                last = pe.transpose(E.PS[:, 4, k * P:(k + 1) * P], hid[:, k, :], E.ident[:, :])
            last.then_inc(self.hid_turned, 1)

        def outputs(j, slot, turn):
            pe.wait_ge(self.w2_loaded[slot], turn * 16 + 16)
            pe.wait_ge(self.hid_copied, j + 1)
            pe.wait_ge(self.y_act, j + 1)
            pe.wait_ge(self.y_dve, j + 1)
            for a in range(2):
                for k in range(2):
                    last = pe.matmul(E.PS[:, 6 + a, :], E.hT[:, k * P:(k + 1) * P],
                                     self.w2s[:, slot, k, a * 512:(a + 1) * 512], start=(k == 0), stop=(k == 1))
            last.then_inc(self.y_done, 1)
        turn_x(0, 0, 0)

        def body(j, slot, turn):
            before, after = self.neighbours(j, slot, turn)
            hidden(j, slot, turn)
            if before:
                outputs(j - 1, *before)
            if after:
                turn_x(j + 1, *after)
            turn_hidden(j)
        self.in_turn(pe, body)
        outputs(N_EXP - 1, 1, N_EXP // 2 - 1)

    def scalar(self, act):
        E = self.E
        act.sem_inc(self.y_act, 1)

        def copy_x(j):
            act.wait_ge(self.x_turned, j + 1)
            act.copy(E.xT[:, 0:512], E.PS[:, 0, :]).then_inc(self.x_act, 1)

        def copy_y(j, slot, turn):
            act.wait_ge(self.y_done, j + 1)
            act.wait_ge(self.y_stored[slot], turn * 16)
            act.copy(E.yo[:, slot, 0:512], E.PS[:, 6, :]).then_inc(self.y_act, 1)
        copy_x(0)

        def body(j, slot, turn):
            before, after = self.neighbours(j, slot, turn)
            act.wait_ge(self.h_done, j + 1)
            if before:
                act.wait_ge(self.hid_done, j)
            act.activation(E.hs, E.PS[:, 2 + slot, 0:E_HID], ACT.Silu).then_inc(self.silu_done, 1)
            if before:
                copy_y(j - 1, *before)
            if after:
                copy_x(j + 1)
        self.in_turn(act, body)
        copy_y(N_EXP - 1, 1, N_EXP // 2 - 1)

    def vector(self, dve):
        E = self.E
        dve.sem_inc(self.y_dve, 1)

        def copy_x(j):
            dve.wait_ge(self.x_turned, j + 1)
            dve.tensor_copy(E.xT[:, 512:1024], E.PS[:, 1, :]).then_inc(self.x_dve, 1)

        def copy_y(j, slot, turn):
            dve.wait_ge(self.y_done, j + 1)
            dve.wait_ge(self.y_stored[slot], turn * 16)
            dve.tensor_copy(E.yo[:, slot, 512:1024], E.PS[:, 7, :]).then_inc(self.y_dve, 1)
        copy_x(0)

        def body(j, slot, turn):
            before, after = self.neighbours(j, slot, turn)
            dve.wait_ge(self.silu_done, j + 1)
            dve.tensor_tensor(E.hg, E.hs, E.PS[:, 2 + slot, E_HID:2 * E_HID], ALU.mult).then_inc(self.hid_done, 1)
            if before:
                copy_y(j - 1, *before)
            if after:
                copy_x(j + 1)
            dve.wait_ge(self.hid_turned, j + 1)
            dve.tensor_copy(E.hT, E.PS[:, 4, 0:2 * P]).then_inc(self.hid_copied, 1)
        self.in_turn(dve, body)
        copy_y(N_EXP - 1, 1, N_EXP // 2 - 1)


class DenseExperts:

    def __init__(self, S, E):
        self.E = E
        self.loaded = [S.take("w_loaded_0"), S.take("w_loaded_1")]
        self.done = S.take("tile_done")
        self.act_out = S.take("silu_out")
        self.dve_out = S.take("dve_out")
        self.own = S.take("hidden_steps")
        self.scaled = S.take("residual_scaled")

    def sync(self, sp):
        E, A, li, dve_out = self.E, self.E.A, self.E.li, self.dve_out
        w1 = A["moe_w1_2"][li].rearrange("e (k p) m -> e p k m", p=P)
        w3 = A["moe_w3_2"][li].rearrange("e (k p) m -> e p k m", p=P)
        w2 = A["moe_w2_2"][li].rearrange("e (k p) m -> e p k m", p=P)

        def load(j, slot, turn):
            sp.wait_ge(dve_out, j * 10 + 10)
            for dst, src in ((E.w1s[:, slot], w1[j]), (E.w3s[:, slot], w3[j]), (E.w2s[:, slot], w2[j]),
                             (E.gate_row[:, slot, :], E.gates_dram[j].partition_broadcast(P))):
                sp.dma_start(dst, src).then_inc(self.loaded[slot], 16)
        in_pairs(sp, N_EXP, load)

    def tensor(self, pe):
        E, dve_out = self.E, self.dve_out

        def body(j, slot, turn):
            def tile(q, w, rhs, nk):
                s = 2 * (q % 4)
                for k in range(nk):
                    for a in range(2):
                        last = pe.matmul(E.PS[:, s + a, 0:HALF], w(k), halves(rhs(k), 2)[:, a, :],
                                         start=(k == 0), stop=(k == nk - 1))
                last.then_inc(self.done, 1)
            pe.wait_ge(self.loaded[slot], turn * 64 + 64)
            for m in range(2):
                for n, w in enumerate((E.w1s, E.w3s)):
                    pe.wait_ge(dve_out, j * 10 + (17 + 2 * m + n))
                    tile(2 * m + n, lambda k: w[:, slot, k, m * P:(m + 1) * P], lambda k: E.h[:, k, :], KT)
            pe.wait_ge(dve_out, j * 10 + 22)
            for m in range(KT):
                if m >= 4:
                    pe.wait_ge(dve_out, j * 10 + (23 + m - 4))
                tile(4 + m, lambda k: E.w2s[:, slot, k, m * P:(m + 1) * P], lambda k: E.hid[:, k, :], 2)
        in_pairs(pe, N_EXP, body)

    def scalar(self, act):
        E = self.E

        def body(j, slot, turn):
            for m in range(2):
                act.wait_ge(self.done, j * 12 + (2 * m + 1))
                act.activation(halves(E.silu[:, m, :], 2), E.PS[:, 4 * m:4 * m + 2, 0:HALF],
                               ACT.Silu).then_inc(self.act_out, 1)
        in_pairs(act, N_EXP, body)

    def vector(self, dve):
        E, done, own, dve_out = self.E, self.done, self.own, self.dve_out
        dve.tensor_scalar(E.h1[:, :, :], E.h[:, :, :], ALPHA, None, ALU.mult).then_inc(self.scaled, 1)
        dve.wait_ge(self.scaled, 1)
        dve.sem_inc(dve_out, 20)

        def body(j, slot, turn):
            dve.wait_ge(self.loaded[slot], turn * 64 + 64)
            for m in range(2):
                dve.wait_ge(self.act_out, j * 2 + (m + 1))
                dve.tensor_tensor(E.silu[:, m, :], E.silu[:, m, :], E.gate_row[:, slot, :],
                                  ALU.mult).then_inc(own, 1)
                dve.wait_ge(done, j * 12 + (2 * m + 2))
                dve.wait_ge(own, j * 2 + (m + 1))
                dve.tensor_tensor(halves(E.hid[:, m, :], 2), halves(E.silu[:, m, :], 2),
                                  E.PS[:, 4 * m + 2:4 * m + 4, 0:HALF], ALU.mult).then_inc(dve_out, 1)
            for m in range(KT):
                dve.wait_ge(done, j * 12 + (5 + m))
                s = 2 * (m % 4)
                dve.tensor_tensor(halves(E.h1[:, m, :], 2), halves(E.h1[:, m, :], 2), E.PS[:, s:s + 2, 0:HALF],
                                  ALU.add).then_inc(dve_out, 1)
        in_pairs(dve, N_EXP, body)


def combine(nc, S, E):
    S.open()
    loaded = S.take("outputs_loaded")
    first = S.take("first_scaled")
    mixed = S.take("outputs_mixed")
    turned = S.take("turned")
    added = S.take("added")
    nt = len(TOK)

    def load(sp):
        for t, (t0, rows) in enumerate(TOK):
            if t:
                sp.wait_ge(loaded, 32 * t)
            for w in range(2):
                sp.dma_start(E.parts[w][0:rows, t, :], E.out_dram[w * L + t0:w * L + t0 + rows, :]).then_inc(loaded, 16)

    def mix(dve):
        for t, (t0, rows) in enumerate(TOK):
            a, b = (x[0:rows, t, :] for x in E.parts)
            dve.wait_ge(loaded, 32 * t + 32)
            dve.tensor_scalar(a, a, E.gates[0][0:rows, t:t + 1], None, ALU.mult).then_inc(first, 1)
            dve.wait_ge(first, t + 1)
            dve.scalar_tensor_tensor(a, b, E.gates[1][0:rows, t:t + 1], a, ALU.mult, ALU.add).then_inc(mixed, 1)
        for k in range(KT):
            dve.wait_ge(turned, k + 1)
            dve.scalar_tensor_tensor(E.h1[:, k, 0:SEQ], E.h[:, k, 0:SEQ], ALPHA, E.PS[:, k % 4, :],
                                     ALU.mult, ALU.add).then_inc(added, 1)
        dve.scalar_tensor_tensor(E.h1[:, :, SEQ:L], E.h[:, :, SEQ:L], ALPHA,
                                 E.PS[:, 7, 0:KT * N_META].rearrange("p (k n) -> p k n", k=KT), ALU.mult, ALU.add)

    def turn(pe):
        for k in range(KT):
            if k >= 4:
                pe.wait_ge(added, k - 3)
            for t, (t0, rows) in enumerate(TOK):
                if k == 0:
                    pe.wait_ge(mixed, t + 1)
                dst = E.PS[:, k % 4, t0:t0 + rows] if t < nt - 1 else E.PS[:, 7, k * N_META:(k + 1) * N_META]
                last = pe.transpose(dst, E.parts[0][0:rows, t, k * P:(k + 1) * P], E.ident[0:rows, 0:rows])
            last.then_inc(turned, 1)
    with nc.Block() as block:
        @block.gpsimd
        def _(pool):
            S.clear_old(pool)

        @block.sync
        def _(sp):
            most = sp.value_load(E.most[0:1, 0:1])
            with sp.If(most <= CAP):
                load(sp)

        @block.vector
        def _(dve):
            most = dve.value_load(E.most[0:1, 0:1])
            with dve.If(most <= CAP):
                mix(dve)

        @block.tensor
        def _(pe):
            most = pe.value_load(E.most[0:1, 0:1])
            with pe.If(most <= CAP):
                turn(pe)


def store_output(nc, S, E):
    S.open()
    turned = S.take("turned")
    copied = S.take("copied")
    stored = S.take("output_stored")
    out = E.out[0].rearrange("(t p) d -> t p d", p=P)
    with nc.Block() as block:
        @block.gpsimd
        def _(pool):
            S.clear_old(pool)

        @block.tensor
        def _(pe):
            for t in range(4):
                if t >= 2:
                    pe.wait_ge(copied, t - 1)
                for k in range(KT):
                    last = pe.transpose(E.PS[:, 2 * (t % 2) + k // 4, (k % 4) * P:(k % 4 + 1) * P],
                                        E.h[:, k, N_META + t * P:N_META + (t + 1) * P], E.ident[:, :])
                last.then_inc(turned, 1)

        @block.scalar
        def _(act):
            for t in range(4):
                act.wait_ge(turned, t + 1)
                act.copy(E.outbuf[:, t, :].rearrange("p (b n) -> p b n", b=2),
                         E.PS[:, 2 * (t % 2):2 * (t % 2) + 2, :]).then_inc(copied, 1)

        @block.sync
        def _(sp):
            for t in range(4):
                sp.wait_ge(copied, t + 1)
                sp.dma_start(out[t], E.outbuf[:, t, :]).then_inc(stored, 16)
            sp.wait_ge(stored, 64)


def second_block(nc, S, E, scope):
    A = E.A

    def sb(name, shape, dt=F32):
        return scope.enter_context(nc.sbuf_tensor(name, shape, dt))
    E.zt = sb("zt", [P, 19 * LP])
    E.zs = [E.zt[:, i * LP:i * LP + L] for i in range(19)]
    E.zr = E.zt[:, T_R * LP:(T_R + 12) * LP].rearrange("p (a n) -> p a n", a=12)
    E.kdbuf = sb("kd", [P, WIDE])
    E.kd = E.kdbuf[:, :].rearrange("p (d m n) -> p d m n", d=2, m=4)
    E.vfirst = sb("vfirst", [P, 4, L])
    E.head_ones = sb("head_ones", [P, P])
    E.head_mean = sb("head_mean", [P, P])
    E.level = sb("level", [P, 2, LEVELS, CH])
    E.pair = sb("pair", [P, 2, CH])
    E.eye2 = sb("eye2", [P, CH])
    E.total = sb("total", [P, 4 * N_CH])
    E.state = sb("state", [P, 4, 2, CH])
    E.pend = sb("pend", [P, 4, 2])
    E.invf = sb("invf", [P, 1])
    E.mx2 = sb("mx2", [P, 20])
    E.sums2 = sb("sums2", [P, 20])
    E.ovar = sb("ovar", [P, 20])

    def four(x, i):
        return x[:, i * 4 * LP:(i + 1) * 4 * LP].rearrange("p (m n) -> p m n", m=4)
    E.cum = [four(E.n_flat, 0), four(E.n_flat, 1)]
    E.ld = [four(E.h1_flat, 0), four(E.h1_flat, 1)]
    E.ba = [four(E.norm_flat, 0), four(E.norm_flat, 1)]
    E.pos_int = E.n_flat[:, 0:SEQ].bitcast(I32)
    E.shifted = E.norm_flat[:, 0:4 * L].rearrange("p (a n) -> p a n", a=4)
    E.qn, E.kn = E.h1[:, 0:4, :], E.h1[:, 4:8, :]
    E.qp = E.norm_flat[:, 2560:2560 + 2 * L].rearrange("p (a n) -> p a n", a=2)
    E.vn2 = E.norm_flat[:, 0:2560].rearrange("p (t n) -> p t n", t=5)
    E.prob2 = E.n_flat[:, 0:2 * L].rearrange("p (a n) -> p a n", a=2)
    E.probT2 = E.n_flat[:, 2 * L:2 * L + 2 * 5 * P].rearrange("p (a b n) -> p a b n", a=2, b=5)
    flat = E.wring[:, :, :, :].rearrange("p s k m -> p (s k m)")
    E.on = flat[:, 0:2560].rearrange("p (t n) -> p t n", t=5)
    E.osq = E.norm_flat[:, 0:2560].rearrange("p (t n) -> p t n", t=5)
    E.onorm = flat[:, 2560:3072]
    tmp = E.y[:, 4:8, :].rearrange("p m n -> p (m n)")
    E.tmp4 = E.y[:, 4:8, :]
    E.tmp4b = E.rotbuf[:, :, :, :].rearrange("p a b n -> p (a b) n")
    E.lora = sb("lora", [P, 2, L])
    E.low = E.lora[0:32, 0, :]
    E.kk = E.zt[:, 0:4 * LP].rearrange("p (m n) -> p m n", m=4)
    E.tmp8a = E.h1[:, 0:4, :]
    E.tmp8b = E.h1[:, 4:8, :]

    rot = E.rotbuf[:, :, :, :].rearrange("p a b n -> p (a b n)")
    spare = [(flat, 512, 4096), (rot, 0, 2112), (tmp, 0, 2112), (E.zt, T_WD * LP, T_GD * LP), (E.stat, 0, L),
             (E.lora[:, 0, :], 0, L), (E.lora[:, 1, :], 0, L)]

    def cut(n, name):
        for i, (x, a, z) in enumerate(spare):
            if z - a >= n:
                spare[i] = (x, a + n, z)
                return x[:, a:a + n]
        return sb(name, [P, n])[:, :]
    N = 8 * CH
    E.ex, E.ep, E.en, E.bb, E.kb, E.vb = (cut(N, x).rearrange("p (m d n) -> p m d n", m=4, d=2)
                                          for x in ("ex", "ep", "en", "bb", "kb", "vb"))
    E.ar = cut(2 * N, "ar").rearrange("p (m d r n) -> p m d r n", m=4, d=2, r=2)
    E.lb, E.mk = (cut(2 * N, x).rearrange("p (h r n) -> p h r n", h=8, r=2) for x in ("lb", "mk"))
    E.vtok, E.btok, E.ktok = (cut(N, x) for x in ("vtok", "btok", "ktok"))
    E.x, E.xt = (cut(N, x).rearrange("p (h n) -> p h n", h=8) for x in ("x", "xt"))
    E.mjt = [cut(N, f"mjt{j}").rearrange("p (h n) -> p h n", h=8) for j in range(1, LEVELS)]
    E.t1 = cut(N, "t1").rearrange("p (h n) -> p h n", h=8)
    E.f, E.sa = E.mjt[0], E.x
    E.keep = flat[:, 2176:2176 + LP]
    E.bonus = E.zr[:, T_K - T_R:T_K - T_R + 4, 0:L]

    E.w1s, E.w3s = (E.zt[:, i * 4096:(i + 1) * 4096].rearrange("p (s k m) -> p s k m", s=2, k=KT) for i in range(2))
    E.w2s = flat.rearrange("p (s k m) -> p s k m", s=2, k=2)
    E.router = E.norm_flat
    E.gT = E.n_flat[0:32, 0:L]
    E.silu = E.n[:, 0:2, :]
    E.hid = E.n[:, 2:4, :]
    E.gate_row = E.n[:, 4:6, :]
    E.outbuf = E.n_flat[:, 0:4096].rearrange("p (t d) -> p t d", t=4)
    E.w13 = E.zt[:, 0:2 * 4096].rearrange("p (s w k m) -> p s w k m", s=2, w=2, k=KT)
    E.natural = E.zt[:, 0:5 * D].rearrange("p (t d) -> p t d", t=5)
    E.parts = [E.zt[:, i * 5 * D:(i + 1) * 5 * D].rearrange("p (t d) -> p t d", t=5) for i in range(2)]
    E.xg = E.n_flat[:, 0:2 * D].rearrange("p (s d) -> p s d", s=2)
    E.yo = E.n_flat[:, 2 * D:4 * D].rearrange("p (s d) -> p s d", s=2)
    E.xT = E.h1_flat[:, 0:D]
    E.hs, E.hg, E.hT = (E.h1_flat[:, D + i * E_HID:D + (i + 1) * E_HID] for i in range(3))
    E.most = sb("most", [P, 1], I32)
    E.x_index, E.y_index = sb("x_index", [P, 2], I32), sb("y_index", [P, 2], I32)
    E.h_dram = nc.dram_tensor("h_tokens", (L, D), F32, kind="Internal").ap()
    E.out_dram = nc.dram_tensor("expert_out", (2 * L, D), F32, kind="Internal").ap()
    E.list_dram = nc.dram_tensor("expert_lists", (CAP * N_EXP, 1), F32, kind="Internal").ap()
    E.gates_dram = nc.dram_tensor("gates", (N_EXP, L), F32, kind="Internal").ap()

    meta = E.norm_flat[0:N_META, 0:D]
    load_constants(nc, S, [(E.head_ones[:, :], A["head_ones"]), (E.head_mean[:, :], A["head_mean"]),
                           (E.level[:, :, :, :], A["level_masks"]), (E.pair[:, :, :], A["pair_masks"]),
                           (E.eye2[:, :], A["eye2"]), (meta, A["meta_tokens_2"])])
    transpose_rows(nc, S, E, lambda k: E.h1[:, k, 0:N_META], KT, parts=[(meta, 0, N_META)])
    norm(nc, S, E, lambda k: E.h1[:, k, :], lambda k: E.h[:, k, :], KT, 2, HALF, lambda k: E.par[:, 8 + k:9 + k], 1e-5,
         b=lambda k: E.par[:, 16 + k:17 + k])
    angles(nc, S, E)
    clear_vfirst(nc, S, E)
    sweep(nc, S)
    with nc.Fori(0, E.depth) as li:
        E.li = li

        def rows(name, n, *ix):
            x = A[name][li]
            for i in ix:
                x = x[i]
            return x.rearrange("(t p) -> t p", p=P)[0:n]

        def par(r):
            return lambda k: E.par[:, r + k:r + k + 1]
        load_params(nc, S, E, [
            (Q_QN, 2, rows("mla_q_norm_2", 2), 0, P), (Q_KVN, 1, rows("mla_kv_norm_2", 1), 0, P),
            (Q_MP, 15, rows("rwkv_mu_prev_2", 15), 0, P), (Q_MN, 15, rows("rwkv_mu_next_2", 15), 0, P),
            (Q_W0, 8, A["rwkv_w0_2"][li].rearrange("d (t p) -> (d t) p", p=P), 0, P),
            (Q_A0, 8, A["rwkv_a0_2"][li].rearrange("d (t p) -> (d t) p", p=P), 0, P),
            (Q_KK, 4, rows("rwkv_k_k_2", 4), 0, P), (Q_KA, 4, rows("rwkv_k_a_2", 4), 0, P),
            (Q_RK, 4, A["rwkv_r_k_2"][li].rearrange("(t h) n -> t (h n)", h=2), 0, P),
            (Q_GG, 4, rows("rwkv_gn_g_2", 4), 0, P), (Q_GB, 4, rows("rwkv_gn_b_2", 4), 0, P),
            (Q_V0, 4, A["rwkv_v0_2"][0].rearrange("(t p) -> t p", p=P), 0, P),
            (Q_L1G, 8, rows("ln1_g_2", 8), 0, P), (Q_L1B, 8, rows("ln1_b_2", 8), 0, P),
            (Q_L2G, 8, rows("ln2_g_2", 8), 0, P), (Q_L2B, 8, rows("ln2_b_2", 8), 0, P),
            (Q_FIRST, 1, A["is_first"][li].unsqueeze(0), 0, P)])
        project_tail(nc, S, E)
        w_in = A["w_in_2"][li].rearrange("(k p) m -> p k m", p=P)
        zall = E.zt[:, :].rearrange("p (a n) -> p a n", n=LP)

        def to_z(eng, j, t, psum):
            q = j * 2 + (t + T_R)
            return eng.activation(zall[:, bass.ds(q, 1), 0:L].rearrange("p o (a n) -> p (o a) n", a=2), psum, ACT.Identity)
        project(nc, S, E, lambda j: w_in[:, :, bass.ds(j * 256 + 448, 256)], lambda k: E.h[:, k, :], KT, 7, 2, HALF, to_z)
        norm(nc, S, E, lambda k: E.zs[T_CQ + k], lambda k: E.n[:, k, :], 2, 2, HALF, par(Q_QN), 1e-6)
        norm(nc, S, E, lambda k: E.zs[T_CKV], lambda k: E.n[:, 2, :], 1, 2, HALF, par(Q_KVN), 1e-6)
        mla_project(nc, S, E)
        rotate(nc, S, E, [E.qp[:, 0, :], E.qp[:, 1, :], E.zs[T_KPE]], L, 2)
        mla_attend(nc, S, E)
        mla_out(nc, S, E)
        shift(nc, S, E)
        load_constants(nc, S, [*lora_loads(E), (E.keep, A["keep"])])
        value_mix(nc, S, E)
        removal_keys(nc, S, E)
        rates(nc, S, E, 0)
        rates(nc, S, E, 1)
        bonus(nc, S, E)
        recurrence(nc, S, E)
        head_norm(nc, S, E)
        w_out = A["w_out_2"][li].rearrange("(k p) m -> p k m", p=P)

        def add_h(eng, j, t, psum):
            q = j * 2 + t

            def tile(x):
                return x[:, bass.ds(q, 1), :].rearrange("p o (a n) -> p (o a) n", a=2)
            return eng.scalar_tensor_tensor(tile(E.h1), tile(E.h), ALPHA, psum, ALU.mult, ALU.add)
        project(nc, S, E, lambda j: w_out[:, :, bass.ds(j * 256, 256)], lambda k: E.y[:, k, :], KT, KT // 2,
                2, HALF, add_h, on="vector")
        norm(nc, S, E, lambda k: E.h1[:, k, :], lambda k: E.h[:, k, :], KT, 2, HALF, par(Q_L1G), 1e-5, b=par(Q_L1B))
        route(nc, S, E)
        dispatch(nc, S, E)
        experts(nc, S, E)
        combine(nc, S, E)
        norm(nc, S, E, lambda k: E.h1[:, k, :], lambda k: E.h[:, k, :], KT, 2, HALF, par(Q_L2G), 1e-5, b=par(Q_L2B))
        sweep(nc, S)
    store_output(nc, S, E)


def clear_vfirst(nc, S, E):
    S.open()
    with nc.Block() as block:
        @block.gpsimd
        def _(pool):
            S.clear_old(pool)
            pool.memset(E.vfirst[:, :, :], 0.0)


def program(nc, A, out):
    E = Env()
    E.A, E.out = A, out
    E.depth = DEPTH
    S = Sems(nc)
    with ExitStack() as ctx:
        def sb(name, shape, dt=F32):
            return ctx.enter_context(nc.sbuf_tensor(name, shape, dt))
        E.PS = ctx.enter_context(nc.psum_tensor("PS", [P, 8, 512], F32))
        E.ident = sb("ident", [P, P])
        E.ones = sb("ones", [P, P])
        E.rot = sb("rot", [P, P])
        E.cos = sb("cos", [P, L])
        E.sin = sb("sin", [P, L])
        E.praw = sb("praw", [P, P])
        E.par = sb("par", [P, P])
        E.stat = sb("stat", [P, L])
        E.rotbuf = sb("rotbuf", [P, 2, 2, L])
        E.h = sb("h", [P, KT, L])
        E.h1_flat = sb("h1", [P, WIDE])
        E.n_flat = sb("n", [P, WIDE])
        E.norm_flat = sb("normbuf", [P, WIDE])
        E.h1, E.n, E.normbuf = (x[:, 0:KT * L].rearrange("p (k n) -> p k n", k=KT)
                                for x in (E.h1_flat, E.n_flat, E.norm_flat))
        E.y = sb("y", [P, KT, L])
        E.wring = sb("wring", [P, 2, KT, 256])
        load_constants(nc, S, [(E.ident[:, :], A["ident"]), (E.ones[:, :], A["ones"]), (E.rot[:, :], A["rot"])])
        with ExitStack() as scope:
            first_block(nc, S, E, scope)
        with ExitStack() as scope:
            second_block(nc, S, E, scope)
        sweep(nc, S)


def shape_constants():
    f = np.float32
    rot = np.zeros((P, P), f)
    for m in range(P):
        if m % 64 < 32:
            rot[m + 32, m] = -1.0
        else:
            rot[m - 32, m] = 1.0
    half = 32
    inv = (f(10000.0) ** (-np.arange(half, dtype=f) / f(half))).astype(f)
    ang = (np.arange(SEQ, dtype=f)[None, :] * inv[:, None]).astype(f)
    t = np.arange(SEQ)
    cnt = np.zeros((P, 2, SEQ), f)
    for g, win in enumerate((2, 4, 8, 16)):
        cnt[(g % 2) * 64:(g % 2) * 64 + 64, g // 2] = 1.0 / np.minimum(t + 1, win)
    inv2 = (f(10000.0) ** (-np.arange(0, 64, 2, dtype=f) / f(64))).astype(f)
    s_, t_ = np.arange(CH)[:, None], np.arange(CH)[None, :]
    strict = (t_ < s_).astype(f)
    level = np.zeros((P, 2, LEVELS, CH), f)
    for j in range(LEVELS):
        b = 1 << j
        m = ((s_ // (2 * b) == t_ // (2 * b)) & (s_ // b > t_ // b)).astype(f)
        level[:CH, 0, j], level[CH:, 0, j] = m, m.T
        level[:CH, 1, j], level[CH:, 1, j] = m.T, m
    pair = np.zeros((P, 2, CH), f)
    pair[:CH, 0], pair[CH:, 0] = strict.T, strict
    pair[:CH, 1], pair[CH:, 1] = strict.T + np.eye(CH, dtype=f), strict + np.eye(CH, dtype=f)
    keep = np.ones((P, LP), f)
    keep[:, ::CH] = 0.0
    keep_group = np.tile((np.arange(20) % 4 != 0).astype(f), (P, 1))
    keep_expert = np.tile((np.arange(160) % 32 != 0).astype(f), (P, 1))
    token = np.arange(5)[None, :] * P + np.arange(P)[:, None]
    valid = (token < L).astype(f)
    choice = np.concatenate([token, token + L], axis=1).astype(f)
    beyond = np.tile((1 - valid) * f(1e6), (1, 2)).astype(f)
    heads = np.zeros((P, P), f)
    heads[:64, :64] = heads[64:, 64:] = 1.0
    return {
        "ident": np.eye(P, dtype=f), "ones": np.ones((P, P), f), "rot": rot,
        "cos1": np.tile(np.cos(ang), (4, 1)).astype(f), "sin1": np.tile(np.sin(ang), (4, 1)).astype(f),
        "invcnt": cnt, "onesrow": np.ones((P, SEQ), f),
        "inv_freq": np.tile(inv2, 4)[:, None].copy(), "meta_pos": np.tile(np.arange(N_META, dtype=f), (P, 1)),
        "level_masks": level, "pair_masks": pair, "eye2": np.tile(np.eye(CH, dtype=f), (2, 1)),
        "keep": keep, "keep_group": keep_group, "keep_expert": keep_expert, "head_ones": heads, "head_mean": heads / f(64),
        "valid_token": valid, "choice": choice, "beyond": beyond,
        "before": np.triu(np.ones((P, P), f), 1), "expert_index": np.tile(np.arange(160) % 32, (P, 1)).astype(f),
        "is_first": np.repeat(np.arange(DEPTH)[:, None] == 0, P, axis=1).astype(f),
    }


def kernel(**inputs):
    import concourse.bacc as bacc
    from concourse.bass_utils import run_bass_kernel_spmd

    nc = bacc.Bacc("TRN2", target_bir_lowering=False, num_devices=1)
    arrays, aps = {}, {}
    for name, a in {**inputs, **shape_constants()}.items():
        a = np.ascontiguousarray(a)
        arrays[f"in_{name}"] = a
        aps[name] = nc.dram_tensor(f"in_{name}", a.shape, mybir.dt.from_np(a.dtype), kind="ExternalInput").ap()
    out = nc.dram_tensor("out", (1, SEQ, D), F32, kind="ExternalOutput").ap()
    program(nc, aps, out)
    r = run_bass_kernel_spmd(nc, [arrays], core_ids=[0])
    return r.results[0]["out"]
```

```python
from contextlib import ExitStack

import numpy as np

import concourse.bass as bass
from concourse import mybir

F32 = mybir.dt.float32
I32 = mybir.dt.int32
ALU = mybir.AluOpType
ACT = mybir.ActivationFunctionType
AX = mybir.AxisListType.X

P = 128
D = 1024
KT = D // P
SEQ = 512
DEPTH = 2
BIG = 1e30

CONV_K = 31
TOPK = 128
IDX_HEADS = 4
Z_TILES = 30
Z_VAL, Z_GLU, Z_CGATE, Z_PIN, Z_PGATE, Z_Q, Z_K, Z_V, Z_AGATE, Z_QI, Z_KI, Z_WI = (
    0, 2, 4, 6, 8, 10, 14, 18, 22, 26, 28, 29)
PAIRS1 = 14

N_META = 16
L = SEQ + N_META
HALF = L // 2
H_A = 4
MLA_SCALE = 192 ** -0.5
RW_TILES = 4
CH = 64
N_CH = -(-L // CH)
LP = N_CH * CH
WIDE = 2 * RW_TILES * LP
LEVELS = 6
N_EXP = 32
E_HID = 256
CAP = P
ALPHA = (2 * DEPTH) ** 0.25
EXP_HALF = float(np.exp(-0.5))
T_CQ, T_CKV, T_KPE, T_R, T_K, T_V, T_WD, T_AD, T_GD = 0, 2, 3, 4, 8, 12, 16, 17, 18
TOK = [(t * P, min(P, L - t * P)) for t in range(-(-L // P))]


POOL_DMA_SEMS = ("x_gathered_0", "x_gathered_1", "y_stored_0", "y_stored_1")


class Sems:

    def __init__(self, nc):
        self.nc = nc
        self.old = []
        self.new = []
        self.stack = ExitStack()
        self.last = ExitStack()
        self.forever = ExitStack()
        self.own = {name: self.forever.enter_context(nc.semaphore(name)) for name in POOL_DMA_SEMS}
        self.stage = 0

    def open(self):
        self.last.close()
        self.stage += 1
        self.old, self.new = self.new, []
        self.last, self.stack = self.stack, ExitStack()

    def take(self, name):
        s = self.stack.enter_context(self.nc.semaphore(f"{name}_{self.stage}"))
        self.new.append(s)
        return s

    def take_own(self, name):
        self.new.append(self.own[name])
        return self.own[name]

    def clear_old(self, pool):
        if any(s in self.own.values() for s in self.old):
            pool.dma_reset()
        for s in self.old:
            pool.sem_clear(s)


class Chain:

    def __init__(self, eng, sem):
        self.eng, self.sem, self.n = eng, sem, 0

    def add(self, ins):
        ins.then_inc(self.sem, 1)
        self.n += 1
        return self.n

    def wait(self, n=None):
        self.eng.wait_ge(self.sem, self.n if n is None else n)

    def link(self, ins):
        self.add(ins)
        self.wait()


def in_pairs(eng, n, body):
    if n >= 2:
        with eng.Fori(0, n // 2) as i:
            body(i * 2, 0, i)
            body(i * 2 + 1, 1, i)
    if n % 2:
        body(n - 1, 0, n // 2)


def halves(ap, nh):
    return ap.rearrange("p (a n) -> p a n", a=nh)


class Env:
    pass


def sweep(nc, S):
    S.open()
    with nc.Block() as block:
        @block.gpsimd
        def _(pool):
            S.clear_old(pool)
    S.open()


def fetch_beside(block, S, pairs):
    if pairs:
        fetched = S.take("fetched")

        @block.sync
        def _(sp):
            for dst, src in pairs:
                sp.dma_start(dst, src).then_inc(fetched, 16)
            sp.wait_ge(fetched, 16 * len(pairs))


def load_constants(nc, S, pairs):
    S.open()
    loaded = S.take("constants_loaded")
    with nc.Block() as block:
        @block.gpsimd
        def _(pool):
            S.clear_old(pool)

        @block.sync
        def _(sp):
            for dst, src in pairs:
                sp.dma_start(dst, src).then_inc(loaded, 16)
            sp.wait_ge(loaded, 16 * len(pairs))


def transpose_rows(nc, S, E, dst, ntiles, parts):
    S.open()
    turned = S.take("turned")
    copied = S.take("copied")
    with nc.Block() as block:
        @block.gpsimd
        def _(pool):
            S.clear_old(pool)

        @block.tensor
        def _(pe):
            for k in range(ntiles):
                if k >= 8:
                    pe.wait_ge(copied, k - 7)
                for n, (tile_ap, c0, rows_n) in enumerate(parts):
                    last = pe.transpose(E.PS[:, k % 8, c0:c0 + rows_n], tile_ap[:, k * P:(k + 1) * P],
                                        E.ident[0:rows_n, 0:rows_n])
                last.then_inc(turned, 1)

        @block.scalar
        def _(act):
            w = parts[-1][1] + parts[-1][2]
            for k in range(ntiles):
                act.wait_ge(turned, k + 1)
                act.copy(dst(k), E.PS[:, k % 8, 0:w]).then_inc(copied, 1)


def load_params(nc, S, E, rows, also=()):
    S.open()
    blank = S.take("blank")
    loaded = S.take("rows_loaded")
    turned = S.take("turned")
    also_loaded = S.take("also_loaded")
    with nc.Block() as block:
        @block.gpsimd
        def _(pool):
            S.clear_old(pool)

        @block.vector
        def _(dve):
            dve.memset(E.praw[:, :], 0.0).then_inc(blank, 1)

        @block.sync
        def _(sp):
            sp.wait_ge(blank, 1)
            for r, n, src, c0, w in rows[0::2]:
                sp.dma_start(E.praw[r:r + n, c0:c0 + w], src).then_inc(loaded, 16)
            for dst, src in also:
                sp.dma_start(dst, src).then_inc(also_loaded, 16)
            if also:
                sp.wait_ge(also_loaded, 16 * len(also))

        @block.tensor
        def _(pe):
            pe.wait_ge(loaded, 16 * len(rows))
            pe.transpose(E.PS[:, 0, 0:P], E.praw[:, :], E.ident[:, :]).then_inc(turned, 1)

        @block.scalar
        def _(act):
            act.wait_ge(blank, 1)
            for r, n, src, c0, w in rows[1::2]:
                act.dma_start(E.praw[r:r + n, c0:c0 + w], src).then_inc(loaded, 16)
            act.wait_ge(turned, 1)
            act.copy(E.par[:, :], E.PS[:, 0, 0:P])


def norm(nc, S, E, src, dst, nk, nh, nw, g, eps, b=None, func=None, fetch=()):
    S.open()
    centred = b is not None
    sum_ready = S.take("sum_ready")
    xc_ready = S.take("xc_ready")
    sq_ready = S.take("sq_ready")
    ssq_ready = S.take("ssq_ready")
    var_ready = S.take("var_ready")
    std_ready = S.take("std_ready")
    scaled = S.take("scaled")
    own = S.take("dve_steps")
    width = nk * P
    bank_sum = E.PS[:, 0:nh, 0:nw]
    bank_sq = E.PS[:, 2:2 + nh, 0:nw]
    sq = E.normbuf
    stat = halves(E.stat[:, 0:nh * nw], nh)

    with nc.Block() as block:
        fetch_beside(block, S, fetch)

        @block.gpsimd
        def _(pool):
            S.clear_old(pool)

        @block.tensor
        def _(pe):
            if centred:
                for k in range(nk):
                    for a in range(nh):
                        last = pe.matmul(E.PS[:, a, 0:nw], E.ones[:, :], halves(src(k), nh)[:, a, :],
                                         start=(k == 0), stop=(k == nk - 1))
                last.then_inc(sum_ready, 1)
            for k in range(nk):
                pe.wait_ge(sq_ready, k + 1)
                for a in range(nh):
                    last = pe.matmul(E.PS[:, 2 + a, 0:nw], E.ones[:, :],
                                     halves(sq[:, k, 0:nh * nw], nh)[:, a, :],
                                     start=(k == 0), stop=(k == nk - 1))
            last.then_inc(ssq_ready, 1)

        @block.scalar
        def _(act):
            for k in range(nk):
                if centred:
                    act.wait_ge(xc_ready, k + 1)
                act.activation(sq[:, k, 0:nh * nw], dst(k) if centred else src(k),
                               ACT.Square).then_inc(sq_ready, 1)
            act.wait_ge(var_ready, 1)
            act.activation(stat, stat, ACT.Sqrt).then_inc(std_ready, 1)
            if centred:
                for k in range(nk):
                    act.wait_ge(scaled, k + 1)
                    act.activation(dst(k), dst(k), func or ACT.Identity, bias=b(k))

        @block.vector
        def _(dve):
            c = Chain(dve, own)
            if centred:
                dve.wait_ge(sum_ready, 1)
                c.link(dve.tensor_scalar(stat, bank_sum, 1.0 / width, None, ALU.mult))
                for k in range(nk):
                    dve.tensor_tensor(dst(k), src(k), E.stat[:, 0:nh * nw], ALU.subtract).then_inc(xc_ready, 1)
                dve.wait_ge(xc_ready, nk)
            dve.wait_ge(ssq_ready, 1)
            dve.tensor_scalar(stat, bank_sq, 1.0 / width, eps, ALU.mult, ALU.add).then_inc(var_ready, 1)
            dve.wait_ge(std_ready, 1)
            c.link(dve.reciprocal(E.stat[:, 0:nh * nw], E.stat[:, 0:nh * nw]))
            for k in range(nk):
                dve.scalar_tensor_tensor(dst(k), dst(k) if centred else src(k), g(k), E.stat[:, 0:nh * nw],
                                         ALU.mult, ALU.mult).then_inc(scaled, 1)


def project(nc, S, E, w_of, rhs, nk, npairs, nh, nw, evac, on="scalar", beside=None, also=(), ready=False):
    S.open()
    steps = S.take("beside_steps")
    also_loaded = S.take("also_loaded")
    loaded = [S.take("w_loaded_0"), S.take("w_loaded_1")]
    done = S.take("tile_done")
    freed = S.take("tile_out")
    with nc.Block() as block:
        @block.gpsimd
        def _(pool):
            S.clear_old(pool)

        @block.sync
        def _(sp):
            def load(j, slot, turn):
                sp.wait_ge(done, j * 2 + 1)
                sp.dma_start(E.wring[:, slot, 0:nk, :], w_of(j)).then_inc(loaded[slot], 16)
            for dst, src in also:
                sp.dma_start(dst, src).then_inc(also_loaded, 16)
            if ready:
                sp.sem_inc(loaded[0], 16)
                with sp.Fori(0, (npairs - 1) // 2) as i:
                    load(i * 2 + 1, 1, i)
                    load(i * 2 + 2, 0, i)
                if npairs % 2 == 0:
                    load(npairs - 1, 1, npairs // 2)
            else:
                in_pairs(sp, npairs, load)
            if also:
                sp.wait_ge(also_loaded, 16 * len(also))

        @block.tensor
        def _(pe):
            pe.sem_inc(done, 3)

            def multiply(j, slot, turn):
                pe.wait_ge(loaded[slot], turn * 16 + 16)
                for t in range(2):
                    pe.wait_ge(freed, j * 2 + (t + 1))
                    for k in range(nk):
                        for a in range(nh):
                            last = pe.matmul(E.PS[:, 4 * slot + 2 * t + a, 0:nw],
                                             E.wring[:, slot, k, t * P:(t + 1) * P],
                                             halves(rhs(k), nh)[:, a, :], start=(k == 0), stop=(k == nk - 1))
                    last.then_inc(done, 1)
            in_pairs(pe, npairs, multiply)

        def take_out(eng):
            eng.sem_inc(freed, 4)

            def body(j, slot, turn):
                for t in range(2):
                    eng.wait_ge(done, j * 2 + (t + 4))
                    b = 4 * slot + 2 * t
                    evac(eng, j, t, E.PS[:, b:b + nh, 0:nw]).then_inc(freed, 1)
            in_pairs(eng, npairs, body)

        if on == "scalar":
            @block.scalar
            def _(act):
                take_out(act)
            if beside:
                @block.vector
                def _(dve):
                    beside(dve, steps)
        else:
            @block.vector
            def _(dve):
                take_out(dve)


def conv_gate(nc, S, E, fetch):
    S.open()
    sig_ready = S.take("sig_ready")
    pad = CONV_K - 1
    with nc.Block() as block:
        fetch_beside(block, S, fetch)

        @block.gpsimd
        def _(pool):
            S.clear_old(pool)

        @block.scalar
        def _(act):
            act.activation(E.z[:, Z_GLU:Z_GLU + 2, :], E.z[:, Z_GLU:Z_GLU + 2, :],
                           ACT.Sigmoid).then_inc(sig_ready, 1)

        @block.vector
        def _(dve):
            dve.memset(E.upad[:, :, 0:pad], 0.0)
            dve.wait_ge(sig_ready, 1)
            dve.tensor_tensor(E.upad[:, :, pad:pad + SEQ], E.z[:, Z_VAL:Z_VAL + 2, :],
                              E.z[:, Z_GLU:Z_GLU + 2, :], ALU.mult)


def conv_taps(E, dve, steps):
    c = Chain(dve, steps)
    for tap in range(CONV_K):
        for t in range(2):
            acc, u = E.conv[:, t, :], E.upad[:, t, tap:tap + SEQ]
            w = E.par[:, R_DW + 2 * tap + t:R_DW + 2 * tap + t + 1]
            if tap == 0:
                c.add(dve.tensor_scalar(acc, u, w, E.par[:, R_DWB + t:R_DWB + t + 1], ALU.mult, ALU.add))
            else:
                c.wait(2 * tap - 1 + t)
                c.add(dve.scalar_tensor_tensor(acc, u, w, acc, ALU.mult, ALU.add))


def conv_point(nc, S, E):
    S.open()
    silu_ready = S.take("silu_ready")
    done = S.take("point_done")
    with nc.Block() as block:
        @block.gpsimd
        def _(pool):
            S.clear_old(pool)

        @block.scalar
        def _(act):
            act.activation(E.z[:, Z_CGATE:Z_CGATE + 2, :], E.z[:, Z_CGATE:Z_CGATE + 2, :],
                           ACT.Silu).then_inc(silu_ready, 1)

        @block.tensor
        def _(pe):
            for m in range(2):
                for k in range(2):
                    last = pe.matmul(E.PS[:, m, :], E.wring[:, 0, k, m * P:(m + 1) * P], E.conv[:, k, :],
                                     start=(k == 0), stop=(k == 1))
                last.then_inc(done, 1)

        @block.vector
        def _(dve):
            dve.wait_ge(silu_ready, 1)
            for m in range(2):
                dve.wait_ge(done, m + 1)
                dve.scalar_tensor_tensor(E.y[:, m, 0:SEQ], E.PS[:, m, :], E.par[:, R_PWB + m:R_PWB + m + 1],
                                         E.z[:, Z_CGATE + m, :], ALU.add, ALU.mult)


def pool_windows(E, dve, steps):
    c = Chain(dve, steps)
    G = 64
    x = E.z[:, Z_PIN:Z_PIN + 2, :]
    a, b = E.win[:, 0, :, :], E.win[:, 1, :, :]
    c.add(dve.memset(E.win[:, :, :, 0:16], 0.0))
    c.link(dve.tensor_copy(a[:, :, 16:16 + SEQ], x))

    def double(dst, src, by):
        c.link(dve.tensor_tensor(dst[:, :, 16:16 + SEQ], src[:, :, 16:16 + SEQ],
                                 src[:, :, 16 - by:16 - by + SEQ], ALU.add))

    def use(src, g):
        r, t = (g % 2) * G, g // 2
        c.add(dve.tensor_copy(E.avg[r:r + G, t, :], src[r:r + G, t, 16:16 + SEQ]))
    double(b, a, 1)
    use(b, 0)
    double(a, b, 2)
    use(a, 1)
    double(b, a, 4)
    use(b, 2)
    double(a, b, 8)
    use(a, 3)
    c.wait()
    c.link(dve.tensor_tensor(E.avg, E.avg, E.invcnt[:, :, :], ALU.mult))
    dve.tensor_tensor(E.avg, E.avg, x, ALU.subtract)


def pool_mix(nc, S, E):
    S.open()
    scaled = S.take("scaled")
    silu_ready = S.take("silu_ready")
    done = S.take("pool_done")
    G = 64
    with nc.Block() as block:
        @block.gpsimd
        def _(pool):
            S.clear_old(pool)

        @block.scalar
        def _(act):
            act.activation(E.z[:, Z_PGATE:Z_PGATE + 2, :], E.z[:, Z_PGATE:Z_PGATE + 2, :],
                           ACT.Silu).then_inc(silu_ready, 1)

        @block.vector
        def _(dve):
            dve.wait_ge(done, 1)
            for t in range(2):
                dve.tensor_scalar(E.avg[:, t, :], E.PS[:, t, :], E.par[:, R_PB + t:R_PB + t + 1],
                                  E.par[:, R_PS + t:R_PS + t + 1], ALU.add, ALU.mult).then_inc(scaled, 1)
            dve.wait_ge(silu_ready, 1)
            dve.wait_ge(scaled, 2)
            dve.tensor_tensor(E.y[:, 2:4, 0:SEQ], E.avg, E.z[:, Z_PGATE:Z_PGATE + 2, :], ALU.mult)

        @block.tensor
        def _(pe):
            for g in range(4):
                r, t = (g % 2) * G, g // 2
                last = pe.matmul(E.PS[r:r + G, t, :], E.wring[r:r + G, 1, 0, t * G:t * G + G],
                                 E.avg[r:r + G, t, :], start=True, stop=True)
            last.then_inc(done, 1)


def rotate(nc, S, E, tiles, n_tokens, nh):
    S.open()
    turned = S.take("turned")
    cos_done = S.take("cos_done")
    sin_done = S.take("sin_done")
    added = S.take("added")
    nw = n_tokens // nh
    with nc.Block() as block:
        @block.gpsimd
        def _(pool):
            S.clear_old(pool)
            for i, x in enumerate(tiles):
                pool.wait_ge(cos_done, i + 1)
                pool.wait_ge(sin_done, i + 1)
                pool.tensor_tensor(x, E.rotbuf[:, 0, i % 2, 0:n_tokens], E.rotbuf[:, 1, i % 2, 0:n_tokens],
                                   ALU.add).then_inc(added, 1)

        @block.tensor
        def _(pe):
            for i, x in enumerate(tiles):
                if i >= 4:
                    pe.wait_ge(sin_done, i - 3)
                for a in range(nh):
                    last = pe.matmul(E.PS[:, 2 * (i % 4) + a, 0:nw], E.rot[:, :], halves(x, nh)[:, a, :],
                                     start=True, stop=True)
                last.then_inc(turned, 1)

        @block.vector
        def _(dve):
            for i, x in enumerate(tiles):
                if i >= 2:
                    dve.wait_ge(added, i - 1)
                dve.tensor_tensor(E.rotbuf[:, 0, i % 2, 0:n_tokens], x, E.cos[:, 0:n_tokens],
                                  ALU.mult).then_inc(cos_done, 1)
                dve.wait_ge(turned, i + 1)
                b = 2 * (i % 4)
                dve.tensor_tensor(halves(E.rotbuf[:, 1, i % 2, 0:n_tokens], nh), E.PS[:, b:b + nh, 0:nw],
                                  halves(E.sin[:, 0:n_tokens], nh), ALU.mult).then_inc(sin_done, 1)


def turn_values(nc, S, E, fetch):
    S.open()
    turned = S.take("turned")
    with nc.Block() as block:
        fetch_beside(block, S, fetch)

        @block.gpsimd
        def _(pool):
            S.clear_old(pool)

        @block.tensor
        def _(pe):
            for t in range(4):
                for m in range(4):
                    last = pe.transpose(E.PS[:, t, m * P:(m + 1) * P], E.z[:, Z_V + m, t * P:(t + 1) * P],
                                        E.ident[:, :])
                last.then_inc(turned, 1)

        @block.scalar
        def _(act):
            for t in range(4):
                act.wait_ge(turned, t + 1)
                act.copy(E.vn[:, t, :], E.PS[:, t, :])


def index_scores(nc, S, E, fetch):
    S.open()
    s_done = S.take("s_done")
    relu_done = S.take("relu_done")
    score_done = S.take("score_done")
    causal = S.take("causal")
    own = S.take("select_steps")
    blank = S.take("blank")
    turned = S.take("weights_turned")
    copied = S.take("weights_copied")
    units = [(qb, h) for qb in (1, 2, 3) for h in range(IDX_HEADS)]
    with nc.Block() as block:
        fetch_beside(block, S, fetch)

        @block.tensor
        def _(pe):
            for t in range(4):
                last = pe.transpose(E.PS[:, 7, 4 * t:4 * t + 4], E.z[0:4, Z_WI, t * P:(t + 1) * P],
                                    E.ident[0:4, 0:4])
            last.then_inc(turned, 1)
            for i, (qb, h) in enumerate(units):
                if i >= 7:
                    pe.wait_ge(relu_done, i - 6)
                r, nk = (h % 2) * 64, (qb + 1) * P
                pe.matmul(E.PS[:, i % 7, 0:nk], E.z[r:r + 64, Z_QI + h // 2, qb * P:(qb + 1) * P],
                          E.z[r:r + 64, Z_KI, 0:nk], start=True, stop=True).then_inc(s_done, 1)

        @block.scalar
        def _(act):
            act.wait_ge(turned, 1)
            act.copy(E.wi[:, :], E.PS[:, 7, 0:16]).then_inc(copied, 1)
            for i, (qb, h) in enumerate(units):
                act.wait_ge(s_done, i + 1)
                if i >= 4:
                    act.wait_ge(own, i - 3)
                nk = (qb + 1) * P
                act.activation(E.index_relu[:, i % 4, 0:nk], E.PS[:, i % 7, 0:nk], ACT.Relu,
                               scale=0.125).then_inc(relu_done, 1)

        @block.gpsimd
        def _(pool):
            S.clear_old(pool)
            pool.memset(E.mask[:, 0, 0:P], 0.0).then_inc(blank, 1)
            pool.wait_ge(blank, 1)
            pool.affine_select(out=E.mask[:, 0, 0:P], in_=E.mask[:, 0, 0:P], compare_op=ALU.is_ge, fill=-BIG,
                               base=0, pattern=[[-1, P]], channel_multiplier=1)
            for n, qb in enumerate((1, 2, 3)):
                pool.wait_ge(score_done, n + 1)
                x = E.score[:, qb, qb * P:(qb + 1) * P]
                pool.affine_select(out=x, in_=x, compare_op=ALU.is_ge, fill=-3e38, base=0,
                                   pattern=[[-1, P]], channel_multiplier=1).then_inc(causal, 1)

        @block.vector
        def _(dve):
            c = Chain(dve, own)
            dve.wait_ge(copied, 1)
            for i, (qb, h) in enumerate(units):
                dve.wait_ge(relu_done, i + 1)
                nk = (qb + 1) * P
                acc, w = E.score[:, qb, 0:nk], E.wi[:, 4 * qb + h:4 * qb + h + 1]
                if h == 0:
                    c.link(dve.tensor_scalar(acc, E.index_relu[:, i % 4, 0:nk], w, None, ALU.mult))
                else:
                    c.link(dve.scalar_tensor_tensor(acc, E.index_relu[:, i % 4, 0:nk], w, acc, ALU.mult, ALU.add))
                if h == IDX_HEADS - 1:
                    dve.sem_inc(score_done, 1)


def select_keys(E, dve, steps):
    c = Chain(dve, steps)
    ROUNDS = TOPK // 8
    for r in range(ROUNDS):
        for qb in (1, 2, 3):
            nk = (qb + 1) * P
            if r:
                c.wait(last_rep[qb])
            src = E.work[:, qb, 0:nk] if r else E.score[:, qb, 0:nk]
            c.add(dve.max(out=E.best[:, qb, :], in_=src))
        top = c.n
        last_rep = {}
        for qb in (1, 2, 3):
            nk = (qb + 1) * P
            c.wait(top)
            src = E.work[:, qb, 0:nk] if r else E.score[:, qb, 0:nk]
            if r < ROUNDS - 1:
                last_rep[qb] = c.add(dve.match_replace(out=E.work[:, qb, 0:nk], in_to_replace=E.best[:, qb, :],
                                                       in_values=src, imm_value=-3e38))
    for qb in (1, 2, 3):
        nk = (qb + 1) * P
        s, m = E.score[:, qb, 0:nk], E.mask[:, qb, 0:nk]
        eq, cum = E.work[:, qb, 0:nk], E.index_relu[:, qb, 0:nk]
        thr, need = E.best[:, qb, 7:8], E.count[:, qb:qb + 1]
        c.add(dve.tensor_scalar(eq, s, thr, None, ALU.is_equal))
        c.link(dve.tensor_scalar(m, s, thr, 0.0, ALU.is_gt, ALU.add, accum_out=need))
        c.add(dve.tensor_scalar(need, need, -1.0, float(TOPK), ALU.mult, ALU.add))
        c.link(dve.tensor_tensor_scan(cum, E.onesrow[:, 0:nk], eq, 0.0, ALU.mult, ALU.add))
        c.link(dve.scalar_tensor_tensor(eq, cum, need, eq, ALU.is_le, ALU.mult))
        c.link(dve.tensor_tensor(m, m, eq, ALU.add))
        c.add(dve.tensor_scalar(m, m, BIG, -BIG, ALU.mult, ALU.add))
    c.wait()


def attend(nc, S, E):
    S.open()
    logit_done = S.take("logit_done")
    masked = S.take("masked")
    neg_max = S.take("neg_max")
    exp_done = S.take("exp_done")
    turned = S.take("probs_turned")
    copied = S.take("probs_copied")
    pv_done = S.take("pv_done")
    rsum = S.take("sum_inverse")
    normed = S.take("probs_normed")
    gate = S.take("gate_ready")
    used = S.take("o_used")
    units = [(qb, h) for qb in range(4) for h in range(8)]
    SCALE = 0.125
    LOGIT_BANKS = (0, 1, 7)
    with nc.Block() as block:
        @block.gpsimd
        def _(pool):
            S.clear_old(pool)

        @block.tensor
        def _(pe):
            def logits(i):
                qb, h = units[i]
                r, nk = (h % 2) * 64, (qb + 1) * P
                if i >= 3:
                    pe.wait_ge(masked, i - 2)
                pe.matmul(E.PS[:, LOGIT_BANKS[i % 3], 0:nk], E.z[r:r + 64, Z_Q + h // 2, qb * P:(qb + 1) * P],
                          E.z[r:r + 64, Z_K + h // 2, 0:nk], start=True, stop=True).then_inc(logit_done, 1)

            def turn(i):
                qb, h = units[i]
                pe.wait_ge(normed, i + 1)
                if i >= 2:
                    pe.wait_ge(copied, i - 1)
                for kb in range(qb + 1):
                    last = pe.transpose(E.PS[:, 2 + i % 2, kb * P:(kb + 1) * P],
                                        E.prob[:, i % 3, kb * P:(kb + 1) * P], E.ident[:, :])
                last.then_inc(turned, 1)

            def values(i):
                qb, h = units[i]
                pe.wait_ge(copied, i + 1)
                if h == 0 and qb >= 2:
                    pe.wait_ge(used, qb - 1)
                r = (h % 2) * 64
                for kb in range(qb + 1):
                    last = pe.matmul(E.PS[r:r + 64, 4 + qb % 2, (h // 2) * P:(h // 2 + 1) * P],
                                     E.vn[:, kb, h * 64:h * 64 + 64], E.probT[:, i % 2, kb * P:(kb + 1) * P],
                                     start=(kb == 0), stop=(kb == qb))
                last.then_inc(pv_done, 1)

            n = len(units)
            logits(0)
            logits(1)
            for i in range(n + 1):
                if i + 2 < n:
                    logits(i + 2)
                if i < n:
                    turn(i)
                if i >= 1:
                    values(i - 1)

        @block.vector
        def _(dve):
            def mask(i):
                qb, h = units[i]
                nk = (qb + 1) * P
                dve.wait_ge(logit_done, i + 1)
                if i >= 3:
                    dve.wait_ge(exp_done, i - 2)
                dve.tensor_tensor_reduce(E.logit[:, i % 3, 0:nk], E.PS[:, LOGIT_BANKS[i % 3], 0:nk], E.mask[:, qb, 0:nk],
                                         1.0, -3e38, ALU.add, ALU.max, E.mx[:, i:i + 1]).then_inc(masked, 1)
                dve.wait_ge(masked, i + 1)
                dve.tensor_scalar(E.mx[:, i:i + 1], E.mx[:, i:i + 1], -SCALE, None, ALU.mult).then_inc(neg_max, 1)

            def copy(i):
                qb, h = units[i]
                nk = (qb + 1) * P
                dve.wait_ge(turned, i + 1)
                if i >= 2:
                    dve.wait_ge(pv_done, i - 1)
                dve.tensor_copy(E.probT[:, i % 2, 0:nk], E.PS[:, 2 + i % 2, 0:nk]).then_inc(copied, 1)

            def normalise(i):
                nk = (units[i][0] + 1) * P
                prob = E.prob[:, i % 3, 0:nk]
                dve.wait_ge(exp_done, i + 1)
                dve.reciprocal(E.sums[:, i:i + 1], E.sums[:, i:i + 1]).then_inc(rsum, 1)
                dve.wait_ge(rsum, i + 1)
                dve.tensor_scalar(prob, prob, E.sums[:, i:i + 1], None, ALU.mult).then_inc(normed, 1)

            def store(qb):
                dve.wait_ge(pv_done, 8 * qb + 8)
                dve.wait_ge(gate, 1)
                dve.tensor_tensor(E.y[:, 4:8, qb * P:(qb + 1) * P],
                                  E.PS[:, 4 + qb % 2, :].rearrange("p (m n) -> p m n", m=4),
                                  E.z[:, Z_AGATE:Z_AGATE + 4, qb * P:(qb + 1) * P], ALU.mult).then_inc(used, 1)

            n = len(units)
            mask(0)
            mask(1)
            normalise(0)
            for i in range(n + 1):
                if i + 2 < n:
                    mask(i + 2)
                if i + 1 < n:
                    normalise(i + 1)
                if i < n:
                    copy(i)
                if i >= 8 and i % 8 == 0:
                    store(i // 8 - 1)

        @block.scalar
        def _(act):
            act.activation(E.z[:, Z_AGATE:Z_AGATE + 4, :], E.z[:, Z_AGATE:Z_AGATE + 4, :],
                           ACT.Silu).then_inc(gate, 1)
            for i, (qb, h) in enumerate(units):
                nk = (qb + 1) * P
                act.wait_ge(neg_max, i + 1)
                if i >= 3:
                    act.wait_ge(turned, i - 2)
                act.activation(E.prob[:, i % 3, 0:nk], E.logit[:, i % 3, 0:nk], ACT.Exp, bias=E.mx[:, i:i + 1],
                               scale=SCALE, accum_out=E.sums[:, i:i + 1]).then_inc(exp_done, 1)


def index_weights(nc, S, E, beside):
    S.open()
    steps = S.take("beside_steps")
    done = S.take("tile_done")
    with nc.Block() as block:
        @block.gpsimd
        def _(pool):
            S.clear_old(pool)

        @block.vector
        def _(dve):
            beside(dve, steps)

        @block.tensor
        def _(pe):
            for n, (c0, m) in enumerate(((0, P), (P, 4))):
                for k in range(KT):
                    last = pe.matmul(E.PS[0:m, n, :], E.index_w[:, k, c0:c0 + m], E.n[:, k, 0:SEQ],
                                     start=(k == 0), stop=(k == KT - 1))
                last.then_inc(done, 1)

        @block.scalar
        def _(act):
            for n, m in enumerate((P, 4)):
                act.wait_ge(done, n + 1)
                act.activation(E.z[0:m, Z_KI + n, :], E.PS[0:m, n, :], ACT.Identity,
                               bias=E.par[0:m, R_B + Z_KI + n:R_B + Z_KI + n + 1])


def gated_skip(nc, S, E):
    S.open()
    done = S.take("tile_done")
    times = S.take("times_gate")
    with nc.Block() as block:
        @block.gpsimd
        def _(pool):
            S.clear_old(pool)
            for m in range(KT):
                pool.wait_ge(times, m + 1)
                pool.tensor_tensor(E.h[:, m, 0:SEQ], E.h1[:, m, 0:SEQ], E.n[:, m, 0:SEQ], ALU.add)

        @block.tensor
        def _(pe):
            for m in range(KT):
                for k in range(2):
                    last = pe.matmul(E.PS[:, m, :], E.plew[:, k, m * P:(m + 1) * P], E.pT[:, k, :],
                                     start=(k == 0), stop=(k == 1))
                last.then_inc(done, 1)

        @block.vector
        def _(dve):
            for m in range(KT):
                dve.wait_ge(done, m + 1)
                dve.tensor_tensor(E.n[:, m, 0:SEQ], E.PS[:, m, :], E.n[:, m, 0:SEQ], ALU.mult).then_inc(times, 1)


R_NG, R_B, R_DW, R_DWB, R_LG, R_LB, R_PWB, R_PB, R_PS = 0, 8, 38, 100, 102, 104, 106, 108, 110


def first_block(nc, S, E, scope):
    A = E.A

    def sb(name, shape):
        return scope.enter_context(nc.sbuf_tensor(name, shape, F32))
    E.z = sb("z", [P, Z_TILES, SEQ])
    h1 = E.h1_flat
    padded = SEQ + CONV_K - 1
    E.upad = h1[:, 0:2 * padded].rearrange("p (a n) -> p a n", a=2)
    at = 2 * padded
    E.conv = h1[:, at:at + 2 * SEQ].rearrange("p (a n) -> p a n", a=2)
    at += 2 * SEQ
    E.win = h1[:, at:at + 4 * (SEQ + 16)].rearrange("p (b a n) -> p b a n", b=2, a=2)
    E.avg = E.y[:, 2:4, 0:SEQ]
    E.index_w = E.norm_flat[:, 0:KT * 132].rearrange("p (k m) -> p k m", k=KT)
    E.index_relu = E.y[:, 4:8, 0:SEQ]
    n = E.n_flat
    E.vn = n[:, 0:4 * SEQ].rearrange("p (a n) -> p a n", a=4)
    E.relu = n[:, 4 * SEQ:8 * SEQ].rearrange("p (a n) -> p a n", a=4)
    E.invcnt = sb("invcnt", [P, 2, SEQ])
    E.wi = sb("wi", [P, 16])
    E.score = sb("score", [P, 4, SEQ])
    E.work = E.normbuf[:, 0:4, 0:SEQ]
    E.mask = E.normbuf[:, 4:8, 0:SEQ]
    E.best = sb("best", [P, 4, 8])
    E.count = sb("count", [P, 4])
    E.onesrow = sb("onesrow", [P, SEQ])
    E.logit = E.normbuf[:, 0:3, 0:SEQ]
    E.prob = E.relu[:, 0:3, :]
    E.probT = E.score[:, 0:2, :]
    E.mx = sb("mx", [P, 32])
    E.sums = sb("sums", [P, 32])
    E.plew = E.z[:, 0:4, :].rearrange("p a n -> p (a n)").rearrange("p (k m) -> p k m", k=2)
    E.pT = E.z[:, 4:6, :]
    xn = E.z[:, 0:8, :].rearrange("p a n -> p (a n)").rearrange("p (t d) -> p t d", t=4)
    pn = E.z[:, 8:10, :].rearrange("p a n -> p (a n)").rearrange("p (t d) -> p t d", t=4)

    load_constants(nc, S, [(E.invcnt[:, :, :], A["invcnt"]), (E.cos[:, 0:SEQ], A["cos1"]), (E.sin[:, 0:SEQ], A["sin1"]),
                           (E.onesrow[:, :], A["onesrow"]),
                           (xn, A["x"][0].rearrange("(t p) d -> p t d", p=P))])
    transpose_rows(nc, S, E, lambda k: E.h[:, k, 0:SEQ], KT,
                   parts=[(xn[:, t, :], t * P, P) for t in range(4)])
    sweep(nc, S)
    with nc.Fori(0, E.depth) as li:
        E.li = li

        def rows(name, n):
            return A[name][li].rearrange("(t p) -> t p", p=P)[0:n]
        b = A["b_in"][li]
        ki0 = Z_KI * P
        load_params(nc, S, E, [
            (R_NG, 8, rows("norm_g", 8), 0, P),
            (R_B, 28, b[0:28 * P].rearrange("(t p) -> t p", p=P), 0, P),
            (R_B + 28, 1, b[ki0:ki0 + 64].unsqueeze(0), 0, 64),
            (R_B + 28, 1, b[ki0:ki0 + 64].unsqueeze(0), 64, 64),
            (R_B + 29, 1, b[ki0 + 64:ki0 + 68].unsqueeze(0), 0, 4),
            (R_DW, 62, A["conv_dw_w"][li].rearrange("k (t p) -> (k t) p", p=P), 0, P),
            (R_DWB, 2, rows("conv_dw_b", 2), 0, P), (R_LG, 2, rows("conv_ln_g", 2), 0, P),
            (R_LB, 2, rows("conv_ln_b", 2), 0, P), (R_PWB, 2, rows("conv_pw_b", 2), 0, P),
            (R_PB, 2, rows("pool_b", 2), 0, P), (R_PS, 2, rows("pool_scale", 2), 0, P)])

        def par(r):
            return lambda k: E.par[:, r + k:r + k + 1]
        w_in = A["w_in"][li].rearrange("(k p) m -> p k m", p=P)

        def pair(w, j):
            return [(E.wring[:, 0, :, :], w[:, :, j * 256:(j + 1) * 256])]
        norm(nc, S, E, lambda k: E.h[:, k, 0:SEQ], lambda k: E.n[:, k, 0:SEQ], KT, 1, SEQ, par(R_NG), 1e-6,
             fetch=pair(w_in, 0))
        par_b = E.par[:, R_B:R_B + 30]

        def to_z(eng, j, t, psum):
            q = j * 2 + t
            return eng.activation(E.z[:, bass.ds(q, 1), :], psum, ACT.Identity, bias=par_b[:, bass.ds(q, 1)])

        def project_in(first, count, beside=None, also=()):
            def evac(eng, j, t, psum):
                return to_z(eng, j + first, t, psum)
            project(nc, S, E, lambda j: w_in[:, :, bass.ds((j + first) * 256, 256)], lambda k: E.n[:, k, 0:SEQ], KT,
                    count, 1, SEQ, evac, beside=beside, also=also, ready=True)
        project_in(0, Z_Q // 2)
        split = (Z_V + 2) // 2
        conv_gate(nc, S, E, pair(w_in, split))
        project_in(split, PAIRS1 - split, beside=lambda dve, steps: conv_taps(E, dve, steps),
                   also=[(E.index_w[:, :, c:c + n], w_in[:, :, ki0 + at:ki0 + at + n])
                         for c, at, n in ((0, 0, 64), (64, 0, 64), (128, 64, 4))])
        index_weights(nc, S, E, lambda dve, steps: pool_windows(E, dve, steps))
        norm(nc, S, E, lambda k: E.conv[:, k, :], lambda k: E.conv[:, k, :], 2, 1, SEQ, par(R_LG), 1e-6,
             b=par(R_LB), func=ACT.Silu,
             fetch=[(E.wring[:, 0, 0:2, :], A["conv_pw_w"][li].rearrange("(k p) m -> p k m", p=P))] + [
                 (E.wring[(g % 2) * 64:(g % 2) * 64 + 64, 1, 0, (g // 2) * 64:(g // 2) * 64 + 64], A["pool_w"][li, g])
                 for g in range(4)])
        conv_point(nc, S, E)
        pool_mix(nc, S, E)
        rotate(nc, S, E, [E.z[:, m, :] for m in (Z_QI, Z_QI + 1, Z_KI)], SEQ, 1)
        index_scores(nc, S, E, pair(w_in, Z_Q // 2))
        project_in(Z_Q // 2, split - Z_Q // 2, beside=lambda dve, steps: select_keys(E, dve, steps))
        rotate(nc, S, E, [E.z[:, m, :] for m in range(Z_Q, Z_V)], SEQ, 1)
        w_out = A["w_out"][li].rearrange("(k p) m -> p k m", p=P)
        turn_values(nc, S, E, pair(w_out, 0))
        attend(nc, S, E)

        def add_h(eng, j, t, psum):
            q = j * 2 + t
            return eng.tensor_tensor(E.h1[:, bass.ds(q, 1), 0:SEQ], psum, E.h[:, bass.ds(q, 1), 0:SEQ], ALU.add)
        project(nc, S, E, lambda j: w_out[:, :, bass.ds(j * 256, 256)], lambda k: E.y[:, k, 0:SEQ], KT, KT // 2,
                1, SEQ, add_h, on="vector", ready=True)
        ple_gate = A["ple_gate_w"][li].rearrange("(k p) m -> p k m", p=P)

        def sigmoids(eng, j, t, psum):
            return eng.activation(E.n[:, bass.ds(j * 2 + t, 1), 0:SEQ], psum, ACT.Sigmoid)
        project(nc, S, E, lambda j: ple_gate[:, :, bass.ds(j * 256, 256)], lambda k: E.h1[:, k, 0:SEQ], KT, KT // 2,
                1, SEQ, sigmoids, also=[(pn, A["p"][li, 0].rearrange("(t p) d -> p t d", p=P)),
                                        (E.plew, A["ple_w"][li].rearrange("(k p) m -> p k m", p=P))])
        transpose_rows(nc, S, E, lambda k: E.pT[:, k, :], 2, parts=[(pn[:, t, :], t * P, P) for t in range(4)])
        gated_skip(nc, S, E)
        sweep(nc, S)
    load_params(nc, S, E, [(0, 8, A["final_norm_g"].rearrange("(t p) -> t p", p=P), 0, P),
                           (8, 8, A["emb_ln_g_2"].rearrange("(t p) -> t p", p=P), 0, P),
                           (16, 8, A["emb_ln_b_2"].rearrange("(t p) -> t p", p=P), 0, P)])
    norm(nc, S, E, lambda k: E.h[:, k, 0:SEQ], lambda k: E.h1[:, k, N_META:L], KT, 1, SEQ,
         lambda k: E.par[:, k:k + 1], 1e-6)


(Q_QN, Q_KVN, Q_MP, Q_MN, Q_W0, Q_A0, Q_KK, Q_KA, Q_RK, Q_GG, Q_GB, Q_V0, Q_L1G, Q_L1B, Q_L2G, Q_L2B, Q_FIRST,
 Q_C0) = (0, 2, 3, 18, 33, 41, 49, 53, 57, 61, 65, 69, 73, 81, 89, 97, 105, 106)


def angles(nc, S, E):
    S.open()
    loaded = S.take("positions_loaded")
    own = S.take("angle_steps")
    r_ready = S.take("r_ready")
    TURN = 2 * np.pi
    C1 = 6.28125
    C2 = float(np.float32(np.round((TURN - C1) * 2 ** 21) / 2 ** 21))
    C3 = TURN - C1 - C2
    MAGIC = 1.5 * 2 ** 23
    with nc.Block() as block:
        @block.gpsimd
        def _(pool):
            S.clear_old(pool)

        @block.sync
        def _(sp):
            sp.dma_start(E.pos_int[:, :], E.A["positions_2"][0].partition_broadcast(P)).then_inc(loaded, 16)
            sp.dma_start(E.cos[:, 0:N_META], E.A["meta_pos"]).then_inc(loaded, 16)
            sp.dma_start(E.invf[:, :], E.A["inv_freq"]).then_inc(loaded, 16)
            sp.wait_ge(loaded, 48)

        @block.vector
        def _(dve):
            c = Chain(dve, own)
            dve.wait_ge(loaded, 48)
            c.link(dve.tensor_copy(E.cos[:, N_META:L], E.pos_int[:, :]))
            c.link(dve.tensor_scalar(E.cos[:, N_META:L], E.cos[:, N_META:L], float(N_META), None, ALU.add))
            c.link(dve.tensor_scalar(E.cos[:, :], E.cos[:, :], E.invf[:, 0:1], None, ALU.mult))
            turns = E.stat[:, 0:L]
            c.link(dve.tensor_scalar(turns, E.cos[:, :], 1.0 / TURN, MAGIC, ALU.mult, ALU.add))
            c.link(dve.tensor_scalar(turns, turns, -MAGIC, None, ALU.add))
            for part in (C1, C2, C3):
                c.link(dve.scalar_tensor_tensor(E.cos[:, :], turns, -part, E.cos[:, :], ALU.mult, ALU.add))
            PI = 3.1415925
            c.link(dve.tensor_scalar(E.cos[:, :], E.cos[:, :], PI, -PI, ALU.min, ALU.max))
            c.link(dve.tensor_scalar(E.stat[:, 0:L], E.cos[:, :], -1.0, None, ALU.mult))
            c.link(dve.tensor_tensor(E.stat[:, 0:L], E.stat[:, 0:L], E.cos[:, :], ALU.max))
            dve.tensor_scalar(E.stat[:, 0:L], E.stat[:, 0:L], -1.0, float(np.pi / 2), ALU.mult,
                              ALU.add).then_inc(r_ready, 1)

        @block.scalar
        def _(act):
            act.wait_ge(r_ready, 1)
            act.activation(E.sin[:, :], E.cos[:, :], ACT.Sin).then_inc(r_ready, 1)
            act.wait_ge(r_ready, 2)
            act.activation(E.cos[:, :], E.stat[:, 0:L], ACT.Sin)


def project_tail(nc, S, E):
    S.open()
    done = S.take("tile_done")
    out = S.take("tile_out")
    c0_ready = S.take("c0_ready")
    own = S.take("shift_steps")
    centre = S.take("centre_ready")
    both = S.take("neighbours_added")
    back = S.take("copied_back")
    tiles = (T_GD, 0, 1, 2, 3)
    wt, w_gd = E.tail_w, E.last_w
    n_t = 15
    with nc.Block() as block:
        @block.gpsimd
        def _(pool):
            S.clear_old(pool)

        @block.tensor
        def _(pe):
            for i, m in enumerate(tiles):
                if i == 4:
                    pe.wait_ge(out, 1)
                for k in range(KT):
                    wk = wt[:, k, (i - 1) * P:i * P] if i else w_gd[:, k, :]
                    for a in range(2):
                        last = pe.matmul(E.PS[:, 2 * (i % 4) + a, 0:HALF], wk,
                                         halves(E.h[:, k, :], 2)[:, a, :], start=(k == 0), stop=(k == KT - 1))
                last.then_inc(done, 1)

        @block.scalar
        def _(act):
            def take_out(i):
                act.wait_ge(done, i + 1)
                act.activation(halves(E.zs[tiles[i]], 2), E.PS[:, 2 * (i % 4):2 * (i % 4) + 2, 0:HALF],
                               ACT.Identity).then_inc(out, 1)

            def return_tile(i):
                act.wait_ge(both, i + 1)
                act.copy(E.zs[T_R + i], E.shifted[:, i % 4, :]).then_inc(back, 1)
            act.wait_ge(c0_ready, 1)
            for i in range(n_t):
                if i >= 4:
                    act.wait_ge(back, i - 3)
                if i % 4 == 2:
                    take_out(i // 4)
                if i == n_t - 1:
                    act.wait_ge(out, 1)
                act.mul(E.shifted[:, i % 4, :], E.zs[T_R + i], E.par[:, Q_C0 + i:Q_C0 + i + 1]).then_inc(centre, 1)
                if i >= 2:
                    return_tile(i - 2)
            for i in (n_t - 2, n_t - 1):
                return_tile(i)
            take_out(4)

        @block.vector
        def _(dve):
            c = Chain(dve, own)
            c0 = E.par[:, Q_C0:Q_C0 + n_t]
            c.link(dve.tensor_tensor(c0, E.par[:, Q_MP:Q_MP + n_t], E.par[:, Q_MN:Q_MN + n_t], ALU.add))
            dve.tensor_scalar(c0, c0, -1.0, 1.0, ALU.mult, ALU.add).then_inc(c0_ready, 1)
            for i in range(n_t):
                x, u = E.zs[T_R + i], E.shifted[:, i % 4, :]
                dve.wait_ge(centre, i + 1)
                c.link(dve.scalar_tensor_tensor(u[:, 1:L], x[:, 0:L - 1], E.par[:, Q_MP + i:Q_MP + i + 1],
                                                u[:, 1:L], ALU.mult, ALU.add))
                dve.scalar_tensor_tensor(u[:, 0:L - 1], x[:, 1:L], E.par[:, Q_MN + i:Q_MN + i + 1],
                                         u[:, 0:L - 1], ALU.mult, ALU.add).then_inc(both, 1)


def mla_project(nc, S, E):
    S.open()
    done = S.take("tile_done")
    out = S.take("tile_out")
    uq, ukv, pe_w = E.uq, E.ukv, E.pe_w
    tiles = [([uq[:, k, h, 0:P] for k in range(2)], 0, E.qn[:, h, :]) for h in range(H_A)]
    tiles += [([pe_w[:, k, 2 * j:2 * j + 2, :].rearrange("p h c -> p (h c)") for k in range(2)], 0, E.qp[:, j, :])
              for j in range(2)]
    tiles += [([ukv[:, h, 0:P]], 2, E.kn[:, h, :]) for h in range(H_A)]
    with nc.Block() as block:
        @block.gpsimd
        def _(pool):
            S.clear_old(pool)

        @block.tensor
        def _(pe):
            for i, (w, k0, _) in enumerate(tiles):
                if i >= 4:
                    pe.wait_ge(out, i - 3)
                for k in range(len(w)):
                    for a in range(2):
                        last = pe.matmul(E.PS[:, 2 * (i % 4) + a, 0:HALF], w[k],
                                         halves(E.n[:, k0 + k, :], 2)[:, a, :], start=(k == 0), stop=(k == len(w) - 1))
                last.then_inc(done, 1)
            pe.wait_ge(out, 10)
            for t, (t0, rows) in enumerate(TOK):
                last = pe.matmul(E.PS[0:rows, t, :], E.n[:, 2, t0:t0 + rows], ukv[:, :, P:2 * P], start=True, stop=True)
                last.then_inc(done, 1)

        @block.scalar
        def _(act):
            for i, (_, _, dst) in enumerate(tiles):
                act.wait_ge(done, i + 1)
                act.activation(halves(dst, 2), E.PS[:, 2 * (i % 4):2 * (i % 4) + 2, 0:HALF],
                               ACT.Identity).then_inc(out, 1)
            for t, (t0, rows) in enumerate(TOK):
                act.wait_ge(done, 11 + t)
                act.copy(E.vn2[0:rows, t, :], E.PS[0:rows, t, :])


def mla_loads(E):
    w = E.A["mla_w_uq_2"][E.li].rearrange("(k p) (h c) -> p k h c", p=P, h=H_A)
    loads = [(E.ukv, E.A["mla_w_ukv_2"][E.li].rearrange("p (h c) -> p h c", h=H_A))]
    for k in range(2):
        loads += [(E.uq[:, k], w[:, k]), (E.pe_w[:, k], w[:, k, :, P:192])]
    return loads


def mla_attend(nc, S, E, fetch):
    S.open()
    logit_done = S.take("logit_done")
    neg_max = S.take("neg_max")
    max_steps = S.take("max_steps")
    exp_done = S.take("exp_done")
    turned = S.take("probs_turned")
    copied = S.take("probs_copied")
    copied_end = S.take("probs_end_copied")
    pv_done = S.take("pv_done")
    inv_ready = S.take("sum_inverse")
    o_ready = S.take("o_ready")
    blank = S.take("blank")
    units = [(t, h) for t in range(len(TOK)) for h in range(H_A)]
    n = len(units)
    nt = len(TOK)
    with nc.Block() as block:
        fetch_beside(block, S, fetch)

        @block.gpsimd
        def _(pool):
            S.clear_old(pool)
            pool.memset(E.on[:, nt - 1, :], 1.0).then_inc(blank, 1)

        @block.tensor
        def _(pe):
            def logits(i):
                t, h = units[i]
                t0, rows = TOK[t]
                r = (h % 2) * 64
                if i >= 2:
                    pe.wait_ge(exp_done, i - 1)
                for a in range(2):
                    dst = E.PS[0:rows, 2 * (i % 2) + a, 0:HALF]
                    pe.matmul(dst, E.qn[:, h, t0:t0 + rows], halves(E.kn[:, h, :], 2)[:, a, :], start=True, stop=False)
                    last = pe.matmul(dst, E.qp[r:r + 64, h // 2, t0:t0 + rows],
                                     halves(E.zs[T_KPE], 2)[r:r + 64, a, :], start=False, stop=True)
                last.then_inc(logit_done, 1)

            def turn(i):
                t, h = units[i]
                rows = TOK[t][1]
                pe.wait_ge(exp_done, i + 1)
                if i >= 2:
                    pe.wait_ge(copied, i - 1)
                    pe.wait_ge(copied_end, i - 1)
                for b, (b0, br) in enumerate(TOK):
                    dst = (E.PS[0:br, 4 + i % 2, b * P:b * P + rows] if b < 4 else
                           E.PS[0:br, 6, (i % 2) * P:(i % 2) * P + rows])
                    last = pe.transpose(dst, E.prob2[0:rows, i % 2, b0:b0 + br], E.ident[0:rows, 0:rows])
                last.then_inc(turned, 1)

            def values(i):
                t, h = units[i]
                rows = TOK[t][1]
                pe.wait_ge(copied, i + 1)
                pe.wait_ge(copied_end, i + 1)
                if h == 0 and t >= 1:
                    pe.wait_ge(o_ready, t)
                for b, (b0, br) in enumerate(TOK):
                    last = pe.matmul(E.PS[0:rows, 7, h * P:(h + 1) * P], E.probT2[0:br, i % 2, b, 0:rows],
                                     E.vn2[0:br, b, h * P:(h + 1) * P], start=(b == 0), stop=(b == nt - 1))
                last.then_inc(pv_done, 1)

            logits(0)
            for i in range(n + 1):
                if i + 1 < n:
                    logits(i + 1)
                if i < n:
                    turn(i)
                if i >= 1:
                    values(i - 1)

        @block.vector
        def _(dve):
            def top(i):
                t, h = units[i]
                rows = TOK[t][1]
                dve.wait_ge(logit_done, i + 1)
                dve.tensor_reduce(E.mx2[0:rows, i:i + 1], E.PS[0:rows, 2 * (i % 2):2 * (i % 2) + 2, 0:HALF],
                                  mybir.AxisListType.XY, ALU.max).then_inc(max_steps, 1)
                dve.wait_ge(max_steps, i + 1)
                dve.tensor_scalar(E.mx2[0:rows, i:i + 1], E.mx2[0:rows, i:i + 1], -MLA_SCALE, None,
                                  ALU.mult).then_inc(neg_max, 1)

            def copy(i):
                t, h = units[i]
                rows = TOK[t][1]
                dve.wait_ge(turned, i + 1)
                if i >= 2:
                    dve.wait_ge(pv_done, i - 1)
                dve.tensor_copy(E.probT2[:, i % 2, 0:4, 0:rows],
                                E.PS[:, 4 + i % 2, :].rearrange("p (b n) -> p b n", b=4)[:, :, 0:rows]).then_inc(copied, 1)

            def out(t):
                rows = TOK[t][1]
                s = E.sums2[0:rows, 4 * t:4 * t + 4]
                dve.wait_ge(exp_done, 4 * t + 4)
                dve.reciprocal(s, s).then_inc(inv_ready, 1)
                dve.wait_ge(pv_done, 4 * t + 4)
                dve.wait_ge(inv_ready, t + 1)
                if t == nt - 1:
                    dve.wait_ge(blank, 1)
                dve.tensor_tensor(E.on[0:rows, t, :].rearrange("p (h n) -> p h n", h=H_A),
                                  E.PS[0:rows, 7, :].rearrange("p (h n) -> p h n", h=H_A),
                                  s.unsqueeze(2).broadcast_to([rows, H_A, P]), ALU.mult).then_inc(o_ready, 1)

            top(0)
            for i in range(n + 2):
                if i + 1 < n:
                    top(i + 1)
                if i < n:
                    copy(i)
                if i >= 4 and i % 4 == 0:
                    out(i // 4 - 1)

        @block.scalar
        def _(act):
            for i, (t, h) in enumerate(units):
                rows = TOK[t][1]
                act.wait_ge(neg_max, i + 1)
                if i >= 2:
                    act.wait_ge(turned, i - 1)
                act.activation(halves(E.prob2[0:rows, i % 2, :], 2), E.PS[0:rows, 2 * (i % 2):2 * (i % 2) + 2, 0:HALF],
                               ACT.Exp, bias=E.mx2[0:rows, i:i + 1], scale=MLA_SCALE,
                               accum_out=E.sums2[0:rows, i:i + 1]).then_inc(exp_done, 1)
                act.wait_ge(turned, i + 1)
                if i >= 2:
                    act.wait_ge(pv_done, i - 1)
                act.copy(E.probT2[0:N_META, i % 2, 4, 0:rows],
                         E.PS[0:N_META, 6, (i % 2) * P:(i % 2) * P + rows]).then_inc(copied_end, 1)


def mla_out(nc, S, E):
    S.open()
    own = S.take("norm_steps")
    sq_ready = S.take("sq_ready")
    var_ready = S.take("var_ready")
    std_ready = S.take("std_ready")
    o_ready = S.take("o_ready")
    turned = S.take("turned")
    copied = S.take("copied")
    nt = len(TOK)
    with nc.Block() as block:
        @block.gpsimd
        def _(pool):
            S.clear_old(pool)

        @block.scalar
        def _(act):
            act.activation(E.osq[:, :, :], E.on[:, :, :], ACT.Square).then_inc(sq_ready, 1)
            act.wait_ge(var_ready, 1)
            act.activation(E.ovar[:, :], E.ovar[:, :], ACT.Sqrt).then_inc(std_ready, 1)
            for m in range(4):
                act.wait_ge(turned, m + 1)
                act.copy(E.y[:, m, 0:512], E.PS[:, 2 * (m % 2), :])
                act.copy(E.y[:, m, 512:L], E.PS[:, 2 * (m % 2) + 1, 0:N_META]).then_inc(copied, 1)

        @block.vector
        def _(dve):
            c = Chain(dve, own)
            dve.wait_ge(sq_ready, 1)
            c.link(dve.tensor_reduce(E.ovar[:, :], E.osq[:, :, :].rearrange("p t (h n) -> p (t h) n", h=H_A), AX, ALU.add))
            dve.tensor_scalar(E.ovar[:, :], E.ovar[:, :], 1.0 / P, 1e-6, ALU.mult, ALU.add).then_inc(var_ready, 1)
            dve.wait_ge(std_ready, 1)
            c.link(dve.reciprocal(E.ovar[:, :], E.ovar[:, :]))
            v = E.on[:, :, :].rearrange("p t (h n) -> p (t h) n", h=H_A)
            c.link(dve.tensor_tensor(v, v, E.ovar[:, :].unsqueeze(2).broadcast_to([P, nt * H_A, P]), ALU.mult))
            dve.tensor_tensor(E.on[:, :, :], E.on[:, :, :], E.onorm[:, :].unsqueeze(1).broadcast_to([P, nt, 512]),
                              ALU.mult).then_inc(o_ready, 1)

        @block.tensor
        def _(pe):
            pe.wait_ge(o_ready, 1)
            for m in range(4):
                if m >= 2:
                    pe.wait_ge(copied, m - 1)
                for t, (t0, rows) in enumerate(TOK):
                    dst = E.PS[:, 2 * (m % 2) + t // 4, (t % 4) * P:(t % 4) * P + rows]
                    last = pe.transpose(dst, E.on[0:rows, t, m * P:(m + 1) * P], E.ident[0:rows, 0:rows])
                last.then_inc(turned, 1)


def lora_loads(E):
    A, li = E.A, E.li
    flat = E.wring[:, :, :, :].rearrange("p s k m -> p (s k m)")
    E.w2, E.a2 = flat[:, 512:1024], flat[:, 1024:1536]
    E.v1 = flat[:, 1536:1664].rearrange("p (k m) -> p k m", k=4)
    E.v2 = flat[0:32, 1664:2176]
    return [(E.w2, A["rwkv_w2_2"][li].rearrange("d j m -> (d j) m")),
            (E.a2, A["rwkv_a2_2"][li].rearrange("d j m -> (d j) m")),
            (E.v1, A["rwkv_v1_2"][0].rearrange("(k p) m -> p k m", p=P)),
            (E.v2, A["rwkv_v2_2"][0])]


def value_mix(nc, S, E):
    S.open()
    own = S.take("mix_steps")
    low_done = S.take("low_done")
    low_ready = S.take("low_ready")
    up_done = S.take("up_done")
    sig = S.take("sig_ready")
    v, vf, d = E.zr[:, T_V - T_R:T_V - T_R + 4, 0:L], E.vfirst[:, :, :], E.tmp4
    with nc.Block() as block:
        @block.gpsimd
        def _(pool):
            S.clear_old(pool)

        @block.tensor
        def _(pe):
            for k in range(4):
                for a in range(2):
                    last = pe.matmul(E.PS[0:32, a, 0:HALF], E.v1[:, k, :], halves(v[:, k, :], 2)[:, a, :],
                                     start=(k == 0), stop=(k == 3))
            last.then_inc(low_done, 1)
            pe.wait_ge(low_ready, 1)
            for m in range(4):
                if m >= 3:
                    pe.wait_ge(sig, m - 2)
                for a in range(2):
                    last = pe.matmul(E.PS[:, 2 + 2 * (m % 3) + a, 0:HALF], E.v2[:, m * P:(m + 1) * P],
                                     halves(E.low[:, :], 2)[:, a, :], start=True, stop=True)
                last.then_inc(up_done, 1)

        @block.scalar
        def _(act):
            act.wait_ge(low_done, 1)
            act.copy(halves(E.low[:, :], 2), E.PS[0:32, 0:2, 0:HALF]).then_inc(low_ready, 1)
            for m in range(4):
                act.wait_ge(up_done, m + 1)
                b = 2 + 2 * (m % 3)
                act.activation(halves(E.tmp4b[:, m, :], 2), E.PS[:, b:b + 2, 0:HALF], ACT.Sigmoid,
                               bias=E.par[:, Q_V0 + m:Q_V0 + m + 1]).then_inc(sig, 1)

        @block.vector
        def _(dve):
            c = Chain(dve, own)
            c.link(dve.tensor_tensor(d, v, vf, ALU.subtract))
            c.link(dve.scalar_tensor_tensor(vf, d, E.par[:, Q_FIRST:Q_FIRST + 1], vf, ALU.mult, ALU.add))
            c.link(dve.tensor_tensor(d, vf, v, ALU.subtract))
            dve.wait_ge(sig, 4)
            dve.wait_ge(low_done, 1)
            c.link(dve.tensor_tensor(d, d, E.tmp4b, ALU.mult))
            dve.tensor_tensor(v, v, d, ALU.add)


def removal_keys(nc, S, E):
    S.open()
    raw = S.take("raw_ready")
    sq = S.take("sq_ready")
    ssq = S.take("ssq_ready")
    var = S.take("var_ready")
    std = S.take("std_ready")
    inv = S.take("inverse_ready")
    spread = S.take("inverse_spread")
    k = E.zr[:, T_K - T_R:T_K - T_R + 4, 0:L]
    with nc.Block() as block:
        @block.gpsimd
        def _(pool):
            S.clear_old(pool)
            pool.memset(E.kk[:, :, L:LP], 0.0)

        @block.tensor
        def _(pe):
            for m in range(4):
                pe.wait_ge(sq, m + 1)
                for a in range(2):
                    last = pe.matmul(E.PS[0:8, a, 0:HALF], E.head_in[:, m * 8:(m + 1) * 8],
                                     halves(E.tmp4[:, m, :], 2)[:, a, :], start=(m == 0), stop=(m == 3))
            last.then_inc(ssq, 1)
            pe.wait_ge(inv, 1)
            for m in range(4):
                for a in range(2):
                    last = pe.matmul(E.PS[:, (2 + 2 * m) % 8 + a, 0:HALF], E.head_out[:, m * P:(m + 1) * P],
                                     halves(E.by_head, 2)[:, a, :], start=True, stop=True)
                last.then_inc(spread, 1)

        @block.scalar
        def _(act):
            for m in range(4):
                act.wait_ge(raw, m + 1)
                act.activation(E.tmp4[:, m, :], E.kk[:, m, 0:L], ACT.Square).then_inc(sq, 1)
            act.wait_ge(var, 1)
            act.activation(E.by_head, E.by_head, ACT.Sqrt).then_inc(std, 1)

        @block.vector
        def _(dve):
            for m in range(4):
                dve.tensor_scalar(E.kk[:, m, 0:L], k[:, m, :], E.par[:, Q_KK + m:Q_KK + m + 1], None,
                                  ALU.mult).then_inc(raw, 1)
            dve.wait_ge(ssq, 1)
            dve.tensor_scalar(halves(E.by_head, 2), E.PS[0:8, 0:2, 0:HALF], 1e-12, None, ALU.add).then_inc(var, 1)
            dve.wait_ge(std, 1)
            dve.reciprocal(E.by_head, E.by_head).then_inc(inv, 1)
            for m in range(4):
                dve.wait_ge(spread, m + 1)
                b = (2 + 2 * m) % 8
                dve.tensor_tensor(halves(E.kk[:, m, 0:L], 2), halves(E.kk[:, m, 0:L], 2), E.PS[:, b:b + 2, 0:HALF],
                                  ALU.mult)


def rates(nc, S, E):
    S.open()
    act_ready = S.take("tanh_ready")
    w_done = S.take("w_done")
    a_done = S.take("a_done")
    w_sig = S.take("w_sig")
    a_sig = S.take("a_sig")
    blank = S.take("blank")
    own = S.take("rate_steps")
    units = [(d, m) for d in range(2) for m in range(4)]
    k = E.zr[:, T_K - T_R:T_K - T_R + 4, 0:L]
    with nc.Block() as block:
        @block.gpsimd
        def _(pool):
            S.clear_old(pool)
            for d in range(2):
                for x in (E.ld[d], E.ba[d], E.kd[:, d]):
                    pool.memset(x[:, :, L:LP], 0.0).then_inc(blank, 1)

        @block.tensor
        def _(pe):
            pe.wait_ge(act_ready, 1)
            for i, (d, m) in enumerate(units):
                r = d * 64
                if i >= 2:
                    pe.wait_ge(w_sig, i - 1)
                for a in range(2):
                    last = pe.matmul(E.PS[:, 4 * (i % 2) + a, 0:HALF], E.w2[r:r + 64, m * P:(m + 1) * P],
                                     halves(E.lora[:, 0, :], 2)[r:r + 64, a, :], start=True, stop=True)
                last.then_inc(w_done, 1)
                if i >= 2:
                    pe.wait_ge(a_sig, i - 1)
                for a in range(2):
                    last = pe.matmul(E.PS[:, 4 * (i % 2) + 2 + a, 0:HALF], E.a2[r:r + 64, m * P:(m + 1) * P],
                                     halves(E.zs[T_AD], 2)[r:r + 64, a, :], start=True, stop=True)
                last.then_inc(a_done, 1)

        @block.scalar
        def _(act):
            act.activation(E.lora[:, 0, :], E.zs[T_WD], ACT.Tanh).then_inc(act_ready, 1)
            for i, (d, m) in enumerate(units):
                b = 4 * (i % 2)
                act.wait_ge(w_done, i + 1)
                act.activation(halves(E.ld[d][:, m, 0:L], 2), E.PS[:, b:b + 2, 0:HALF], ACT.Sigmoid,
                               bias=E.par[:, Q_W0 + 4 * d + m:Q_W0 + 4 * d + m + 1]).then_inc(w_sig, 1)
                act.wait_ge(a_done, i + 1)
                act.activation(halves(E.ba[d][:, m, 0:L], 2), E.PS[:, b + 2:b + 4, 0:HALF], ACT.Sigmoid,
                               bias=E.par[:, Q_A0 + 4 * d + m:Q_A0 + 4 * d + m + 1]).then_inc(a_sig, 1)

        @block.vector
        def _(dve):
            c = Chain(dve, own)
            dve.wait_ge(blank, 6)
            for i, (d, m) in enumerate(units):
                ld, cum, ba, kd = E.ld[d], E.cum[d], E.ba[d], E.kd[:, d]
                dve.wait_ge(w_sig, i + 1)
                c.link(dve.tensor_scalar(ld[:, m, 0:L], ld[:, m, 0:L], -EXP_HALF, None, ALU.mult))
                c.add(dve.tensor_tensor_scan(cum[:, m, :], E.keep[:, :], ld[:, m, :], 0.0, ALU.mult, ALU.add))
                dve.wait_ge(a_sig, i + 1)
                ka = E.par[:, Q_KA + m:Q_KA + m + 1]
                c.link(dve.tensor_scalar(kd[:, m, 0:L], ba[:, m, 0:L], -1.0, ka, ALU.add, ALU.mult))
                c.add(dve.scalar_tensor_tensor(kd[:, m, 0:L], kd[:, m, 0:L], 1.0, k[:, m, :], ALU.add, ALU.mult))
                c.add(dve.tensor_tensor(ba[:, m, 0:L], ba[:, m, 0:L], E.kk[:, m, 0:L], ALU.mult))
            c.wait()
            cum, ld = E.cum[1], E.ld[1]
            x = cum.rearrange("p m (c n) -> p (m c) n", n=CH)
            c.link(dve.tensor_copy(E.total[:, :], x[:, :, CH - 1]))
            c.link(dve.tensor_tensor(x, E.total[:, :].unsqueeze(2).broadcast_to([P, 4 * N_CH, CH]), x, ALU.subtract))
            c.link(dve.tensor_tensor(cum, cum, ld, ALU.add))


def bonus(nc, S, E):
    S.open()
    own = S.take("bonus_steps")
    x_ready = S.take("x_ready")
    done = S.take("head_sum_done")
    r, v = E.zr[:, 0:4, 0:L], E.zr[:, T_V - T_R:T_V - T_R + 4, 0:L]
    with nc.Block() as block:
        @block.gpsimd
        def _(pool):
            S.clear_old(pool)
            pool.memset(E.zr[:, 0:12, L:LP], 0.0)
            pool.memset(E.state[:, :, :, :], 0.0)

        @block.vector
        def _(dve):
            c = Chain(dve, own)
            for m in range(4):
                c.link(dve.tensor_tensor(E.tmp4[:, m, :], E.kd[:, 0, m, 0:L], E.kd[:, 1, m, 0:L], ALU.add))
                dve.scalar_tensor_tensor(E.tmp4[:, m, :], E.tmp4[:, m, :], E.par[:, Q_RK + m:Q_RK + m + 1], r[:, m, :],
                                         ALU.mult, ALU.mult).then_inc(x_ready, 1)
            for m in range(4):
                dve.wait_ge(done, m + 1)
                dve.tensor_tensor(halves(E.bonus[:, m, :], 2), E.PS[:, 2 * m:2 * m + 2, 0:HALF],
                                  halves(v[:, m, :], 2), ALU.mult)

        @block.tensor
        def _(pe):
            for m in range(4):
                pe.wait_ge(x_ready, m + 1)
                for a in range(2):
                    last = pe.matmul(E.PS[:, 2 * m + a, 0:HALF], E.head_ones[:, :], halves(E.tmp4[:, m, :], 2)[:, a, :],
                                     start=True, stop=True)
                last.then_inc(done, 1)


def recurrence(nc, S, E):
    sweep(nc, S)
    names_a = ["end_ready", "products", "x_turned", "pair_copied", "own_a"]
    names_b = ["before_ready", "exp_ready", "levels_ready", "mk_ready", "own_b"] + [f"{x}_{g}" for g in range(2) for x in (
        "f_done", "f_half", "f_ready", "t1_done", "t1_ready", "x_done", "x_ready", "xt_done", "xt_ready",
        "sa_done", "sa_ready", "y_state", "y_half", "y_done")]
    with ExitStack() as stack:
        a = {x: stack.enter_context(nc.semaphore("chunk_" + x)) for x in names_a}
        b = {x: stack.enter_context(nc.semaphore("chunk_" + x)) for x in names_b}
        prep = Preparation(E, 0, b)
        with nc.Block() as block:
            @block.scalar
            def _(act):
                prep.decays(act, 0)
                prep.decays(act, 1)
                prep.before(act)
                prep.values(act)

            @block.vector
            def _(dve):
                prep.differences(dve)
                prep.removals(dve)

            @block.gpsimd
            def _(pool):
                prep.keys(pool)
        with nc.Fori(0, N_CH - 1) as c:
            _chunk_products(nc, E, a, b)
            _chunk_solve(nc, E, c, a, b, Preparation(E, c + 1, b))
        _chunk_products(nc, E, a, b)
        _chunk_solve(nc, E, N_CH - 1, a, b, None)
        with nc.Block() as block:
            @block.gpsimd
            def _(pool):
                for s in [*a.values(), *b.values()]:
                    pool.sem_clear(s)


class Preparation:

    def __init__(self, E, c, b):
        self.E, self.b = E, b
        self.at = [c * CH, (N_CH - 1 - c) * CH]

    def piece(self, x, d):
        return x[:, :, bass.ds(self.at[d], CH)]

    def decays(self, act, d):
        E = self.E
        act.activation(E.ep[:, :, d, :], self.piece(E.cum[d], d), ACT.Exp).then_inc(self.b["exp_ready"], 1)
        act.activation(E.en[:, :, d, :], self.piece(E.cum[d], d), ACT.Exp, scale=-1.0).then_inc(self.b["exp_ready"], 1)

    def differences(self, dve):
        E = self.E
        for d in range(2):
            dve.tensor_tensor(E.ex[:, :, d, :], self.piece(E.cum[d], d), self.piece(E.ld[d], d),
                              ALU.subtract).then_inc(self.b["before_ready"], 1)

    def before(self, act):
        act.wait_ge(self.b["before_ready"], 2)
        act.activation(self.E.ex, self.E.ex, ACT.Exp).then_inc(self.b["exp_ready"], 1)

    def values(self, act):
        E = self.E
        for d in range(2):
            act.copy(E.vb[:, :, d, :], self.piece(E.zr[:, T_V - T_R:T_V - T_R + 4, :], d))

    def removals(self, dve):
        E = self.E
        dve.wait_ge(self.b["exp_ready"], 5)
        for d in range(2):
            dve.tensor_tensor(E.bb[:, :, d, :], self.piece(E.ba[d], d), E.en[:, :, d, :], ALU.mult)
            dve.tensor_tensor(E.ar[:, :, d, 0, :], self.piece(E.kk, d), E.ex[:, :, d, :], ALU.mult)

    def keys(self, pool):
        E = self.E
        pool.wait_ge(self.b["exp_ready"], 5)
        for d in range(2):
            pool.tensor_tensor(E.ar[:, :, d, 1, :], self.piece(E.zr[:, 0:4, :], d), E.ep[:, :, d, :], ALU.mult)
            pool.tensor_tensor(E.kb[:, :, d, :], self.piece(E.kd[:, d], d), E.en[:, :, d, :], ALU.mult)


def _heads():
    return [(d, h, (h % 2) * 64, d * 64) for h in range(8) for d in range(2)]


def _by_parity(x):
    return x.rearrange("p (m q) n -> p q m n", q=2)


def _pair_masks(E):
    return E.pair[:, :, :].rearrange("p r n -> p (r n)").unsqueeze(1).unsqueeze(1).broadcast_to([P, 2, 4, 2 * CH])


def _both(x):
    return _by_parity(x.rearrange("p h r n -> p h (r n)"))


MK_BANKS = (3, 7)


def _chunk_products(nc, E, a, b):
    ar, bb, kb, vb = E.ar, E.bb, E.kb, E.vb
    with nc.Block() as block:
        @block.gpsimd
        def _(pool):
            for s in b.values():
                pool.sem_clear(s)

        @block.vector
        def _(dve):
            for d in range(2):
                dve.tensor_copy(E.pend[:, :, d], E.ep[:, :, d, CH - 1 if d == 0 else 0])
            own = Chain(dve, a["own_a"])
            eye = E.eye2[:, :].unsqueeze(1).broadcast_to([P, 8, CH])
            m0 = E.level[:, 0, 0, :].unsqueeze(1).broadcast_to([P, 8, CH])
            dve.wait_ge(a["products"], 1)
            own.link(dve.tensor_tensor(_by_parity(E.x), E.PS[:, 0:2, 0:4 * CH].rearrange("p q (m n) -> p q m n", m=4),
                                       _by_parity(m0), ALU.mult))
            own.add(dve.tensor_tensor(E.x[:, :, :], eye, E.x[:, :, :], ALU.subtract))
            dve.wait_ge(a["products"], 2)
            own.link(dve.tensor_tensor(_both(E.lb), E.PS[:, 4:6, :].rearrange("p q (m n) -> p q m n", m=4),
                                       _pair_masks(E), ALU.mult))
            m0t = E.level[:, 1, 0, :].unsqueeze(1).broadcast_to([P, 8, CH])
            m1t = E.level[:, 1, 1, :].unsqueeze(1).broadcast_to([P, 8, CH])
            own.add(dve.tensor_tensor(E.mjt[0], E.lb[:, :, 0, :], m1t, ALU.mult))
            own.link(dve.tensor_tensor(E.xt[:, :, :], E.lb[:, :, 0, :], m0t, ALU.mult))
            dve.tensor_tensor(E.xt[:, :, :], eye, E.xt[:, :, :], ALU.subtract)

        @block.scalar
        def _(act):
            for n, dst in enumerate((E.vtok, E.btok, E.ktok)):
                act.wait_ge(a["x_turned"], n + 1)
                act.copy(dst[:, :], E.PS[:, (6, 2, 6)[n], :]).then_inc(a["pair_copied"], 1)

        @block.tensor
        def _(pe):
            def turn(src, bank):
                for hp in range(4):
                    last = pe.transpose(E.PS[:, bank, hp * P:(hp + 1) * P],
                                        src[:, hp, :, :].rearrange("p d n -> p (d n)"), E.ident[:, :])
                last.then_inc(a["x_turned"], 1)
            for d, h, hr, tr in _heads():
                last = pe.matmul(E.PS[tr:tr + CH, h % 2, (h // 2) * CH:(h // 2 + 1) * CH], ar[hr:hr + 64, h // 2, d, 0, :],
                                 bb[hr:hr + 64, h // 2, d, :], start=True, stop=True)
            last.then_inc(a["products"], 1)

            def pairs(src, banks):
                for d, h, hr, tr in _heads():
                    last = pe.matmul(E.PS[tr:tr + CH, banks[h % 2], (h // 2) * 2 * CH:(h // 2 + 1) * 2 * CH],
                                     src[hr:hr + 64, h // 2, d, :],
                                     ar[hr:hr + 64, h // 2, d, :, :].rearrange("p r n -> p (r n)"),
                                     start=True, stop=True)
                return last
            pairs(bb, (4, 5)).then_inc(a["products"], 1)
            turn(vb, 6)
            turn(bb, 2)
            pairs(kb, MK_BANKS)
            pe.wait_ge(a["pair_copied"], 1)
            turn(kb, 6)


def _chunk_solve(nc, E, c, a, b, prep):
    at = [c * CH, (N_CH - 1 - c) * CH]

    def group(x, g):
        return _by_parity(x)[:, g]

    def psum(g, bank):
        return E.PS[:, 4 * g + bank, 0:256].rearrange("p (m n) -> p m n", m=4)
    with nc.Block() as block:
        @block.gpsimd
        def _(pool):
            for s in a.values():
                pool.sem_clear(s)
            for j in range(2, LEVELS):
                mj = E.level[:, 1, j, :].unsqueeze(1).broadcast_to([P, 8, CH])
                pool.tensor_tensor(E.mjt[j - 1], E.lb[:, :, 0, :], mj, ALU.mult).then_inc(b["levels_ready"], 1)
            if prep:
                for g in range(2):
                    pool.wait_ge(b[f"f_done_{g}"], 1)
                prep.keys(pool)

        @block.tensor
        def _(pe):
            def tokens_product(g, bank, left, right):
                for m in range(4):
                    for d in range(2):
                        tr, h, col = d * CH, 2 * m + g, m * CH
                        last = pe.matmul(E.PS[tr:tr + CH, 4 * g + bank, col:col + CH], left[tr:tr + CH, h, :],
                                         right[tr:tr + CH, h, :], start=True, stop=True)
                return last

            def by_head(x):
                return x.rearrange("p (h n) -> p h n", h=8)

            def old_state():
                for g in range(2):
                    hr = g * 64
                    for m in range(4):
                        for d in range(2):
                            cols = (m * 2 + d) * CH
                            last = pe.matmul(E.PS[hr:hr + 64, 4 * g + 2, cols:cols + CH], E.state[hr:hr + 64, m, d, :],
                                             E.ar[hr:hr + 64, m, d, 1, :], start=True, stop=True)
                    last.then_inc(b[f"y_state_{g}"], 1)
                for g in range(2):
                    pe.wait_ge(b["mk_ready"], g + 1)
                    hr = g * 64
                    for m in range(4):
                        for d in range(2):
                            pe.matmul(E.PS[d * CH:d * CH + CH, 4 * g + 3, m * CH:(m + 1) * CH],
                                      E.ar[hr:hr + 64, m, d, 0, :], E.state[hr:hr + 64, m, d, :],
                                      start=True, stop=True)
                    tokens_product(g, 1, E.mk[:, :, 0, :], by_head(E.vtok)).then_inc(b[f"f_done_{g}"], 1)

            for j in range(1, LEVELS):
                if j > 1:
                    pe.wait_ge(b["levels_ready"], j - 1)
                for g in range(2):
                    if j > 1:
                        pe.wait_ge(b[f"x_ready_{g}"], j - 1)
                    tokens_product(g, 0, E.mjt[j - 1], E.x).then_inc(b[f"t1_done_{g}"], 1)
                if j == 1:
                    old_state()
                for g in range(2):
                    pe.wait_ge(b[f"t1_ready_{g}"], j)
                    if j > 1:
                        pe.wait_ge(b[f"xt_ready_{g}"], j - 1)
                    else:
                        pe.wait_ge(b[f"f_half_{g}"], 1)
                        pe.wait_ge(b[f"y_half_{g}"], 2)
                    if j < LEVELS - 1:
                        tokens_product(g, 1, E.xt, E.t1).then_inc(b[f"x_done_{g}"], 1)
                    tokens_product(g, 2, E.t1, E.xt).then_inc(b[f"xt_done_{g}"], 1)
            for g in range(2):
                pe.wait_ge(b[f"f_ready_{g}"], 1)
                pe.wait_ge(b[f"xt_ready_{g}"], LEVELS - 1)
                tokens_product(g, 0, E.xt, E.f).then_inc(b[f"sa_done_{g}"], 1)
            for g in range(2):
                hr = g * 64
                pe.wait_ge(b[f"sa_ready_{g}"], 1)
                for m in range(4):
                    for d in range(2):
                        tr, h = d * CH, 2 * m + g
                        dst = E.PS[hr:hr + 64, 4 * g + 1 + d, m * CH:(m + 1) * CH]
                        pe.matmul(dst, E.ktok[tr:tr + CH, h * CH:(h + 1) * CH], E.vtok[tr:tr + CH, h * CH:(h + 1) * CH],
                                  start=True, stop=False)
                        pe.matmul(dst, E.btok[tr:tr + CH, h * CH:(h + 1) * CH], E.sa[tr:tr + CH, h, :],
                                  start=False, stop=True)
                for m in range(4):
                    for d in range(2):
                        tr, h = d * CH, 2 * m + g
                        dst = E.PS[hr:hr + 64, 4 * g + 1 + d, 256 + m * CH:256 + (m + 1) * CH]
                        pe.matmul(dst, E.vtok[tr:tr + CH, h * CH:(h + 1) * CH], E.mk[tr:tr + CH, h, 1, :],
                                  start=True, stop=False)
                        last = pe.matmul(dst, E.sa[tr:tr + CH, h, :], E.lb[tr:tr + CH, h, 1, :], start=False, stop=True)
                last.then_inc(b[f"y_done_{g}"], 1)

        @block.scalar
        def _(act):
            for j in range(1, LEVELS):
                for g in range(2):
                    act.wait_ge(b[f"t1_done_{g}"], j)
                    act.copy(group(E.t1, g), psum(g, 0)).then_inc(b[f"t1_ready_{g}"], 1)
                if j == 1:
                    for g in range(2):
                        hr = slice(g * 64, g * 64 + 64)
                        act.wait_ge(b[f"y_state_{g}"], 1)
                        y = E.PS[hr, 4 * g + 2, :].rearrange("p (m d n) -> p m d n", m=4, d=2)
                        for d in range(2):
                            act.copy(E.ba[d][hr, :, bass.ds(at[d], CH)], y[:, :, d, :]).then_inc(b[f"y_half_{g}"], 1)
                    for g in range(2):
                        act.wait_ge(b[f"f_done_{g}"], 1)
                        act.copy(group(E.f, g), psum(g, 1)).then_inc(b[f"f_half_{g}"], 1)
                if prep and j == 2:
                    prep.decays(act, 0)
                if prep and j == 3:
                    prep.decays(act, 1)
                if prep and j == 4:
                    prep.before(act)
                    prep.values(act)
            for g in range(2):
                act.wait_ge(b[f"sa_done_{g}"], 1)
                act.mul(group(E.sa, g), psum(g, 0), -1.0).then_inc(b[f"sa_ready_{g}"], 1)

        @block.vector
        def _(dve):
            def subtract(x, g, bank, ready):
                dve.tensor_tensor(group(x, g), group(x, g), psum(g, bank), ALU.subtract).then_inc(ready, 1)
            for q, bank in enumerate(MK_BANKS):
                dve.tensor_tensor(_both(E.mk)[:, q], E.PS[:, bank, :].rearrange("p (m n) -> p m n", m=4),
                                  _pair_masks(E)[:, q], ALU.mult).then_inc(b["mk_ready"], 1)
            for g in range(2):
                dve.wait_ge(b[f"f_half_{g}"], 1)
                dve.tensor_tensor(group(E.f, g), group(E.f, g), psum(g, 3), ALU.add).then_inc(b[f"f_ready_{g}"], 1)
            for j in range(1, LEVELS):
                for g in range(2):
                    if j < LEVELS - 1:
                        dve.wait_ge(b[f"x_done_{g}"], j)
                        subtract(E.x, g, 1, b[f"x_ready_{g}"])
                    dve.wait_ge(b[f"xt_done_{g}"], j)
                    subtract(E.xt, g, 2, b[f"xt_ready_{g}"])
                if prep and j == 2:
                    prep.differences(dve)
            if prep:
                prep.removals(dve)
            for g in range(2):
                hr = slice(g * 64, g * 64 + 64)
                st = E.state[hr, :, :, :]
                dve.wait_ge(b[f"y_done_{g}"], 1)
                dve.tensor_tensor(st, st, E.PS[hr, 4 * g + 1:4 * g + 3, 0:256].rearrange("p d (m n) -> p m d n", m=4),
                                  ALU.add).then_inc(b["own_b"], 1)
                for d in range(2):
                    y = E.ba[d][hr, :, bass.ds(at[d], CH)]
                    dve.tensor_tensor(y, y, E.PS[hr, 4 * g + 1 + d, 256:512].rearrange("p (m n) -> p m n", m=4), ALU.add)
                dve.wait_ge(b["own_b"], g + 1)
                dve.tensor_tensor(st, st, E.pend[hr, :, :].unsqueeze(3).broadcast_to([64, 4, 2, CH]), ALU.mult)


def head_norm(nc, S, E, fetch):
    S.open()
    fetched = S.take("fetched")
    y_ready = S.take("y_ready")
    mean_done = S.take("mean_done")
    xc_ready = S.take("xc_ready")
    sq_ready = S.take("sq_ready")
    var_done = S.take("var_done")
    var_ready = S.take("var_ready")
    std_ready = S.take("std_ready")
    inv = S.take("inverse_ready")
    loaded = S.take("head_rows_loaded")
    spread = S.take("inverse_spread")
    own = S.take("norm_steps")
    g_in = S.take("g_in_ready")
    g_done = S.take("g_done")
    biased = S.take("biased")
    yf, yb = E.ba
    out = E.y[:, 4:8, :]
    x = E.tmp8a
    sq = E.tmp8b
    with nc.Block() as block:
        @block.gpsimd
        def _(pool):
            S.clear_old(pool)
            for m in range(4):
                pool.tensor_tensor(x[:, m, :], yf[:, m, 0:L], yb[:, m, 0:L], ALU.add).then_inc(y_ready, 1)

        @block.sync
        def _(sp):
            sp.dma_start(E.head_out, E.A["head_out"]).then_inc(loaded, 16)
            sp.dma_start(E.g2, E.A["rwkv_g2_2"][E.li]).then_inc(loaded, 16)
            for dst, src in fetch:
                sp.dma_start(dst, src).then_inc(fetched, 16)
            sp.wait_ge(loaded, 32)
            sp.wait_ge(fetched, 16 * len(fetch))

        @block.tensor
        def _(pe):
            for m in range(4):
                pe.wait_ge(y_ready, m + 1)
                for a in range(2):
                    last = pe.matmul(E.PS[:, 2 * m + a, 0:HALF], E.head_mean[:, :], halves(x[:, m, :], 2)[:, a, :],
                                     start=True, stop=True)
                last.then_inc(mean_done, 1)
            for m in range(4):
                pe.wait_ge(sq_ready, m + 1)
                for a in range(2):
                    last = pe.matmul(E.PS[0:8, a, 0:HALF], E.head_in[:, m * 8:(m + 1) * 8],
                                     halves(sq[:, m, :], 2)[:, a, :], start=(m == 0), stop=(m == 3))
            last.then_inc(var_done, 1)
            pe.wait_ge(loaded, 32)
            pe.wait_ge(inv, 1)
            for m in range(4):
                for a in range(2):
                    last = pe.matmul(E.PS[:, (2 + 2 * m) % 8 + a, 0:HALF], E.head_out[:, m * P:(m + 1) * P],
                                     halves(E.by_head, 2)[:, a, :], start=True, stop=True)
                last.then_inc(spread, 1)
            pe.wait_ge(g_in, 1)
            for m in range(4):
                pe.wait_ge(own, m + 1)
                for a in range(2):
                    last = pe.matmul(E.PS[:, (2 + 2 * m) % 8 + a, 0:HALF], E.g2[:, m * P:(m + 1) * P],
                                     halves(E.lora[:, 1, :], 2)[:, a, :], start=True, stop=True)
                last.then_inc(g_done, 1)

        @block.scalar
        def _(act):
            act.activation(E.lora[:, 1, :], E.zs[T_GD], ACT.Sigmoid).then_inc(g_in, 1)
            for m in range(4):
                act.wait_ge(xc_ready, m + 1)
                act.activation(sq[:, m, :], x[:, m, :], ACT.Square).then_inc(sq_ready, 1)
            act.wait_ge(var_ready, 1)
            act.activation(E.by_head, E.by_head, ACT.Sqrt).then_inc(std_ready, 1)

        @block.vector
        def _(dve):
            c = Chain(dve, own)
            for m in range(4):
                dve.wait_ge(mean_done, m + 1)
                dve.tensor_tensor(halves(x[:, m, :], 2), halves(x[:, m, :], 2), E.PS[:, 2 * m:2 * m + 2, 0:HALF],
                                  ALU.subtract).then_inc(xc_ready, 1)
            dve.wait_ge(var_done, 1)
            dve.tensor_scalar(halves(E.by_head, 2), E.PS[0:8, 0:2, 0:HALF], 1.0 / 64, 64e-5, ALU.mult,
                              ALU.add).then_inc(var_ready, 1)
            dve.wait_ge(std_ready, 1)
            dve.reciprocal(E.by_head, E.by_head).then_inc(inv, 1)
            for m in range(4):
                b = (2 + 2 * m) % 8
                dve.wait_ge(spread, m + 1)
                c.add(dve.scalar_tensor_tensor(halves(x[:, m, :], 2), halves(x[:, m, :], 2),
                                               E.par[:, Q_GG + m:Q_GG + m + 1], E.PS[:, b:b + 2, 0:HALF],
                                               ALU.mult, ALU.mult))
            for m in range(4):
                b = (2 + 2 * m) % 8
                c.wait(m + 1)
                c.link(dve.scalar_tensor_tensor(x[:, m, :], x[:, m, :], E.par[:, Q_GB + m:Q_GB + m + 1],
                                                E.bonus[:, m, :], ALU.add, ALU.add))
                dve.wait_ge(g_done, m + 1)
                dve.tensor_tensor(halves(out[:, m, :], 2), halves(x[:, m, :], 2), E.PS[:, b:b + 2, 0:HALF], ALU.mult)


def route(nc, S, E):
    S.open()
    loaded = S.take("tables_loaded")
    blank = S.take("blank")
    done = S.take("logits_done")
    own = S.take("route_steps")
    e_in = S.take("exp_in")
    e_out = S.take("exp_out")
    g_ready = S.take("gates_ready")
    turned = S.take("turned")
    copied = S.take("copied")
    stored = S.take("stored")
    expert_loaded = S.take("expert_0_loaded")
    nt = len(TOK)
    R = E.router
    wr, bias = E.router_w, E.router_b
    at = [0]

    def buf(*shape):
        n = int(np.prod(shape))
        x = R[:, at[0]:at[0] + n]
        at[0] += n
        if len(shape) == 2:
            return x.rearrange("p (a b) -> p a b", a=shape[0])
        return x
    lg = buf(nt, 36)
    gl, gx, gs, gc = (buf(nt, 4) for _ in range(4))
    el, ex, s1, s2, cum = (buf(nt, 32) for _ in range(5))
    gm, gsum, m1, m2, z = (buf(nt) for _ in range(5))
    keep_g, keep_e = buf(20), buf(160)
    E.sel = [buf(nt, 32), buf(nt, 32)]
    E.gates = [buf(nt), buf(nt)]
    valid = buf(nt)
    E.router_used = at[0]

    def over(x, n):
        return x.unsqueeze(2).broadcast_to([P, nt, n])

    def flat(x):
        return x.rearrange("p a b -> p (a b)")
    with nc.Block() as block:
        @block.gpsimd
        def _(pool):
            S.clear_old(pool)
            pool.memset(lg, 0.0).then_inc(blank, 1)

        @block.sync
        def _(sp):
            A = E.A
            sp.dma_start(keep_g, A["keep_group"]).then_inc(loaded, 16)
            sp.dma_start(keep_e, A["keep_expert"]).then_inc(loaded, 16)
            sp.dma_start(valid, A["valid_token"]).then_inc(loaded, 16)
            load_expert(E, sp, 0, 0, expert_loaded, expert_loaded)
            sp.wait_ge(copied, 2)
            sp.dma_start(E.gates_dram, E.gT[:, :]).then_inc(stored, 16)
            sp.wait_ge(stored, 16)
            sp.wait_ge(expert_loaded, 48)

        @block.tensor
        def _(pe):
            for t, (t0, rows) in enumerate(TOK):
                for k in range(KT):
                    last = pe.matmul(E.PS[0:rows, 0, t * 36:(t + 1) * 36], E.h[:, k, t0:t0 + rows], wr[:, k, :],
                                     start=(k == 0), stop=(k == KT - 1))
            last.then_inc(done, 1)
            pe.wait_ge(g_ready, 1)
            for t, (t0, rows) in enumerate(TOK):
                last = pe.transpose(E.PS[0:32, 1 + t // 4, (t % 4) * P:(t % 4) * P + rows], ex[0:rows, t, :],
                                    E.ident[0:rows, 0:rows])
            last.then_inc(turned, 1)

        @block.scalar
        def _(act):
            act.wait_ge(e_in, 1)
            act.activation(gx, gx, ACT.Exp).then_inc(e_out, 1)
            act.wait_ge(e_in, 2)
            act.activation(ex, ex, ACT.Exp).then_inc(e_out, 1)
            act.wait_ge(e_in, 3)
            act.activation(m2, m2, ACT.Exp).then_inc(e_out, 1)
            act.wait_ge(turned, 1)
            act.copy(E.gT[:, 0:512], E.PS[0:32, 1, :]).then_inc(copied, 1)
            act.copy(E.gT[:, 512:L], E.PS[0:32, 2, 0:N_META]).then_inc(copied, 1)

        @block.vector
        def _(dve):
            c = Chain(dve, own)
            tt, ts, stt = dve.tensor_tensor, dve.tensor_scalar, dve.scalar_tensor_tensor
            dve.wait_ge(blank, 1)
            dve.wait_ge(loaded, 48)
            dve.wait_ge(done, 1)
            for t, (_, rows) in enumerate(TOK):
                c.add(tt(lg[0:rows, t, :], E.PS[0:rows, 0, t * 36:(t + 1) * 36], bias[0:rows, :], ALU.add))
            c.wait()
            c.link(dve.tensor_copy(gl, lg[:, :, 0:4]))
            c.link(dve.tensor_reduce(gm, gl, AX, ALU.max))
            tt(gx, gl, over(gm, 4), ALU.subtract).then_inc(e_in, 1)
            c.link(tt(gs, gl, over(gm, 4), ALU.is_equal))
            c.link(dve.tensor_tensor_scan(flat(gc), keep_g, flat(gs), 0.0, ALU.mult, ALU.add))
            c.link(stt(gs, gc, 1.0, gs, ALU.is_le, ALU.mult))
            c.link(ts(gs, gs, BIG, -BIG, ALU.mult, ALU.add))
            c.link(tt(el.rearrange("p a (g n) -> p a g n", g=4), lg[:, :, 4:36].rearrange("p a (g n) -> p a g n", g=4),
                      gs.unsqueeze(3).broadcast_to([P, nt, 4, 8]), ALU.add))
            c.link(dve.tensor_reduce(m1, el, AX, ALU.max))
            tt(ex, el, over(m1, 32), ALU.subtract).then_inc(e_in, 1)

            def first_of(sel, top):
                c.link(tt(sel, el, over(top, 32), ALU.is_equal))
                c.link(dve.tensor_tensor_scan(flat(cum), keep_e, flat(sel), 0.0, ALU.mult, ALU.add))
                c.link(stt(sel, cum, 1.0, sel, ALU.is_le, ALU.mult))
            first_of(s1, m1)
            c.link(stt(el, s1, -3 * BIG, el, ALU.mult, ALU.add))
            c.link(dve.tensor_reduce(m2, el, AX, ALU.max))
            first_of(s2, m2)
            c.add(tt(E.sel[0], s1, over(valid, 32), ALU.mult))
            c.link(tt(E.sel[1], s2, over(valid, 32), ALU.mult))
            tt(m2, m2, m1, ALU.subtract).then_inc(e_in, 1)
            dve.wait_ge(e_out, 2)
            c.add(dve.tensor_reduce(gsum, gx, AX, ALU.add))
            c.link(dve.tensor_reduce(z, ex, AX, ALU.add))
            c.link(tt(z, z, gsum, ALU.mult))
            c.link(dve.reciprocal(z, z))
            dve.wait_ge(e_out, 3)
            c.add(dve.tensor_copy(E.gates[0], z))
            c.add(tt(E.gates[1], z, m2, ALU.mult))
            c.link(tt(s2, s2, over(m2, 32), ALU.mult))
            c.link(tt(s1, s1, s2, ALU.add))
            tt(ex, s1, over(z, 32), ALU.mult).then_inc(g_ready, 1)


def dispatch(nc, S, E):
    S.open()
    loaded = S.take("tables_loaded")
    both = S.take("both_ready")
    counted = S.take("counted")
    own = S.take("place_steps")
    placed = S.take("places_ready")
    listed = S.take("choices_listed")
    turned = S.take("tokens_turned")
    copied = S.take("tokens_copied")
    stored = S.take("tokens_stored")
    expert_loaded = S.take("expert_1_loaded")
    nt = len(TOK)
    R = E.router
    at = [E.router_used]

    def buf(n):
        at[0] += n
        return R[:, at[0] - n:at[0]]
    before, slot_index, choice = buf(P), buf(P), buf(10)
    both_sel, within, at_place, earlier, total = buf(160), buf(160), buf(160), buf(160), buf(160)
    numbered = [buf(160), buf(160)]
    place, top = buf(10), buf(1)
    empty, number, tokens = buf(32), buf(32), buf(33)
    E.choice_list, E.token_list = buf(32).bitcast(I32), buf(33).bitcast(I32)
    is_place = E.h1_flat[:, D:D + 10 * P].rearrange("p (q s) -> p q s", q=10)
    lists = E.PS[:, 0, 256:288]

    def by_tile(x):
        return x.rearrange("p (t e) -> p t e", t=nt)
    flat_sel = [x.rearrange("p t e -> p (t e)") for x in E.sel]
    with nc.Block() as block:
        @block.gpsimd
        def _(pool):
            S.clear_old(pool)

        @block.sync
        def _(sp):
            for dst, name in ((before, "before"), (choice, "choice"), (slot_index, "slot_index")):
                sp.dma_start(dst, E.A[name]).then_inc(loaded, 16)
            load_expert(E, sp, 1, 1, expert_loaded, expert_loaded)
            for t, (t0, rows) in enumerate(TOK):
                sp.wait_ge(copied, 2 * t + 2)
                sp.dma_start(E.h_dram[t0:t0 + rows, :], E.natural[t][0:rows, :]).then_inc(stored, 16)
            sp.wait_ge(stored, 16 * nt)
            sp.wait_ge(expert_loaded, 48)

        @block.tensor
        def _(pe):
            pe.wait_ge(loaded, 48)
            pe.wait_ge(both, 1)
            pe.matmul(E.PS[:, 0, 0:160], before, both_sel, start=True, stop=True)
            pe.matmul(E.PS[:, 1, 0:160], E.ones[:, :], both_sel, start=True, stop=True).then_inc(counted, 1)
            for t, (t0, rows) in enumerate(TOK):
                b = 2 + 2 * (t % 3)
                if t >= 3:
                    pe.wait_ge(copied, 2 * t - 4)
                for k in range(KT):
                    last = pe.transpose(E.PS[0:rows, b + k // 4, (k % 4) * P:(k % 4 + 1) * P], E.h[:, k, t0:t0 + rows],
                                        E.ident[:, :])
                last.then_inc(turned, 1)
            for q in range(2 * nt):
                pe.wait_ge(placed, q + 1)
                last = pe.matmul(lists, is_place[:, q, :], by_tile(numbered[q // nt])[:, q % nt, :],
                                 start=(q == 0), stop=(q == 2 * nt - 1))
            last.then_inc(listed, 1)

        @block.scalar
        def _(act):
            for t, (t0, rows) in enumerate(TOK):
                b = 2 + 2 * (t % 3)
                act.wait_ge(turned, t + 1)
                for a in range(2):
                    act.copy(E.natural[t][0:rows, a * 512:(a + 1) * 512], E.PS[0:rows, b + a, :]).then_inc(copied, 1)

        @block.vector
        def _(dve):
            c = Chain(dve, own)
            dve.tensor_tensor(both_sel, flat_sel[0], flat_sel[1], ALU.add).then_inc(both, 1)
            dve.wait_ge(loaded, 48)
            for w in range(2):
                c.add(dve.tensor_tensor(by_tile(numbered[w]), E.sel[w],
                                        choice[:, w * nt:(w + 1) * nt].unsqueeze(2).broadcast_to([P, nt, 32]), ALU.mult))
            dve.wait_ge(counted, 1)
            c.add(dve.tensor_copy(total, E.PS[:, 1, 0:160]))
            c.link(dve.memset(earlier[:, 0:32], 0.0))
            for t in range(1, nt):
                c.link(dve.tensor_tensor(by_tile(earlier)[:, t, :], by_tile(earlier)[:, t - 1, :],
                                         by_tile(total)[:, t - 1, :], ALU.add))
            c.link(dve.tensor_tensor(within, E.PS[:, 0, 0:160], earlier, ALU.add))
            for w in range(2):
                c.link(dve.tensor_tensor(at_place, within, flat_sel[w], ALU.mult))
                c.link(dve.tensor_reduce(place[:, w * nt:(w + 1) * nt], by_tile(at_place), AX, ALU.add))
            for q in range(2 * nt):
                dve.tensor_scalar(is_place[:, q, :], slot_index, place[:, q:q + 1], None,
                                  ALU.is_equal).then_inc(placed, 1)
            c.link(dve.tensor_tensor(total[:, 0:32], by_tile(earlier)[:, nt - 1, :], by_tile(total)[:, nt - 1, :],
                                     ALU.add))
            c.link(dve.tensor_reduce(top, total[:, 0:32], AX, ALU.max))
            c.link(dve.tensor_copy(E.most[:, :], top))
            c.add(dve.memset(tokens[:, 32:33], float(16 * L)))
            dve.wait_ge(listed, 1)
            c.link(dve.tensor_scalar(empty, lists, 0.0, float(16 * L), ALU.is_equal, ALU.mult))
            c.link(dve.scalar_tensor_tensor(number, lists, -1.0, empty, ALU.add, ALU.add))
            c.link(dve.tensor_scalar(tokens[:, 0:32], number, float(L), float(-L), ALU.is_ge, ALU.mult))
            c.add(dve.tensor_copy(E.choice_list, number))
            c.link(dve.tensor_tensor(tokens[:, 0:32], tokens[:, 0:32], number, ALU.add))
            dve.tensor_copy(E.token_list, tokens)


def experts(nc, S, E):
    S.open()
    sparse, dense = SparseExperts(S, E), DenseExperts(S, E)
    with nc.Block() as block:
        @block.gpsimd
        def _(pool):
            S.clear_old(pool)
            most = pool.value_load(E.most[0:1, 0:1])
            with pool.If(most > CAP):
                pass
            with pool.Else():
                sparse.pool(pool)

        @block.sync
        def _(sp):
            most = sp.value_load(E.most[0:1, 0:1])
            with sp.If(most > CAP):
                dense.sync(sp)
            with sp.Else():
                sparse.sync(sp)

        @block.tensor
        def _(pe):
            most = pe.value_load(E.most[0:1, 0:1])
            with pe.If(most > CAP):
                dense.tensor(pe)
            with pe.Else():
                sparse.tensor(pe)

        @block.scalar
        def _(act):
            most = act.value_load(E.most[0:1, 0:1])
            with act.If(most > CAP):
                dense.scalar(act)
            with act.Else():
                sparse.scalar(act)

        @block.vector
        def _(dve):
            most = dve.value_load(E.most[0:1, 0:1])
            with dve.If(most > CAP):
                dense.vector(dve)
            with dve.Else():
                sparse.vector(dve)


def load_expert(E, sp, j, slot, loaded_13, loaded_2, parts=(0, 1)):
    A, li = E.A, E.li

    def rows(name):
        return A[name][li].rearrange("e (p k) m -> e p k m", p=P)[j]
    if 0 in parts:
        sp.dma_start(E.w13[:, slot, 0], rows("moe_w1_2")).then_inc(loaded_13, 16)
        sp.dma_start(E.w13[:, slot, 1], rows("moe_w3_2")).then_inc(loaded_13, 16)
    if 1 in parts:
        sp.dma_start(E.w2_sparse[:, slot], rows("moe_w2_2")).then_inc(loaded_2, 16)


class SparseExperts:

    def __init__(self, S, E):
        self.E = E
        self.w13_loaded = [S.take("w13_loaded_0"), S.take("w13_loaded_1")]
        self.w2_loaded = [S.take("w2_loaded_0"), S.take("w2_loaded_1")]
        self.x_blank = S.take("x_blank")
        self.x_indexed, self.y_indexed = S.take("x_indexed"), S.take("y_indexed")
        self.x_gathered = [S.take_own("x_gathered_0"), S.take_own("x_gathered_1")]
        self.x_turned = S.take("x_turned")
        self.x_act = S.take("x_copied_act")
        self.x_dve = S.take("x_copied_dve")
        self.h_done = S.take("h_done")
        self.silu_done = S.take("h_silu")
        self.hid_done = S.take("hid_done")
        self.hid_turned = S.take("hid_turned")
        self.hid_copied = S.take("hid_copied")
        self.y_done = S.take("y_done")
        self.y_act = S.take("y_copied_act")
        self.y_dve = S.take("y_copied_dve")
        self.y_stored = [S.take_own("y_stored_0"), S.take_own("y_stored_1")]

    @staticmethod
    def in_turn(eng, body):
        body(0, 0, 0)
        with eng.Fori(0, N_EXP // 2 - 1) as i:
            body(i * 2 + 1, 1, i)
            body(i * 2 + 2, 0, i + 1)
        body(N_EXP - 1, 1, N_EXP // 2 - 1)

    @staticmethod
    def neighbours(j, slot, turn):
        first = isinstance(j, int) and j == 0
        last = isinstance(j, int) and j == N_EXP - 1
        before = None if first else (1 - slot, turn if slot else turn - 1)
        after = None if last else (1 - slot, turn + 1 if slot else turn)
        return before, after

    def sync(self, sp):
        E = self.E

        for slot in range(2):
            sp.sem_inc(self.w13_loaded[slot], 32)
            sp.sem_inc(self.w2_loaded[slot], 16)
        with sp.Fori(0, N_EXP // 2 - 1) as i:
            for slot in range(2):
                where = (i * 2 + (slot + 2), slot, self.w13_loaded[slot], self.w2_loaded[slot])
                sp.wait_ge(self.h_done, i * 2 + (slot + 1))
                load_expert(E, sp, *where, parts=(0,))
                sp.wait_ge(self.y_done, i * 2 + (slot + 1))
                load_expert(E, sp, *where, parts=(1,))

    def pool(self, pool):
        E = self.E

        def gather(j, slot):
            pool.tensor_copy(E.x_index[:, slot:slot + 1], E.token_list[:, bass.ds(j, 1)]).then_inc(self.x_indexed, 1)
            pool.wait_ge(self.x_indexed, 1)
            pool.sem_clear(self.x_indexed)
            pool.indirect_dma_start(
                out=E.xg[:, slot, :], out_offset=None, in_=E.h_dram[:, :],
                in_offset=bass.IndirectOffsetOnAxis(ap=E.x_index[:, slot:slot + 1], axis=0),
                bounds_check=L - 1, oob_is_err=False).then_inc(self.x_gathered[slot], 16)

        def scatter(j, slot):
            pool.wait_ge(self.y_act, j + 2)
            pool.wait_ge(self.y_dve, j + 2)
            pool.tensor_copy(E.y_index[:, slot:slot + 1], E.choice_list[:, bass.ds(j, 1)]).then_inc(self.y_indexed, 1)
            pool.wait_ge(self.y_indexed, 1)
            pool.sem_clear(self.y_indexed)
            pool.indirect_dma_start(
                out=E.out_dram[:, :], out_offset=bass.IndirectOffsetOnAxis(ap=E.y_index[:, slot:slot + 1], axis=0),
                in_=E.yo[:, slot, :], in_offset=None,
                bounds_check=2 * L - 1, oob_is_err=False).then_inc(self.y_stored[slot], 16)
        pool.memset(E.xg, 0.0).then_inc(self.x_blank, 1)
        pool.wait_ge(self.x_blank, 1)
        gather(0, 0)
        gather(1, 1)

        def body(j, slot, turn):
            before, after = self.neighbours(j, slot, turn)
            if after:
                pool.wait_ge(self.x_turned, j + 1)
                gather(j + 2, slot)
            if before:
                scatter(j - 1, before[0])
        self.in_turn(pool, body)
        scatter(N_EXP - 1, 1)
        for slot in range(2):
            pool.wait_ge(self.y_stored[slot], 16 * (N_EXP // 2))
            pool.wait_ge(self.x_gathered[slot], 16 * (N_EXP // 2 + 1 - slot))

    def tensor(self, pe):
        E = self.E

        def turn_x(j, slot, turn):
            pe.wait_ge(self.x_gathered[slot], turn * 16 + 16)
            x = E.xg[:, slot, :].rearrange("s (p k) -> s k p", k=KT)
            for k in range(KT):
                last = pe.transpose(E.PS[:, k // 4, (k % 4) * P:(k % 4 + 1) * P], x[:, k, :], E.ident[:, :])
            last.then_inc(self.x_turned, 1)

        def hidden(j, slot, turn):
            pe.wait_ge(self.w13_loaded[slot], turn * 32 + 32)
            pe.wait_ge(self.x_act, j + 1)
            pe.wait_ge(self.x_dve, j + 1)
            for k in range(KT):
                last = pe.matmul(E.PS[:, 2 + slot, :].rearrange("p (w m) -> p w m", w=2), E.xT[:, k * P:(k + 1) * P],
                                 E.w13[:, slot, :, k, :], start=(k == 0), stop=(k == KT - 1))
            last.then_inc(self.h_done, 1)

        def turn_hidden(j):
            pe.wait_ge(self.hid_done, j + 1)
            hid = E.hg.rearrange("s (p k) -> s k p", k=2)
            for k in range(2):
                last = pe.transpose(E.PS[:, 4, k * P:(k + 1) * P], hid[:, k, :], E.ident[:, :])
            last.then_inc(self.hid_turned, 1)

        def outputs(j, slot, turn):
            pe.wait_ge(self.w2_loaded[slot], turn * 16 + 16)
            pe.wait_ge(self.hid_copied, j + 1)
            pe.wait_ge(self.y_act, j + 1)
            pe.wait_ge(self.y_dve, j + 1)
            for a in range(2):
                for k in range(2):
                    last = pe.matmul(E.PS[:, 6 + a, :], E.hT[:, k * P:(k + 1) * P],
                                     E.w2_sparse[:, slot, k, a * 512:(a + 1) * 512], start=(k == 0), stop=(k == 1))
            last.then_inc(self.y_done, 1)
        turn_x(0, 0, 0)

        def body(j, slot, turn):
            before, after = self.neighbours(j, slot, turn)
            hidden(j, slot, turn)
            if after:
                turn_x(j + 1, *after)
            if before:
                outputs(j - 1, *before)
            turn_hidden(j)
        self.in_turn(pe, body)
        outputs(N_EXP - 1, 1, N_EXP // 2 - 1)

    def scalar(self, act):
        E = self.E
        act.sem_inc(self.y_act, 1)

        def copy_x(j):
            act.wait_ge(self.x_turned, j + 1)
            act.copy(E.xT[:, 0:512], E.PS[:, 0, :]).then_inc(self.x_act, 1)

        def copy_y(j, slot, turn):
            act.wait_ge(self.y_done, j + 1)
            act.wait_ge(self.y_stored[slot], turn * 16)
            act.copy(E.yo[:, slot, 0:512], E.PS[:, 6, :]).then_inc(self.y_act, 1)
        copy_x(0)

        def body(j, slot, turn):
            before, after = self.neighbours(j, slot, turn)
            act.wait_ge(self.h_done, j + 1)
            if before:
                act.wait_ge(self.hid_done, j)
            act.activation(E.hs, E.PS[:, 2 + slot, 0:E_HID], ACT.Silu).then_inc(self.silu_done, 1)
            if after:
                copy_x(j + 1)
            if before:
                copy_y(j - 1, *before)
        self.in_turn(act, body)
        copy_y(N_EXP - 1, 1, N_EXP // 2 - 1)

    def vector(self, dve):
        E = self.E
        dve.sem_inc(self.y_dve, 1)

        def copy_x(j):
            dve.wait_ge(self.x_turned, j + 1)
            dve.tensor_copy(E.xT[:, 512:1024], E.PS[:, 1, :]).then_inc(self.x_dve, 1)

        def copy_y(j, slot, turn):
            dve.wait_ge(self.y_done, j + 1)
            dve.wait_ge(self.y_stored[slot], turn * 16)
            dve.tensor_copy(E.yo[:, slot, 512:1024], E.PS[:, 7, :]).then_inc(self.y_dve, 1)
        copy_x(0)

        def body(j, slot, turn):
            before, after = self.neighbours(j, slot, turn)
            dve.wait_ge(self.silu_done, j + 1)
            dve.tensor_tensor(E.hg, E.hs, E.PS[:, 2 + slot, E_HID:2 * E_HID], ALU.mult).then_inc(self.hid_done, 1)
            if after:
                copy_x(j + 1)
            if before:
                copy_y(j - 1, *before)
            dve.wait_ge(self.hid_turned, j + 1)
            dve.tensor_copy(E.hT, E.PS[:, 4, 0:2 * P]).then_inc(self.hid_copied, 1)
        self.in_turn(dve, body)
        copy_y(N_EXP - 1, 1, N_EXP // 2 - 1)


class DenseExperts:

    def __init__(self, S, E):
        self.E = E
        self.loaded = [S.take("w_loaded_0"), S.take("w_loaded_1")]
        self.done = S.take("tile_done")
        self.act_out = S.take("silu_out")
        self.dve_out = S.take("dve_out")
        self.own = S.take("hidden_steps")
        self.scaled = S.take("residual_scaled")

    def sync(self, sp):
        E, A, li, dve_out = self.E, self.E.A, self.E.li, self.dve_out
        w1 = A["moe_w1_2"][li].rearrange("e (k p) m -> e p k m", p=P)
        w3 = A["moe_w3_2"][li].rearrange("e (k p) m -> e p k m", p=P)
        w2 = A["moe_w2_2"][li].rearrange("e (k p) m -> e p k m", p=P)

        def load(j, slot, turn):
            sp.wait_ge(dve_out, j * 10 + 10)
            for dst, src in ((E.w1s[:, slot], w1[j]), (E.w3s[:, slot], w3[j]), (E.w2s[:, slot], w2[j]),
                             (E.gate_row[:, slot, :], E.gates_dram[j].partition_broadcast(P))):
                sp.dma_start(dst, src).then_inc(self.loaded[slot], 16)
        in_pairs(sp, N_EXP, load)

    def tensor(self, pe):
        E, dve_out = self.E, self.dve_out

        def body(j, slot, turn):
            def tile(q, w, rhs, nk):
                s = 2 * (q % 4)
                for k in range(nk):
                    for a in range(2):
                        last = pe.matmul(E.PS[:, s + a, 0:HALF], w(k), halves(rhs(k), 2)[:, a, :],
                                         start=(k == 0), stop=(k == nk - 1))
                last.then_inc(self.done, 1)
            pe.wait_ge(self.loaded[slot], turn * 64 + 64)
            for m in range(2):
                for n, w in enumerate((E.w1s, E.w3s)):
                    pe.wait_ge(dve_out, j * 10 + (17 + 2 * m + n))
                    tile(2 * m + n, lambda k: w[:, slot, k, m * P:(m + 1) * P], lambda k: E.h[:, k, :], KT)
            pe.wait_ge(dve_out, j * 10 + 22)
            for m in range(KT):
                if m >= 4:
                    pe.wait_ge(dve_out, j * 10 + (23 + m - 4))
                tile(4 + m, lambda k: E.w2s[:, slot, k, m * P:(m + 1) * P], lambda k: E.hid[:, k, :], 2)
        in_pairs(pe, N_EXP, body)

    def scalar(self, act):
        E = self.E

        def body(j, slot, turn):
            for m in range(2):
                act.wait_ge(self.done, j * 12 + (2 * m + 1))
                act.activation(halves(E.silu[:, m, :], 2), E.PS[:, 4 * m:4 * m + 2, 0:HALF],
                               ACT.Silu).then_inc(self.act_out, 1)
        in_pairs(act, N_EXP, body)

    def vector(self, dve):
        E, done, own, dve_out = self.E, self.done, self.own, self.dve_out
        dve.tensor_scalar(E.h1[:, :, :], E.h[:, :, :], ALPHA, None, ALU.mult).then_inc(self.scaled, 1)
        dve.wait_ge(self.scaled, 1)
        dve.sem_inc(dve_out, 20)

        def body(j, slot, turn):
            dve.wait_ge(self.loaded[slot], turn * 64 + 64)
            for m in range(2):
                dve.wait_ge(self.act_out, j * 2 + (m + 1))
                dve.tensor_tensor(E.silu[:, m, :], E.silu[:, m, :], E.gate_row[:, slot, :],
                                  ALU.mult).then_inc(own, 1)
                dve.wait_ge(done, j * 12 + (2 * m + 2))
                dve.wait_ge(own, j * 2 + (m + 1))
                dve.tensor_tensor(halves(E.hid[:, m, :], 2), halves(E.silu[:, m, :], 2),
                                  E.PS[:, 4 * m + 2:4 * m + 4, 0:HALF], ALU.mult).then_inc(dve_out, 1)
            for m in range(KT):
                dve.wait_ge(done, j * 12 + (5 + m))
                s = 2 * (m % 4)
                dve.tensor_tensor(halves(E.h1[:, m, :], 2), halves(E.h1[:, m, :], 2), E.PS[:, s:s + 2, 0:HALF],
                                  ALU.add).then_inc(dve_out, 1)
        in_pairs(dve, N_EXP, body)


def combine(nc, S, E):
    S.open()
    loaded = [S.take(f"outputs_loaded_{t}") for t in range(len(TOK))]
    first = S.take("first_scaled")
    mixed = S.take("outputs_mixed")
    turned = S.take("turned")
    added = S.take("added")
    nt = len(TOK)

    def load(sp):
        for t, (t0, rows) in enumerate(TOK):
            for w in range(2):
                sp.dma_start(E.parts[w][0:rows, t, :], E.out_dram[w * L + t0:w * L + t0 + rows, :]).then_inc(loaded[t], 16)

    def mix(dve):
        for t, (t0, rows) in enumerate(TOK):
            a, b = (x[0:rows, t, :] for x in E.parts)
            dve.wait_ge(loaded[t], 32)
            dve.tensor_scalar(a, a, E.gates[0][0:rows, t:t + 1], None, ALU.mult).then_inc(first, 1)
            dve.wait_ge(first, t + 1)
            dve.scalar_tensor_tensor(a, b, E.gates[1][0:rows, t:t + 1], a, ALU.mult, ALU.add).then_inc(mixed, 1)
        for k in range(KT):
            dve.wait_ge(turned, k + 1)
            dve.scalar_tensor_tensor(E.h1[:, k, 0:SEQ], E.h[:, k, 0:SEQ], ALPHA, E.PS[:, k % 4, :],
                                     ALU.mult, ALU.add).then_inc(added, 1)
        dve.scalar_tensor_tensor(E.h1[:, :, SEQ:L], E.h[:, :, SEQ:L], ALPHA,
                                 E.PS[:, 7, 0:KT * N_META].rearrange("p (k n) -> p k n", k=KT), ALU.mult, ALU.add)

    def turn(pe):
        for k in range(KT):
            if k >= 4:
                pe.wait_ge(added, k - 3)
            for t, (t0, rows) in enumerate(TOK):
                if k == 0:
                    pe.wait_ge(mixed, t + 1)
                dst = E.PS[:, k % 4, t0:t0 + rows] if t < nt - 1 else E.PS[:, 7, k * N_META:(k + 1) * N_META]
                last = pe.transpose(dst, E.parts[0][0:rows, t, k * P:(k + 1) * P], E.ident[0:rows, 0:rows])
            last.then_inc(turned, 1)
    with nc.Block() as block:
        @block.gpsimd
        def _(pool):
            S.clear_old(pool)

        @block.sync
        def _(sp):
            most = sp.value_load(E.most[0:1, 0:1])
            with sp.If(most <= CAP):
                load(sp)

        @block.vector
        def _(dve):
            most = dve.value_load(E.most[0:1, 0:1])
            with dve.If(most <= CAP):
                mix(dve)

        @block.tensor
        def _(pe):
            most = pe.value_load(E.most[0:1, 0:1])
            with pe.If(most <= CAP):
                turn(pe)


def store_output(nc, S, E):
    S.open()
    turned = S.take("turned")
    copied = S.take("copied")
    stored = S.take("output_stored")
    out = E.out[0].rearrange("(t p) d -> t p d", p=P)
    with nc.Block() as block:
        @block.gpsimd
        def _(pool):
            S.clear_old(pool)

        @block.tensor
        def _(pe):
            for t in range(4):
                if t >= 2:
                    pe.wait_ge(copied, t - 1)
                for k in range(KT):
                    last = pe.transpose(E.PS[:, 2 * (t % 2) + k // 4, (k % 4) * P:(k % 4 + 1) * P],
                                        E.h[:, k, N_META + t * P:N_META + (t + 1) * P], E.ident[:, :])
                last.then_inc(turned, 1)

        @block.scalar
        def _(act):
            for t in range(4):
                act.wait_ge(turned, t + 1)
                act.copy(E.outbuf[:, t, :].rearrange("p (b n) -> p b n", b=2),
                         E.PS[:, 2 * (t % 2):2 * (t % 2) + 2, :]).then_inc(copied, 1)

        @block.sync
        def _(sp):
            for t in range(4):
                sp.wait_ge(copied, t + 1)
                sp.dma_start(out[t], E.outbuf[:, t, :]).then_inc(stored, 16)
            sp.wait_ge(stored, 64)


def second_block(nc, S, E, scope):
    A = E.A

    def sb(name, shape, dt=F32):
        return scope.enter_context(nc.sbuf_tensor(name, shape, dt))
    E.zt = sb("zt", [P, 19 * LP])
    E.zs = [E.zt[:, i * LP:i * LP + L] for i in range(19)]
    E.zr = E.zt[:, T_R * LP:(T_R + 12) * LP].rearrange("p (a n) -> p a n", a=12)
    E.kdbuf = sb("kd", [P, WIDE])
    E.kd = E.kdbuf[:, :].rearrange("p (d m n) -> p d m n", d=2, m=4)
    E.vfirst = sb("vfirst", [P, 4, L])
    E.head_ones = sb("head_ones", [P, P])
    E.head_mean = sb("head_mean", [P, P])
    E.level = sb("level", [P, 2, LEVELS, CH])
    E.pair = sb("pair", [P, 2, CH])
    E.eye2 = sb("eye2", [P, CH])
    E.total = sb("total", [P, 4 * N_CH])
    E.state = sb("state", [P, 4, 2, CH])
    E.pend = sb("pend", [P, 4, 2])
    E.invf = sb("invf", [P, 1])
    E.mx2 = sb("mx2", [P, 20])
    E.sums2 = sb("sums2", [P, 20])
    E.ovar = sb("ovar", [P, 20])

    def four(x, i):
        return x[:, i * 4 * LP:(i + 1) * 4 * LP].rearrange("p (m n) -> p m n", m=4)
    E.cum = [four(E.n_flat, 0), four(E.n_flat, 1)]
    E.ld = [four(E.h1_flat, 0), four(E.h1_flat, 1)]
    E.ba = [four(E.norm_flat, 0), four(E.norm_flat, 1)]
    E.pos_int = E.n_flat[:, 0:SEQ].bitcast(I32)
    E.shifted = E.h1[:, 0:4, :]
    E.qn, E.kn = E.h1[:, 0:4, :], E.h1[:, 4:8, :]
    E.qp = E.norm_flat[:, 2560:2560 + 2 * L].rearrange("p (a n) -> p a n", a=2)
    E.vn2 = E.norm_flat[:, 0:2560].rearrange("p (t n) -> p t n", t=5)
    E.prob2 = E.n_flat[:, 0:2 * L].rearrange("p (a n) -> p a n", a=2)
    E.probT2 = E.n_flat[:, 2 * L:2 * L + 2 * 5 * P].rearrange("p (a b n) -> p a b n", a=2, b=5)
    flat = E.wring[:, :, :, :].rearrange("p s k m -> p (s k m)")
    E.on = E.kdbuf[:, 0:2560].rearrange("p (t n) -> p t n", t=5)
    E.osq = E.norm_flat[:, 0:2560].rearrange("p (t n) -> p t n", t=5)
    E.onorm = E.kdbuf[:, 2560:3072]
    E.uq = flat[:, 0:1536].rearrange("p (k h c) -> p k h c", k=2, h=H_A)
    E.ukv = flat[:, 1536:2560].rearrange("p (h c) -> p h c", h=H_A)
    E.pe_w = flat[:, 2560:3072].rearrange("p (k h c) -> p k h c", k=2, h=H_A)
    E.tail_w = E.norm_flat[:, 0:KT * 512].rearrange("p (k m) -> p k m", k=KT)
    E.last_w = E.h1_flat[:, 4 * L:4 * L + KT * P].rearrange("p (k m) -> p k m", k=KT)
    E.y_flat = E.y[:, :, :].rearrange("p m n -> p (m n)")
    tmp = E.y[:, 4:8, :].rearrange("p m n -> p (m n)")
    E.tmp4 = E.y[:, 4:8, :]
    E.tmp4b = E.rotbuf[:, :, :, :].rearrange("p a b n -> p (a b) n")
    E.lora = sb("lora", [P, 2, L])
    E.low = E.lora[0:32, 0, :]
    E.kk = E.zt[:, 0:4 * LP].rearrange("p (m n) -> p m n", m=4)
    E.tmp8a = E.h1[:, 0:4, :]
    E.tmp8b = E.h1[:, 4:8, :]

    rot = E.rotbuf[:, :, :, :].rearrange("p a b n -> p (a b n)")
    spare = [(flat, 0, 4096), (rot, 0, 2112), (tmp, 0, 2112), (E.zt, T_WD * LP, T_GD * LP), (E.stat, 0, L),
             (E.lora[:, 0, :], 0, L), (E.lora[:, 1, :], 0, L)]

    def cut(n, name):
        for i, (x, a, z) in enumerate(spare):
            if z - a >= n:
                spare[i] = (x, a + n, z)
                return x[:, a:a + n]
        return sb(name, [P, n])[:, :]
    N = 8 * CH
    E.ex, E.ep, E.en, E.bb, E.kb, E.vb = (cut(N, x).rearrange("p (m d n) -> p m d n", m=4, d=2)
                                          for x in ("ex", "ep", "en", "bb", "kb", "vb"))
    E.ar = cut(2 * N, "ar").rearrange("p (m d r n) -> p m d r n", m=4, d=2, r=2)
    E.lb, E.mk = (cut(2 * N, x).rearrange("p (h r n) -> p h r n", h=8, r=2) for x in ("lb", "mk"))
    E.vtok, E.btok, E.ktok = (cut(N, x) for x in ("vtok", "btok", "ktok"))
    E.x, E.xt = (cut(N, x).rearrange("p (h n) -> p h n", h=8) for x in ("x", "xt"))
    E.mjt = [cut(N, f"mjt{j}").rearrange("p (h n) -> p h n", h=8) for j in range(1, LEVELS)]
    E.t1 = cut(N, "t1").rearrange("p (h n) -> p h n", h=8)
    E.f, E.sa = E.mjt[0], E.x
    E.keep = flat[:, 2176:2176 + LP]
    E.g2 = E.kdbuf[:, 0:512]
    E.head_out = flat[0:8, 2752:2752 + 4 * P]
    E.by_head = E.stat[0:8, 0:L]
    E.head_in = sb("head_in", [P, 32])
    E.bonus = E.zr[:, T_K - T_R:T_K - T_R + 4, 0:L]

    E.w1s, E.w3s = (E.zt[:, i * 4096:(i + 1) * 4096].rearrange("p (s k m) -> p s k m", s=2, k=KT) for i in range(2))
    E.w2s = flat.rearrange("p (s k m) -> p s k m", s=2, k=2)
    E.router = E.norm_flat[:, 0:KT * L]
    E.router_w = E.norm_flat[:, KT * L:KT * L + 288].rearrange("p (k m) -> p k m", k=KT)
    E.router_b = E.norm_flat[:, KT * L + 288:KT * L + 324]
    E.gT = E.n_flat[0:32, 0:L]
    E.silu = E.n[:, 0:2, :]
    E.hid = E.n[:, 2:4, :]
    E.gate_row = E.n[:, 4:6, :]
    E.outbuf = E.n_flat[:, 0:4096].rearrange("p (t d) -> p t d", t=4)
    E.w13 = E.zt[:, 0:2 * 4096].rearrange("p (s w k m) -> p s w k m", s=2, w=2, k=KT)
    E.natural = [E.y_flat[:, t * D:(t + 1) * D] for t in range(4)] + [E.h1_flat[:, 0:D]]
    E.parts = [E.zt[:, i * 5 * D:(i + 1) * 5 * D].rearrange("p (t d) -> p t d", t=5) for i in range(2)]
    E.w2_sparse = flat.rearrange("p (s k m) -> p s k m", s=2, k=2)
    E.xg = E.n_flat[:, 0:2 * D].rearrange("p (s d) -> p s d", s=2)
    E.yo = E.n_flat[:, 2 * D:4 * D].rearrange("p (s d) -> p s d", s=2)
    E.xT = E.h1_flat[:, 0:D]
    E.hs, E.hg, E.hT = (E.h1_flat[:, D + i * E_HID:D + (i + 1) * E_HID] for i in range(3))
    E.most = sb("most", [P, 1], I32)
    E.x_index, E.y_index = sb("x_index", [P, 2], I32), sb("y_index", [P, 2], I32)
    E.h_dram = nc.dram_tensor("h_tokens", (L, D), F32, kind="Internal").ap()
    E.out_dram = nc.dram_tensor("expert_out", (2 * L, D), F32, kind="Internal").ap()
    E.gates_dram = nc.dram_tensor("gates", (N_EXP, L), F32, kind="Internal").ap()

    meta = E.norm_flat[0:N_META, 0:D]
    load_constants(nc, S, [(E.head_ones[:, :], A["head_ones"]), (E.head_mean[:, :], A["head_mean"]),
                           (E.head_in[:, :], A["head_in"]),
                           (E.level[:, :, :, :], A["level_masks"]), (E.pair[:, :, :], A["pair_masks"]),
                           (E.eye2[:, :], A["eye2"]), (meta, A["meta_tokens_2"])])
    transpose_rows(nc, S, E, lambda k: E.h1[:, k, 0:N_META], KT, parts=[(meta, 0, N_META)])
    norm(nc, S, E, lambda k: E.h1[:, k, :], lambda k: E.h[:, k, :], KT, 2, HALF, lambda k: E.par[:, 8 + k:9 + k], 1e-5,
         b=lambda k: E.par[:, 16 + k:17 + k])
    angles(nc, S, E)
    clear_vfirst(nc, S, E)
    sweep(nc, S)
    with nc.Fori(0, E.depth) as li:
        E.li = li

        def rows(name, n, *ix):
            x = A[name][li]
            for i in ix:
                x = x[i]
            return x.rearrange("(t p) -> t p", p=P)[0:n]

        def par(r):
            return lambda k: E.par[:, r + k:r + k + 1]
        w_in = A["w_in_2"][li].rearrange("(k p) m -> p k m", p=P)
        load_params(nc, S, E, [
            (Q_QN, 2, rows("mla_q_norm_2", 2), 0, P), (Q_KVN, 1, rows("mla_kv_norm_2", 1), 0, P),
            (Q_MP, 15, rows("rwkv_mu_prev_2", 15), 0, P), (Q_MN, 15, rows("rwkv_mu_next_2", 15), 0, P),
            (Q_W0, 8, A["rwkv_w0_2"][li].rearrange("d (t p) -> (d t) p", p=P), 0, P),
            (Q_A0, 8, A["rwkv_a0_2"][li].rearrange("d (t p) -> (d t) p", p=P), 0, P),
            (Q_KK, 4, rows("rwkv_k_k_2", 4), 0, P), (Q_KA, 4, rows("rwkv_k_a_2", 4), 0, P),
            (Q_RK, 4, A["rwkv_r_k_2"][li].rearrange("(t h) n -> t (h n)", h=2), 0, P),
            (Q_GG, 4, rows("rwkv_gn_g_2", 4), 0, P), (Q_GB, 4, rows("rwkv_gn_b_2", 4), 0, P),
            (Q_V0, 4, A["rwkv_v0_2"][0].rearrange("(t p) -> t p", p=P), 0, P),
            (Q_L1G, 8, rows("ln1_g_2", 8), 0, P), (Q_L1B, 8, rows("ln1_b_2", 8), 0, P),
            (Q_L2G, 8, rows("ln2_g_2", 8), 0, P), (Q_L2B, 8, rows("ln2_b_2", 8), 0, P),
            (Q_FIRST, 1, A["is_first"][li].unsqueeze(0), 0, P)], also=[(E.wring[:, 0, :, :], w_in[:, :, 448:704])])
        zall = E.zt[:, :].rearrange("p (a n) -> p a n", n=LP)

        def to_z(eng, j, t, psum):
            q = j * 2 + (t + T_R)
            return eng.activation(zall[:, bass.ds(q, 1), 0:L].rearrange("p o (a n) -> p (o a) n", a=2), psum, ACT.Identity)
        project(nc, S, E, lambda j: w_in[:, :, bass.ds(j * 256 + 448, 256)], lambda k: E.h[:, k, :], KT, 7, 2, HALF, to_z,
                ready=True, also=[(E.last_w, w_in[:, :, 448 + 14 * P:448 + 15 * P]),
                                  (E.tail_w[:, :, 0:448], w_in[:, :, 0:448]), (E.tail_w[:, :, 448:512], w_in[:, :, 384:448])])
        project_tail(nc, S, E)
        norm(nc, S, E, lambda k: E.zs[T_CQ + k], lambda k: E.n[:, k, :], 2, 2, HALF, par(Q_QN), 1e-6,
             fetch=mla_loads(E))
        norm(nc, S, E, lambda k: E.zs[T_CKV], lambda k: E.n[:, 2, :], 1, 2, HALF, par(Q_KVN), 1e-6)
        mla_project(nc, S, E)
        rotate(nc, S, E, [E.qp[:, 0, :], E.qp[:, 1, :], E.zs[T_KPE]], L, 2)
        mla_attend(nc, S, E, [*lora_loads(E), (E.keep, A["keep"]), (E.head_out, A["head_out"]),
                              (E.onorm, A["mla_out_norm_2"][li].partition_broadcast(P))])
        mla_out(nc, S, E)
        value_mix(nc, S, E)
        removal_keys(nc, S, E)
        rates(nc, S, E)
        bonus(nc, S, E)
        recurrence(nc, S, E)
        w_out = A["w_out_2"][li].rearrange("(k p) m -> p k m", p=P)
        head_norm(nc, S, E, [(E.wring[:, 0, :, :], w_out[:, :, 0:256])])

        def add_h(eng, j, t, psum):
            q = j * 2 + t

            def tile(x):
                return x[:, bass.ds(q, 1), :].rearrange("p o (a n) -> p (o a) n", a=2)
            return eng.scalar_tensor_tensor(tile(E.h1), tile(E.h), ALPHA, psum, ALU.mult, ALU.add)
        project(nc, S, E, lambda j: w_out[:, :, bass.ds(j * 256, 256)], lambda k: E.y[:, k, :], KT, KT // 2,
                2, HALF, add_h, on="vector", ready=True)
        norm(nc, S, E, lambda k: E.h1[:, k, :], lambda k: E.h[:, k, :], KT, 2, HALF, par(Q_L1G), 1e-5, b=par(Q_L1B),
             fetch=[(E.router_w[:, :, 0:4], A["moe_w_group_2"][li].rearrange("(k p) m -> p k m", p=P)),
                    (E.router_w[:, :, 4:36], A["moe_w_expert_2"][li].rearrange("(k p) m -> p k m", p=P)),
                    (E.router_b[:, 0:4], A["moe_b_group_2"][li].partition_broadcast(P)),
                    (E.router_b[:, 4:36], A["moe_b_expert_2"][li].partition_broadcast(P))])
        route(nc, S, E)
        dispatch(nc, S, E)
        experts(nc, S, E)
        combine(nc, S, E)
        norm(nc, S, E, lambda k: E.h1[:, k, :], lambda k: E.h[:, k, :], KT, 2, HALF, par(Q_L2G), 1e-5, b=par(Q_L2B))
        sweep(nc, S)
    store_output(nc, S, E)


def clear_vfirst(nc, S, E):
    S.open()
    with nc.Block() as block:
        @block.gpsimd
        def _(pool):
            S.clear_old(pool)
            pool.memset(E.vfirst[:, :, :], 0.0)


def program(nc, A, out):
    E = Env()
    E.A, E.out = A, out
    E.depth = DEPTH
    S = Sems(nc)
    with ExitStack() as ctx:
        def sb(name, shape, dt=F32):
            return ctx.enter_context(nc.sbuf_tensor(name, shape, dt))
        E.PS = ctx.enter_context(nc.psum_tensor("PS", [P, 8, 512], F32))
        E.ident = sb("ident", [P, P])
        E.ones = sb("ones", [P, P])
        E.rot = sb("rot", [P, P])
        E.cos = sb("cos", [P, L])
        E.sin = sb("sin", [P, L])
        E.praw = sb("praw", [P, P])
        E.par = sb("par", [P, P])
        E.stat = sb("stat", [P, L])
        E.rotbuf = sb("rotbuf", [P, 2, 2, L])
        E.h = sb("h", [P, KT, L])
        E.h1_flat = sb("h1", [P, WIDE])
        E.n_flat = sb("n", [P, WIDE])
        E.norm_flat = sb("normbuf", [P, WIDE])
        E.h1, E.n, E.normbuf = (x[:, 0:KT * L].rearrange("p (k n) -> p k n", k=KT)
                                for x in (E.h1_flat, E.n_flat, E.norm_flat))
        E.y = sb("y", [P, KT, L])
        E.wring = sb("wring", [P, 2, KT, 256])
        load_constants(nc, S, [(E.ident[:, :], A["ident"]), (E.ones[:, :], A["ones"]), (E.rot[:, :], A["rot"])])
        with ExitStack() as scope:
            first_block(nc, S, E, scope)
        with ExitStack() as scope:
            second_block(nc, S, E, scope)
        sweep(nc, S)


def shape_constants():
    f = np.float32
    rot = np.zeros((P, P), f)
    for m in range(P):
        if m % 64 < 32:
            rot[m + 32, m] = -1.0
        else:
            rot[m - 32, m] = 1.0
    half = 32
    inv = (f(10000.0) ** (-np.arange(half, dtype=f) / f(half))).astype(f)
    ang = (np.arange(SEQ, dtype=f)[None, :] * inv[:, None]).astype(f)
    t = np.arange(SEQ)
    cnt = np.zeros((P, 2, SEQ), f)
    for g, win in enumerate((2, 4, 8, 16)):
        cnt[(g % 2) * 64:(g % 2) * 64 + 64, g // 2] = 1.0 / np.minimum(t + 1, win)
    inv2 = (f(10000.0) ** (-np.arange(0, 64, 2, dtype=f) / f(64))).astype(f)
    s_, t_ = np.arange(CH)[:, None], np.arange(CH)[None, :]
    strict = (t_ < s_).astype(f)
    level = np.zeros((P, 2, LEVELS, CH), f)
    for j in range(LEVELS):
        b = 1 << j
        m = ((s_ // (2 * b) == t_ // (2 * b)) & (s_ // b > t_ // b)).astype(f)
        level[:CH, 0, j], level[CH:, 0, j] = m, m.T
        level[:CH, 1, j], level[CH:, 1, j] = m.T, m
    pair = np.zeros((P, 2, CH), f)
    pair[:CH, 0], pair[CH:, 0] = strict.T, strict
    pair[:CH, 1], pair[CH:, 1] = strict.T + np.eye(CH, dtype=f), strict + np.eye(CH, dtype=f)
    keep = np.ones((P, LP), f)
    keep[:, ::CH] = 0.0
    keep_group = np.tile((np.arange(20) % 4 != 0).astype(f), (P, 1))
    keep_expert = np.tile((np.arange(160) % 32 != 0).astype(f), (P, 1))
    token = np.arange(5)[None, :] * P + np.arange(P)[:, None]
    valid = (token < L).astype(f)
    choice = (np.concatenate([token, token + L], axis=1) + 1).astype(f)
    heads = np.zeros((P, P), f)
    heads[:64, :64] = heads[64:, 64:] = 1.0
    head_in = np.zeros((P, 4, 8), f)
    for m in range(4):
        head_in[:64, m, 2 * m] = head_in[64:, m, 2 * m + 1] = 1.0
    return {
        "ident": np.eye(P, dtype=f), "ones": np.ones((P, P), f), "rot": rot,
        "cos1": np.tile(np.cos(ang), (4, 1)).astype(f), "sin1": np.tile(np.sin(ang), (4, 1)).astype(f),
        "invcnt": cnt, "onesrow": np.ones((P, SEQ), f),
        "inv_freq": np.tile(inv2, 4)[:, None].copy(), "meta_pos": np.tile(np.arange(N_META, dtype=f), (P, 1)),
        "level_masks": level, "pair_masks": pair, "eye2": np.tile(np.eye(CH, dtype=f), (2, 1)),
        "keep": keep, "keep_group": keep_group, "keep_expert": keep_expert, "head_ones": heads, "head_mean": heads / f(64),
        "head_in": head_in.reshape(P, 32), "head_out": head_in.transpose(2, 1, 0).reshape(8, 4 * P).copy(),
        "valid_token": valid, "choice": choice,
        "before": np.triu(np.ones((P, P), f), 1), "slot_index": np.tile(np.arange(P), (P, 1)).astype(f),
        "is_first": np.repeat(np.arange(DEPTH)[:, None] == 0, P, axis=1).astype(f),
    }


def kernel(**inputs):
    import concourse.bacc as bacc
    from concourse.bass_utils import run_bass_kernel_spmd

    nc = bacc.Bacc("TRN2", target_bir_lowering=False, num_devices=1)
    arrays, aps = {}, {}
    for name, a in {**inputs, **shape_constants()}.items():
        a = np.ascontiguousarray(a)
        arrays[f"in_{name}"] = a
        aps[name] = nc.dram_tensor(f"in_{name}", a.shape, mybir.dt.from_np(a.dtype), kind="ExternalInput").ap()
    out = nc.dram_tensor("out", (1, SEQ, D), F32, kind="ExternalOutput").ap()
    program(nc, aps, out)
    r = run_bass_kernel_spmd(nc, [arrays], core_ids=[0])
    return r.results[0]["out"]
```
